# Optimizing a Trainium2 kernel written in Bass

```python
import jax, jax.numpy as jnp
from jax import lax
import numpy as np
import math

D_MODEL = 1024
BATCH = 1
SEQ = 1024
DEPTH = 2

GRID_W = 64
CTX_LEN = 256
ATT_HEADS = 8
ATT_KV_HEADS = 2
ATT_HEAD_DIM = 64
ATT_WIDTH = ATT_HEADS * ATT_HEAD_DIM
KV_WIDTH = ATT_KV_HEADS * ATT_HEAD_DIM
WINDOW = 128
BLOCK = 128
ROPE_BASE = 10000.0
M_HEADS = 4
M_HEAD_DIM = 128
M_WIDTH = M_HEADS * M_HEAD_DIM
CONV_K = 5
CHUNK = 128
N_DIR = 2
MIX_WIDTH = ATT_WIDTH + M_WIDTH
EPS = 1e-6
SPLIT_SIZES = (ATT_WIDTH, KV_WIDTH, KV_WIDTH, ATT_WIDTH, M_WIDTH, M_WIDTH, M_WIDTH, M_WIDTH, M_WIDTH, N_DIR * M_HEADS, N_DIR * M_HEADS)
IN_COLS = 2 * ATT_WIDTH + 2 * KV_WIDTH + 5 * M_WIDTH + 2 * N_DIR * M_HEADS


def rmsnorm(x, g):
    xf = x.astype(jnp.float32)
    y = xf * lax.rsqrt(jnp.mean(xf * xf, axis=-1, keepdims=True) + EPS)
    return (y * g.astype(jnp.float32)).astype(x.dtype)

def project(xn, w_in):
    idx = np.cumsum(SPLIT_SIZES)[:-1].tolist()
    return jnp.split(xn @ w_in, idx, axis=-1)

def axial_rope_tables(T):
    rows = T // GRID_W
    row = jnp.repeat(jnp.arange(rows), GRID_W).astype(jnp.float32)
    col = jnp.tile(jnp.arange(GRID_W), rows).astype(jnp.float32)
    half = ATT_HEAD_DIM // 2
    inv = ROPE_BASE ** (-jnp.arange(0, half, 2, dtype=jnp.float32) / half)
    ang_r = row[:, None] * inv
    ang_c = col[:, None] * inv
    return (jnp.cos(ang_r)[:, None, :], jnp.sin(ang_r)[:, None, :],
            jnp.cos(ang_c)[:, None, :], jnp.sin(ang_c)[:, None, :])

def rope_2d(u, tables):
    cos_r, sin_r, cos_c, sin_c = [t.astype(u.dtype) for t in tables]

    def rot(a, cos, sin):
        a1, a2 = jnp.split(a, 2, axis=-1)
        return jnp.concatenate([a1 * cos - a2 * sin, a2 * cos + a1 * sin], axis=-1)

    ur, uc = jnp.split(u, 2, axis=-1)
    return jnp.concatenate([rot(ur, cos_r, sin_r), rot(uc, cos_c, sin_c)], axis=-1)

def window_ctx_attention(q, k, v, kc, vc, sink):
    B, T, H, dh = q.shape
    G = H // ATT_KV_HEADS
    NB = T // BLOCK
    scale = dh ** -0.5
    qb = q.reshape(B, NB, BLOCK, ATT_KV_HEADS, G, dh)
    pad = ((0, 0), (BLOCK, BLOCK), (0, 0), (0, 0))
    kp = jnp.pad(k, pad).reshape(B, NB + 2, BLOCK, ATT_KV_HEADS, dh)
    vp = jnp.pad(v, pad).reshape(B, NB + 2, BLOCK, ATT_KV_HEADS, dh)
    kw = jnp.concatenate([kp[:, :-2], kp[:, 1:-1], kp[:, 2:]], axis=2)
    vw = jnp.concatenate([vp[:, :-2], vp[:, 1:-1], vp[:, 2:]], axis=2)
    s_win = jnp.einsum('bnqhgd,bnkhd->bhgnqk', qb, kw).astype(jnp.float32) * scale
    qpos = jnp.arange(NB)[:, None, None] * BLOCK + jnp.arange(BLOCK)[None, :, None]
    kpos = (jnp.arange(NB)[:, None, None] - 1) * BLOCK + jnp.arange(3 * BLOCK)[None, None, :]
    valid = (jnp.abs(qpos - kpos) <= WINDOW) & (kpos >= 0) & (kpos < T)
    s_win = jnp.where(valid, s_win, -jnp.inf)
    s_ctx = jnp.einsum('bnqhgd,bchd->bhgnqc', qb, kc).astype(jnp.float32) * scale
    s_sink = jnp.broadcast_to(sink.astype(jnp.float32).reshape(1, ATT_KV_HEADS, G, 1, 1, 1),
                              s_win.shape[:-1] + (1,))
    p = jax.nn.softmax(jnp.concatenate([s_win, s_ctx, s_sink], axis=-1), axis=-1)
    Lw = 3 * BLOCK
    Lc = kc.shape[1]
    p_win = p[..., :Lw].astype(v.dtype)
    p_ctx = p[..., Lw:Lw + Lc].astype(v.dtype)
    out = (jnp.einsum('bhgnqk,bnkhd->bnqhgd', p_win, vw)
           + jnp.einsum('bhgnqc,bchd->bnqhgd', p_ctx, vc))
    return out.reshape(B, T, H * dh)

def ctx_attention(qc, kc, vc, sink):
    B, Lc, H, dh = qc.shape
    G = H // ATT_KV_HEADS
    qg = qc.reshape(B, Lc, ATT_KV_HEADS, G, dh)
    s = jnp.einsum('bqhgd,bkhd->bhgqk', qg, kc).astype(jnp.float32) * dh ** -0.5
    s_sink = jnp.broadcast_to(sink.astype(jnp.float32).reshape(1, ATT_KV_HEADS, G, 1, 1),
                              s.shape[:-1] + (1,))
    p = jax.nn.softmax(jnp.concatenate([s, s_sink], axis=-1), axis=-1)
    out = jnp.einsum('bhgqk,bkhd->bqhgd', p[..., :Lc].astype(vc.dtype), vc)
    return out.reshape(B, Lc, H * dh)

def dwconv(u, w, b):
    C = u.shape[-1]
    y = lax.conv_general_dilated(u, w[:, None, :].astype(u.dtype), window_strides=(1,),
                                 padding=[(CONV_K // 2, CONV_K // 2)],
                                 dimension_numbers=('NWC', 'WIO', 'NWC'), feature_group_count=C)
    return y + b.astype(u.dtype)

def mlstm_init_state(B):
    N = N_DIR * B * M_HEADS
    return (jnp.zeros((N, M_HEAD_DIM, M_HEAD_DIM), jnp.float32),
            jnp.zeros((N, M_HEAD_DIM), jnp.float32),
            jnp.full((N,), -jnp.inf, jnp.float32))

def mlstm_chunkwise(q, k, v, i_pre, f_pre, state):
    N, T, dh = q.shape
    NC = T // CHUNK
    f32 = jnp.float32

    def chunks(u):
        return u.astype(f32).reshape((N, NC, CHUNK) + u.shape[2:]).swapaxes(0, 1)

    qc = chunks(q)
    kc = chunks(k) * dh ** -0.5
    vc = chunks(v)
    lf = chunks(jax.nn.log_sigmoid(f_pre.astype(f32)))
    ic = chunks(i_pre)
    lower = jnp.tril(jnp.ones((CHUNK, CHUNK), bool))

    def step(carry, inp):
        C, n, m = carry
        qq, kk, vv, lfc, ii = inp
        b = jnp.cumsum(lfc, axis=-1)
        dmat = jnp.where(lower, b[:, :, None] - b[:, None, :] + ii[:, None, :], -jnp.inf)
        inter = b + m[:, None]
        m_t = jnp.maximum(inter, jnp.max(dmat, axis=-1))
        w_inter = jnp.exp(inter - m_t)
        qk = jnp.einsum('ntd,nsd->nts', qq, kk) * jnp.exp(dmat - m_t[:, :, None])
        num = (w_inter[..., None] * jnp.einsum('nvd,ntd->ntv', C, qq)
               + jnp.einsum('nts,nsv->ntv', qk, vv))
        den = w_inter * jnp.einsum('nd,ntd->nt', n, qq) + qk.sum(-1)
        h = num / jnp.maximum(jnp.abs(den), jnp.exp(-m_t))[..., None]
        bL = b[:, -1]
        g = bL[:, None] - b + ii
        m_new = jnp.maximum(bL + m, jnp.max(g, axis=-1))
        a = jnp.exp(bL + m - m_new)
        w = jnp.exp(g - m_new[:, None])
        C_new = a[:, None, None] * C + jnp.einsum('ns,nsv,nsd->nvd', w, vv, kk)
        n_new = a[:, None] * n + jnp.einsum('ns,nsd->nd', w, kk)
        return (C_new, n_new, m_new), h

    state, h = lax.scan(step, state, (qc, kc, vc, lf, ic))
    h = h.swapaxes(0, 1).reshape(N, T, dh)
    return h.astype(q.dtype), state

def mlstm_bidir(q, k, v, i_pre, f_pre, state):
    B, T, _ = q.shape

    def heads(u):
        u = u.reshape(B, T, M_HEADS, M_HEAD_DIM).transpose(0, 2, 1, 3)
        return jnp.stack([u, jnp.flip(u, axis=2)]).reshape(N_DIR * B * M_HEADS, T, M_HEAD_DIM)

    def gates(gt):
        gt = gt.reshape(B, T, N_DIR, M_HEADS).transpose(2, 0, 3, 1)
        return jnp.stack([gt[0], jnp.flip(gt[1], axis=-1)]).reshape(N_DIR * B * M_HEADS, T)

    h, state = mlstm_chunkwise(heads(q), heads(k), heads(v), gates(i_pre), gates(f_pre), state)
    h = h.reshape(N_DIR, B, M_HEADS, T, M_HEAD_DIM)
    h = h[0] + jnp.flip(h[1], axis=2)
    return h.transpose(0, 2, 1, 3).reshape(B, T, M_WIDTH), state

def mlstm_post(h, o_pre, z, head_g):
    B, T, _ = h.shape
    h = jax.nn.sigmoid(o_pre) * h
    hh = rmsnorm(h.reshape(B, T, M_HEADS, M_HEAD_DIM), head_g.reshape(M_HEADS, M_HEAD_DIM))
    return hh.reshape(B, T, M_WIDTH) * jax.nn.silu(z)

def mlstm_qk(mq, mk, conv_w, conv_b):
    qk = jax.nn.silu(dwconv(jnp.concatenate([mq, mk], axis=-1), conv_w, conv_b))
    return jnp.split(qk, 2, axis=-1)

def hybrid_layer(x, ctx, mod_x, mod_c, tables, norm_g, w_in, conv_w, conv_b, gate_b, sink,
                 head_g, w_out, last):
    shift_x, scale_x, gate_x = mod_x
    shift_c, scale_c, gate_c = mod_c
    B, T, _ = x.shape
    Lc = ctx.shape[1]
    b_i, b_f = jnp.split(gate_b, 2)
    xn = rmsnorm(x, norm_g) * (1 + scale_x) + shift_x
    cn = rmsnorm(ctx, norm_g) * (1 + scale_c) + shift_c
    aq, ak, av, az, mq, mk, mv, mo, mz, mi, mf = project(xn, w_in)
    caq, cak, cav, caz, cmq, cmk, cmv, cmo, cmz, cmi, cmf = project(cn, w_in)

    q = rope_2d(aq.reshape(B, T, ATT_HEADS, ATT_HEAD_DIM), tables)
    k = rope_2d(ak.reshape(B, T, ATT_KV_HEADS, ATT_HEAD_DIM), tables)
    v = av.reshape(B, T, ATT_KV_HEADS, ATT_HEAD_DIM)
    kc = cak.reshape(B, Lc, ATT_KV_HEADS, ATT_HEAD_DIM)
    vc = cav.reshape(B, Lc, ATT_KV_HEADS, ATT_HEAD_DIM)
    att_x = window_ctx_attention(q, k, v, kc, vc, sink) * jax.nn.silu(az)

    cq, ck = mlstm_qk(cmq, cmk, conv_w, conv_b)
    xq, xk = mlstm_qk(mq, mk, conv_w, conv_b)
    h_ctx, ctx_state = mlstm_bidir(cq, ck, cmv, cmi + b_i, cmf + b_f, mlstm_init_state(B))
    h_lat, _ = mlstm_bidir(xq, xk, mv, mi + b_i, mf + b_f, ctx_state)
    m_x = mlstm_post(h_lat, mo, mz, head_g)

    out_x = jnp.concatenate([att_x, m_x], axis=-1) @ w_out
    x = x + gate_x * out_x
    if not last:
        qc = caq.reshape(B, Lc, ATT_HEADS, ATT_HEAD_DIM)
        att_c = ctx_attention(qc, kc, vc, sink) * jax.nn.silu(caz)
        m_c = mlstm_post(h_ctx, cmo, cmz, head_g)
        out_c = jnp.concatenate([att_c, m_c], axis=-1) @ w_out
        ctx = ctx + gate_c * out_c
    return x, ctx

def first_inputs(seed: int = 0) -> dict:
    key = jax.random.key(seed)
    ks = jax.random.split(key, 16)
    f32 = jnp.float32
    nrm = lambda k, s: jax.random.normal(k, s, f32)
    f_bias = jnp.tile(jnp.linspace(3.0, 6.0, M_HEADS), N_DIR)
    gate_b = jnp.concatenate([0.1 * nrm(ks[8], (DEPTH, N_DIR * M_HEADS)),
                              f_bias[None, :] + 0.1 * nrm(ks[9], (DEPTH, N_DIR * M_HEADS))], axis=-1)
    return {
        "x": nrm(ks[0], (BATCH, SEQ, D_MODEL)),
        "c": nrm(ks[1], (BATCH, D_MODEL)),
        "ctx": nrm(ks[2], (BATCH, CTX_LEN, D_MODEL)),
        "c_ctx": nrm(ks[3], (D_MODEL,)),
        "w_ada": 0.5 * D_MODEL ** -0.5 * nrm(ks[4], (DEPTH, D_MODEL, 3 * D_MODEL)),
        "b_ada": 0.01 * nrm(ks[5], (DEPTH, 3 * D_MODEL)),
        "norm_g": 1.0 + 0.02 * nrm(ks[6], (DEPTH, D_MODEL)),
        "w_in": D_MODEL ** -0.5 * nrm(ks[7], (DEPTH, D_MODEL, IN_COLS)),
        "conv_w": CONV_K ** -0.5 * nrm(ks[10], (DEPTH, CONV_K, 2 * M_WIDTH)),
        "conv_b": 0.01 * nrm(ks[11], (DEPTH, 2 * M_WIDTH)),
        "gate_b": gate_b,
        "sink": 0.5 * nrm(ks[12], (DEPTH, ATT_HEADS)),
        "head_g": 1.0 + 0.02 * nrm(ks[13], (DEPTH, M_WIDTH)),
        "w_out": MIX_WIDTH ** -0.5 * nrm(ks[14], (DEPTH, MIX_WIDTH, D_MODEL)),
        "final_g": 1.0 + 0.02 * nrm(ks[15], (D_MODEL,)),
    }

def first_block(x, c, ctx, c_ctx, w_ada, b_ada, norm_g, w_in, conv_w, conv_b, gate_b, sink,
              head_g, w_out, final_g):
    T = x.shape[1]
    tables = axial_rope_tables(T)
    sc = jax.nn.silu(c)
    scc = jax.nn.silu(c_ctx)
    for l in range(DEPTH):
        mod_x = jnp.split((sc @ w_ada[l] + b_ada[l])[:, None, :], 3, axis=-1)
        mod_c = jnp.split(scc @ w_ada[l] + b_ada[l], 3, axis=-1)
        x, ctx = hybrid_layer(x, ctx, mod_x, mod_c, tables, norm_g[l], w_in[l], conv_w[l],
                              conv_b[l], gate_b[l], sink[l], head_g[l], w_out[l],
                              last=(l == DEPTH - 1))
    return rmsnorm(x, final_g)


DEPTH_2 = 1

MIX_WIDTH_2 = D_MODEL
N_MIXERS = 4
GROUP_WIDTH = MIX_WIDTH_2 // N_MIXERS
ATT_HEADS_2 = 4
ATT_VDIM = GROUP_WIDTH // ATT_HEADS_2
ATT_QK = ATT_VDIM // 2
Q_BLOCK = 128
CONV_WIDTH = 31
CONV_GROUPS = 4
FNET_GROUPS = 4
SGU_CHUNK = 128
SGU_GROUPS = 4
D_FF = 4 * D_MODEL
A_COLS = 3 * GROUP_WIDTH
B_COLS = 2 * GROUP_WIDTH
C_COLS = GROUP_WIDTH
D_COLS = 2 * GROUP_WIDTH
IN_COLS_2 = A_COLS + B_COLS + C_COLS + D_COLS


def _rmsnorm(x, g):
    xf = x.astype(jnp.float32)
    y = xf * lax.rsqrt(jnp.mean(xf * xf, axis=-1, keepdims=True) + EPS)
    return (y * g.astype(jnp.float32)).astype(x.dtype)

def _layernorm(x, g, b):
    xf = x.astype(jnp.float32)
    mu = jnp.mean(xf, axis=-1, keepdims=True)
    xc = xf - mu
    var = jnp.mean(xc * xc, axis=-1, keepdims=True)
    y = xc * lax.rsqrt(var + EPS) * g.astype(jnp.float32) + b.astype(jnp.float32)
    return y.astype(x.dtype)

def _alibi_slopes(n):
    return jnp.asarray([2.0 ** (-8.0 * (i + 1) / n) for i in range(n)], dtype=jnp.float32)

def _diff_attention(q, k, v, lam, lam_init, subln_g):
    bsz, seq = q.shape[0], q.shape[1]
    nb = seq // Q_BLOCK
    scale = ATT_QK ** -0.5
    slopes = _alibi_slopes(ATT_HEADS_2)
    kpos = jnp.arange(seq, dtype=jnp.float32)
    qb = q.reshape(bsz, nb, Q_BLOCK, ATT_HEADS_2, 2, ATT_QK).transpose(1, 0, 2, 3, 4, 5)

    def block(args):
        q_blk, i = args
        qpos = (i * Q_BLOCK + jnp.arange(Q_BLOCK)).astype(jnp.float32)
        bias = -slopes[:, None, None] * jnp.abs(qpos[:, None] - kpos[None, :])
        s = jnp.einsum('bqhmd,bkhmd->bhmqk', q_blk, k,
                       preferred_element_type=jnp.float32) * scale + bias[None, :, None]
        p = jax.nn.softmax(s, axis=-1)
        w = p[:, :, 0] - lam * p[:, :, 1]
        return jnp.einsum('bhqk,bkhe->bqhe', w.astype(v.dtype), v)

    o = lax.map(block, (qb, jnp.arange(nb)))
    o = o.transpose(1, 0, 2, 3, 4).reshape(bsz, seq, ATT_HEADS_2, ATT_VDIM)
    o = _rmsnorm(o, subln_g) * (1.0 - lam_init)
    return o.reshape(bsz, seq, GROUP_WIDTH)

def _conformer_conv(h, dw_w, dw_b, ln_g, ln_b, pw_w, pw_b):
    a, g = jnp.split(h, 2, axis=-1)
    z = a * jax.nn.sigmoid(g)
    z = lax.conv_general_dilated(
        z, dw_w[:, None, :], window_strides=(1,),
        padding=[(CONV_WIDTH // 2, CONV_WIDTH // 2)],
        dimension_numbers=('NWC', 'WIO', 'NWC'),
        feature_group_count=GROUP_WIDTH) + dw_b
    zg = z.reshape(z.shape[0], z.shape[1], CONV_GROUPS, GROUP_WIDTH // CONV_GROUPS)
    zg = _layernorm(zg, ln_g.reshape(CONV_GROUPS, -1), ln_b.reshape(CONV_GROUPS, -1))
    z = jax.nn.silu(zg.reshape(z.shape))
    return z @ pw_w + pw_b

def _fourier_mix(c, w, b):
    bsz, seq = c.shape[0], c.shape[1]
    cg = c.reshape(bsz, seq, FNET_GROUPS, GROUP_WIDTH // FNET_GROUPS).astype(jnp.float32)
    f = jnp.fft.fft2(cg, axes=(1, 3), norm='ortho').real.astype(c.dtype)
    return jnp.einsum('bsgc,gce->bsge', f, w).reshape(bsz, seq, GROUP_WIDTH) + b

def _spatial_gate(h, ln_g, ln_b, w_s, b_s):
    bsz, seq = h.shape[0], h.shape[1]
    u, v = jnp.split(h, 2, axis=-1)
    v = _layernorm(v, ln_g, ln_b)
    nc = seq // SGU_CHUNK
    vg = v.reshape(bsz, nc, SGU_CHUNK, SGU_GROUPS, GROUP_WIDTH // SGU_GROUPS)
    sv = jnp.einsum('gts,bnsgc->bntgc', w_s, vg) + b_s.T[None, None, :, :, None]
    return u * sv.reshape(bsz, seq, GROUP_WIDTH)

def second_inputs(seed: int = 0) -> dict:
    key = jax.random.key(seed)
    ks = jax.random.split(key, 26)

    def nrm(k, shape, scale):
        return jax.random.normal(k, shape, jnp.float32) * scale

    def gain(k, shape):
        return 1.0 + 0.02 * jax.random.normal(k, shape, jnp.float32)

    gw = GROUP_WIDTH
    return {
        "x": nrm(ks[0], (BATCH, SEQ, D_MODEL), 1.0),
        "norm1_g": gain(ks[1], (DEPTH_2, D_MODEL)),
        "w_in": nrm(ks[2], (DEPTH_2, D_MODEL, IN_COLS_2), D_MODEL ** -0.5),
        "lam_q1": nrm(ks[3], (DEPTH_2, ATT_QK), 0.1),
        "lam_k1": nrm(ks[4], (DEPTH_2, ATT_QK), 0.1),
        "lam_q2": nrm(ks[5], (DEPTH_2, ATT_QK), 0.1),
        "lam_k2": nrm(ks[6], (DEPTH_2, ATT_QK), 0.1),
        "subln_g": gain(ks[7], (DEPTH_2, ATT_VDIM)),
        "conv_dw_w": nrm(ks[8], (DEPTH_2, CONV_WIDTH, gw), CONV_WIDTH ** -0.5),
        "conv_dw_b": nrm(ks[9], (DEPTH_2, gw), 0.02),
        "conv_ln_g": gain(ks[10], (DEPTH_2, gw)),
        "conv_ln_b": nrm(ks[11], (DEPTH_2, gw), 0.02),
        "conv_pw_w": nrm(ks[12], (DEPTH_2, gw, gw), gw ** -0.5),
        "conv_pw_b": nrm(ks[13], (DEPTH_2, gw), 0.02),
        "fnet_w": nrm(ks[14], (DEPTH_2, FNET_GROUPS, gw // FNET_GROUPS, gw // FNET_GROUPS),
                      (gw // FNET_GROUPS) ** -0.5),
        "fnet_b": nrm(ks[15], (DEPTH_2, gw), 0.02),
        "sgu_ln_g": gain(ks[16], (DEPTH_2, gw)),
        "sgu_ln_b": nrm(ks[17], (DEPTH_2, gw), 0.02),
        "sgu_w": nrm(ks[18], (DEPTH_2, SGU_GROUPS, SGU_CHUNK, SGU_CHUNK), SGU_CHUNK ** -0.5),
        "sgu_b": gain(ks[19], (DEPTH_2, SGU_GROUPS, SGU_CHUNK)),
        "w_out": nrm(ks[20], (DEPTH_2, MIX_WIDTH_2, D_MODEL), MIX_WIDTH_2 ** -0.5),
        "norm2_g": gain(ks[21], (DEPTH_2, D_MODEL)),
        "w_up": nrm(ks[22], (DEPTH_2, D_MODEL, D_FF), D_MODEL ** -0.5),
        "w_down": nrm(ks[23], (DEPTH_2, D_FF, D_MODEL), D_FF ** -0.5),
        "final_g": gain(ks[24], (D_MODEL,)),
    }

def second_block(x, norm1_g, w_in, lam_q1, lam_k1, lam_q2, lam_k2, subln_g,
              conv_dw_w, conv_dw_b, conv_ln_g, conv_ln_b, conv_pw_w, conv_pw_b,
              fnet_w, fnet_b, sgu_ln_g, sgu_ln_b, sgu_w, sgu_b,
              w_out, norm2_g, w_up, w_down, final_g):
    bsz, seq = x.shape[0], x.shape[1]
    splits = [GROUP_WIDTH, 2 * GROUP_WIDTH, A_COLS, A_COLS + B_COLS, A_COLS + B_COLS + C_COLS]
    for l in range(DEPTH_2):
        xn = _rmsnorm(x, norm1_g[l])
        h = xn @ w_in[l]
        hq, hk, hv, hb, hc, hd = jnp.split(h, splits, axis=-1)
        q = hq.reshape(bsz, seq, ATT_HEADS_2, 2, ATT_QK)
        k = hk.reshape(bsz, seq, ATT_HEADS_2, 2, ATT_QK)
        v = hv.reshape(bsz, seq, ATT_HEADS_2, ATT_VDIM)
        lam_init = 0.8 - 0.6 * math.exp(-0.3 * l)
        lam = (jnp.exp(jnp.sum((lam_q1[l] * lam_k1[l]).astype(jnp.float32)))
               - jnp.exp(jnp.sum((lam_q2[l] * lam_k2[l]).astype(jnp.float32)))
               + lam_init)
        y_a = _diff_attention(q, k, v, lam, lam_init, subln_g[l])
        y_b = _conformer_conv(hb, conv_dw_w[l], conv_dw_b[l], conv_ln_g[l], conv_ln_b[l],
                              conv_pw_w[l], conv_pw_b[l])
        y_c = _fourier_mix(hc, fnet_w[l], fnet_b[l])
        y_d = _spatial_gate(hd, sgu_ln_g[l], sgu_ln_b[l], sgu_w[l], sgu_b[l])
        y = jnp.concatenate([y_a, y_b, y_c, y_d], axis=-1)
        x = x + y @ w_out[l]
        xn2 = _rmsnorm(x, norm2_g[l])
        x = x + jnp.square(jax.nn.relu(xn2 @ w_up[l])) @ w_down[l]
    return _rmsnorm(x, final_g)


_first_inputs = second_inputs


def second_inputs(seed=0):
    import zlib

    import numpy as np

    out = dict(_first_inputs(seed))
    spreads = {}
    factors = {'norm1_g': 2.756,
     'lam_q1': 6.011,
     'lam_q2': 2.811,
     'lam_k2': 7.161,
     'subln_g': 64.0,
     'conv_dw_b': 21.455,
     'conv_ln_g': 64.0,
     'conv_ln_b': 64.0,
     'conv_pw_b': 56.08,
     'fnet_b': 61.344,
     'sgu_ln_g': 27.546,
     'sgu_ln_b': 30.233,
     'sgu_b': 31.34,
     'norm2_g': 11.736,
     'final_g': 8.206}
    for name, (base, spread) in spreads.items():
        noise = np.random.default_rng([zlib.crc32(name.encode()), seed]).standard_normal(out[name].shape)
        drawn = base * np.exp(spread * noise) if base else spread * noise
        out[name] = __import__('jax').numpy.asarray(drawn.astype(out[name].dtype))
    for name, factor in factors.items():
        out[name] = (out[name] * factor).astype(out[name].dtype)
    return out


_narrow_inputs = second_inputs


def second_inputs(seed=0):

    out = dict(_narrow_inputs(seed))
    wider = {'subln_g': 7.03,
     'conv_ln_g': 8.15,
     'conv_ln_b': 8.11,
     'conv_pw_b': 6.38,
     'fnet_w': 3.84,
     'fnet_b': 6.43,
     'sgu_ln_g': 4.78,
     'sgu_ln_b': 4.8,
     'sgu_b': 4.79,
     'final_g': 3.24}
    for name, times in wider.items():
        mean = out[name].mean()
        out[name] = (mean + times * (out[name] - mean)).astype(out[name].dtype)
    return out


def setup_inputs(seed=0):
    out = dict(first_inputs(seed))
    for name, value in second_inputs(seed + 1).items():
        if name != "x":
            out[name + "_2"] = value
    return out


def reference(
    x, c, ctx, c_ctx, w_ada, b_ada, norm_g, w_in, conv_w, conv_b, gate_b, sink, head_g, w_out,
    final_g, norm1_g_2, w_in_2, lam_q1_2, lam_k1_2, lam_q2_2, lam_k2_2, subln_g_2, conv_dw_w_2,
    conv_dw_b_2, conv_ln_g_2, conv_ln_b_2, conv_pw_w_2, conv_pw_b_2, fnet_w_2, fnet_b_2,
    sgu_ln_g_2, sgu_ln_b_2, sgu_w_2, sgu_b_2, w_out_2, norm2_g_2, w_up_2, w_down_2, final_g_2,
):
    x = first_block(
        x, c, ctx, c_ctx, w_ada, b_ada, norm_g, w_in, conv_w, conv_b, gate_b, sink, head_g,
        w_out, final_g,
    )
    return second_block(
        x, norm1_g_2, w_in_2, lam_q1_2, lam_k1_2, lam_q2_2, lam_k2_2, subln_g_2, conv_dw_w_2,
        conv_dw_b_2, conv_ln_g_2, conv_ln_b_2, conv_pw_w_2, conv_pw_b_2, fnet_w_2, fnet_b_2,
        sgu_ln_g_2, sgu_ln_b_2, sgu_w_2, sgu_b_2, w_out_2, norm2_g_2, w_up_2, w_down_2,
        final_g_2,
    )


_drawn_inputs = setup_inputs


def setup_inputs(seed=0):
    import zlib

    import numpy as np

    out = dict(_drawn_inputs(seed))
    spreads = {}
    factors = {'norm_g': 4.315, 'conv_b': 24.695, 'sink': 8.0, 'head_g': 5.747}
    for name, (base, spread) in spreads.items():
        noise = np.random.default_rng([zlib.crc32(name.encode()), seed]).standard_normal(out[name].shape)
        drawn = base * np.exp(spread * noise) if base else spread * noise
        out[name] = __import__('jax').numpy.asarray(drawn.astype(out[name].dtype))
    for name, factor in factors.items():
        out[name] = (out[name] * factor).astype(out[name].dtype)
    return out
```

```python
from contextlib import ExitStack

import numpy as np

import concourse.bass as bass
from concourse import mybir

F32 = mybir.dt.float32
BF16 = mybir.dt.bfloat16
F16 = mybir.dt.float16
ACT = mybir.ActivationFunctionType
ALU = mybir.AluOpType
AX_X = mybir.AxisListType.X

P = 128
D_MODEL = 1024
KT = D_MODEL // P
SEQ, CTX = 1024, 256
NX, NC = SEQ // P, CTX // P
NTOK = SEQ + CTX
NTILE = NX + NC
DEPTH = 2
HEADS, KV, DH = 8, 2, 64
MH, MD = 4, 128
MW = MH * MD
CONV_K = 5
EPS = 1e-6
BIG = 1e30
WIN = 3 * P
KPAD = P + SEQ + P
NKEY = WIN + CTX
F_TILES = 18
N_GATE, N_K, N_Q, N_AZ, N_MQ, N_MK = 0, 1, 2, 6, 10, 14
CONV_LEN = SEQ + CTX + 8
ACC_LEN = CONV_LEN - 4
GW = D_MODEL // 4
DW_K = 31
D_FF = 4 * D_MODEL
ALIBI_LEN = SEQ - P + SEQ
LAM_INIT = float(0.8 - 0.6 * np.exp(0.0))
SMALL = 3264
LN_KSCALE = float(-0.5 * np.log(MD))


class Chain:

    def __init__(self, sem):
        self.sem, self.base, self.n = sem, 0, 0

    def start(self, base):
        self.base, self.n = base, 0

    def __call__(self, eng, ins):
        ins.then_inc(self.sem, 1)
        self.n += 1
        eng.wait_ge(self.sem, self.base + self.n)


def host_constants():
    f = np.float32
    out = {"ident": np.eye(P, dtype=f)}
    rot = np.zeros((P, P), f)
    for b in range(0, P, 32):
        for j in range(16):
            rot[b + 16 + j, b + j] = -1.0
            rot[b + j, b + 16 + j] = 1.0
    out["rot"] = rot
    sel = np.zeros((36, 2 * MH, P), f)
    for d in range(2):
        for h in range(MH):
            sel[32 * d + h, d * MH + h] = 1.0
    out["sel"] = sel
    s, t = np.arange(P)[:, None], np.arange(P)[None, :]
    out["tri"] = np.stack([np.where(s <= t, 0.0, BIG), np.where(s >= t, 0.0, BIG)], 1).astype(f)
    half = DH // 2
    inv = (10000.0 ** (-np.arange(0, half, 2, dtype=f) / f(half))).astype(f)
    tok = np.arange(SEQ)
    ang = np.concatenate([np.tile((tok // 64).astype(f)[None] * inv[:, None], (2, 1)),
                          np.tile((tok % 64).astype(f)[None] * inv[:, None], (2, 1))], 0)
    ang = np.tile(ang.astype(f), (2, 1)).astype(np.float64)
    out["cos"], out["sin"] = np.cos(ang).astype(f), np.sin(ang).astype(f)
    q, k = np.arange(P)[:, None], np.arange(WIN)[None, :] - P
    band = np.abs(q - k) <= P
    mask = np.zeros((P, NX, WIN), f)
    for b in range(NX):
        kpos = b * P + k
        mask[:, b] = np.where(band & (kpos >= 0) & (kpos < SEQ), 0.0, -BIG)
    out["wmask"] = mask
    out["alibi"] = np.abs(np.arange(P)[:, None] - (np.arange(ALIBI_LEN)[None, :] - (SEQ - P))).astype(np.float16)
    slopes = 2.0 ** (-8.0 * (np.arange(4) + 1) / 4)
    out["slope"] = (-slopes[None, :, None] * np.eye(P)[:, None, :]).astype(np.float16)
    n = np.arange(SEQ)
    ang = 2 * np.pi * ((n[:, None] * n[None, :]) % SEQ) / SEQ
    half = SEQ // 2
    out["cos_s"] = np.cos(ang[:, 0:half + 1]).reshape(NX, P, half + 1).transpose(1, 0, 2).astype(f)
    out["sin_s"] = np.sin(ang[:, 1:half]).reshape(NX, P, half - 1).transpose(1, 0, 2).astype(f)
    c = np.arange(DH)
    ang = 2 * np.pi * ((c[:, None] * c[None, :]) % DH) / DH
    norm = (SEQ * DH) ** -0.5
    diag = np.eye(P // DH)
    out["dft_c"] = np.stack([np.kron(diag, np.cos(ang) * norm), np.kron(diag, -np.sin(ang) * norm)], 1).astype(f)
    out["mean64"] = np.kron(diag, np.full((DH, DH), 1.0 / DH)).astype(f)
    out["map_rows"] = (np.arange(P)[:, None] // 32 == np.arange(4)[None, :]).astype(f)
    return out


def pairs(eng, n, body):
    for t in range(2):
        body(t, t)
    with eng.Fori(1, n) as i:
        for u in range(2):
            body(2 * i + u, u)


def host_layout(inputs):
    f = np.float32

    def rows(w):
        return w.reshape(w.shape[0] // P, P, w.shape[1]).transpose(1, 0, 2)

    def cols(v):
        v = v.reshape(v.shape[:-1] + (v.shape[-1] // P, P))
        return np.moveaxis(v, -1, 0)

    def spread(v):
        return np.broadcast_to(v[None], (P,) + v.shape)

    i = {k: np.asarray(v) for k, v in inputs.items()}
    o = dict(host_constants())
    o["wmask"] = (o["wmask"].view(np.uint32) >> 16).astype(np.uint16)
    o["xall"] = np.concatenate([i["x"][0], i["ctx"][0]], 0).reshape(NTILE, P, D_MODEL)
    o["cc"] = np.stack([cols(i["c"][0]), cols(i["c_ctx"])], 2)
    o["w_ada"] = np.stack([np.stack([rows(w[:, 512 * b:512 * b + 512]) for b in range(6)]) for w in i["w_ada"]])
    o["b_ada"] = cols(i["b_ada"][:, 0:2 * D_MODEL])
    o["b_gate"] = spread(i["b_ada"][:, 2 * D_MODEL:])
    o["norm_g"], o["conv_b"], o["head_g"] = cols(i["norm_g"]), cols(i["conv_b"]), cols(i["head_g"])
    o["conv_w"] = cols(i["conv_w"]).transpose(0, 1, 3, 2)
    gate = np.zeros((36, DEPTH, 2), f)
    for d in range(2):
        for n in range(2):
            at = 2 * MH * n + MH * d
            gate[32 * d:32 * d + MH, :, n] = i["gate_b"][:, at:at + MH].T
    o["gate_b"] = gate
    o["sink"], o["final_g"] = spread(i["sink"]), spread(i["final_g"])
    cut = np.cumsum((HEADS * DH, KV * DH, KV * DH, HEADS * DH, MW, MW, MW, MW, MW, 2 * MH, 2 * MH))
    w_tm, w_v, w_ft = [], [], []
    for w in i["w_in"]:
        aq, ak, av, az, mq, mk, mv, mo, mz, mi, mf, _ = np.split(w, cut, 1)
        w_tm.append(np.stack([rows(m) for m in (mv, mz, mo)]))
        w_v.append(rows(av))
        gates = np.zeros((D_MODEL, P), f)
        for n, m in enumerate((mi, mf)):
            for d in range(2):
                gates[:, 64 * n + 32 * d:64 * n + 32 * d + MH] = m[:, MH * d:MH * (d + 1)]
        q = [np.concatenate([aq[:, DH * j:DH * (j + 1)], aq[:, DH * (j + 4):DH * (j + 5)]], 1) for j in range(4)]
        w_ft.append(np.stack([rows(m) for m in [gates, ak] + q + sum([np.split(m, 4, 1) for m in (az, mq, mk)], [])]))
    o["w_tm"], o["w_v"], o["w_ft"] = np.stack(w_tm), np.stack(w_v), np.stack(w_ft)
    o["w_out"] = np.stack([rows(w) for w in i["w_out"]])
    two = {k[:-2]: v[0] for k, v in i.items() if k.endswith("_2") and k != "final_g_2"}
    w = two["w_in"]
    hq, hk, hv, ha, hg, hc, hu, hvv = np.split(w, 8, 1)
    blocks = (np.concatenate([hg[:, 0:P], ha[:, 0:P], hg[:, P:], ha[:, P:]], 1), np.concatenate([hc, hv], 1),
              np.concatenate([hu, hvv], 1), np.concatenate([hq, hk], 1))
    o["w_in2"] = np.stack([rows(b) for b in blocks])
    o["w_out2"] = np.stack([rows(b) for b in np.split(two["w_out"], 2, 1)])
    o["w_up"] = np.stack([rows(b) for b in np.split(two["w_up"], D_FF // 512, 1)])
    o["w_down"] = np.stack([rows(b) for b in np.split(two["w_down"], D_FF // 512, 0)])
    o["lam"] = spread(np.stack([two[n] for n in ("lam_q1", "lam_k1", "lam_q2", "lam_k2")]))
    o["subln_g"] = np.tile(two["subln_g"], 2)[:, None]
    o["norm1_g"], o["norm2_g"], o["final_g2"] = cols(two["norm1_g"]), cols(two["norm2_g"]), spread(i["final_g_2"])
    o["dw_w"] = cols(two["conv_dw_w"]).transpose(0, 2, 1)
    for name, src in (("dw_b", "conv_dw_b"), ("cln_g", "conv_ln_g"), ("cln_b", "conv_ln_b"), ("pw_b", "conv_pw_b"), ("fnet_b", "fnet_b")):
        o[name] = cols(two[src])
    o["pw_w"] = rows(two["conv_pw_w"])
    fw = np.zeros((P, 2, P), f)
    for g in range(4):
        at = DH * (g % 2)
        fw[at:at + DH, g // 2, at:at + DH] = two["fnet_w"][g]
    o["fnet_w"] = fw
    o["sgu_rows"] = spread(np.stack([two["sgu_ln_g"], two["sgu_ln_b"]]))
    o["sgu_w"] = two["sgu_w"].transpose(2, 0, 1)
    o["sgu_b"] = two["sgu_b"].T
    return {k: np.ascontiguousarray(v) for k, v in o.items()}




def build(nc, A, out):
    with ExitStack() as ctx:
        def sb(name, shape, dt=F32):
            return ctx.enter_context(nc.sbuf_tensor(f"{name}_sb", shape, dt))

        ident = sb("ident", [P, P])
        rot = sb("rot", [P, P])
        small = sb("small", [P, SMALL])
        sel = small[0:36, 0:1024].rearrange("p (n m) -> p n m", n=2 * MH)
        tri = sb("tri", [P, 2, P])
        ident_bf = sb("ident_bf", [P, P], BF16)
        gate_c = small[:, 1024:2048]
        cc = sb("cc", [P, KT, 2])
        scc = sb("scc", [P, KT, 2])
        b_ada = sb("b_ada", [P, DEPTH, 2 * KT])
        norm_g = sb("norm_g", [P, DEPTH, KT])
        mod_shift = sb("mod_shift", [P, DEPTH, 2, KT])
        mod_scale = sb("mod_scale", [P, DEPTH, 2, KT])
        conv_w = sb("conv_w", [P, DEPTH, KT, CONV_K])
        conv_b = sb("conv_b", [P, DEPTH, KT])
        gate_b = sb("gate_b", [36, DEPTH, 2])
        head_g = sb("head_g", [P, DEPTH, MH])
        sink = sb("sink", [P, DEPTH, HEADS])
        neg_sink = sb("neg_sink", [P, DEPTH, HEADS])
        minus_half = sb("minus_half", [P, MH])
        k_scale = sb("k_scale", [P, 1])
        stat = sb("stat", [P, 4, 8])
        cols = small[:, 2048:2048 + 3 * NTILE * 36].rearrange("p (n t r) -> p n t r", n=3, t=NTILE)
        decay_b = sb("decay_b", [P, 2 * MH, NTILE])
        m_state = sb("m_state", [36, 16])
        m_dec = sb("m_dec", [36, NTILE])
        lsum = sb("lsum", [P, 2, HEADS])
        neg_max = sb("neg_max", [P, 2, HEADS])
        row_max = sb("row_max", [P, 2, HEADS])
        sink_e = sb("sink_e", [P, 2, HEADS])
        recip = sb("recip", [P, 2, HEADS])
        den = sb("den", [P, 2, 4, MH])

        ARENA = 47700
        arena = sb("arena", [P, ARENA])
        XN, QKV, MV, MQK, G, S, WFT = 0, 10240, 19968, 25136, 35376, 41776, 45652

        def part(at, *shape):
            n = int(np.prod(shape))
            assert at + n <= ARENA, (at, shape)
            v = arena[:, at:at + n]
            names = "abcde"[:len(shape)]
            if len(shape) == 1:
                return v
            return v.rearrange(f"p ({' '.join(names)}) -> p {' '.join(names)}",
                               **{c: s for c, s in zip(names[1:], shape[1:])})

        xn_t = part(XN, KT, NTILE, P)
        xn_flat = part(XN, KT, NTOK)
        att_t = part(XN, 4, NTILE, P)
        h_dir = [part(XN + 5120, NTILE, MW), part(QKV, NTILE, MW)]
        q_t = part(QKV, 4, NTILE, P)
        q_flat = part(QKV, 4, NTOK)
        kz = part(QKV + 5120, KV, KPAD + CTX)
        v_tm = part(QKV + 8192, NTILE + 2, P)
        mv_tm = part(MV, NTILE, MH, MD + 1)
        mqk_t = part(MQK, 2 * MH, NTILE, P)
        mqk_flat = part(MQK, 2 * MH, NTOK)
        ada_w = [part(XN + 4096 * u, KT, 512) for u in range(2)]
        ada_sc = part(XN + 8192, 2, KT, P)
        gates = part(MQK + 2 * KT * 512, DEPTH, D_MODEL)
        w_mv, w_mz, w_mo = part(MQK, KT, 512), part(MQK + 4096, KT, 512), part(QKV, KT, 512)
        w_v = part(QKV + 4096, KT, P)
        xt = [part(G + 1024 * u, D_MODEL) for u in range(2)]
        xs = [part(G + 2048 + 1024 * u, D_MODEL) for u in range(2)]
        xst = [part(G + 4096 + 1024 * u, KT, P) for u in range(2)]
        junk = [part(G + 6144 + 3072 * u, D_MODEL) for u in range(2)]
        z_st = [part(G + 7168 + 512 * u, MW) for u in range(2)]
        o_st = [part(G + 8192 + 512 * u, MW) for u in range(2)]
        w_ft = [part(WFT + 1024 * u, KT, P) for u in range(2)]
        cst = [part(S + 1292 * u, 1292) for u in range(2)]
        acc = part(S + 2584, 1292)
        cos_t, sin_t = part(MQK, SEQ), part(MQK + 1024, SEQ)
        rope_a = [part(MQK + 2048 + 1024 * u, SEQ) for u in range(2)]
        rope_b = [part(MQK + 4096 + 1024 * u, SEQ) for u in range(2)]
        row_a, row_b, row_m, row_w, row_i = [arena[0:36, G + NTOK * n:G + NTOK * (n + 1)] for n in range(5)]
        prob = [part(XN + 5120 + NKEY * u, NKEY) for u in range(2)]
        prob_t = [part(XN + 6400 + NKEY * u, NKEY // P, P) for u in range(2)]
        q_st = [part(XN + 7680 + 512 * u, 4, P) for u in range(2)]
        az_st = [part(XN + 8704 + 512 * u, 4, P) for u in range(2)]
        att_tm = part(S, HEADS, DH)
        wmask = part(S + 512, NX * WIN // 2).bitcast(BF16).rearrange("p (b k) -> p b k", b=NX)
        c_state = part(QKV + 5120, 2 * MH, MD + 1)
        qk_st = [part(QKV + 6152 + 1024 * d, 2 * MH, P) for d in range(2)]
        dec_y = [part(QKV + 8200 + 512 * d, MH, P) for d in range(2)]
        p_t = [part(S + 512 * d, MH, P) for d in range(2)]
        q_w = [part(S + 1024 + 512 * d, MH, P) for d in range(2)]
        k_w = [part(S + 2048 + 512 * d, MH, P) for d in range(2)]
        w_out = part(MQK, KT, D_MODEL)
        mix_st = [part(MV + 1024 * u, KT, P) for u in range(2)]
        x_new = [part(MV + 2048 + 1024 * u, D_MODEL) for u in range(2)]
        gated = part(MV + 4096, D_MODEL)
        x_in = [part(G + 1024 * u, D_MODEL) for u in range(2)]
        o_in = [part(G + 2048 + 512 * u, MW) for u in range(2)]
        z_in = [part(G + 3072 + 512 * u, MW) for u in range(2)]
        h_sum = [part(G + 4096 + 512 * u, MW) for u in range(2)]
        h_g = [part(G + 5120 + 512 * u, MW) for u in range(2)]
        gate, final_g = part(WFT, D_MODEL), part(WFT + 1024, D_MODEL)
        sq_junk = part(S, D_MODEL)
        sq_last = part(S + 2560, D_MODEL)
        h_n = part(S + 1024, MW)
        h_z = [part(S + 1536 + 512 * u, MW) for u in range(2)]

        ps = ctx.enter_context(nc.psum_tensor("ps", [P, 8, 512], F32))
        ps_flat = ps[:, :, :].rearrange("p b n -> p (b n)")

        X2, XNT, YT, W2, M2 = 0, 8192, 16384, 24576, 32768
        x_res = part(X2, NX, D_MODEL)
        xn2_t = part(XNT, KT, SEQ)
        y_t = part(YT, KT, SEQ)
        nx_s = [part(YT + 1024 * u, D_MODEL) for u in range(2)]
        w_in2 = [part(W2 + 4096 * u, KT, 512) for u in range(2)]
        q2_t, k2_t = part(M2, 2, SEQ), part(M2 + 2048, 2, SEQ)
        v2_tm = part(M2 + 4096, NX, GW)
        z_pad = part(M2 + 6144, 2, SEQ + DW_K - 1)
        z_flat = part(M2 + 6144, 2, SEQ)
        c2_t = part(M2 + 8256, 2, SEQ)
        uv_tm = part(M2 + 10304, NX, 2 * GW)
        o_tm, o_sq = part(M2 + 14400, GW), part(M2 + 14656, GW)
        dw_acc = y_t[:, 2:4, :]
        sig = [part(YT + 4096 + 1024 * u, SEQ) for u in range(2)]
        v_sq = part(YT + 6144, NX, GW)
        prob2 = [[part(W2 + 2048 * u + 1024 * m, SEQ) for m in range(2)] for u in range(2)]
        w_t = [part(W2 + 4096 + 1024 * u, NX, P) for u in range(2)]
        q2_st = [part(W2 + 6144 + 1024 * u, 8, P) for u in range(2)]
        HALF = SEQ // 2
        cos_s = arena[:, XNT:XNT + KT * (HALF + 1)].rearrange("p (k n) -> p k n", k=KT)
        sin_s = arena[:, XNT + KT * (HALF + 1):XNT + 8192].rearrange("p (k n) -> p k n", k=KT)
        u_tm = part(M2, NX, 2, 2, P)
        odd = [part(YT + 6144 + 512 * j, HALF) for j in range(2)]
        w_out2 = part(W2, 2, KT, 512)
        y_st = [part(M2 + 8192 + 1024 * u, KT, P) for u in range(2)]
        nx_s2 = [part(M2 + 12288 + 1024 * u, D_MODEL) for u in range(2)]
        w_up = [part(M2 + 4096 * u, KT, 512) for u in range(2)]
        w_down = [part(W2 + 4096 * u, 4, D_MODEL) for u in range(2)]
        h_t = [part(M2 + 8192, 4, SEQ), part(YT, 4, SEQ)]
        final_g2 = part(YT + 4096, D_MODEL)
        out_s = [part(YT + 5120 + 1024 * u, D_MODEL) for u in range(2)]
        alibi = sb("alibi", [P, ALIBI_LEN], F16)
        stat2 = sb("stat2", [P, 6, 8])
        eps_col = sb("eps_col", [P, 1])
        neg_lam = sb("neg_lam", [P, 1])
        lam_s = sb("lam_s", [P, 2])
        sub_g = sb("sub_g", [P, 1])
        at2 = 0

        def small_part(*shape):
            nonlocal at2
            n = int(np.prod(shape))
            at2 += n
            assert at2 <= SMALL, at2
            v = small[:, at2 - n:at2]
            return v if len(shape) == 1 else v.rearrange(
                f"p ({' '.join('abc'[:len(shape)])}) -> p {' '.join('abc'[:len(shape)])}",
                **{c: s for c, s in zip("bc", shape[1:])})

        slope = small_part(4 * P // 2).bitcast(F16).rearrange("p (h q) -> p h q", h=4)
        pw_w, fnet_w, dft_c = small_part(2, GW), small_part(2, P), small_part(2, P)
        chan_w = small_part(2, 2, P)
        sgu_rows, sgu_w = small_part(2, GW), small_part(4, P)
        lam_in, lam_p = small_part(4, 32), small_part(2, 32)
        dw_w, dw_b = small_part(2, DW_K), small_part(2)
        cln_g, cln_b, pw_b, fnet_b = [small_part(2) for _ in range(4)]
        subln_g, norm1_g, norm2_g, sgu_b = small_part(1), small_part(KT), small_part(KT), small_part(4)
        map_rows = small_part(4)
        mean64 = small_part(P)

        def dram(name, shape):
            return nc.dram_tensor(f"{name}_dram", shape, F32).ap()

        gates_dram = dram("gates", [P, DEPTH, D_MODEL])
        z_dram = [dram(f"z_{l}", [NTILE, P, MW]) for l in range(DEPTH)]
        o_dram = [dram(f"o_{l}", [NTILE, P, MW]) for l in range(DEPTH)]
        az_dram = [dram(f"az_{l}", [4, P, NTILE, P]) for l in range(DEPTH)]
        x_dram = [A["xall"]] + [dram(f"x_{l + 1}", [NTILE, P, D_MODEL]) for l in range(DEPTH)]

        def layer_tiles(l):
            return NTILE if l < DEPTH - 1 else NX

        def first_block_layer(l, block, sems):

            def sem(name):
                sems.append(nc.alloc_semaphore(name=f"{name}_{l}"))
                return sems[-1]

            def sem_per_layer(name):
                return {l: sem(name)}

            def sem_per_slot(name):
                return {l: [sem(f"{name}{u}") for u in range(2)]}

            const_ld = sem("const_ld")
            CONSTS = [(ident[:, :], "ident"), (rot[:, :], "rot"), (sel[:, :, :], "sel"), (tri[:, :, :], "tri"),
                      (cc[:, :, :], "cc"), (b_ada[:, :, :], "b_ada"), (norm_g[:, :, :], "norm_g"),
                      (conv_w[:, :, :, :], "conv_w"), (conv_b[:, :, :], "conv_b"), (gate_b[:, :, :], "gate_b"),
                      (head_g[:, :, :], "head_g"), (sink[:, :, :], "sink"),
                      (gates, "b_gate")]
            CONST_ALL = 16 * len(CONSTS)
            setup_dve = sem("setup_dve")
            ada_ld, ada_use = [sem(f"ada_ld{u}") for u in range(2)], sem("ada_use")
            silu_c, silu_cb = sem("silu_c"), sem("silu_cb")
            ada_done, gates_st = sem("ada_done"), sem("gates_st")
            nt_w = {l: [sem(f"nt_w{n}") for n in range(4)]}
            nt_ld = sem_per_slot("nt_ld")
            nt_sq, nt_ms, nt_rs, nt_xs, nt_tr = [sem_per_layer(n) for n in ("nt_sq", "nt_ms", "nt_rs", "nt_xs", "nt_tr")]
            nt_ev_act, nt_ev_dve, nt_cp = [sem_per_layer(n) for n in ("nt_ev_act", "nt_ev_dve", "nt_cp")]
            nt_mv, nt_mz, nt_mo, nt_v = [sem_per_layer(n) for n in ("nt_mv", "nt_mz", "nt_mo", "nt_v")]
            nt_mv_ev, nt_mz_ev, nt_mo_ev, nt_v_ev = [sem_per_layer(n) for n in ("nt_mv_ev", "nt_mz_ev", "nt_mo_ev", "nt_v_ev")]
            nt_z_st, nt_o_st = sem_per_slot("nt_z_st"), sem_per_slot("nt_o_st")
            pads = sem_per_layer("pads")
            ft_w = sem_per_slot("ft_w")
            ft_trig, ft_mm, ft_ev, ft_rot, ft_rope_a, ft_rope, ft_conv, ft_silu = [sem_per_layer(n) for n in (
                "ft_trig", "ft_mm", "ft_ev", "ft_rot", "ft_rope_a", "ft_rope", "ft_conv", "ft_silu")]
            ft_rotfree = sem_per_layer("ft_rotfree")
            ft_az_st = sem_per_slot("ft_az_st")
            ft_chain = {l: Chain(sem("ft_chain"))}
            g_abs, g_ln, g_rows, g_exp, g_tr, g_cols = [sem_per_layer(n) for n in (
                "g_abs", "g_ln", "g_rows", "g_exp", "g_tr", "g_cols")]
            g_chain = {l: Chain(sem("g_chain"))}
            g_act_chain = {l: Chain(sem("g_act_chain"))}
            a_mask = sem_per_layer("a_mask")
            a_az = sem_per_slot("a_az")
            a_q, a_s, a_nm, a_e, a_t, a_t_act, a_t_dve, a_pv = [sem_per_layer(n) for n in (
                "a_q", "a_s", "a_nm", "a_e", "a_t", "a_t_act", "a_t_dve", "a_pv")]
            a_sink, a_sink_e, a_att, a_att_tr, a_out = [sem_per_layer(n) for n in (
                "a_sink", "a_sink_e", "a_att", "a_att_tr", "a_out")]
            a_chain = {l: Chain(sem("a_chain"))}
            m_st, m_s, m_k, m_m, m_w, m_y, m_d, m_kw, m_qs, m_p, m_num, m_del, m_c, m_h, m_init = [sem_per_layer(n) for n in (
                "m_st", "m_s", "m_k", "m_m", "m_w", "m_y", "m_d", "m_kw", "m_qs", "m_p", "m_num", "m_del", "m_c", "m_h", "m_init")]
            m_chain = {l: Chain(sem("m_chain"))}
            p_w, p_gates = sem_per_layer("p_w"), sem_per_layer("p_gates")
            p_x, p_o, p_z, p_store = [sem_per_slot(n) for n in ("p_x", "p_o", "p_z", "p_store")]
            p_sig, p_sum, p_hg, p_sq, p_ms, p_rs, p_hn, p_hz, p_tr, p_ev, p_att, p_mm, p_gated, p_new = [sem_per_layer(n) for n in (
                "p_sig", "p_sum", "p_hg", "p_sq", "p_ms", "p_rs", "p_hn", "p_hz", "p_tr", "p_ev", "p_att", "p_mm", "p_gated", "p_new")]
            f_sq, f_ms, f_rs, f_x = sem("f_sq"), sem("f_ms"), sem("f_rs"), sem("f_x")

            @block.sync
            def _(sp):
                if l == 0:
                    for view, name in CONSTS:
                        sp.dma_start(view, A[name]).then_inc(const_ld, 16)

                def modulation():
                    for n in range(DEPTH * 6):
                        if n >= 2:
                            sp.wait_ge(ada_use, n - 1)
                        sp.dma_start(ada_w[n % 2], A["w_ada"][n // 6, n % 6]).then_inc(ada_ld[n % 2], 16)

                def norm_tm(l):
                    sp.dma_start(w_mv, A["w_tm"][l, 0]).then_inc(nt_w[l][0], 16)
                    sp.dma_start(w_mz, A["w_tm"][l, 1]).then_inc(nt_w[l][1], 16)
                    sp.dma_start(w_mo, A["w_tm"][l, 2]).then_inc(nt_w[l][2], 16)
                    sp.dma_start(w_v, A["w_v"][l]).then_inc(nt_w[l][3], 16)

                    for u in range(2):
                        sp.dma_start(w_ft[u], A["w_ft"][l, u]).then_inc(ft_w[l][u], 16)

                    def load_x(t, u):
                        sp.dma_start(xt[u], x_dram[l][t]).then_inc(nt_ld[l][u], 16)

                    def store(t, u):
                        sp.wait_ge(nt_mz_ev[l], t + 1)
                        sp.dma_start(z_dram[l][t], z_st[u]).then_inc(nt_z_st[l][u], 16)
                        sp.wait_ge(nt_mo_ev[l], t + 1)
                        sp.dma_start(o_dram[l][t], o_st[u]).then_inc(nt_o_st[l][u], 16)

                    for u in range(2):
                        load_x(u, u)
                    with sp.Fori(0, NX // 2) as i:
                        for u in range(2):
                            sp.wait_ge(nt_xs[l], 2 * i + u + 1)
                            load_x(2 * i + u + 2, u)
                            store(2 * i + u, u)
                    if l < DEPTH - 1:
                        for t in range(NX, NTILE):
                            store(t, t % 2)

                def ft(l):
                    sp.wait_ge(nt_mv[l], NTILE)
                    sp.dma_start(cos_t, A["cos"]).then_inc(ft_trig[l], 16)
                    sp.dma_start(sin_t, A["sin"]).then_inc(ft_trig[l], 16)
                    with sp.Fori(1, F_TILES // 2) as i:
                        for u in range(2):
                            sp.wait_ge(ft_mm[l], 2 * i + u - 1)
                            sp.dma_start(w_ft[u], A["w_ft"][l, 2 * i + u]).then_inc(ft_w[l][u], 16)

                def attention(l):
                    sp.wait_ge(ft_silu[l], 8)
                    sp.dma_start(wmask, A["wmask"].bitcast(BF16)).then_inc(a_mask[l], 16)
                    for u in range(2):
                        sp.wait_ge(ft_az_st[l][u], 16 * 2)

                    def load_az(b, u):
                        sp.dma_start(az_st[u], az_dram[l][:, :, b, :].rearrange("j p n -> p j n")).then_inc(a_az[l][u], 16)

                    load_az(0, 0)
                    load_az(1, 1)
                    with sp.Fori(0, NX // 2 - 1) as i:
                        for u in range(2):
                            sp.wait_ge(a_out[l], 2 * i + u + 1)
                            load_az(2 * i + u + 2, u)
                    if l < DEPTH - 1:
                        for t in range(NX, NTILE):
                            sp.wait_ge(a_out[l], t - 1)
                            load_az(t, t % 2)

                def output(l):
                    nt = layer_tiles(l)
                    sp.wait_ge(m_st[l], 2 * NTILE)
                    sp.dma_start(w_out, A["w_out"][l]).then_inc(p_w[l], 16)
                    sp.dma_start(gate, gates_dram[:, l, :]).then_inc(p_gates[l], 16)
                    if l == DEPTH - 1:
                        sp.dma_start(final_g, A["final_g"]).then_inc(p_gates[l], 16)
                    sp.wait_ge(m_h[l], 2 * nt)
                    sp.wait_ge(m_del[l], 2 * NTILE)
                    sp.wait_ge(m_w[l], 2 * nt)
                    for s in (nt_z_st, nt_o_st):
                        for u in range(2):
                            sp.wait_ge(s[l][u], 16 * (nt // 2))

                    def load(t, u):
                        sp.dma_start(o_in[u], o_dram[l][t]).then_inc(p_o[l][u], 16)
                        sp.dma_start(z_in[u], z_dram[l][t]).then_inc(p_z[l][u], 16)

                    def load_x(t, u):
                        sp.dma_start(x_in[u], x_dram[l][t]).then_inc(p_x[l][u], 16)

                    def store(t, u):
                        sp.wait_ge(p_new[l], t + 1) if l == 0 else sp.wait_ge(f_x, t + 1)
                        sp.dma_start(x_dram[l + 1][t], x_new[u]).then_inc(p_store[l][u], 16)

                    def next_loads(t, u):
                        sp.wait_ge(p_hz[l], t + 1)
                        load(t + 2, u)

                    for t in range(2):
                        load(t, t)
                        load_x(t, t)
                    with sp.Fori(0, NX // 2 - 1) as i:
                        for u in range(2):
                            next_loads(2 * i + u, u)
                            store(2 * i + u, u)
                            load_x(2 * i + u + 2, u)
                    for t in range(NX - 2, nt):
                        if t + 2 < nt:
                            next_loads(t, t % 2)
                        store(t, t % 2)
                        if t + 2 < nt:
                            load_x(t + 2, t % 2)
                    for u in range(2):
                        sp.wait_ge(p_store[l][u], 16 * (nt // 2))

                if l == 0:
                    modulation()
                norm_tm(l)
                ft(l)
                attention(l)
                output(l)

            @block.tensor
            def _(pe):
                def modulation():
                    pe.wait_ge(silu_c, 1)
                    pe.wait_ge(const_ld, CONST_ALL)
                    for l in range(DEPTH):
                        for blk in range(6):
                            n = 6 * l + blk
                            pe.wait_ge(ada_ld[n % 2], 16 * (n // 2 + 1))
                            w = ada_w[n % 2]
                            if blk < 4:
                                for f in range(4):
                                    at = 2 * (4 * blk + f)
                                    for k in range(KT):
                                        mm = pe.matmul(ps[:, l, at:at + 2], w[:, k, f * P:(f + 1) * P], scc[:, k, :],
                                                       start=k == 0, stop=k == KT - 1)
                                mm.then_inc(ada_use, 1)
                            else:
                                if n == 4:
                                    pe.wait_ge(silu_cb, 1)
                                for v in range(2 if l == 0 else 1):
                                    bank = (2 + 2 * v if l == 0 else 6) + blk - 4
                                    for k in range(KT):
                                        mm = pe.matmul(ps[:, bank, :], ada_sc[:, v, k, :], w[:, k, :],
                                                       start=k == 0, stop=k == KT - 1)
                                mm.then_inc(ada_use, 1)

                def norm_tm(l):
                    def turn(t, u):
                        pe.wait_ge(nt_xs[l], t + 1)
                        for k in range(KT):
                            mm = pe.transpose(ps[:, 2 * u + k // 4, (k % 4) * P:(k % 4 + 1) * P],
                                              xs[u][:, k * P:(k + 1) * P], ident[:, :])
                        mm.then_inc(nt_tr[l], 1)

                    def products(t, u, gates=True):
                        pe.wait_ge(nt_ev_act[l], t + 1)
                        pe.wait_ge(nt_ev_dve[l], t + 1)
                        for n, w, width, done, free in ((0, w_mv, 512, nt_mv, nt_mv_ev), (1, w_mz, 512, nt_mz, nt_mz_ev),
                                                        (2, w_mo, 512, nt_mo, nt_mo_ev), (3, w_v, P, nt_v, nt_v_ev)):
                            if n in (1, 2) and not gates:
                                continue
                            pe.wait_ge(nt_w[l][n], 16)
                            if not isinstance(t, int) or t > 0:
                                pe.wait_ge(free[l], t)
                            for k in range(KT):
                                mm = pe.matmul(ps[:, 4 + n, 0:width], xst[u][:, k, :], w[:, k, :],
                                               start=k == 0, stop=k == KT - 1)
                            mm.then_inc(done[l], 1)

                    if l == 0:
                        pe.wait_ge(ada_done, 1)
                    turn(0, 0)
                    turn(1, 1)
                    products(0, 0)
                    turn(2, 0)
                    products(1, 1)
                    with pe.Fori(1, NX // 2) as i:
                        turn(2 * i + 1, 1)
                        products(2 * i, 0)
                        turn(2 * i + 2, 0)
                        products(2 * i + 1, 1)
                    turn(9, 1)
                    products(8, 0, l < DEPTH - 1)
                    products(9, 1, l < DEPTH - 1)

                def ft(l):
                    nt = layer_tiles(l)
                    for s, n in ((nt_ev_act, NTILE), (nt_ev_dve, NTILE), (nt_mv_ev, NTILE), (nt_mz_ev, nt), (nt_mo_ev, nt), (nt_v_ev, NTILE)):
                        pe.wait_ge(s[l], n)
                    pe.wait_ge(nt_cp[l], NTILE)

                    def tile(n, i, u, ntok):
                        pe.wait_ge(ft_w[l][u], 16 * i + 16)
                        if not isinstance(n, int) or n >= 2:
                            pe.wait_ge(ft_ev[l], n - 1)
                        for c, at in enumerate(range(0, ntok, 512)):
                            size = min(512, ntok - at)
                            for k in range(KT):
                                mm = pe.matmul(ps[:, 3 * u + c, 0:size], w_ft[u][:, k, :], xn_flat[:, k, at:at + size],
                                               start=k == 0, stop=k == KT - 1)
                        mm.then_inc(ft_mm[l], 1)

                    def rotate(r, n, u):
                        pe.wait_ge(ft_ev[l], n + 1)
                        if not isinstance(r, int) or r > 0:
                            pe.wait_ge(ft_rotfree[l], r)
                        for c in range(2):
                            mm = pe.matmul(ps[:, 6 + c, :], rot[:, :], cst[u][:, 512 * c:512 * c + 512], start=True, stop=True)
                        mm.then_inc(ft_rot[l], 1)

                    tile(N_GATE, 0, 0, NTOK)
                    tile(N_K, 0, 1, NTOK)
                    rotate(0, N_K, 1)
                    with pe.Fori(0, 2) as j:
                        for u in range(2):
                            tile(N_Q + 2 * j + u, j + N_Q // 2, u, nt * P)
                        for u in range(2):
                            rotate(2 * j + u + 1, N_Q + 2 * j + u, u)
                    with pe.Fori(N_AZ // 2, N_MK // 2) as j:
                        for u in range(2):
                            tile(2 * j + u, j, u, nt * P)
                    with pe.Fori(N_MK // 2, F_TILES // 2) as j:
                        for u in range(2):
                            tile(2 * j + u, j, u, NTOK)
                    pe.wait_ge(g_exp[l], 4)
                    pe.wait_ge(ft_rotfree[l], 5)
                    pe.wait_ge(ft_ev[l], F_TILES)
                    for n, row in enumerate((row_a, row_w, row_b)):
                        for t in range(NTILE):
                            mm = pe.transpose(ps[:, n, 36 * t:36 * t + 36], row[:, t * P:(t + 1) * P], ident[0:36, 0:36])
                        mm.then_inc(g_tr[l], 1)
                    for n in range(2 * MH):
                        mm = pe.matmul(ps[:, 3, NTILE * n:NTILE * (n + 1)], sel[:, n, :], m_dec[:, :], start=True, stop=True)
                    mm.then_inc(g_tr[l], 1)

                def attention(l):
                    pe.wait_ge(g_cols[l], 4)
                    pe.wait_ge(ft_rope[l], 5)
                    pe.wait_ge(a_mask[l], 16)

                    def scores(s, b, u, h, n_win):
                        r, j, g = h % 2, h % 4, h // 4
                        if n_win:
                            pe.matmul(ps[:, 2 * r, P:512], q_st[u][:, j, :], kz[:, g, bass.ds(b * P, WIN)], start=True, stop=False)
                            pe.matmul(ps[:, 2 * r, P:512], ident_bf[:, :], wmask[:, b, :], start=False, stop=True)
                        pe.matmul(ps[:, 2 * r + 1, 0:CTX], q_st[u][:, j, :], kz[:, g, KPAD:KPAD + CTX], start=True, stop=True)\
                            .then_inc(a_s[l], 1)

                    def turn(s, h, n_win):
                        pe.wait_ge(a_e[l], s + 1)
                        if not isinstance(s, int) or s > 0:
                            pe.wait_ge(a_t_act[l], s)
                            pe.wait_ge(a_t_dve[l], s)
                        for n in range((n_win + CTX) // P):
                            bank, at = (4, n * P) if n < 4 else (5, 0)
                            if not n_win:
                                bank, at = 4 + n, 0
                            mm = pe.transpose(ps[:, bank, at:at + P], prob[h % 2][:, n * P:(n + 1) * P], ident[:, :])
                        mm.then_inc(a_t[l], 1)

                    def values(s, b, h, n_win):
                        pe.wait_ge(a_t_act[l], s + 1)
                        pe.wait_ge(a_t_dve[l], s + 1)
                        g, n_all = h // 4, (n_win + CTX) // P
                        for n in range(n_all):
                            tile = b + n if n < n_win // P else NX + 2 + n - n_win // P
                            mm = pe.matmul(ps[:, 6, DH * h:DH * (h + 1)], prob_t[h % 2][:, n, :],
                                           v_tm[:, tile, g * DH:(g + 1) * DH], start=n == 0, stop=n == n_all - 1)
                        mm.then_inc(a_pv[l], 1)

                    def query_block(b, u, n_win):
                        s0 = b * HEADS
                        pe.wait_ge(a_q[l], b + 1)
                        if not isinstance(b, int) or b > 0:
                            pe.wait_ge(a_e[l], s0)
                        scores(s0, b, u, 0, n_win)
                        scores(s0 + 1, b, u, 1, n_win)
                        for h in range(HEADS):
                            turn(s0 + h, h, n_win)
                            if h + 2 < HEADS:
                                scores(s0 + h + 2, b, u, h + 2, n_win)
                            if h == 0 and (not isinstance(b, int) or b > 0):
                                pe.wait_ge(a_att[l], b)
                            values(s0 + h, b, h, n_win)
                        pe.wait_ge(a_att[l], b + 1)
                        if not isinstance(b, int) or b > 0:
                            pe.wait_ge(a_out[l], b)
                        att = att_tm.rearrange("p h d -> p (h d)")
                        for j in range(4):
                            mm = pe.transpose(ps[:, 7, j * P:(j + 1) * P], att[:, j * P:(j + 1) * P], ident[:, :])
                        mm.then_inc(a_att_tr[l], 1)

                    pairs(pe, NX // 2, lambda b, u: query_block(b, u, WIN))
                    for b in range(NX, layer_tiles(l)):
                        query_block(b, b % 2, 0)

                def mlstm(l):
                    nt = layer_tiles(l)
                    pe.wait_ge(a_out[l], nt)
                    pe.wait_ge(m_init[l], 1)

                    def front(n, d, tile, outputs):
                        pe.wait_ge(m_st[l], n + 1)
                        if outputs:
                            c = n - 2 * (NTILE - nt)
                            first = isinstance(c, int) and c == 0
                            if not first:
                                pe.wait_ge(m_y[l], c)
                            for h in range(MH):
                                mm = pe.matmul(ps[:, 1, h * P:(h + 1) * P], sel[:, d * MH + h, :], row_m[:, bass.ts(tile, P)], start=True, stop=True)
                            mm.then_inc(m_m[l], 1)
                            if not first:
                                pe.wait_ge(m_qs[l], c)
                            for h in range(MH):
                                mm = pe.matmul(ps[:, 2, h * P:(h + 1) * P], sel[:, d * MH + h, :], row_i[:, bass.ts(tile, P)], start=True, stop=True)
                            mm.then_inc(m_w[l], 1)
                        if not isinstance(n, int) or n > 0:
                            pe.wait_ge(m_kw[l], n)
                        for h in range(MH):
                            mm = pe.transpose(ps[:, 3, h * P:(h + 1) * P], qk_st[d][:, MH + h, :], ident[:, :])
                        mm.then_inc(m_k[l], 1)

                    def scores(n, d):
                        c = n - 2 * (NTILE - nt)
                        if not isinstance(c, int) or c > 0:
                            pe.wait_ge(m_p[l], c)
                        for h in range(MH):
                            mm = pe.matmul(ps[:, 0, h * P:(h + 1) * P], qk_st[d][:, MH + h, :], qk_st[d][:, h, :], start=True, stop=True)
                        mm.then_inc(m_s[l], 1)

                    def back(n, d, tile, outputs):
                        if outputs:
                            c = n - 2 * (NTILE - nt)
                            pe.wait_ge(m_p[l], c + 1)
                            pe.wait_ge(m_qs[l], c + 1)
                            if not isinstance(c, int) or c > 0:
                                pe.wait_ge(m_h[l], c)
                            if not isinstance(n, int) or n >= 2:
                                pe.wait_ge(m_c[l], n - 1)
                            for h in range(MH):
                                o = ps[:, 4 + h // 2, (MD + 1) * (h % 2):(MD + 1) * (h % 2 + 1)]
                                pe.matmul(o, p_t[d][:, h, :], mv_tm[:, tile, h, :], start=True, stop=False)
                                mm = pe.matmul(o, q_w[d][:, h, :], c_state[:, d * MH + h, :], start=False, stop=True)
                            mm.then_inc(m_num[l], 1)
                        pe.wait_ge(m_kw[l], n + 1)
                        if not isinstance(n, int) or n > 0:
                            pe.wait_ge(m_c[l], n)
                        for h in range(MH):
                            mm = pe.matmul(ps[:, 6 + h // 2, (MD + 1) * (h % 2):(MD + 1) * (h % 2 + 1)],
                                           k_w[d][:, h, :], mv_tm[:, tile, h, :], start=True, stop=True)
                        mm.then_inc(m_del[l], 1)

                    def step(j, tiles, outputs):
                        for d in range(2):
                            front(2 * j + d, d, tiles[d], outputs)
                            if outputs:
                                scores(2 * j + d, d)
                        for d in range(2):
                            back(2 * j + d, d, tiles[d], outputs)

                    for j in range(NC):
                        step(j, (NX + j, NX + NC - 1 - j), l < DEPTH - 1)
                    if l == DEPTH - 1:
                        step(NC, (0, NX - 1), True)
                    with pe.Fori(0 if l < DEPTH - 1 else 1, NX) as i:
                        step(i + NC, (i, i * -1 + (NX - 1)), True)

                def output(l):
                    nt = layer_tiles(l)
                    pe.wait_ge(m_h[l], 2 * nt)
                    pe.wait_ge(m_c[l], 2 * NTILE)

                    def turn(t, u):
                        pe.wait_ge(p_hz[l], t + 1)
                        if not isinstance(t, int) or t >= 2:
                            pe.wait_ge(p_ev[l], t - 1)
                        for j in range(MH):
                            mm = pe.transpose(ps[:, 4 + u, j * P:(j + 1) * P], h_z[u][:, j * P:(j + 1) * P], ident[:, :])
                        mm.then_inc(p_tr[l], 1)

                    def product(t, u):
                        pe.wait_ge(p_ev[l], t + 1)
                        pe.wait_ge(p_att[l], t + 1)
                        if not isinstance(t, int) or t >= 2:
                            pe.wait_ge(p_gated[l], t - 1)
                        for c in range(2):
                            for k in range(KT):
                                mm = pe.matmul(ps[:, 2 * u + c, :], mix_st[u][:, k, :], w_out[:, k, 512 * c:512 * (c + 1)],
                                               start=k == 0, stop=k == KT - 1)
                        mm.then_inc(p_mm[l], 1)

                    turn(0, 0)
                    pe.wait_ge(p_w[l], 16)
                    turn(1, 1)
                    product(0, 0)
                    turn(2, 0)
                    product(1, 1)
                    last = NX // 2 if nt > NX else NX // 2 - 1
                    with pe.Fori(1, last) as i:
                        turn(2 * i + 1, 1)
                        product(2 * i, 0)
                        turn(2 * i + 2, 0)
                        product(2 * i + 1, 1)
                    turn(nt - 1, 1)
                    product(nt - 2, 0)
                    product(nt - 1, 1)

                if l == 0:
                    modulation()
                norm_tm(l)
                ft(l)
                attention(l)
                mlstm(l)
                output(l)

            @block.vector
            def _(dve):
                def bcast(col, n):
                    return col.unsqueeze(2).to_broadcast([col.shape[0], col.shape[1], n])

                def setup():
                    dve.memset(minus_half[:, :], -0.5)
                    dve.memset(k_scale[:, :], LN_KSCALE)
                    dve.memset(m_dec[:, :], 0.0).then_inc(setup_dve, 1)
                    dve.wait_ge(const_ld, CONST_ALL)
                    dve.tensor_copy(ident_bf[:, :], ident[:, :]).then_inc(setup_dve, 1)
                    dve.tensor_scalar(neg_sink[:, :, :], sink[:, :, :], -1.0, None, ALU.mult).then_inc(setup_dve, 1)

                def modulation():
                    for l in range(DEPTH):
                        dve.wait_ge(ada_use, 6 * l + 4)
                        got = ps[:, l, 0:4 * KT].rearrange("p (k v) -> p v k", v=2)
                        b = b_ada[:, l, :].unsqueeze(1).to_broadcast([P, 2, 2 * KT])
                        dve.tensor_tensor(mod_shift[:, l], got[:, :, 0:KT], b[:, :, 0:KT], ALU.add)
                        dve.scalar_tensor_tensor(out=mod_scale[:, l], in0=got[:, :, KT:], scalar=1.0, in1=b[:, :, KT:],
                                                 op0=ALU.add, op1=ALU.add).then_inc(setup_dve, 1)
                        dve.wait_ge(setup_dve, 4 + l)
                        dve.tensor_tensor(mod_scale[:, l], mod_scale[:, l],
                                          norm_g[:, l, :].unsqueeze(1).to_broadcast([P, 2, KT]), ALU.mult)
                    dve.wait_ge(ada_use, 6 * DEPTH)
                    dve.tensor_tensor(gate_c[:, :], ps_flat[:, 2048:3072], gates[:, 0], ALU.add)
                    dve.tensor_tensor(gates[:, 0], ps_flat[:, 1024:2048], gates[:, 0], ALU.add)
                    dve.tensor_tensor(gates[:, 1], ps_flat[:, 3072:4096], gates[:, 1], ALU.add).then_inc(ada_done, 1)

                def norm_tm(l):
                    def scale_rows(t, u):
                        dve.wait_ge(nt_sq[l], t + 1)
                        dve.tensor_scalar(stat[:, 1, u:u + 1], stat[:, 0, u:u + 1], 1.0 / D_MODEL, EPS, ALU.mult, ALU.add)\
                            .then_inc(nt_ms[l], 1)
                        dve.wait_ge(nt_rs[l], t + 1)
                        if not isinstance(t, int) or t >= 2:
                            dve.wait_ge(nt_tr[l], t - 1)
                        dve.tensor_scalar(xs[u], xt[u], stat[:, 2, u:u + 1], None, ALU.mult).then_inc(nt_xs[l], 1)

                    def modulate(t, u, v):
                        dve.wait_ge(nt_tr[l], t + 1)
                        if not isinstance(t, int) or t >= 2:
                            dve.wait_ge(nt_v[l], t - 1)
                            dve.wait_ge(nt_cp[l], t - 1)
                        for k in range(4, KT):
                            ins = dve.tensor_scalar(xst[u][:, k, :], ps[:, 2 * u + 1, (k - 4) * P:(k - 3) * P],
                                                    mod_scale[:, l, v, k:k + 1], mod_shift[:, l, v, k:k + 1], ALU.mult, ALU.add)
                        ins.then_inc(nt_ev_dve[l], 1)

                    def outputs(t, u, gates=True):
                        dve.wait_ge(nt_mv[l], t + 1)
                        dve.tensor_copy(mv_tm[:, t, :, 0:MD], ps[:, 4, :].rearrange("p (h d) -> p h d", h=MH))\
                            .then_inc(nt_mv_ev[l], 1)
                        if gates:
                            dve.wait_ge(nt_mo[l], t + 1)
                            if not isinstance(t, int) or t >= 2:
                                dve.wait_ge(nt_o_st[l][u], 16 * ((t - u) // 2) if isinstance(t, int) else 8 * (t - u))
                            dve.tensor_copy(o_st[u], ps[:, 6, :]).then_inc(nt_mo_ev[l], 1)
                        dve.wait_ge(nt_v[l], t + 1)
                        dve.tensor_copy(v_tm[:, t + 1 if not isinstance(t, int) or t < NX else t + 2, :], ps[:, 7, 0:P])\
                            .then_inc(nt_v_ev[l], 1)

                    dve.memset(kz, 0.0)
                    dve.memset(v_tm[:, 0, :], 0.0)
                    dve.memset(v_tm[:, NX + 1, :], 0.0)
                    dve.memset(mv_tm[:, :, :, MD:MD + 1], 1.0).then_inc(pads[l], 1)
                    for t in range(2):
                        scale_rows(t, t)
                        modulate(t, t, 0)
                    scale_rows(2, 0)
                    outputs(0, 0)
                    def tile(t, u):
                        modulate(t + 2, u, 0)
                        scale_rows(t + 3, 1 - u)
                        outputs(t + 1, 1 - u)

                    pairs(dve, NX // 2 - 1, tile)
                    modulate(8, 0, 1)
                    scale_rows(9, 1)
                    outputs(7, 1)
                    modulate(9, 1, 1)
                    outputs(8, 0, l < DEPTH - 1)
                    outputs(9, 1, l < DEPTH - 1)

                def rope(l, r, n, u, dest, ctx_dest):
                    if ctx_dest is not None:
                        dve.wait_ge(ft_ev[l], n + 1)
                        for at, rows in ctx_dest:
                            dve.tensor_copy(at, cst[u][rows, SEQ:NTOK])
                    dve.wait_ge(ft_rot[l], r + 1)
                    dve.wait_ge(ft_rope_a[l], r + 1)
                    dve.tensor_tensor(rope_b[u], ps_flat[:, 3072:4096], sin_t, ALU.mult).then_inc(ft_rotfree[l], 1)
                    dve.wait_ge(ft_rotfree[l], r + 1)
                    for at, rows in dest:
                        ins = dve.tensor_tensor(at, rope_a[u][rows, :], rope_b[u][rows, :], ALU.add)
                    ins.then_inc(ft_rope[l], 1)

                def gate_scans(l):
                    ch = g_chain[l]
                    dve.wait_ge(g_ln[l], 1)
                    ch.start(1)
                    fwd, bwd = slice(0, MH), slice(32, 32 + MH)
                    tiles_w, tiles_m, tiles_i, tiles_b, tiles_a = [
                        r.rearrange("p (t n) -> p t n", n=P) for r in (row_w, row_m, row_i, row_b, row_a)]
                    dve.scalar_tensor_tensor(out=row_b, in0=row_b, scalar=0.0, in1=row_i, op0=ALU.min, op1=ALU.subtract)
                    ch(dve, dve.memset(row_m, 1.0))
                    dve.memset(tiles_m[fwd, :, 0:1], 0.0)
                    ch(dve, dve.memset(tiles_m[bwd, :, P - 1:P], 0.0))
                    dve.tensor_tensor_scan(row_i[fwd], row_m[fwd], row_b[fwd], 0.0, ALU.mult, ALU.add)
                    dve.tensor_tensor_scan(row_i[bwd, ::-1], row_m[bwd, ::-1], row_b[bwd, ::-1], 0.0, ALU.mult, ALU.add)
                    ch(dve, dve.memset(row_w, 0.0))
                    dve.tensor_tensor(row_a, row_a, row_i, ALU.subtract)
                    dve.tensor_copy(tiles_w[fwd, 1:, 0], tiles_i[fwd, 0:NTILE - 1, P - 1])
                    dve.tensor_copy(tiles_w[fwd, 0:1, 0], tiles_i[fwd, NTILE - 1:, P - 1])
                    ch(dve, dve.tensor_copy(tiles_w[bwd, 0:NTILE - 1, P - 1], tiles_i[bwd, 1:, 0]))
                    dve.tensor_tensor_scan(row_m[bwd, ::-1], row_w[bwd, ::-1], row_a[bwd, ::-1], -BIG, ALU.add, ALU.max)
                    ch(dve, dve.tensor_tensor_scan(row_m[fwd, SEQ:], row_w[fwd, SEQ:], row_a[fwd, SEQ:], -BIG, ALU.add, ALU.max))
                    ch(dve, dve.tensor_tensor_scan(row_m[fwd, 0:SEQ], row_w[fwd, 0:SEQ], row_a[fwd, 0:SEQ], row_m[fwd, NTOK - 1:],
                                                   ALU.add, ALU.max))
                    dve.tensor_tensor(m_state[fwd, 1:NTILE], tiles_w[fwd, 1:, 0], tiles_m[fwd, 0:NTILE - 1, P - 1], ALU.add)
                    dve.tensor_tensor(m_state[fwd, 0:1], tiles_w[fwd, 0:1, 0], tiles_m[fwd, NTILE - 1:, P - 1], ALU.add)
                    dve.tensor_tensor(m_state[bwd, 0:NTILE - 1], tiles_w[bwd, 0:NTILE - 1, P - 1], tiles_m[bwd, 1:, 0], ALU.add)
                    ch(dve, dve.memset(m_state[bwd, NTILE - 1:NTILE], -BIG))
                    ch(dve, dve.memset(m_state[fwd, NX:NX + 1], -BIG))
                    for r, end in ((fwd, P - 1), (bwd, 0)):
                        m_last = tiles_m[r, :, end]
                        dve.tensor_tensor(tiles_w[r], tiles_a[r], bcast(m_last, P), ALU.subtract)
                        dve.tensor_tensor(m_dec[r, 0:NTILE], m_state[r, 0:NTILE], m_last, ALU.subtract)
                        ins = dve.tensor_tensor(row_b[r], row_i[r], row_m[r], ALU.add)
                    ch(dve, ins)
                    for r in (fwd, bwd):
                        ins = dve.tensor_tensor(tiles_i[r], bcast(m_state[r, 0:NTILE], P), tiles_m[r], ALU.subtract)
                    ins.then_inc(g_rows[l], 1)

                def conv(l, c, u):
                    n = N_MQ + c
                    dve.wait_ge(ft_ev[l], n + 1)
                    if not isinstance(c, int) or c > 0:
                        dve.wait_ge(ft_silu[l], c)
                    ch = ft_chain[l]
                    ch.start((CONV_K - 1) * c)
                    w = conv_w[:, l, :, :].rearrange("p c k -> p (c k)")

                    def tap(k):
                        return w[:, bass.ds(c * CONV_K + k, 1)]

                    a = acc[:, 0:ACC_LEN]
                    ch(dve, dve.tensor_scalar(a, cst[u][:, 0:ACC_LEN], tap(0), None, ALU.mult))
                    for k in range(1, CONV_K):
                        ins = dve.scalar_tensor_tensor(out=a, in0=cst[u][:, k:k + ACC_LEN], scalar=tap(k), in1=a,
                                                       op0=ALU.mult, op1=ALU.add)
                        if k < CONV_K - 1:
                            ch(dve, ins)
                    ins.then_inc(ft_conv[l], 1)
                    assert ch.n == CONV_K - 1

                def ft(l):
                    nt = layer_tiles(l)
                    ch = g_chain[l]
                    dve.wait_ge(ft_ev[l], 1)
                    ch.start(0)
                    ch(dve, dve.tensor_scalar(row_b, row_b, gate_b[:, l, 1:2], None, ALU.add))
                    dve.scalar_tensor_tensor(out=row_m, in0=row_b, scalar=-1.0, in1=row_b, op0=ALU.mult, op1=ALU.min)\
                        .then_inc(g_abs[l], 1)
                    dve.wait_ge(ft_trig[l], 32)
                    halves = [slice(g * DH, (g + 1) * DH) for g in range(KV)]
                    rope(l, 0, N_K, 1, [(kz[r, g, P:P + SEQ], r) for g, r in enumerate(halves)],
                         [(kz[r, g, KPAD:KPAD + CTX], r) for g, r in enumerate(halves)])
                    everything = slice(0, P)
                    with dve.Fori(0, 2) as j:
                        for u in range(2):
                            n = 2 * j + u
                            rope(l, n + 1, N_Q + n, u, [(q_flat[:, n, 0:SEQ], everything)],
                                 [(q_flat[:, n, SEQ:NTOK], everything)] if nt > NX else None)
                    gate_scans(l)
                    for u in range(2):
                        dve.wait_ge(ft_az_st[l][u], 32)
                        dve.memset(cst[u][:, 0:2], 0.0)
                        dve.memset(cst[u][:, SEQ + 2:SEQ + 6], 0.0)
                        ins = dve.memset(cst[u][:, CONV_LEN - 2:CONV_LEN], 0.0)
                    ins.then_inc(pads[l], 1)
                    pairs(dve, 4, lambda c, u: conv(l, c, u))
                    for n in range(3):
                        dve.wait_ge(g_tr[l], n + 1)
                        dve.tensor_copy(cols[:, n].rearrange("p t r -> p (t r)"), ps[:, n, 0:36 * NTILE]).then_inc(g_cols[l], 1)
                    dve.wait_ge(g_tr[l], 4)
                    dve.tensor_copy(decay_b[:, :, :].rearrange("p n j -> p (n j)"), ps[:, 3, 0:2 * MH * NTILE]).then_inc(g_cols[l], 1)

                def attention(l):
                    ch = a_chain[l]

                    def head_max(s, u, h, n_win):
                        dve.wait_ge(a_s[l], s + 1)
                        r = h % 2
                        at = ps_flat[:, 1024 * r + P:1024 * r + P + NKEY] if n_win else ps[:, 2 * r + 1, 0:CTX]
                        ch(dve, dve.tensor_reduce(row_max[:, u, h:h + 1], at, AX_X, ALU.max, negate=True))
                        dve.tensor_scalar(neg_max[:, u, h:h + 1], row_max[:, u, h:h + 1], DH ** -0.5, neg_sink[:, l, h:h + 1],
                                          ALU.mult, ALU.min).then_inc(a_nm[l], 1)

                    def query_block(b, u, n_win):
                        s0 = HEADS * b
                        ch.start((HEADS + 2) * b)
                        head_max(s0, u, 0, n_win)
                        head_max(s0 + 1, u, 1, n_win)
                        for h in range(HEADS):
                            dve.wait_ge(a_t[l], s0 + h + 1)
                            n = 4 if n_win else 1
                            dve.tensor_copy(prob_t[h % 2][:, 0:n, :], ps[:, 4, 0:n * P].rearrange("p (n q) -> p n q", n=n))\
                                .then_inc(a_t_dve[l], 1)
                            if h + 2 < HEADS:
                                head_max(s0 + h + 2, u, h + 2, n_win)
                            if h == HEADS - 3:
                                dve.wait_ge(a_nm[l], s0 + HEADS)
                                dve.tensor_tensor(sink_e[:, u, :], neg_max[:, u, :], sink[:, l, :], ALU.add).then_inc(a_sink[l], 1)
                        dve.wait_ge(a_sink_e[l], b + 1)
                        ch(dve, dve.tensor_tensor(lsum[:, u, :], lsum[:, u, :], sink_e[:, u, :], ALU.add))
                        ch(dve, dve.reciprocal(recip[:, u, :], lsum[:, u, :]))
                        dve.wait_ge(a_pv[l], s0 + HEADS)
                        if not isinstance(b, int) or b > 0:
                            dve.wait_ge(a_att_tr[l], b)
                        dve.tensor_tensor(att_tm, ps[:, 6, :].rearrange("p (h d) -> p h d", h=HEADS), bcast(recip[:, u, :], DH), ALU.mult)\
                            .then_inc(a_att[l], 1)
                        dve.wait_ge(a_att_tr[l], b + 1)
                        dve.wait_ge(a_az[l][u], (8 * (b - u) if not isinstance(b, int) else 16 * (b // 2)) + 16)
                        dve.tensor_tensor(att_t[:, :, b, :], ps[:, 7, :].rearrange("p (j n) -> p j n", j=4), az_st[u], ALU.mult)\
                            .then_inc(a_out[l], 1)
                        assert ch.n == HEADS + 2

                    pairs(dve, NX // 2, lambda b, u: query_block(b, u, WIN))
                    for b in range(NX, layer_tiles(l)):
                        query_block(b, b % 2, 0)

                def mlstm(l):
                    nt = layer_tiles(l)
                    ch = m_chain[l]
                    dve.wait_ge(a_out[l], nt)
                    dve.wait_ge(a_pv[l], HEADS * nt)
                    dve.memset(c_state, 0.0).then_inc(m_init[l], 1)

                    def before(n, d, tile):
                        c = n - 2 * (NTILE - nt)
                        dve.wait_ge(m_m[l], c + 1)
                        if not isinstance(c, int) or c >= 2:
                            dve.wait_ge(m_d[l], c - 1)
                        a_col = cols[:, 0].rearrange("p t r -> p (t r)")
                        for h in range(MH):
                            ins = dve.scalar_tensor_tensor(out=dec_y[d][:, h, :], in0=ps[:, 1, h * P:(h + 1) * P],
                                                           scalar=a_col[:, bass.ds(tile * 36 + 32 * d + h, 1)], in1=tri[:, d, :],
                                                           op0=ALU.subtract, op1=ALU.max)
                        ins.then_inc(m_y[l], 1)
                        dve.wait_ge(m_w[l], c + 1)
                        if not isinstance(c, int) or c >= 2:
                            dve.wait_ge(m_num[l], c - 1)
                        dve.tensor_tensor(q_w[d], ps[:, 2, :].rearrange("p (h t) -> p h t", h=MH), qk_st[d][:, 0:MH, :], ALU.mult)\
                            .then_inc(m_qs[l], 1)

                    def weigh(n, d):
                        c = n - 2 * (NTILE - nt)
                        dve.wait_ge(m_s[l], c + 1)
                        dve.wait_ge(m_d[l], c + 1)
                        dve.tensor_tensor(p_t[d], ps[:, 0, :].rearrange("p (h t) -> p h t", h=MH), dec_y[d], ALU.mult)\
                            .then_inc(m_p[l], 1)

                    def after(n, d, tile, outputs):
                        dve.wait_ge(m_del[l], n + 1)
                        dec = decay_b[:, :, :].rearrange("p n j -> p (n j)")
                        for h in range(MH):
                            c_h = c_state[:, d * MH + h, :]
                            ins = dve.scalar_tensor_tensor(out=c_h, in0=c_h, scalar=dec[:, bass.ds((d * MH + h) * NTILE + tile, 1)],
                                                           in1=ps[:, 6 + h // 2, (MD + 1) * (h % 2):(MD + 1) * (h % 2 + 1)],
                                                           op0=ALU.mult, op1=ALU.add)
                        ins.then_inc(m_c[l], 1)
                        if not outputs:
                            return
                        c = n - 2 * (NTILE - nt)
                        ch.start(4 * c)
                        dve.wait_ge(m_num[l], c + 1)
                        num = ps[:, 4:6, 0:2 * (MD + 1)].rearrange("p b (h v) -> p b h v", h=2)
                        ch(dve, dve.tensor_copy(den[:, d, 0, :].rearrange("p (b h) -> p b h", b=2), num[:, :, :, MD]))
                        ch(dve, dve.scalar_tensor_tensor(out=den[:, d, 1, :], in0=den[:, d, 0, :], scalar=-1.0, in1=den[:, d, 0, :],
                                                         op0=ALU.mult, op1=ALU.max))
                        ch(dve, dve.tensor_tensor(den[:, d, 2, :], den[:, d, 1, :], cols[:, 2, tile, 32 * d:32 * d + MH], ALU.max))
                        ch(dve, dve.reciprocal(den[:, d, 3, :], den[:, d, 2, :]))
                        r = den[:, d, 3, :].rearrange("p (b h) -> p b h", b=2).unsqueeze(3).to_broadcast([P, 2, 2, MD])
                        dve.tensor_tensor(h_dir[d][:, tile, :].rearrange("p (b h v) -> p b h v", b=2, h=2), num[:, :, :, 0:MD], r, ALU.mult)\
                            .then_inc(m_h[l], 1)
                        assert ch.n == 4

                    def step(j, tiles, outputs):
                        if outputs:
                            before(2 * j, 0, tiles[0])
                            before(2 * j + 1, 1, tiles[1])
                            weigh(2 * j, 0)
                            weigh(2 * j + 1, 1)
                        for d in range(2):
                            after(2 * j + d, d, tiles[d], outputs)

                    for j in range(NC):
                        step(j, (NX + j, NX + NC - 1 - j), l < DEPTH - 1)
                    if l == DEPTH - 1:
                        step(NC, (0, NX - 1), True)
                    with dve.Fori(0 if l < DEPTH - 1 else 1, NX) as i:
                        step(i + NC, (i, i * -1 + (NX - 1)), True)

                def output(l):
                    nt = layer_tiles(l)

                    def heads_norm(t, u):
                        dve.wait_ge(p_sig[l], t + 1)
                        dve.wait_ge(p_sum[l], t + 1)
                        dve.tensor_tensor(h_g[u], h_sum[u], o_in[u], ALU.mult).then_inc(p_hg[l], 1)
                        dve.wait_ge(p_sq[l], t + 1)
                        dve.tensor_scalar(stat[:, 1, 0:MH], stat[:, 0, 0:MH], 1.0 / MD, EPS, ALU.mult, ALU.add).then_inc(p_ms[l], 1)
                        dve.wait_ge(p_rs[l], t + 1)
                        if not isinstance(t, int) or t > 0:
                            dve.wait_ge(p_hz[l], t)
                        dve.tensor_tensor(h_n.rearrange("p (h v) -> p h v", h=MH), h_g[u].rearrange("p (h v) -> p h v", h=MH),
                                          bcast(stat[:, 2, 0:MH], MD), ALU.mult).then_inc(p_hn[l], 1)

                    def residual(t, u, gate):
                        dve.wait_ge(p_mm[l], t + 1)
                        if not isinstance(t, int) or t > 0:
                            dve.wait_ge(p_new[l], t)
                        dve.tensor_tensor(gated, ps_flat[:, 1024 * u:1024 * u + 1024], gate, ALU.mult).then_inc(p_gated[l], 1)
                        dve.wait_ge(p_gated[l], t + 1)
                        dve.wait_ge(p_x[l][u], (8 * (t - u) if not isinstance(t, int) else 16 * (t // 2)) + 16)
                        if not isinstance(t, int) or t >= 2:
                            dve.wait_ge(p_store[l][u], 8 * (t - u) if not isinstance(t, int) else 16 * (t // 2))
                        dve.tensor_tensor(x_new[u], gated, x_in[u], ALU.add).then_inc(p_new[l], 1)
                        if l == DEPTH - 1:
                            dve.wait_ge(f_sq, t + 1)
                            dve.tensor_scalar(stat[:, 1, 4:5], stat[:, 0, 4:5], 1.0 / D_MODEL, EPS, ALU.mult, ALU.add).then_inc(f_ms, 1)
                            dve.wait_ge(f_rs, t + 1)
                            dve.scalar_tensor_tensor(out=x_new[u], in0=x_new[u], scalar=stat[:, 2, 4:5], in1=final_g,
                                                     op0=ALU.mult, op1=ALU.mult).then_inc(f_x, 1)

                    dve.wait_ge(p_gates[l], 16 if l < DEPTH - 1 else 32)
                    heads_norm(0, 0)
                    heads_norm(1, 1)
                    def tile(t, u):
                        heads_norm(t + 2, u)
                        residual(t, u, gate)

                    pairs(dve, NX // 2 - 1, tile)
                    for t in range(NX - 2, nt):
                        if t + 2 < nt:
                            heads_norm(t + 2, t % 2)
                        residual(t, t % 2, gate if t < NX else gate_c[:, :])

                if l == 0:
                    setup()
                    modulation()
                norm_tm(l)
                ft(l)
                attention(l)
                mlstm(l)
                output(l)

            @block.scalar
            def _(act):
                def modulation():
                    act.wait_ge(const_ld, CONST_ALL)
                    act.activation(scc[:, :, :], cc[:, :, :], ACT.Silu).then_inc(silu_c, 1)

                def norm_tm(l):
                    def squares(t, u):
                        act.wait_ge(nt_ld[l][u], (8 * (t - u) if not isinstance(t, int) else 16 * (t // 2)) + 16)
                        act.activation(junk[u], xt[u], ACT.Square, accum_out=stat[:, 0, u:u + 1]).then_inc(nt_sq[l], 1)

                    def modulate(t, u, v):
                        act.wait_ge(nt_tr[l], t + 1)
                        if not isinstance(t, int) or t >= 2:
                            act.wait_ge(nt_v[l], t - 1)
                            act.wait_ge(nt_cp[l], t - 1)
                        for k in range(4):
                            ins = act.activation(xst[u][:, k, :], ps[:, 2 * u, k * P:(k + 1) * P], ACT.Identity,
                                                 bias=mod_shift[:, l, v, k:k + 1], scale=mod_scale[:, l, v, k:k + 1])
                        ins.then_inc(nt_ev_act[l], 1)

                    def gate(t, u):
                        act.wait_ge(nt_mz[l], t + 1)
                        if not isinstance(t, int) or t >= 2:
                            act.wait_ge(nt_z_st[l][u], 16 * (t // 2) if isinstance(t, int) else 8 * (t - u))
                        act.activation(z_st[u], ps[:, 5, :], ACT.Silu).then_inc(nt_mz_ev[l], 1)

                    if l == 0:
                        act.wait_ge(ada_done, 1)
                        act.dma_start(gates_dram, gates).then_inc(gates_st, 16)
                    for t in range(2):
                        squares(t, t)
                    for t in range(2):
                        modulate(t, t, 0)
                    squares(2, 0)
                    gate(0, 0)
                    def tile(t, u):
                        modulate(t + 2, u, 0)
                        squares(t + 3, 1 - u)
                        gate(t + 1, 1 - u)

                    pairs(act, NX // 2 - 1, tile)
                    modulate(8, 0, 1)
                    squares(9, 1)
                    gate(7, 1)
                    modulate(9, 1, 1)
                    if l < DEPTH - 1:
                        gate(8, 0)
                        gate(9, 1)

                def ft(l):
                    nt = layer_tiles(l)
                    for stored in (nt_z_st[l], nt_o_st[l]):
                        for u in range(2):
                            act.wait_ge(stored[u], 16 * (nt // 2))
                    act.wait_ge(ft_mm[l], 1)
                    act.activation(row_a, ps_flat[0:36, 0:NTOK], ACT.Identity, bias=gate_b[:, l, 0:1])
                    act.activation(row_b, ps_flat[64:100, 0:NTOK], ACT.Copy).then_inc(ft_ev[l], 1)
                    act.wait_ge(g_abs[l], 1)
                    ch = g_act_chain[l]
                    ch(act, act.activation(row_w, row_m, ACT.Exp))
                    act.activation(row_i, row_w, ACT.Ln, bias=1.0).then_inc(g_ln[l], 1)

                    def raw(r, n, u, ntok):
                        act.wait_ge(ft_mm[l], n + 1)
                        if not isinstance(r, int) or r >= 2:
                            act.wait_ge(ft_rope[l], r - 1)
                        act.activation(cst[u][:, 0:ntok], ps_flat[:, 1536 * u:1536 * u + ntok], ACT.Copy).then_inc(ft_ev[l], 1)

                    raw(0, N_K, 1, NTOK)
                    raw(1, N_Q, 0, nt * P)
                    raw(2, N_Q + 1, 1, nt * P)
                    raw(3, N_Q + 2, 0, nt * P)
                    raw(4, N_Q + 3, 1, nt * P)
                    for j in range(4):
                        u = j % 2
                        act.wait_ge(ft_mm[l], N_AZ + j + 1)
                        if j < 2:
                            act.wait_ge(ft_rope[l], 4 + u)
                        else:
                            act.wait_ge(ft_az_st[l][u], 16)
                        act.activation(cst[u][:, 0:nt * P], ps_flat[:, 1536 * u:1536 * u + nt * P], ACT.Silu).then_inc(ft_ev[l], 1)
                        act.wait_ge(ft_ev[l], N_AZ + j + 1)
                        act.dma_start(az_dram[l][j, :, 0:nt, :], cst[u][:, 0:nt * P].rearrange("p (t n) -> p t n", n=P))\
                            .then_inc(ft_az_st[l][u], 16)
                    act.wait_ge(g_rows[l], 1)
                    act.activation(row_w, row_w, ACT.Exp, bias=k_scale[0:36, :]).then_inc(g_exp[l], 1)
                    act.activation(row_i, row_i, ACT.Exp).then_inc(g_exp[l], 1)
                    act.activation(row_b, row_b, ACT.Exp, scale=-1.0).then_inc(g_exp[l], 1)
                    act.activation(m_dec[:, :], m_dec[:, :], ACT.Exp).then_inc(g_exp[l], 1)
                    act.wait_ge(pads[l], 2)
                    act.wait_ge(ft_rope[l], 5)

                    def taps_in(c, u, ntok):
                        act.wait_ge(ft_mm[l], N_MQ + c + 1)
                        if not isinstance(c, int) or c >= 2:
                            act.wait_ge(ft_conv[l], c - 1)
                        if ntok > SEQ:
                            act.activation(cst[u][:, SEQ + 6:SEQ + 6 + CTX], ps_flat[:, 1536 * u + SEQ:1536 * u + NTOK], ACT.Copy)
                        act.activation(cst[u][:, 2:2 + SEQ], ps_flat[:, 1536 * u:1536 * u + SEQ], ACT.Copy).then_inc(ft_ev[l], 1)

                    if l == 0:
                        act.wait_ge(gates_st, 16)

                    def silu(c, ntok):
                        act.wait_ge(ft_conv[l], c + 1)
                        bias = conv_b[:, l, bass.ds(c, 1)]
                        ins = act.activation(mqk_flat[:, c, 0:SEQ], acc[:, 0:SEQ], ACT.Silu, bias=bias)
                        if ntok > SEQ:
                            ins = act.activation(mqk_flat[:, c, SEQ:NTOK], acc[:, SEQ + 4:ACC_LEN], ACT.Silu, bias=bias)
                        ins.then_inc(ft_silu[l], 1)

                    def pair(i, ntok):
                        for u in range(2):
                            taps_in(2 * i + u, u, ntok)
                        for u in range(2):
                            silu(2 * i + u, ntok)

                    for i in range(2):
                        pair(i, nt * P)
                    with act.Fori(2, 4) as i:
                        pair(i, NTOK)

                def attention(l):
                    def exps(s, u, h, n_win):
                        act.wait_ge(a_nm[l], s + 1)
                        r, n = h % 2, n_win + CTX
                        at = ps_flat[:, 1024 * r + P:1024 * r + P + NKEY] if n_win else ps[:, 2 * r + 1, 0:CTX]
                        act.activation(prob[r][:, 0:n], at, ACT.Exp, bias=neg_max[:, u, h:h + 1], scale=DH ** -0.5,
                                       accum_out=lsum[:, u, h:h + 1]).then_inc(a_e[l], 1)

                    def query_block(b, u, n_win):
                        s0 = HEADS * b
                        if not isinstance(b, int) or b > 0:
                            act.wait_ge(a_t[l], s0)
                        exps(s0, u, 0, n_win)
                        exps(s0 + 1, u, 1, n_win)
                        for h in range(HEADS):
                            act.wait_ge(a_t[l], s0 + h + 1)
                            n = 4 if n_win else 1
                            act.activation(prob_t[h % 2][:, n, :], ps[:, 5, 0:P], ACT.Copy).then_inc(a_t_act[l], 1)
                            if h + 2 < HEADS:
                                exps(s0 + h + 2, u, h + 2, n_win)
                        act.wait_ge(a_sink[l], b + 1)
                        act.activation(sink_e[:, u, :], sink_e[:, u, :], ACT.Exp).then_inc(a_sink_e[l], 1)

                    pairs(act, NX // 2, lambda b, u: query_block(b, u, WIN))
                    for b in range(NX, layer_tiles(l)):
                        query_block(b, b % 2, 0)

                def mlstm(l):
                    nt = layer_tiles(l)

                    def weigh_keys(n, d, tile):
                        act.wait_ge(m_k[l], n + 1)
                        if not isinstance(n, int) or n >= 2:
                            act.wait_ge(m_del[l], n - 1)
                        w_col = cols[:, 1].rearrange("p t r -> p (t r)")
                        for h in range(MH):
                            ins = act.activation(k_w[d][:, h, :], ps[:, 3, h * P:(h + 1) * P], ACT.Copy,
                                                 scale=w_col[:, bass.ds(tile * 36 + 32 * d + h, 1)])
                        ins.then_inc(m_kw[l], 1)

                    def decays(n, d):
                        c = n - 2 * (NTILE - nt)
                        act.wait_ge(m_y[l], c + 1)
                        act.activation(dec_y[d], dec_y[d], ACT.Exp, scale=-1.0, bias=k_scale[:, :]).then_inc(m_d[l], 1)

                    def step(j, tiles, outputs):
                        for d in range(2):
                            if outputs:
                                decays(2 * j + d, d)
                            weigh_keys(2 * j + d, d, tiles[d])

                    act.wait_ge(m_init[l], 1)
                    for j in range(NC):
                        step(j, (NX + j, NX + NC - 1 - j), l < DEPTH - 1)
                    if l == DEPTH - 1:
                        step(NC, (0, NX - 1), True)
                    with act.Fori(0 if l < DEPTH - 1 else 1, NX) as i:
                        step(i + NC, (i, i * -1 + (NX - 1)), True)

                def output(l):
                    nt = layer_tiles(l)

                    def gate(t, u):
                        act.wait_ge(p_o[l][u], (8 * (t - u) if not isinstance(t, int) else 16 * (t // 2)) + 16)
                        act.activation(o_in[u], o_in[u], ACT.Sigmoid).then_inc(p_sig[l], 1)
                        act.wait_ge(p_hg[l], t + 1)
                        if not isinstance(t, int) or t > 0:
                            act.wait_ge(p_ms[l], t)
                        for h in range(MH):
                            ins = act.activation(sq_junk[:, h * P:(h + 1) * P], h_g[u][:, h * MD:(h + 1) * MD], ACT.Square,
                                                 accum_out=stat[:, 0, h:h + 1])
                        ins.then_inc(p_sq[l], 1)

                    def gains(t, u):
                        act.wait_ge(p_tr[l], t + 1)
                        if not isinstance(t, int) or t >= 2:
                            act.wait_ge(p_mm[l], t - 1)
                        for j in range(MH):
                            ins = act.activation(mix_st[u][:, 4 + j, :], ps[:, 4 + u, j * P:(j + 1) * P], ACT.Copy,
                                                 scale=head_g[:, l, j:j + 1])
                        ins.then_inc(p_ev[l], 1)

                    def last_norm(t, u):
                        if l < DEPTH - 1:
                            return
                        act.wait_ge(p_new[l], t + 1)
                        act.activation(sq_last, x_new[u], ACT.Square, accum_out=stat[:, 0, 4:5]).then_inc(f_sq, 1)

                    act.wait_ge(m_del[l], 2 * NTILE)
                    gate(0, 0)
                    gate(1, 1)
                    gains(0, 0)
                    gains(1, 1)
                    with act.Fori(0, NX // 2 - 1) as i:
                        for u in range(2):
                            gate(2 * i + u + 2, u)
                            last_norm(2 * i + u, u)
                            gains(2 * i + u + 2, u)
                    for t in range(NX - 2, nt):
                        if t + 2 < nt:
                            gate(t + 2, t % 2)
                        last_norm(t, t % 2)
                        if t + 2 < nt:
                            gains(t + 2, t % 2)

                if l == 0:
                    modulation()
                norm_tm(l)
                ft(l)
                attention(l)
                mlstm(l)
                output(l)

            @block.gpsimd
            def _(pool):
                def inverse_root(dst, src, n):
                    return pool.tensor_tensor(dst, src, minus_half[:, 0:n], ALU.pow)

                def modulation():
                    pool.wait_ge(silu_c, 1)
                    for v in range(2):
                        for k in range(KT):
                            ins = pool.tensor_copy(ada_sc[:, v, k, :], scc[:, k, v:v + 1].to_broadcast([P, P]))
                    ins.then_inc(silu_cb, 1)
                    pool.wait_ge(setup_dve, 1)

                def norm_tm(l):
                    def roots(t, u):
                        pool.wait_ge(nt_ms[l], t + 1)
                        inverse_root(stat[:, 2, u:u + 1], stat[:, 1, u:u + 1], 1).then_inc(nt_rs[l], 1)

                    def keep(t, u):
                        pool.wait_ge(nt_ev_act[l], t + 1)
                        pool.wait_ge(nt_ev_dve[l], t + 1)
                        pool.tensor_copy(xn_t[:, :, t, :], xst[u]).then_inc(nt_cp[l], 1)

                    roots(0, 0)
                    roots(1, 1)
                    keep(0, 0)
                    with pool.Fori(0, NX // 2) as i:
                        for u in range(2):
                            roots(2 * i + u + 2, u)
                            keep(2 * i + u + 1, 1 - u)
                    keep(NTILE - 1, 1)

                def ft(l):
                    def rope(r, n, u):
                        pool.wait_ge(ft_ev[l], n + 1)
                        if not isinstance(r, int) or r >= 2:
                            pool.wait_ge(ft_rope[l], r - 1)
                        pool.tensor_tensor(rope_a[u], cst[u][:, 0:SEQ], cos_t, ALU.mult).then_inc(ft_rope_a[l], 1)

                    pool.wait_ge(ft_trig[l], 32)
                    rope(0, N_K, 1)
                    rope(1, N_Q, 0)
                    rope(2, N_Q + 1, 1)
                    rope(3, N_Q + 2, 0)
                    rope(4, N_Q + 3, 1)

                def attention(l):
                    def stage(b, u):
                        if not isinstance(b, int) or b >= 2:
                            pool.wait_ge(a_s[l], HEADS * (b - 1))
                        pool.tensor_copy(q_st[u], q_t[:, :, b, :]).then_inc(a_q[l], 1)

                    pool.wait_ge(ft_rope[l], 5)
                    pool.wait_ge(ft_mm[l], F_TILES)
                    stage(0, 0)
                    stage(1, 1)
                    with pool.Fori(1, NX // 2) as i:
                        for u in range(2):
                            stage(2 * i + u, u)
                    for b in range(NX, layer_tiles(l)):
                        stage(b, b % 2)

                def mlstm(l):
                    nt = layer_tiles(l)

                    def stage(n, d, tile):
                        if not isinstance(n, int) or n >= 2:
                            c = n - 2 * (NTILE - nt)
                            pool.wait_ge(m_k[l], n - 1)
                            if not isinstance(c, int) or c >= 2:
                                pool.wait_ge(m_qs[l], c - 1)
                                pool.wait_ge(m_s[l], c - 1)
                        pool.tensor_copy(qk_st[d], mqk_t[:, :, tile, :]).then_inc(m_st[l], 1)

                    pool.wait_ge(m_init[l], 1)
                    pool.wait_ge(ft_silu[l], 8)

                    def step(j, tiles):
                        for d in range(2):
                            stage(2 * j + d, d, tiles[d])

                    for j in range(NC):
                        step(j, (NX + j, NX + NC - 1 - j))
                    first = 0
                    if l == DEPTH - 1:
                        step(NC, (0, NX - 1))
                        first = 1
                    with pool.Fori(first, NX) as i:
                        step(i + NC, (i, i * -1 + (NX - 1)))

                def output(l):
                    nt = layer_tiles(l)
                    pool.wait_ge(m_h[l], 2 * nt)
                    pool.wait_ge(m_del[l], 2 * NTILE)

                    def join(t, u):
                        if not isinstance(t, int) or t >= 2:
                            pool.wait_ge(p_hg[l], t - 1)
                        pool.tensor_tensor(h_sum[u], h_dir[0][:, t, :], h_dir[1][:, t, :], ALU.add).then_inc(p_sum[l], 1)
                        if not isinstance(t, int) or t >= 2:
                            pool.wait_ge(p_mm[l], t - 1)
                        pool.tensor_copy(mix_st[u][:, 0:4, :], att_t[:, :, t, :]).then_inc(p_att[l], 1)

                    def heads(t, u):
                        pool.wait_ge(p_ms[l], t + 1)
                        inverse_root(stat[:, 2, 0:MH], stat[:, 1, 0:MH], MH).then_inc(p_rs[l], 1)
                        pool.wait_ge(p_hn[l], t + 1)
                        pool.wait_ge(p_z[l][u], (8 * (t - u) if not isinstance(t, int) else 16 * (t // 2)) + 16)
                        if not isinstance(t, int) or t >= 2:
                            pool.wait_ge(p_tr[l], t - 1)
                        pool.tensor_tensor(h_z[u], h_n, z_in[u], ALU.mult).then_inc(p_hz[l], 1)

                    def last_root(t):
                        if l < DEPTH - 1:
                            return
                        pool.wait_ge(f_ms, t + 1)
                        inverse_root(stat[:, 2, 4:5], stat[:, 1, 4:5], 1).then_inc(f_rs, 1)

                    for t in range(2):
                        join(t, t)
                        heads(t, t)
                    with pool.Fori(0, NX // 2 - 1) as i:
                        for u in range(2):
                            t = 2 * i + u
                            join(t + 2, u)
                            heads(t + 2, u)
                            last_root(t)
                    for t in range(NX - 2, nt):
                        if t + 2 < nt:
                            join(t + 2, t % 2)
                            heads(t + 2, t % 2)
                        last_root(t)

                if l == 0:
                    modulation()
                norm_tm(l)
                ft(l)
                attention(l)
                mlstm(l)
                output(l)

        def second_block(number, block, sems):
            def sem(name):
                sems.append(nc.alloc_semaphore(name=f"{name}_{number}"))
                return sems[-1]

            const2 = sem("const2")
            CONST2 = [(alibi[:, :], "alibi"), (slope, "slope"), (pw_w, "pw_w"), (fnet_w, "fnet_w"), (dft_c, "dft_c"),
                      (sgu_rows, "sgu_rows"), (sgu_w, "sgu_w"), (lam_in, "lam"), (dw_w, "dw_w"), (dw_b, "dw_b"),
                      (cln_g, "cln_g"), (cln_b, "cln_b"), (pw_b, "pw_b"), (fnet_b, "fnet_b"), (subln_g, "subln_g"),
                      (norm1_g, "norm1_g"), (norm2_g, "norm2_g"), (sgu_b, "sgu_b"), (mean64, "mean64"), (map_rows, "map_rows")]
            CONST2_ALL = 16 * len(CONST2)
            setup2, lam_sum, lam_e, sub_ready = sem("setup2"), sem("lam_sum"), sem("lam_e"), sem("sub_ready")
            x_ld = [sem(f"x_ld{u}") for u in range(2)]
            norm_sems = {n: {k: sem(f"n{n}_{k}") for k in ("sq", "ms", "rs", "xs", "tr", "ev_act", "ev_dve")} for n in ("1", "2", "f")}
            w2_ld = [sem(f"w2_ld{n}") for n in range(4)]
            cv_mm, cv_sig, cv_z, cv_acc = sem("cv_mm"), sem("cv_sig"), sem("cv_z"), sem("cv_acc")
            cv_tap = sem("cv_tap")
            c_mm, c_ev, v_mm, v_ev, uv_mm, uv_ev = [sem(n) for n in ("c_mm", "c_ev", "v_mm", "v_ev", "uv_mm", "uv_ev")]
            qk_mm, qk_ev = sem("qk_mm"), sem("qk_ev")
            ln_act, ln_rs, ln_v = Chain(sem("ln_act")), sem("ln_rs"), sem("ln_v")
            ln_pool = Chain(sem("ln_pool"))
            ln_var = sem("ln_var")
            d_q, d_s, d_nm, d_e = sem("d_q"), [sem(f"d_s{m}") for m in range(2)], [sem(f"d_nm{m}") for m in range(2)], \
                [sem(f"d_e{m}") for m in range(2)]
            d_w, d_t, d_t_act, d_t_dve, d_pv, d_o = [sem(n) for n in ("d_w", "d_t", "d_t_act", "d_t_dve", "d_pv", "d_o")]
            d_ms, d_rs, d_on, d_att, d_y = [sem(n) for n in ("d_ms", "d_rs", "d_on", "d_att", "d_y")]
            d_chain, d_fin = Chain(sem("d_chain")), Chain(sem("d_fin"))
            tab_ld = [sem(f"tab_ld{n}") for n in range(2)]
            cw_mm, cw_ev, u_mm, u_ev = sem("cw_mm"), sem("cw_ev"), sem("u_mm"), sem("u_ev")
            dft_mm, dft_odd, dft_y = sem("dft_mm"), sem("dft_odd"), sem("dft_y")
            mu_mm, mu_x, mu_sq, var_mm, var_ln, var_rs, cn_z, cn_silu, pw_mm, pw_ev = [sem(n) for n in (
                "mu_mm", "mu_x", "mu_sq", "var_mm", "var_ln", "var_rs", "cn_z", "cn_silu", "pw_mm", "pw_ev")]
            sg_mm, sg_u, sg_tr, sg_ev = [sem(n) for n in ("sg_mm", "sg_u", "sg_tr", "sg_ev")]
            wo_ld, y_rd, wo_mm, x_add = [sem(f"wo_ld{c}") for c in range(2)], sem("y_rd"), sem("wo_mm"), sem("x_add")
            up_ld, dn_ld = [sem(f"up_ld{u}") for u in range(2)], [sem(f"dn_ld{u}") for u in range(2)]
            up_mm, up_relu, up_sq, dn_mm, dn_add = [sem(n) for n in ("up_mm", "up_relu", "up_sq", "dn_mm", "dn_add")]
            fg_ld, out_ready, out_st = sem("fg_ld"), sem("out_ready"), [sem(f"out_st{u}") for u in range(2)]
            DIMS = D_FF // 512

            def pairs_with_ends(eng, n, body):
                for t in range(2):
                    body(t, t)
                with eng.Fori(1, n - 1) as i:
                    for u in range(2):
                        body(2 * i + u, u)
                for t in range(2 * n - 2, 2 * n):
                    body(t, t % 2)

            @block.sync
            def _(sp):
                def load_x(t, u):
                    if not isinstance(t, int) or t >= 2:
                        sp.wait_ge(x_ld[u], 8 * (t - u) if not isinstance(t, int) else 16 * (t // 2))
                    sp.dma_start(x_res[:, t, :], x_dram[DEPTH][t]).then_inc(x_ld[u], 16)

                load_x(0, 0)
                load_x(1, 1)
                for view, name in CONST2:
                    sp.dma_start(view, A[name]).then_inc(const2, 16)
                for n in range(2):
                    sp.dma_start(w_in2[n], A["w_in2"][n]).then_inc(w2_ld[n], 16)
                with sp.Fori(1, NX // 2) as i:
                    for u in range(2):
                        load_x(2 * i + u, u)
                sp.wait_ge(cv_mm, 4)
                sp.dma_start(w_in2[0], A["w_in2"][2]).then_inc(w2_ld[2], 16)
                sp.wait_ge(c_mm, 2)
                sp.wait_ge(v_mm, NX)
                sp.dma_start(w_in2[1], A["w_in2"][3]).then_inc(w2_ld[3], 16)
                sp.wait_ge(qk_mm, 4)
                sp.dma_start(cos_s, A["cos_s"]).then_inc(tab_ld[0], 16)
                sp.dma_start(sin_s, A["sin_s"]).then_inc(tab_ld[1], 16)
                sp.wait_ge(d_pv, 4 * NX)
                for c in range(2):
                    sp.dma_start(w_out2[:, c], A["w_out2"][c]).then_inc(wo_ld[c], 16)

                def load_up(g, u):
                    sp.dma_start(w_up[u], A["w_up"][g]).then_inc(up_ld[u], 16)

                def load_down(g, u):
                    sp.dma_start(w_down[u], A["w_down"][g]).then_inc(dn_ld[u], 16)

                sp.wait_ge(dft_mm, 2)
                sp.wait_ge(pw_mm, 4)
                sp.wait_ge(sg_mm, 4)
                load_up(0, 0)
                load_up(1, 1)
                sp.wait_ge(wo_mm, NX)
                sp.dma_start(final_g2, A["final_g2"]).then_inc(fg_ld, 16)
                load_down(0, 0)
                load_down(1, 1)
                with sp.Fori(1, DIMS // 2) as i:
                    for u in range(2):
                        sp.wait_ge(up_mm, 8 * i + 4 * u - 4)
                        load_up(2 * i + u, u)
                        sp.wait_ge(dn_mm, 32 * i + 16 * u - 16)
                        load_down(2 * i + u, u)

                def store(t, u):
                    sp.wait_ge(out_ready, t + 1)
                    sp.dma_start(out[t], out_s[u]).then_inc(out_st[u], 16)

                pairs(sp, NX // 2, store)
                for u in range(2):
                    sp.wait_ge(out_st[u], 16 * (NX // 2))

            @block.tensor
            def _(pe):
                def turn(n, xs, t, u):
                    s = norm_sems[n]
                    pe.wait_ge(s["xs"], t + 1)
                    if not isinstance(t, int) or t >= 2:
                        pe.wait_ge(s["ev_act"], t - 1)
                        pe.wait_ge(s["ev_dve"], t - 1)
                    for k in range(KT):
                        mm = pe.transpose(ps[:, 2 * u + k // 4, (k % 4) * P:(k % 4 + 1) * P], xs[u][:, k * P:(k + 1) * P], ident[:, :])
                    mm.then_inc(s["tr"], 1)

                def ft_tile(bank, w, done):
                    for c in range(2):
                        for k in range(KT):
                            mm = pe.matmul(ps[:, bank + c, :], w[:, k, :], xn2_t[:, k, 512 * c:512 * (c + 1)],
                                           start=k == 0, stop=k == KT - 1)
                    mm.then_inc(done, 1)

                def tm_tile(bank, t, w, width, done):
                    for k in range(KT):
                        mm = pe.matmul(ps[:, bank, 0:width], xn2_t[:, k, t * P:(t + 1) * P], w[:, k, :], start=k == 0, stop=k == KT - 1)
                    mm.then_inc(done, 1)

                def projections():
                    pe.wait_ge(norm_sems["1"]["ev_act"], NX)
                    pe.wait_ge(norm_sems["1"]["ev_dve"], NX)
                    pe.wait_ge(w2_ld[0], 16)
                    for n in range(4):
                        ft_tile(2 * n, w_in2[0][:, :, n * P:(n + 1) * P], cv_mm)
                    pe.wait_ge(w2_ld[1], 16)
                    for j in range(2):
                        pe.wait_ge(cv_sig, j + 1)
                        ft_tile(4 * j, w_in2[1][:, :, j * P:(j + 1) * P], c_mm)
                    pe.wait_ge(cv_z, 1)
                    for t in range(NX):
                        if t >= 2:
                            pe.wait_ge(v_ev, t - 1)
                        tm_tile(2 + t % 2, t, w_in2[1][:, :, GW:2 * GW], GW, v_mm)
                    pe.wait_ge(cv_z, 2)
                    pe.wait_ge(w2_ld[2], 16)
                    for t in range(NX):
                        if t >= 2:
                            pe.wait_ge(uv_ev, t - 1)
                        tm_tile(6 + t % 2, t, w_in2[0], 512, uv_mm)
                    pe.wait_ge(w2_ld[3], 16)
                    pe.wait_ge(c_ev, 2)
                    pe.wait_ge(v_ev, NX)
                    for n, bank in enumerate((0, 4, 2)):
                        ft_tile(bank, w_in2[1][:, :, n * P:(n + 1) * P], qk_mm)
                    pe.wait_ge(uv_ev, NX)
                    ft_tile(6, w_in2[1][:, :, 3 * P:4 * P], qk_mm)

                def attention():
                    pe.wait_ge(qk_ev, 4)

                    def scores(s, b, u, h):
                        if not isinstance(b, int) or h == 0:
                            pe.wait_ge(d_q, b + 1)
                        for m in range(2):
                            if not isinstance(s, int) or s > 0:
                                pe.wait_ge(d_e[m], s)
                            for c in range(2):
                                pe.matmul(ps[:, 2 * m + c, :], q2_st[u][:, 2 * h + m, :], k2_t[:, h // 2, 512 * c:512 * (c + 1)],
                                          start=True, stop=False)
                                mm = pe.matmul(ps[:, 2 * m + c, :], slope[:, h, :],
                                               alibi[:, bass.ds(b * -P + (SEQ - P + 512 * c), 512)], start=False, stop=True)
                            mm.then_inc(d_s[m], 1)

                    def turn_p(s, h):
                        pe.wait_ge(d_w, s + 1)
                        if not isinstance(s, int) or s > 0:
                            pe.wait_ge(d_t_act, s)
                            pe.wait_ge(d_t_dve, s)
                        for n in range(NX):
                            mm = pe.transpose(ps[:, 4 + n // 4, (n % 4) * P:(n % 4 + 1) * P], prob2[h % 2][0][:, n * P:(n + 1) * P], ident[:, :])
                        mm.then_inc(d_t, 1)

                    def values(s, b, h):
                        pe.wait_ge(d_t_act, s + 1)
                        pe.wait_ge(d_t_dve, s + 1)
                        if h == 0 and (not isinstance(b, int) or b > 0):
                            pe.wait_ge(d_o, b)
                        for n in range(NX):
                            mm = pe.matmul(ps[:, 6, DH * h:DH * (h + 1)], w_t[h % 2][:, n, :], v2_tm[:, n, DH * h:DH * (h + 1)],
                                           start=n == 0, stop=n == NX - 1)
                        mm.then_inc(d_pv, 1)

                    def turn_out(b):
                        pe.wait_ge(d_on, b + 1)
                        if not isinstance(b, int) or b > 0:
                            pe.wait_ge(d_y, b)
                        for j in range(2):
                            mm = pe.transpose(ps[:, 7, j * P:(j + 1) * P], o_tm[:, j * P:(j + 1) * P], ident[:, :])
                        mm.then_inc(d_att, 1)

                    def query_block(b, u):
                        for h in range(4):
                            s = 4 * b + h
                            if h < 3:
                                scores(s + 1, b, u, h + 1)
                            elif not isinstance(b, int) or b < NX - 1:
                                scores(s + 1, b + 1, 1 - u, 0)
                            turn_p(s, h)
                            values(s, b, h)
                            if h == 1 and (not isinstance(b, int) or b > 0):
                                turn_out(b - 1)

                    scores(0, 0, 0, 0)
                    pairs_with_ends(pe, NX // 2, query_block)
                    turn_out(NX - 1)

                def mixers():
                    pe.wait_ge(d_y, NX)
                    pe.wait_ge(d_e[1], 4 * NX)

                    def group_mean(src, n, done):
                        for c in range(2):
                            mm = pe.matmul(ps[:, 2 * n + c, :], mean64, src[:, n, 512 * c:512 * (c + 1)], start=True, stop=True)
                        mm.then_inc(done, 1)

                    pe.wait_ge(cv_acc, 2)
                    for j in range(2):
                        group_mean(dw_acc, j, mu_mm)
                    for j in range(2):
                        for m in range(2):
                            mm = pe.matmul(ps[:, 4 + j, m * P:(m + 1) * P], dft_c[:, m, :], fnet_w[:, j, :], start=True, stop=True)
                    mm.then_inc(cw_mm, 1)
                    pe.wait_ge(cw_ev, 1)
                    for t in range(NX):
                        if t >= 2:
                            pe.wait_ge(u_ev, t - 1)
                        for j in range(2):
                            mm = pe.matmul(ps[:, 6 + t % 2, 2 * P * j:2 * P * (j + 1)], c2_t[:, j, t * P:(t + 1) * P],
                                           chan_w[:, j].rearrange("p m e -> p (m e)"), start=True, stop=True)
                        mm.then_inc(u_mm, 1)
                    for j in range(2):
                        pe.wait_ge(mu_sq, j + 1)
                        group_mean(z_flat, j, var_mm)
                    pe.wait_ge(u_ev, NX)
                    for n in range(2):
                        pe.wait_ge(tab_ld[n], 16)
                    for j in range(2):
                        a, b = (4, 5) if j == 0 else (6, 7)
                        for k in range(NX):
                            pe.matmul(ps[:, a, :], u_tm[:, k, j, 0, :], cos_s[:, k, 0:HALF], start=k == 0, stop=k == NX - 1)
                        for k in range(NX):
                            pe.matmul(ps[:, b, 0:1], u_tm[:, k, j, 0, :], cos_s[:, k, HALF:HALF + 1], start=k == 0, stop=k == NX - 1)
                        for k in range(NX):
                            mm = pe.matmul(ps[:, b, 1:HALF], u_tm[:, k, j, 1, :], sin_s[:, k, :], start=k == 0, stop=k == NX - 1)
                        mm.then_inc(dft_mm, 1)
                    pe.wait_ge(cn_silu, 2)
                    for e in range(2):
                        for c in range(2):
                            for k in range(2):
                                mm = pe.matmul(ps[:, 2 * e + c, :], pw_w[:, k, e * P:(e + 1) * P], z_flat[:, k, 512 * c:512 * (c + 1)],
                                               start=k == 0, stop=k == 1)
                            mm.then_inc(pw_mm, 1)
                    pe.wait_ge(ln_v, 1)
                    for g in range(4):
                        pe.wait_ge(dft_y, 1 if g < 2 else 2)
                        v_g = uv_tm[:, :, GW + DH * g:GW + DH * (g + 1)]
                        pe.matmul(ps[:, 4 + g, :], sgu_w[:, g, :], v_g, start=True, stop=True).then_inc(sg_mm, 1)
                    pe.wait_ge(sg_u, 4)
                    pe.wait_ge(pw_ev, 4)
                    for n in range(4):
                        j, half = n // 2, n % 2
                        for i in range(4):
                            mm = pe.transpose(ps[:, n, i * P:(i + 1) * P], uv_tm[:, 4 * half + i, j * P:(j + 1) * P], ident[:, :])
                        mm.then_inc(sg_tr, 1)

                def output():
                    def product(t, u):
                        pe.wait_ge(y_rd, t + 1)
                        if not isinstance(t, int) or t >= 2:
                            pe.wait_ge(x_add, t - 1)
                        for c in range(2):
                            if isinstance(t, int) and t == 0:
                                pe.wait_ge(wo_ld[c], 16)
                            for k in range(KT):
                                mm = pe.matmul(ps[:, 4 + 2 * u + c, :], y_st[u][:, k, :], w_out2[:, c, k, :], start=k == 0, stop=k == KT - 1)
                        mm.then_inc(wo_mm, 1)

                    pe.wait_ge(sg_ev, 4)
                    for t in range(4):
                        product(t, t % 2)
                        if t >= 2:
                            turn("2", nx_s2, t - 2, t % 2)
                    with pe.Fori(2, NX // 2) as i:
                        for u in range(2):
                            product(2 * i + u, u)
                            turn("2", nx_s2, 2 * i + u - 2, u)
                    for t in range(NX - 2, NX):
                        turn("2", nx_s2, t, t % 2)

                def mlp():
                    pe.wait_ge(norm_sems["2"]["ev_act"], NX)
                    pe.wait_ge(norm_sems["2"]["ev_dve"], NX)
                    pe.wait_ge(x_add, NX)

                    def up(g, u):
                        pe.wait_ge(up_ld[u], 8 * (g - u) + 16)
                        for n in range(4):
                            i = 4 * g + n
                            if not isinstance(i, int) or i >= 2:
                                pe.wait_ge(up_relu, i - 1)
                            for c in range(2):
                                for k in range(KT):
                                    mm = pe.matmul(ps[:, 2 * (n % 2) + c, :], w_up[u][:, k, n * P:(n + 1) * P], xn2_t[:, k, 512 * c:512 * (c + 1)],
                                                   start=k == 0, stop=k == KT - 1)
                            mm.then_inc(up_mm, 1)

                    def down(g, u):
                        pe.wait_ge(dn_ld[u], 8 * (g - u) + 16)
                        pe.wait_ge(up_sq, 4 * g + 4)
                        for t in range(NX):
                            for c in range(2):
                                i = 16 * g + 2 * t + c
                                if not isinstance(i, int) or i >= 4:
                                    pe.wait_ge(dn_add, i - 3)
                                for k in range(4):
                                    mm = pe.matmul(ps[:, 4 + (2 * t + c) % 4, :], h_t[u][:, k, t * P:(t + 1) * P], w_down[u][:, k, 512 * c:512 * (c + 1)],
                                                   start=k == 0, stop=k == 3)
                                mm.then_inc(dn_mm, 1)

                    up(0, 0)
                    up(1, 1)
                    down(0, 0)
                    with pe.Fori(1, DIMS // 2) as i:
                        up(2 * i, 0)
                        down(2 * i - 1, 1)
                        up(2 * i + 1, 1)
                        down(2 * i, 0)
                    down(DIMS - 1, 1)

                pe.wait_ge(const2, CONST2_ALL)
                pairs(pe, NX // 2, lambda t, u: turn("1", nx_s, t, u))
                projections()
                attention()
                mixers()
                output()
                mlp()

            @block.vector
            def _(dve):
                def bcast(col, n):
                    return col.unsqueeze(2).to_broadcast([col.shape[0], col.shape[1], n])

                def mean_square(n, t):
                    s = norm_sems[n]
                    dve.wait_ge(s["sq"], t + 1)
                    dve.tensor_scalar(stat[:, 1, bass.ds(t, 1)], stat[:, 0, bass.ds(t, 1)], 1.0 / D_MODEL, EPS, ALU.mult, ALU.add)\
                        .then_inc(s["ms"], 1)

                def scale_rows(n, xs, t, u):
                    s = norm_sems[n]
                    mean_square(n, t)
                    dve.wait_ge(s["rs"], t + 1)
                    if not isinstance(t, int) or t >= 2:
                        dve.wait_ge(s["tr"], t - 1)
                    dve.tensor_scalar(xs[u], x_res[:, t, :], stat[:, 2, bass.ds(t, 1)], None, ALU.mult).then_inc(s["xs"], 1)

                def gain(n, g, t, u):
                    s = norm_sems[n]
                    dve.wait_ge(s["tr"], t + 1)
                    dve.tensor_tensor(xn2_t[:, 4:8, bass.ts(t, P)], ps[:, 2 * u + 1, :].rearrange("p (k n) -> p k n", k=4),
                                      bcast(g[:, 4:8], P), ALU.mult).then_inc(s["ev_dve"], 1)

                def setup():
                    dve.memset(eps_col[:, :], EPS)
                    dve.memset(z_pad[:, :, 0:DW_K // 2], 0.0)
                    dve.memset(z_pad[:, :, SEQ + DW_K // 2:], 0.0).then_inc(setup2, 1)
                    dve.wait_ge(const2, CONST2_ALL)
                    dve.tensor_scalar(sub_g[:, :], subln_g, 1.0 - LAM_INIT, None, ALU.mult).then_inc(sub_ready, 1)
                    dve.tensor_tensor(lam_p, lam_in[:, 0:4:2], lam_in[:, 1:4:2], ALU.mult).then_inc(setup2, 1)
                    dve.wait_ge(setup2, 2)
                    dve.tensor_reduce(lam_s[:, :], lam_p, AX_X, ALU.add).then_inc(lam_sum, 1)

                def convolution():
                    for j in range(2):
                        dve.wait_ge(cv_mm, 2 * j + 2)
                        dve.wait_ge(cv_sig, j + 1)
                        dve.tensor_tensor(z_pad[:, j, DW_K // 2:DW_K // 2 + SEQ], ps_flat[:, 2048 * j + 1024:2048 * j + 2048], sig[j], ALU.mult)\
                            .then_inc(cv_z, 1)
                    dve.wait_ge(cv_z, 2)
                    for k in range(DW_K):
                        for j in range(2):
                            src, tap = z_pad[:, j, k:k + SEQ], dw_w[:, j, k:k + 1]
                            if k:
                                dve.wait_ge(cv_tap, 2 * k + j - 1)
                                ins = dve.scalar_tensor_tensor(out=dw_acc[:, j], in0=src, scalar=tap, in1=dw_acc[:, j], op0=ALU.mult, op1=ALU.add)
                            else:
                                ins = dve.tensor_scalar(dw_acc[:, j], src, tap, dw_b[:, j:j + 1], ALU.mult, ALU.add)
                            ins.then_inc(cv_acc if k == DW_K - 1 else cv_tap, 1)

                def attention():
                    ch, fin = d_chain, d_fin
                    dve.wait_ge(lam_e, 1)
                    dve.scalar_tensor_tensor(out=neg_lam[:, :], in0=lam_s[:, 1:2], scalar=-LAM_INIT, in1=lam_s[:, 0:1],
                                             op0=ALU.add, op1=ALU.subtract).then_inc(setup2, 1)
                    dve.wait_ge(setup2, 3)

                    def maxima(s, u, h):
                        for m in range(2):
                            dve.wait_ge(d_s[m], s + 1)
                            dve.tensor_reduce(neg_max[:, u, 2 * h + m:2 * h + m + 1], ps_flat[:, 1024 * m:1024 * (m + 1)], AX_X, ALU.max, negate=True)\
                                .then_inc(d_nm[m], 1)

                    def combine(s, u, h):
                        dve.wait_ge(d_e[1], s + 1)
                        dve.wait_ge(d_e[0], s + 1)
                        ch.start(2 * s)
                        c = recip[:, u, 2 * h + 1:2 * h + 2]
                        ch(dve, dve.reciprocal(c, lsum[:, u, 2 * h + 1:2 * h + 2]))
                        ch(dve, dve.scalar_tensor_tensor(out=row_max[:, u, h:h + 1], in0=lsum[:, u, 2 * h:2 * h + 1], scalar=neg_lam[:, :], in1=c,
                                                         op0=ALU.mult, op1=ALU.mult))
                        p0, p1 = prob2[h % 2]
                        dve.scalar_tensor_tensor(out=p0, in0=p1, scalar=row_max[:, u, h:h + 1], in1=p0, op0=ALU.mult, op1=ALU.add)\
                            .then_inc(d_w, 1)

                    def evacuate(s, h):
                        dve.wait_ge(d_t, s + 1)
                        dve.tensor_copy(w_t[h % 2][:, 4:8, :], ps[:, 5, :].rearrange("p (n q) -> p n q", n=4)).then_inc(d_t_dve, 1)

                    def finish(b, u):
                        fin.start(3 * b)
                        fin(dve, dve.reciprocal(den[:, u, 0, :], lsum[:, u, 0:8:2]))
                        dve.wait_ge(d_pv, 4 * b + 4)
                        if not isinstance(b, int) or b > 0:
                            dve.wait_ge(d_att, b)
                        o = o_tm.rearrange("p (h d) -> p h d", h=4)
                        dve.tensor_tensor(o, ps[:, 6, 0:GW].rearrange("p (h d) -> p h d", h=4), bcast(den[:, u, 0, :], DH), ALU.mult)\
                            .then_inc(d_o, 1)
                        dve.wait_ge(d_o, b + 1)
                        fin(dve, dve.tensor_tensor(o_sq, o_tm, o_tm, ALU.mult))
                        fin(dve, dve.tensor_reduce(den[:, u, 1, :], o_sq.rearrange("p (h d) -> p h d", h=4), AX_X, ALU.add))
                        dve.tensor_scalar(den[:, u, 2, :], den[:, u, 1, :], 1.0 / DH, EPS, ALU.mult, ALU.add).then_inc(d_ms, 1)
                        dve.wait_ge(d_rs, b + 1)
                        dve.tensor_tensor(o, o, bcast(den[:, u, 3, :], DH), ALU.mult).then_inc(d_on, 1)

                    def query_block(b, u):
                        for h in range(4):
                            s = 4 * b + h
                            combine(s, u, h)
                            if h < 3:
                                maxima(s + 1, u, h + 1)
                            elif not isinstance(b, int) or b < NX - 1:
                                maxima(s + 1, 1 - u, 0)
                            if h == 0 and (not isinstance(b, int) or b > 0):
                                finish(b - 1, 1 - u)
                            evacuate(s, h)

                    maxima(0, 0, 0)
                    pairs_with_ends(dve, NX // 2, query_block)
                    finish(NX - 1, 1)

                def mixers():
                    for j in range(2):
                        dve.wait_ge(mu_mm, j + 1)
                        dve.tensor_tensor(dw_acc[:, j], dw_acc[:, j], ps_flat[:, 1024 * j:1024 * (j + 1)], ALU.subtract).then_inc(mu_x, 1)
                    for j in range(2):
                        dve.wait_ge(var_rs, j + 1)
                        dve.tensor_tensor(dw_acc[:, j], dw_acc[:, j], z_flat[:, j], ALU.mult).then_inc(cn_z, 1)
                    for j in range(2):
                        dve.wait_ge(dft_mm, j + 1)
                        dve.wait_ge(dft_odd, j + 1)
                        a, y, b = ps[:, (4, 6)[j], :], y_t[:, 4 + j, :], fnet_b[:, j:j + 1]
                        dve.tensor_scalar(y[:, 0:1], a[:, 0:1], b, None, ALU.add)
                        dve.tensor_scalar(y[:, HALF:HALF + 1], odd[j][:, 0:1], b, None, ALU.add)
                        dve.scalar_tensor_tensor(out=y[:, 1:HALF], in0=a[:, 1:HALF], scalar=b, in1=odd[j][:, 1:HALF], op0=ALU.add, op1=ALU.add)
                        dve.scalar_tensor_tensor(out=y[:, :HALF:-1], in0=a[:, 1:HALF], scalar=b, in1=odd[j][:, 1:HALF], op0=ALU.add, op1=ALU.subtract)\
                            .then_inc(dft_y, 1)
                    for g in range(4):
                        dve.wait_ge(sg_mm, g + 1)
                        u = uv_tm[:, :, DH * g:DH * (g + 1)]
                        dve.scalar_tensor_tensor(out=u, in0=ps[:, 4 + g, :].rearrange("p (n c) -> p n c", n=NX), scalar=sgu_b[:, g:g + 1], in1=u,
                                                 op0=ALU.add, op1=ALU.mult).then_inc(sg_u, 1)
                    for n in range(4):
                        dve.wait_ge(sg_tr, n + 1)
                        dve.tensor_copy(y_t[:, 6 + n // 2, 512 * (n % 2):512 * (n % 2 + 1)], ps[:, n, :]).then_inc(sg_ev, 1)

                def output():
                    def residual(t, u):
                        dve.wait_ge(wo_mm, t + 1)
                        dve.tensor_tensor(x_res[:, t, :], x_res[:, t, :], ps_flat[:, 2048 + 1024 * u:3072 + 1024 * u], ALU.add).then_inc(x_add, 1)

                    residual(0, 0)
                    residual(1, 1)
                    for t in range(2):
                        scale_rows("2", nx_s2, t, t)
                        residual(t + 2, t)
                    with dve.Fori(0, 2) as i:
                        for u in range(2):
                            gain("2", norm2_g, 2 * i + u, u)
                            scale_rows("2", nx_s2, 2 * i + u + 2, u)
                            residual(2 * i + u + 4, u)
                    for t in range(4, NX):
                        gain("2", norm2_g, t, t % 2)
                        if t + 2 < NX:
                            scale_rows("2", nx_s2, t + 2, t % 2)

                def mlp():
                    def square(i, n, u):
                        dve.wait_ge(up_relu, i + 1)
                        dve.tensor_tensor(h_t[u][:, n, :], h_t[u][:, n, :], h_t[u][:, n, :], ALU.mult).then_inc(up_sq, 1)

                    def squares(g, u):
                        for n in range(4):
                            square(4 * g + n, n, u)

                    def adds(g, u):
                        for t in range(NX):
                            for c in range(2):
                                dve.wait_ge(dn_mm, 16 * g + 2 * t + c + 1)
                                x = x_res[:, t, 512 * c:512 * (c + 1)]
                                dve.tensor_tensor(x, x, ps[:, 4 + (2 * t + c) % 4, :], ALU.add).then_inc(dn_add, 1)

                    squares(0, 0)
                    squares(1, 1)
                    adds(0, 0)
                    with dve.Fori(1, DIMS // 2) as i:
                        squares(2 * i, 0)
                        adds(2 * i - 1, 1)
                        squares(2 * i + 1, 1)
                        adds(2 * i, 0)
                    adds(DIMS - 1, 1)

                def last_norm(t, u):
                    mean_square("f", t)
                    dve.wait_ge(norm_sems["f"]["rs"], t + 1)
                    if not isinstance(t, int) or t >= 2:
                        dve.wait_ge(out_st[u], 8 * (t - u) if not isinstance(t, int) else 16 * (t // 2))
                    dve.scalar_tensor_tensor(out=out_s[u], in0=x_res[:, t, :], scalar=stat[:, 2, bass.ds(t, 1)], in1=final_g2,
                                             op0=ALU.mult, op1=ALU.mult).then_inc(out_ready, 1)

                setup()
                for t in range(2):
                    scale_rows("1", nx_s, t, t)
                with dve.Fori(0, NX // 2 - 1) as i:
                    for u in range(2):
                        gain("1", norm1_g, 2 * i + u, u)
                        scale_rows("1", nx_s, 2 * i + u + 2, u)
                for t in range(NX - 2, NX):
                    gain("1", norm1_g, t, t % 2)
                convolution()
                attention()
                mixers()
                output()
                mlp()
                dve.wait_ge(fg_ld, 16)
                pairs(dve, NX // 2, last_norm)

            @block.scalar
            def _(act):
                def squares(n, xs, t, u):
                    s = norm_sems[n]
                    if n == "1":
                        act.wait_ge(x_ld[u], 8 * (t - u) + 16 if not isinstance(t, int) else 16 * (t // 2) + 16)
                    elif n == "2":
                        act.wait_ge(x_add, t + 1)
                    else:
                        act.wait_ge(dn_add, 16 * (DIMS - 1) + 2 * t + 2)
                    if not isinstance(t, int) or t >= 2:
                        act.wait_ge(s["tr"] if n != "f" else s["ms"], t - 1)
                    act.activation(xs[u], x_res[:, t, :], ACT.Square, accum_out=stat[:, 0, bass.ds(t, 1)]).then_inc(s["sq"], 1)

                def gain(n, g, t, u):
                    s = norm_sems[n]
                    act.wait_ge(s["tr"], t + 1)
                    for k in range(4):
                        ins = act.activation(xn2_t[:, k, bass.ts(t, P)], ps[:, 2 * u, k * P:(k + 1) * P], ACT.Copy, scale=g[:, k:k + 1])
                    ins.then_inc(s["ev_act"], 1)

                def norm(n, xs, g):
                    for t in range(2):
                        squares(n, xs, t, t)
                    with act.Fori(0, NX // 2 - 1) as i:
                        for u in range(2):
                            gain(n, g, 2 * i + u, u)
                            squares(n, xs, 2 * i + u + 2, u)
                    for t in range(NX - 2, NX):
                        gain(n, g, t, t % 2)

                def projections():
                    for j in range(2):
                        act.wait_ge(cv_mm, 2 * j + 1)
                        act.activation(sig[j], ps_flat[:, 2048 * j:2048 * j + 1024], ACT.Sigmoid).then_inc(cv_sig, 1)
                    for j in range(2):
                        act.wait_ge(c_mm, j + 1)
                        act.activation(c2_t[:, j, :], ps_flat[:, 2048 * j:2048 * j + 1024], ACT.Copy).then_inc(c_ev, 1)
                    for t in range(NX):
                        act.wait_ge(v_mm, t + 1)
                        act.activation(v2_tm[:, t, :], ps[:, 2 + t % 2, 0:GW], ACT.Copy).then_inc(v_ev, 1)
                    for t in range(NX):
                        act.wait_ge(uv_mm, t + 1)
                        act.activation(uv_tm[:, t, 0:GW], ps[:, 6 + t % 2, 0:GW], ACT.Copy)
                        act.activation(uv_tm[:, t, GW:], ps[:, 6 + t % 2, GW:], ACT.Copy, accum_out=stat2[:, 0, t:t + 1]).then_inc(uv_ev, 1)
                    ch = ln_act
                    act.wait_ge(uv_ev, NX)
                    ch(act, act.activation(stat2[:, 1, :], stat2[:, 0, :], ACT.Copy, scale=-1.0 / GW))
                    for n, bank in enumerate((0, 4, 2, 6)):
                        act.wait_ge(qk_mm, n + 1)
                        dst = q2_t[:, n, :] if n < 2 else k2_t[:, n - 2, :]
                        act.activation(dst, ps_flat[:, 512 * bank:512 * bank + 1024], ACT.Copy, scale=32 ** -0.5 if n < 2 else 1.0).then_inc(qk_ev, 1)
                        if n < 2:
                            for t in range(4 * n, 4 * n + 4):
                                v = uv_tm[:, t, GW:]
                                ins = act.activation(v, v, ACT.Identity, bias=stat2[:, 1, t:t + 1])
                            ch(act, ins)
                        else:
                            for t in range(4 * n - 8, 4 * n - 4):
                                ins = act.activation(v_sq[:, t, :], uv_tm[:, t, GW:], ACT.Square, accum_out=stat2[:, 2, t:t + 1])
                            ch(act, ins)
                    act.activation(stat2[:, 3, :], stat2[:, 2, :], ACT.Identity, scale=1.0 / GW, bias=eps_col[:, :]).then_inc(ln_var, 1)

                def attention():
                    act.wait_ge(lam_sum, 1)
                    act.activation(lam_s[:, :], lam_s[:, :], ACT.Exp).then_inc(lam_e, 1)

                    def exps(s, u, h):
                        for m in range(2):
                            act.wait_ge(d_nm[m], s + 1)
                            if m == 0 and (not isinstance(s, int) or s >= 2):
                                act.wait_ge(d_t, s - 1)
                            act.activation(prob2[h % 2][m], ps_flat[:, 1024 * m:1024 * (m + 1)], ACT.Exp, bias=neg_max[:, u, 2 * h + m:2 * h + m + 1],
                                           accum_out=lsum[:, u, 2 * h + m:2 * h + m + 1]).then_inc(d_e[m], 1)

                    def evacuate(s, h):
                        act.wait_ge(d_t, s + 1)
                        act.activation(w_t[h % 2][:, 0:4, :], ps[:, 4, :].rearrange("p (n q) -> p n q", n=4), ACT.Copy).then_inc(d_t_act, 1)

                    def gains(b):
                        act.wait_ge(d_att, b + 1)
                        for j in range(2):
                            ins = act.activation(y_t[:, j, bass.ts(b, P)], ps[:, 7, j * P:(j + 1) * P], ACT.Copy, scale=sub_g[:, :])
                        ins.then_inc(d_y, 1)

                    def query_block(b, u):
                        for h in range(4):
                            s = 4 * b + h
                            if h < 3:
                                exps(s + 1, u, h + 1)
                            elif not isinstance(b, int) or b < NX - 1:
                                exps(s + 1, 1 - u, 0)
                            evacuate(s, h)
                            if h == 2 and (not isinstance(b, int) or b > 0):
                                gains(b - 1)

                    act.wait_ge(sub_ready, 1)
                    exps(0, 0, 0)
                    pairs_with_ends(act, NX // 2, query_block)
                    gains(NX - 1)

                def mixers():
                    act.wait_ge(cw_mm, 1)
                    for j in range(2):
                        ins = act.activation(chan_w[:, j], ps[:, 4 + j, 0:2 * P].rearrange("p (m e) -> p m e", m=2), ACT.Copy)
                    ins.then_inc(cw_ev, 1)
                    for j in range(2):
                        act.wait_ge(mu_x, j + 1)
                        act.activation(z_flat[:, j], dw_acc[:, j], ACT.Square).then_inc(mu_sq, 1)
                    for t in range(NX):
                        act.wait_ge(u_mm, t + 1)
                        act.activation(u_tm[:, t].rearrange("p j m e -> p (j m e)"), ps[:, 6 + t % 2, :], ACT.Copy).then_inc(u_ev, 1)
                    for j in range(2):
                        act.wait_ge(var_mm, j + 1)
                        act.activation(z_flat[:, j], ps_flat[:, 1024 * j:1024 * (j + 1)], ACT.Ln, bias=eps_col[:, :]).then_inc(var_ln, 1)
                    for j in range(2):
                        act.wait_ge(var_ln, j + 1)
                        act.activation(z_flat[:, j], z_flat[:, j], ACT.Exp, scale=-0.5).then_inc(var_rs, 1)
                    for j in range(2):
                        act.wait_ge(cn_z, j + 1)
                        act.activation(z_flat[:, j], dw_acc[:, j], ACT.Silu, scale=cln_g[:, j:j + 1], bias=cln_b[:, j:j + 1]).then_inc(cn_silu, 1)
                    for j in range(2):
                        act.wait_ge(dft_mm, j + 1)
                        act.activation(odd[j], ps[:, (5, 7)[j], :], ACT.Copy).then_inc(dft_odd, 1)
                    for n in range(4):
                        act.wait_ge(pw_mm, n + 1)
                        e, c = n // 2, n % 2
                        act.activation(dw_acc[:, e, 512 * c:512 * (c + 1)], ps[:, n, :], ACT.Identity, bias=pw_b[:, e:e + 1]).then_inc(pw_ev, 1)

                def mlp():
                    def relus(g, u):
                        for n in range(4):
                            act.wait_ge(up_mm, 4 * g + n + 1)
                            if n == 0 and (not isinstance(g, int) or g >= 2):
                                act.wait_ge(dn_mm, 16 * g - 16)
                            act.activation(h_t[u][:, n, :], ps_flat[:, 1024 * (n % 2):1024 * (n % 2 + 1)], ACT.Relu).then_inc(up_relu, 1)

                    pairs(act, DIMS // 2, relus)

                act.wait_ge(const2, CONST2_ALL)
                act.wait_ge(setup2, 1)
                norm("1", nx_s, norm1_g)
                projections()
                attention()
                mixers()
                norm("2", nx_s2, norm2_g)
                mlp()
                pairs(act, NX // 2, lambda t, u: squares("f", nx_s2, t, u))

            @block.gpsimd
            def _(pool):
                def root(n, t):
                    s = norm_sems[n]
                    pool.wait_ge(s["ms"], t + 1)
                    pool.tensor_tensor(stat[:, 2, bass.ds(t, 1)], stat[:, 1, bass.ds(t, 1)], minus_half[:, 0:1], ALU.pow).then_inc(s["rs"], 1)

                def spatial_norm():
                    ch = ln_pool
                    v = uv_tm[:, :, GW:]
                    pool.wait_ge(ln_var, 1)
                    for c in range(2):
                        ins = pool.tensor_tensor(stat2[:, 4, 4 * c:4 * c + 4], stat2[:, 3, 4 * c:4 * c + 4], minus_half[:, :], ALU.pow)
                    ch(pool, ins)
                    ch(pool, pool.tensor_tensor(v, v, stat2[:, 4, :].unsqueeze(2).to_broadcast([P, NX, GW]), ALU.mult))
                    ch(pool, pool.tensor_tensor(v, v, sgu_rows[:, 0:1, :].to_broadcast([P, NX, GW]), ALU.mult))
                    pool.tensor_tensor(v, v, sgu_rows[:, 1:2, :].to_broadcast([P, NX, GW]), ALU.add).then_inc(ln_v, 1)

                def attention():
                    def stage(b, u):
                        if not isinstance(b, int) or b >= 2:
                            pool.wait_ge(d_s[1], 4 * b - 4)
                        for r in range(4):
                            ins = pool.tensor_tensor(q2_st[u][:, r::4, :], q2_t[:, :, bass.ts(b, P)],
                                                     map_rows[:, r:r + 1].unsqueeze(2).to_broadcast([P, 2, P]), ALU.mult)
                        ins.then_inc(d_q, 1)

                    def root_heads(b, u):
                        pool.wait_ge(d_ms, b + 1)
                        pool.tensor_tensor(den[:, u, 3, :], den[:, u, 2, :], minus_half[:, :], ALU.pow).then_inc(d_rs, 1)

                    pool.wait_ge(qk_ev, 4)
                    stage(0, 0)
                    stage(1, 1)
                    spatial_norm()
                    with pool.Fori(1, NX // 2) as i:
                        for u in range(2):
                            root_heads(2 * i + u - 2, u)
                            stage(2 * i + u, u)
                    root_heads(NX - 2, 0)
                    root_heads(NX - 1, 1)

                def output():
                    def stage(t, u):
                        if not isinstance(t, int) or t >= 2:
                            pool.wait_ge(wo_mm, t - 1)
                        pool.tensor_copy(y_st[u], y_t[:, :, bass.ts(t, P)]).then_inc(y_rd, 1)

                    pool.wait_ge(sg_ev, 4)
                    pool.wait_ge(pw_ev, 4)
                    stage(0, 0)
                    stage(1, 1)
                    with pool.Fori(1, NX // 2) as i:
                        for u in range(2):
                            stage(2 * i + u, u)
                            root("2", 2 * i + u - 2)
                    root("2", NX - 2)
                    root("2", NX - 1)

                with pool.Fori(0, NX) as t:
                    root("1", t)
                attention()
                output()
                with pool.Fori(0, NX) as t:
                    root("f", t)

        def run_block(number, program):
            sems = []
            with nc.Block() as block:
                program(number, block, sems)
            nc.clear_and_free_semaphores(sems)
            nc.all_engine_barrier()

        for l in range(DEPTH):
            run_block(l, first_block_layer)
        run_block(DEPTH, second_block)


def kernel(**inputs):
    import concourse.bacc as bacc
    from concourse.bass_utils import run_bass_kernel_spmd

    nc = bacc.Bacc("TRN2", target_bir_lowering=False, num_devices=1)
    arrays = {f"in_{k}": v for k, v in host_layout(inputs).items()}
    access = {k[3:]: nc.dram_tensor(k, v.shape, mybir.dt.from_np(v.dtype), kind="ExternalInput").ap() for k, v in arrays.items()}
    out = nc.dram_tensor("out", (NX, P, D_MODEL), F32, kind="ExternalOutput").ap()
    build(nc, access, out)
    result = run_bass_kernel_spmd(nc, [arrays], core_ids=[0])
    return result.results[0]["out"].reshape(1, SEQ, D_MODEL)
```

```python
from contextlib import ExitStack

import numpy as np

import concourse.bass as bass
from concourse import mybir

F32 = mybir.dt.float32
BF16 = mybir.dt.bfloat16
F16 = mybir.dt.float16
F32R = mybir.dt.float32r
ACT = mybir.ActivationFunctionType
ALU = mybir.AluOpType
AX_X = mybir.AxisListType.X

P = 128
D_MODEL = 1024
KT = D_MODEL // P
SEQ, CTX = 1024, 256
NX, NC = SEQ // P, CTX // P
NTOK = SEQ + CTX
NTILE = NX + NC
DEPTH = 2
HEADS, KV, DH = 8, 2, 64
MH, MD = 4, 128
MW = MH * MD
CONV_K = 5
EPS = 1e-6
BIG = 1e30
WIN = 3 * P
KPAD = P + SEQ + P
NKEY = WIN + CTX
F_TILES = 18
N_GATE, N_K, N_Q, N_AZ, N_MQ, N_MK = 0, 1, 2, 6, 10, 14
CONV_LEN = SEQ + CTX + 8
ACC_LEN = CONV_LEN - 4
GW = D_MODEL // 4
DW_K = 31
D_FF = 4 * D_MODEL
FG = 2 * P
ALIBI_LEN = SEQ - P + SEQ
LAM_INIT = float(0.8 - 0.6 * np.exp(0.0))
SMALL = 3264
LN_KSCALE = float(-0.5 * np.log(MD))


class Chain:

    def __init__(self, sem):
        self.sem, self.base, self.n = sem, 0, 0

    def start(self, base):
        self.base, self.n = base, 0

    def __call__(self, eng, ins):
        ins.then_inc(self.sem, 1)
        self.n += 1
        eng.wait_ge(self.sem, self.base + self.n)


def host_constants():
    f = np.float32
    out = {"ident": np.eye(P, dtype=f)}
    rot = np.zeros((P, P), f)
    for b in range(0, P, 32):
        for j in range(16):
            rot[b + 16 + j, b + j] = -1.0
            rot[b + j, b + 16 + j] = 1.0
    out["rot"] = rot
    sel = np.zeros((36, 2 * MH, P), f)
    for d in range(2):
        for h in range(MH):
            sel[32 * d + h, d * MH + h] = 1.0
    out["sel"] = sel
    s, t = np.arange(P)[:, None], np.arange(P)[None, :]
    out["tri"] = np.stack([np.where(s <= t, 0.0, BIG), np.where(s >= t, 0.0, BIG)], 1).astype(f)
    half = DH // 2
    inv = (10000.0 ** (-np.arange(0, half, 2, dtype=f) / f(half))).astype(f)
    tok = np.arange(SEQ)
    ang = np.concatenate([np.tile((tok // 64).astype(f)[None] * inv[:, None], (2, 1)),
                          np.tile((tok % 64).astype(f)[None] * inv[:, None], (2, 1))], 0)
    ang = np.tile(ang.astype(f), (2, 1)).astype(np.float64)
    out["cos"], out["sin"] = np.cos(ang).astype(f), np.sin(ang).astype(f)
    q, k = np.arange(P)[:, None], np.arange(WIN)[None, :] - P
    band = np.abs(q - k) <= P
    mask = np.zeros((P, NX, WIN), f)
    for b in range(NX):
        kpos = b * P + k
        mask[:, b] = np.where(band & (kpos >= 0) & (kpos < SEQ), 0.0, -BIG)
    out["wmask"] = mask
    out["alibi"] = np.abs(np.arange(P)[:, None] - (np.arange(ALIBI_LEN)[None, :] - (SEQ - P))).astype(np.float16)
    slopes = 2.0 ** (-8.0 * (np.arange(4) + 1) / 4)
    out["slope"] = (-slopes[None, :, None] * np.eye(P)[:, None, :]).astype(np.float16)
    n = np.arange(SEQ)
    ang = 2 * np.pi * ((n[:, None] * n[None, :]) % SEQ) / SEQ
    half = SEQ // 2
    out["cos_s"] = np.cos(ang[:, 0:half + 1]).reshape(NX, P, half + 1).transpose(1, 0, 2).astype(f)
    out["sin_s"] = np.sin(ang[:, 1:half]).reshape(NX, P, half - 1).transpose(1, 0, 2).astype(f)
    c = np.arange(DH)
    ang = 2 * np.pi * ((c[:, None] * c[None, :]) % DH) / DH
    norm = (SEQ * DH) ** -0.5
    diag = np.eye(P // DH)
    out["dft_c"] = np.stack([np.kron(diag, np.cos(ang) * norm), np.kron(diag, -np.sin(ang) * norm)], 1).astype(f)
    out["mean64"] = np.kron(diag, np.full((DH, DH), 1.0 / DH)).astype(f)
    high, low = np.repeat([1, 1, 0, 0], 32), np.repeat([0, 0, 1, 1], 32)
    rows, four = np.arange(P)[:, None, None], np.arange(4)[None, :, None]
    copy = rows == 32 * four + np.arange(P)[None, None, :] % 32
    rep_q = np.stack([copy * high, copy * low], 2).astype(f)
    copy = rows[:, :, 0] % 32 == np.arange(P)[None, :] % 32
    high, low = np.repeat([1, 0, 1, 0], 32), np.repeat([0, 1, 0, 1], 32)
    out["rep"] = np.concatenate([rep_q, np.stack([copy * high, copy * low], 1).astype(f)[:, None]], 1)
    return out


def pairs(eng, n, body):
    for t in range(2):
        body(t, t)
    with eng.Fori(1, n) as i:
        for u in range(2):
            body(2 * i + u, u)


def host_layout(inputs):
    f = np.float32

    def rows(w):
        return w.reshape(w.shape[0] // P, P, w.shape[1]).transpose(1, 0, 2)

    def cols(v):
        v = v.reshape(v.shape[:-1] + (v.shape[-1] // P, P))
        return np.moveaxis(v, -1, 0)

    def spread(v):
        return np.broadcast_to(v[None], (P,) + v.shape)

    i = {k: np.asarray(v) for k, v in inputs.items()}
    o = dict(host_constants())
    o["wmask"] = (o["wmask"].view(np.uint32) >> 16).astype(np.uint16)
    o["xall"] = np.concatenate([i["x"][0], i["ctx"][0]], 0).reshape(NTILE, P, D_MODEL)
    o["cc"] = np.stack([cols(i["c"][0]), cols(i["c_ctx"])], 2)
    o["w_ada"] = np.stack([np.stack([rows(w[:, 512 * b:512 * b + 512]) for b in range(6)]) for w in i["w_ada"]])
    o["b_ada"] = cols(i["b_ada"])
    o["norm_g"], o["conv_b"], o["head_g"] = cols(i["norm_g"]), cols(i["conv_b"]), cols(i["head_g"])
    o["conv_w"] = cols(i["conv_w"]).transpose(0, 1, 3, 2)
    gate = np.zeros((36, DEPTH, 2), f)
    for d in range(2):
        for n in range(2):
            at = 2 * MH * n + MH * d
            gate[32 * d:32 * d + MH, :, n] = i["gate_b"][:, at:at + MH].T
    o["gate_b"] = gate
    o["sink"], o["final_g"] = spread(i["sink"]), spread(i["final_g"])
    cut = np.cumsum((HEADS * DH, KV * DH, KV * DH, HEADS * DH, MW, MW, MW, MW, MW, 2 * MH, 2 * MH))
    w_tm, w_v, w_ft = [], [], []
    for w in i["w_in"]:
        aq, ak, av, az, mq, mk, mv, mo, mz, mi, mf, _ = np.split(w, cut, 1)
        w_tm.append(np.stack([rows(m) for m in (mv, mz, mo)]))
        w_v.append(rows(av))
        gates = np.zeros((D_MODEL, P), f)
        for n, m in enumerate((mi, mf)):
            for d in range(2):
                gates[:, 64 * n + 32 * d:64 * n + 32 * d + MH] = m[:, MH * d:MH * (d + 1)]
        q = [np.concatenate([aq[:, DH * j:DH * (j + 1)], aq[:, DH * (j + 4):DH * (j + 5)]], 1) for j in range(4)]
        w_ft.append(np.stack([rows(m) for m in [gates, ak] + q + sum([np.split(m, 4, 1) for m in (az, mq, mk)], [])]))
    o["w_tm"], o["w_v"], o["w_ft"] = np.stack(w_tm), np.stack(w_v), np.stack(w_ft)
    o["w_out"] = np.stack([rows(w) for w in i["w_out"]])
    two = {k[:-2]: v[0] for k, v in i.items() if k.endswith("_2") and k != "final_g_2"}
    w = two["w_in"]
    hq, hk, hv, ha, hg, hc, hu, hvv = np.split(w, 8, 1)
    blocks = (np.concatenate([hg[:, 0:P], ha[:, 0:P], hg[:, P:], ha[:, P:]], 1), np.concatenate([hc, hv], 1),
              np.concatenate([hu, hvv], 1), np.concatenate([hq, hk], 1))
    o["w_in2"] = np.stack([rows(b) for b in blocks])
    o["w_out2"] = np.stack([rows(b) for b in np.split(two["w_out"], 2, 1)])
    o["w_up"] = np.stack([rows(b) for b in np.split(two["w_up"], D_FF // FG, 1)])
    o["w_down"] = np.stack([rows(b) for b in np.split(two["w_down"], D_FF // FG, 0)])
    o["lam"] = spread(np.stack([two[n] for n in ("lam_q1", "lam_k1", "lam_q2", "lam_k2")]))
    o["subln_g"] = np.tile(two["subln_g"], 2)[:, None]
    o["norm1_g"], o["norm2_g"], o["final_g2"] = cols(two["norm1_g"]), cols(two["norm2_g"]), spread(i["final_g_2"])
    o["dw_w"] = cols(two["conv_dw_w"]).transpose(0, 2, 1)
    for name, src in (("dw_b", "conv_dw_b"), ("cln_g", "conv_ln_g"), ("cln_b", "conv_ln_b"), ("pw_b", "conv_pw_b"), ("fnet_b", "fnet_b")):
        o[name] = cols(two[src])
    o["pw_w"] = rows(two["conv_pw_w"])
    fw = np.zeros((P, 2, P), f)
    for g in range(4):
        at = DH * (g % 2)
        fw[at:at + DH, g // 2, at:at + DH] = two["fnet_w"][g]
    o["fnet_w"] = fw
    o["sgu_rows"] = spread(np.stack([two["sgu_ln_g"], two["sgu_ln_b"]]))
    o["sgu_w"] = two["sgu_w"].transpose(2, 0, 1)
    o["sgu_b"] = two["sgu_b"].T
    return {k: np.ascontiguousarray(v) for k, v in o.items()}




def build(nc, A, out):
    with ExitStack() as ctx:
        def sb(name, shape, dt=F32):
            return ctx.enter_context(nc.sbuf_tensor(f"{name}_sb", shape, dt))

        ident = sb("ident", [P, P])
        rot = sb("rot", [P, P])
        small = sb("small", [P, SMALL])
        sel = small[0:36, 0:1024].rearrange("p (n m) -> p n m", n=2 * MH)
        tri = sb("tri", [P, 2, P])
        ident_bf = sb("ident_bf", [P, P], BF16)
        cc = sb("cc", [P, KT, 2])
        scc = sb("scc", [P, KT, 2])
        b_ada = sb("b_ada", [P, DEPTH, 3 * KT])
        mod = sb("mod", [P, 2, 3 * KT])
        norm_g = sb("norm_g", [P, DEPTH, KT])
        mod_scale = sb("mod_scale", [P, 2, KT])
        ones = small[:, 1024 + 3 * NTILE * 36:][:, 0:P]
        conv_w = sb("conv_w", [P, DEPTH, KT, CONV_K])
        conv_b = sb("conv_b", [P, DEPTH, KT])
        gate_b = sb("gate_b", [36, DEPTH, 2])
        head_g = sb("head_g", [P, DEPTH, MH])
        sink = sb("sink", [P, DEPTH, HEADS])
        neg_sink = sb("neg_sink", [P, DEPTH, HEADS])
        minus_half = sb("minus_half", [P, MH])
        k_scale = sb("k_scale", [P, 1])
        stat = sb("stat", [P, 4, 8])
        cols = small[:, 1024:1024 + 3 * NTILE * 36].rearrange("p (n t r) -> p n t r", n=3, t=NTILE)
        decay_b = sb("decay_b", [P, 2 * MH, NTILE])
        m_state = sb("m_state", [36, 16])
        m_dec = sb("m_dec", [36, NTILE])
        lsum = sb("lsum", [P, 2, HEADS])
        neg_max = sb("neg_max", [P, 2, HEADS])
        row_max = sb("row_max", [P, 2, HEADS])
        sink_e = sb("sink_e", [P, 2, HEADS])
        recip = sb("recip", [P, 2, HEADS])
        den = sb("den", [P, 2, 4, MH])

        ARENA = 47700
        arena = sb("arena", [P, ARENA])
        arena_at = nc.sbuf_base - 4 * ARENA
        XN, QKV, MV, MQK, G, S, WFT = 0, 10240, 19968, 25136, 35376, 41776, 45652

        def shaped(v, shape):
            if len(shape) == 1:
                return v
            names = "abcde"[:len(shape)]
            return v.rearrange(f"p ({' '.join(names)}) -> p {' '.join(names)}",
                               **{c: s for c, s in zip(names[1:], shape[1:])})

        def part(at, *shape):
            n = int(np.prod(shape))
            assert at + n <= ARENA, (at, shape)
            return shaped(arena[:, at:at + n], shape)

        def rounded(name, at, *shape):
            n = int(np.prod(shape))
            assert at + n <= ARENA, (at, shape)
            return shaped(nc.alloc_sbuf_tensor_at(f"{name}_sb", [P, n], F32R, offset=arena_at + 4 * at)[:, :], shape)

        xn_t = part(XN, KT, NTILE, P)
        xn_flat = part(XN, KT, NTOK)
        att_t = part(XN, 4, NTILE, P)
        h_dir = [part(XN + 5120, NTILE, MW), part(QKV, NTILE, MW)]
        q_t = part(QKV, 4, NTILE, P)
        q_flat = part(QKV, 4, NTOK)
        kz = part(QKV + 5120, KV, KPAD + CTX)
        v_tm = part(QKV + 8192, NTILE + 2, P)
        mv_tm = part(MV, NTILE, MH, MD + 1)
        mqk_t = part(MQK, 2 * MH, NTILE, P)
        mqk_flat = part(MQK, 2 * MH, NTOK)
        ada_w = [part(XN + 4096 * u, KT, 512) for u in range(2)]
        gate_diag = part(XN + 5120, 2, KT, P)
        w_mv, w_mz, w_mo = part(MQK, KT, 512), part(MQK + 4096, KT, 512), part(QKV, KT, 512)
        w_v = part(QKV + 4096, KT, P)
        xt = [part(G + 1024 * u, D_MODEL) for u in range(2)]
        xs = [part(G + 2048 + 1024 * u, D_MODEL) for u in range(2)]
        xst = [part(G + 4096 + 1024 * u, KT, P) for u in range(2)]
        junk = [part(G + 6144 + 3072 * u, D_MODEL) for u in range(2)]
        z_st = [part(G + 7168 + 512 * u, MW) for u in range(2)]
        o_st = [part(G + 8192 + 512 * u, MW) for u in range(2)]
        w_ft = [part(WFT + 1024 * u, KT, P) for u in range(2)]
        cst = [part(S + 1292 * u, 1292) for u in range(2)]
        acc = part(S + 2584, 1292)
        cos_t, sin_t = part(MQK, SEQ), part(MQK + 1024, SEQ)
        rope_a = [part(MQK + 2048 + 1024 * u, SEQ) for u in range(2)]
        rope_b = [part(MQK + 4096 + 1024 * u, SEQ) for u in range(2)]
        row_a, row_b, row_m, row_w, row_i = [arena[0:36, G + NTOK * n:G + NTOK * (n + 1)] for n in range(5)]
        prob = [part(XN + 5120 + NKEY * u, NKEY) for u in range(2)]
        prob_t = [part(XN + 6400 + NKEY * u, NKEY // P, P) for u in range(2)]
        q_st = [part(XN + 7680 + 512 * u, 4, P) for u in range(2)]
        az_st = [part(XN + 8704 + 512 * u, 4, P) for u in range(2)]
        att_tm = part(S, HEADS, DH)
        wmask = part(S + 512, NX * WIN // 2).bitcast(BF16).rearrange("p (b k) -> p b k", b=NX)
        c_state = part(QKV + 5120, 2 * MH, MD + 1)
        qk_st = [part(QKV + 6152 + 1024 * d, 2 * MH, P) for d in range(2)]
        dec_y = [part(QKV + 8200 + 512 * d, MH, P) for d in range(2)]
        p_t = [part(S + 512 * d, MH, P) for d in range(2)]
        q_w = [part(S + 1024 + 512 * d, MH, P) for d in range(2)]
        k_w = [part(S + 2048 + 512 * d, MH, P) for d in range(2)]
        w_out = part(MQK, KT, D_MODEL)
        mix_st = [part(MV + 1024 * u, KT, P) for u in range(2)]
        x_new = [part(MV + 2048 + 1024 * u, D_MODEL) for u in range(2)]
        gated = part(MV + 4096, D_MODEL)
        x_in = [part(G + 1024 * u, D_MODEL) for u in range(2)]
        o_in = [part(G + 2048 + 512 * u, MW) for u in range(2)]
        z_in = [part(G + 3072 + 512 * u, MW) for u in range(2)]
        h_sum = [part(G + 4096 + 512 * u, MW) for u in range(2)]
        h_g = [part(G + 5120 + 512 * u, MW) for u in range(2)]
        gate, gate_c, final_g = part(WFT, D_MODEL), part(WFT + 1024, D_MODEL), part(WFT + 1024, D_MODEL)
        sq_junk = part(S, D_MODEL)
        sq_last = part(S + 2560, D_MODEL)
        h_n = part(S + 1024, MW)
        h_z = [part(S + 1536 + 512 * u, MW) for u in range(2)]

        ps = ctx.enter_context(nc.psum_tensor("ps", [P, 8, 512], F32))
        ps_flat = ps[:, :, :].rearrange("p b n -> p (b n)")

        X2, XNT, YT, W2, M2 = 0, 8192, 16384, 24576, 32768
        x_res = part(X2, NX, D_MODEL)
        xn2_t = part(XNT, KT, SEQ)
        y_t = part(YT, KT, SEQ)
        nx_s = [part(YT + 1024 * u, D_MODEL) for u in range(2)]
        w_in2 = [part(W2 + 4096 * u, KT, 512) for u in range(2)]
        q2_t, k2_t = part(M2, 2, SEQ), part(M2 + 2048, 2, SEQ)
        v2_tm = part(M2 + 4096, NX, GW)
        z_pad = part(M2 + 6144, 2, SEQ + DW_K - 1)
        z_flat = part(M2 + 6144, 2, SEQ)
        c2_t = part(M2 + 8256, 2, SEQ)
        uv_tm = part(M2 + 10304, NX, 2 * GW)
        o_tm, o_sq = part(M2 + 14400, GW), part(M2 + 14656, GW)
        dw_acc = y_t[:, 2:4, :]
        sig = [part(YT + 4096 + 1024 * u, SEQ) for u in range(2)]
        v_sq = part(W2, NX, GW)
        prob2 = [[part(W2 + 2048 * u + 1024 * m, SEQ) for m in range(2)] for u in range(2)]
        w_t = [part(W2 + 4096 + 1024 * u, NX, P) for u in range(2)]
        q2_st = [rounded(f"q2_st{u}", W2 + 6144 + 1024 * u, 8, P) for u in range(2)]
        qk_hi = [rounded("q_hi", YT + 6144, 2, SEQ), rounded("k_hi", W2 + 2048, 2, SEQ)]
        qk_lo = [rounded("q_lo", M2, 2, SEQ), rounded("k_lo", M2 + 2048, 2, SEQ)]
        k2_st = rounded("k2_st", XNT, 8, SEQ)
        rep_raw = part(YT + 4096, 5, 2, P)
        rep = rounded("rep", YT + 4096, 5, 2, P)
        rep_q, rep_k = rep[:, 0:4], rep[:, 4]
        HALF = SEQ // 2
        cos_s = arena[:, XNT:XNT + KT * (HALF + 1)].rearrange("p (k n) -> p k n", k=KT)
        sin_s = arena[:, XNT + KT * (HALF + 1):XNT + 8192].rearrange("p (k n) -> p k n", k=KT)
        u_tm = part(M2, NX, 2, 2, P)
        odd = [part(M2 + 6144 + 512 * j, HALF) for j in range(2)]
        w_out2 = part(W2, 2, KT, 512)
        y_st = [part(M2 + 8192 + 1024 * u, KT, P) for u in range(2)]
        nx_s2 = [part(M2 + 12288 + 1024 * u, D_MODEL) for u in range(2)]
        xn2_raw = y_t
        xn2_hi = [rounded(f"xn2_hi{n}", XNT + 4096 * n, 4, SEQ) for n in range(2)]
        xn2_lo = [rounded(f"xn2_lo{n}", YT + 4096 * n, 4, SEQ) for n in range(2)]
        w_up = [part(M2 + 4096 * u, KT, FG) for u in range(2)]
        w_up_hi = [rounded(f"w_up_hi{u}", M2 + 4096 * u + 2048, KT, FG) for u in range(2)]
        w_up_lo = [rounded(f"w_up_lo{u}", M2 + 4096 * u, KT, FG) for u in range(2)]
        w_down, w_down_hi = part(W2, FG // P, D_MODEL), rounded("w_down_hi", W2 + 2048, FG // P, D_MODEL)
        w_down_lo = rounded("w_down_lo", W2, FG // P, D_MODEL)
        h_at = (W2 + 4096, M2 + 8192)
        h_raw = [part(at, FG // P, SEQ) for at in h_at]
        h_hi = [rounded(f"h_hi{u}", at + 2048, FG // P, SEQ) for u, at in enumerate(h_at)]
        h_lo = [rounded(f"h_lo{u}", at, FG // P, SEQ) for u, at in enumerate(h_at)]
        final_g2 = part(YT + 4096, D_MODEL)
        out_s = [part(YT + 5120 + 1024 * u, D_MODEL) for u in range(2)]
        alibi = sb("alibi", [P, ALIBI_LEN], F16)
        stat2 = sb("stat2", [P, 6, 8])
        eps_col = sb("eps_col", [P, 1])
        neg_lam = sb("neg_lam", [P, 1])
        lam_s = sb("lam_s", [P, 2])
        sub_g = sb("sub_g", [P, 1])
        at2 = 0

        def small_part(*shape):
            nonlocal at2
            n = int(np.prod(shape))
            at2 += n
            assert at2 <= SMALL, at2
            v = small[:, at2 - n:at2]
            return v if len(shape) == 1 else v.rearrange(
                f"p ({' '.join('abc'[:len(shape)])}) -> p {' '.join('abc'[:len(shape)])}",
                **{c: s for c, s in zip("bc", shape[1:])})

        slope = small_part(4 * P // 2).bitcast(F16).rearrange("p (h q) -> p h q", h=4)
        pw_w, fnet_w, dft_c = small_part(2, GW), small_part(2, P), small_part(2, P)
        chan_w = small_part(2, 2, P)
        sgu_rows, sgu_w = small_part(2, GW), small_part(4, P)
        lam_in, lam_p = small_part(4, 32), small_part(2, 32)
        dw_w, dw_b = small_part(2, DW_K), small_part(2)
        cln_g, cln_b, pw_b, fnet_b = [small_part(2) for _ in range(4)]
        subln_g, norm1_g, norm2_g, sgu_b = small_part(1), small_part(KT), small_part(KT), small_part(4)
        mean64 = small_part(P)

        def dram(name, shape):
            return nc.dram_tensor(f"{name}_dram", shape, F32).ap()

        z_dram = [dram(f"z_{l}", [NTILE, P, MW]) for l in range(DEPTH)]
        o_dram = [dram(f"o_{l}", [NTILE, P, MW]) for l in range(DEPTH)]
        az_dram = [dram(f"az_{l}", [4, P, NTILE, P]) for l in range(DEPTH)]
        x_dram = [A["xall"]] + [dram(f"x_{l + 1}", [NTILE, P, D_MODEL]) for l in range(DEPTH)]

        def layer_tiles(l):
            return NTILE if l < DEPTH - 1 else NX

        def first_block_layer(l, block, sems):

            def sem(name):
                sems.append(nc.alloc_semaphore(name=f"{name}_{l}"))
                return sems[-1]

            def sem_per_layer(name):
                return {l: sem(name)}

            def sem_per_slot(name):
                return {l: [sem(f"{name}{u}") for u in range(2)]}

            const_ld = sem("const_ld")
            CONSTS = [(ident[:, :], "ident"), (rot[:, :], "rot"), (sel[:, :, :], "sel"), (tri[:, :, :], "tri"),
                      (cc[:, :, :], "cc"), (b_ada[:, :, :], "b_ada"), (norm_g[:, :, :], "norm_g"),
                      (conv_w[:, :, :, :], "conv_w"), (conv_b[:, :, :], "conv_b"), (gate_b[:, :, :], "gate_b"),
                      (head_g[:, :, :], "head_g"), (sink[:, :, :], "sink")]
            CONST_ALL = 16 * len(CONSTS)
            setup_dve = sem("setup_dve")
            ada_ld, ada_use = [sem(f"ada_ld{u}") for u in range(2)], sem("ada_use")
            silu_c, mod_sum, ada_done = sem("silu_c"), sem("mod_sum"), sem("ada_done")
            gt_diag, gt_mm, gt_ev = sem("gt_diag"), sem("gt_mm"), sem("gt_ev")
            nt_w = {l: [sem(f"nt_w{n}") for n in range(4)]}
            nt_ld = sem_per_slot("nt_ld")
            nt_sq, nt_ms, nt_rs, nt_xs, nt_tr = [sem_per_layer(n) for n in ("nt_sq", "nt_ms", "nt_rs", "nt_xs", "nt_tr")]
            nt_ev_act, nt_ev_dve, nt_cp = [sem_per_layer(n) for n in ("nt_ev_act", "nt_ev_dve", "nt_cp")]
            nt_mv, nt_mz, nt_mo, nt_v = [sem_per_layer(n) for n in ("nt_mv", "nt_mz", "nt_mo", "nt_v")]
            nt_mv_ev, nt_mz_ev, nt_mo_ev, nt_v_ev = [sem_per_layer(n) for n in ("nt_mv_ev", "nt_mz_ev", "nt_mo_ev", "nt_v_ev")]
            nt_z_st, nt_o_st = sem_per_slot("nt_z_st"), sem_per_slot("nt_o_st")
            pads = sem_per_layer("pads")
            ft_w = sem_per_slot("ft_w")
            ft_trig, ft_mm, ft_ev, ft_rot, ft_rope_a, ft_rope, ft_conv, ft_silu = [sem_per_layer(n) for n in (
                "ft_trig", "ft_mm", "ft_ev", "ft_rot", "ft_rope_a", "ft_rope", "ft_conv", "ft_silu")]
            ft_rotfree = sem_per_layer("ft_rotfree")
            ft_az_st = sem_per_slot("ft_az_st")
            ft_chain = {l: Chain(sem("ft_chain"))}
            g_abs, g_ln, g_rows, g_exp, g_tr, g_cols = [sem_per_layer(n) for n in (
                "g_abs", "g_ln", "g_rows", "g_exp", "g_tr", "g_cols")]
            g_chain = {l: Chain(sem("g_chain"))}
            g_act_chain = {l: Chain(sem("g_act_chain"))}
            a_mask = sem_per_layer("a_mask")
            a_az = sem_per_slot("a_az")
            a_q, a_s, a_nm, a_e, a_t, a_t_act, a_t_dve, a_pv = [sem_per_layer(n) for n in (
                "a_q", "a_s", "a_nm", "a_e", "a_t", "a_t_act", "a_t_dve", "a_pv")]
            a_sink, a_sink_e, a_att, a_att_tr, a_out = [sem_per_layer(n) for n in (
                "a_sink", "a_sink_e", "a_att", "a_att_tr", "a_out")]
            a_chain, a_fin = {l: Chain(sem("a_chain"))}, {l: Chain(sem("a_fin"))}
            m_st, m_s, m_k, m_m, m_w, m_y, m_d, m_kw, m_qs, m_p, m_num, m_del, m_c, m_h, m_init = [sem_per_layer(n) for n in (
                "m_st", "m_s", "m_k", "m_m", "m_w", "m_y", "m_d", "m_kw", "m_qs", "m_p", "m_num", "m_del", "m_c", "m_h", "m_init")]
            m_chain = {l: Chain(sem("m_chain"))}
            p_w, p_fg = sem_per_layer("p_w"), sem_per_layer("p_fg")
            p_x, p_o, p_z, p_store = [sem_per_slot(n) for n in ("p_x", "p_o", "p_z", "p_store")]
            p_sig, p_sum, p_hg, p_sq, p_ms, p_rs, p_hn, p_hz, p_tr, p_ev, p_att, p_mm, p_gated, p_new = [sem_per_layer(n) for n in (
                "p_sig", "p_sum", "p_hg", "p_sq", "p_ms", "p_rs", "p_hn", "p_hz", "p_tr", "p_ev", "p_att", "p_mm", "p_gated", "p_new")]
            f_sq, f_ms, f_rs, f_x = sem("f_sq"), sem("f_ms"), sem("f_rs"), sem("f_x")

            def query_blocks(eng, body):
                nt = layer_tiles(l)
                for b in range(2):
                    body(b, b, WIN, WIN)
                with eng.Fori(1, NX // 2 - 1) as i:
                    for u in range(2):
                        body(2 * i + u, u, WIN, WIN)
                for b in range(NX - 2, nt):
                    body(b, b % 2, WIN if b < NX else 0, None if b == nt - 1 else WIN if b + 1 < NX else 0)

            def mlstm_steps(eng, step, ctx_outputs):
                for j in range(NC):
                    step(j, (NX + j, NTILE - 1 - j), ctx_outputs, NX + j + 1 if j < NC - 1 else 0, ctx_outputs or j == NC - 1)
                step(NC, (0, NX - 1), True, 1, True)
                with eng.Fori(1, NX - 1) as i:
                    step(i + NC, (i, i * -1 + (NX - 1)), True, i + 1, True)
                step(NC + NX - 1, (NX - 1, 0), True, None, False)

            @block.sync
            def _(sp):
                if l == 0:
                    for view, name in CONSTS:
                        sp.dma_start(view, A[name]).then_inc(const_ld, 16)

                def modulation():
                    for n in range(6):
                        if n >= 2:
                            sp.wait_ge(ada_use, n - 1)
                        sp.dma_start(ada_w[n % 2], A["w_ada"][l, n]).then_inc(ada_ld[n % 2], 16)

                def norm_tm(l):
                    sp.dma_start(w_mv, A["w_tm"][l, 0]).then_inc(nt_w[l][0], 16)
                    sp.dma_start(w_mz, A["w_tm"][l, 1]).then_inc(nt_w[l][1], 16)
                    sp.dma_start(w_mo, A["w_tm"][l, 2]).then_inc(nt_w[l][2], 16)
                    sp.dma_start(w_v, A["w_v"][l]).then_inc(nt_w[l][3], 16)

                    for u in range(2):
                        sp.dma_start(w_ft[u], A["w_ft"][l, u]).then_inc(ft_w[l][u], 16)

                    def load_x(t, u):
                        sp.dma_start(xt[u], x_dram[l][t]).then_inc(nt_ld[l][u], 16)

                    def store(t, u):
                        sp.wait_ge(nt_mz_ev[l], t + 1)
                        sp.dma_start(z_dram[l][t], z_st[u]).then_inc(nt_z_st[l][u], 16)
                        sp.wait_ge(nt_mo_ev[l], t + 1)
                        sp.dma_start(o_dram[l][t], o_st[u]).then_inc(nt_o_st[l][u], 16)

                    for u in range(2):
                        load_x(u, u)
                    with sp.Fori(0, NX // 2) as i:
                        for u in range(2):
                            sp.wait_ge(nt_xs[l], 2 * i + u + 1)
                            load_x(2 * i + u + 2, u)
                            store(2 * i + u, u)
                    if l < DEPTH - 1:
                        for t in range(NX, NTILE):
                            store(t, t % 2)

                def ft(l):
                    sp.wait_ge(nt_mv[l], NTILE)
                    sp.dma_start(cos_t, A["cos"]).then_inc(ft_trig[l], 16)
                    sp.dma_start(sin_t, A["sin"]).then_inc(ft_trig[l], 16)
                    with sp.Fori(1, F_TILES // 2) as i:
                        for u in range(2):
                            sp.wait_ge(ft_mm[l], 2 * i + u - 1)
                            sp.dma_start(w_ft[u], A["w_ft"][l, 2 * i + u]).then_inc(ft_w[l][u], 16)

                def attention(l):
                    sp.wait_ge(ft_silu[l], 8)
                    sp.dma_start(wmask, A["wmask"].bitcast(BF16)).then_inc(a_mask[l], 16)
                    for u in range(2):
                        sp.wait_ge(ft_az_st[l][u], 16 * 2)

                    def load_az(b, u):
                        sp.dma_start(az_st[u], az_dram[l][:, :, b, :].rearrange("j p n -> p j n")).then_inc(a_az[l][u], 16)

                    load_az(0, 0)
                    load_az(1, 1)
                    with sp.Fori(0, NX // 2 - 1) as i:
                        for u in range(2):
                            sp.wait_ge(a_out[l], 2 * i + u + 1)
                            load_az(2 * i + u + 2, u)
                    if l < DEPTH - 1:
                        for t in range(NX, NTILE):
                            sp.wait_ge(a_out[l], t - 1)
                            load_az(t, t % 2)

                def output(l):
                    nt = layer_tiles(l)
                    sp.wait_ge(m_st[l], 2 * NTILE)
                    sp.dma_start(w_out, A["w_out"][l]).then_inc(p_w[l], 16)
                    if l == DEPTH - 1:
                        sp.dma_start(final_g, A["final_g"]).then_inc(p_fg[l], 16)
                    sp.wait_ge(m_h[l], 2 * nt)
                    sp.wait_ge(m_del[l], 2 * NTILE)
                    sp.wait_ge(m_w[l], 2 * nt)
                    for s in (nt_z_st, nt_o_st):
                        for u in range(2):
                            sp.wait_ge(s[l][u], 16 * (nt // 2))

                    def load(t, u):
                        sp.dma_start(o_in[u], o_dram[l][t]).then_inc(p_o[l][u], 16)
                        sp.dma_start(z_in[u], z_dram[l][t]).then_inc(p_z[l][u], 16)

                    def load_x(t, u):
                        sp.dma_start(x_in[u], x_dram[l][t]).then_inc(p_x[l][u], 16)

                    def store(t, u):
                        sp.wait_ge(p_new[l], t + 1) if l == 0 else sp.wait_ge(f_x, t + 1)
                        sp.dma_start(x_dram[l + 1][t], x_new[u]).then_inc(p_store[l][u], 16)

                    def next_loads(t, u):
                        sp.wait_ge(p_hz[l], t + 1)
                        load(t + 2, u)

                    for t in range(2):
                        load(t, t)
                        load_x(t, t)
                    with sp.Fori(0, NX // 2 - 1) as i:
                        for u in range(2):
                            next_loads(2 * i + u, u)
                            store(2 * i + u, u)
                            load_x(2 * i + u + 2, u)
                    for t in range(NX - 2, nt):
                        if t + 2 < nt:
                            next_loads(t, t % 2)
                        store(t, t % 2)
                        if t + 2 < nt:
                            load_x(t + 2, t % 2)
                    for u in range(2):
                        sp.wait_ge(p_store[l][u], 16 * (nt // 2))

                modulation()
                norm_tm(l)
                ft(l)
                attention(l)
                output(l)

            @block.tensor
            def _(pe):
                def modulation():
                    if l == 0:
                        pe.wait_ge(silu_c, 1)
                        pe.wait_ge(const_ld, CONST_ALL)
                    for n in range(6):
                        pe.wait_ge(ada_ld[n % 2], 16 * (n // 2 + 1))
                        for f in range(4):
                            at = 2 * (4 * n + f)
                            for k in range(KT):
                                mm = pe.matmul(ps[:, 0, at:at + 2], ada_w[n % 2][:, k, f * P:(f + 1) * P], scc[:, k, :],
                                               start=k == 0, stop=k == KT - 1)
                        mm.then_inc(ada_use, 1)

                def spread_gates(l):
                    pe.wait_ge(gt_diag, 1)
                    for v in range(2 if l < DEPTH - 1 else 1):
                        for k in range(KT):
                            mm = pe.matmul(ps[:, 4 + 2 * v + k // 4, (k % 4) * P:(k % 4 + 1) * P], ones[:, :], gate_diag[:, v, k, :],
                                           start=True, stop=True)
                    mm.then_inc(gt_mm, 1)

                def norm_tm(l):
                    def turn(t, u):
                        pe.wait_ge(nt_xs[l], t + 1)
                        for k in range(KT):
                            mm = pe.transpose(ps[:, 2 * u + k // 4, (k % 4) * P:(k % 4 + 1) * P],
                                              xs[u][:, k * P:(k + 1) * P], ident[:, :])
                        mm.then_inc(nt_tr[l], 1)

                    def products(t, u, gates=True):
                        pe.wait_ge(nt_ev_act[l], t + 1)
                        pe.wait_ge(nt_ev_dve[l], t + 1)
                        for n, w, width, done, free in ((0, w_mv, 512, nt_mv, nt_mv_ev), (1, w_mz, 512, nt_mz, nt_mz_ev),
                                                        (2, w_mo, 512, nt_mo, nt_mo_ev), (3, w_v, P, nt_v, nt_v_ev)):
                            if n in (1, 2) and not gates:
                                continue
                            pe.wait_ge(nt_w[l][n], 16)
                            if not isinstance(t, int) or t > 0:
                                pe.wait_ge(free[l], t)
                            for k in range(KT):
                                mm = pe.matmul(ps[:, 4 + n, 0:width], xst[u][:, k, :], w[:, k, :],
                                               start=k == 0, stop=k == KT - 1)
                            mm.then_inc(done[l], 1)

                    pe.wait_ge(ada_done, 1)
                    turn(0, 0)
                    turn(1, 1)
                    products(0, 0)
                    turn(2, 0)
                    products(1, 1)
                    with pe.Fori(1, NX // 2) as i:
                        turn(2 * i + 1, 1)
                        products(2 * i, 0)
                        turn(2 * i + 2, 0)
                        products(2 * i + 1, 1)
                    turn(9, 1)
                    products(8, 0, l < DEPTH - 1)
                    products(9, 1, l < DEPTH - 1)

                def ft(l):
                    nt = layer_tiles(l)
                    for s, n in ((nt_ev_act, NTILE), (nt_ev_dve, NTILE), (nt_mv_ev, NTILE), (nt_mz_ev, nt), (nt_mo_ev, nt), (nt_v_ev, NTILE)):
                        pe.wait_ge(s[l], n)
                    pe.wait_ge(nt_cp[l], NTILE)

                    def tile(n, i, u, ntok):
                        pe.wait_ge(ft_w[l][u], 16 * i + 16)
                        if not isinstance(n, int) or n >= 2:
                            pe.wait_ge(ft_ev[l], n - 1)
                        for c, at in enumerate(range(0, ntok, 512)):
                            size = min(512, ntok - at)
                            for k in range(KT):
                                mm = pe.matmul(ps[:, 3 * u + c, 0:size], w_ft[u][:, k, :], xn_flat[:, k, at:at + size],
                                               start=k == 0, stop=k == KT - 1)
                        mm.then_inc(ft_mm[l], 1)

                    def rotate(r, n, u):
                        pe.wait_ge(ft_ev[l], n + 1)
                        if not isinstance(r, int) or r > 0:
                            pe.wait_ge(ft_rotfree[l], r)
                        for c in range(2):
                            mm = pe.matmul(ps[:, 6 + c, :], rot[:, :], cst[u][:, 512 * c:512 * c + 512], start=True, stop=True)
                        mm.then_inc(ft_rot[l], 1)

                    tile(N_GATE, 0, 0, NTOK)
                    tile(N_K, 0, 1, NTOK)
                    rotate(0, N_K, 1)
                    with pe.Fori(0, 2) as j:
                        for u in range(2):
                            tile(N_Q + 2 * j + u, j + N_Q // 2, u, nt * P)
                        for u in range(2):
                            rotate(2 * j + u + 1, N_Q + 2 * j + u, u)
                    with pe.Fori(N_AZ // 2, N_MK // 2) as j:
                        for u in range(2):
                            tile(2 * j + u, j, u, nt * P)
                    with pe.Fori(N_MK // 2, F_TILES // 2) as j:
                        for u in range(2):
                            tile(2 * j + u, j, u, NTOK)
                    pe.wait_ge(g_exp[l], 4)
                    pe.wait_ge(ft_rotfree[l], 5)
                    pe.wait_ge(ft_ev[l], F_TILES)
                    for n, row in enumerate((row_a, row_w, row_b)):
                        for t in range(NTILE):
                            mm = pe.transpose(ps[:, n, 36 * t:36 * t + 36], row[:, t * P:(t + 1) * P], ident[0:36, 0:36])
                        mm.then_inc(g_tr[l], 1)
                    for n in range(2 * MH):
                        mm = pe.matmul(ps[:, 3, NTILE * n:NTILE * (n + 1)], sel[:, n, :], m_dec[:, :], start=True, stop=True)
                    mm.then_inc(g_tr[l], 1)

                def attention(l):
                    pe.wait_ge(g_cols[l], 4)
                    pe.wait_ge(gt_ev, 1)
                    pe.wait_ge(ft_rope[l], 5)
                    pe.wait_ge(a_mask[l], 16)

                    def scores(s, b, u, h, n_win):
                        r, j, g = h % 2, h % 4, h // 4
                        if n_win:
                            pe.matmul(ps[:, 2 * r, P:512], q_st[u][:, j, :], kz[:, g, bass.ds(b * P, WIN)], start=True, stop=False)
                            pe.matmul(ps[:, 2 * r, P:512], ident_bf[:, :], wmask[:, b, :], start=False, stop=True)
                        pe.matmul(ps[:, 2 * r + 1, 0:CTX], q_st[u][:, j, :], kz[:, g, KPAD:KPAD + CTX], start=True, stop=True)\
                            .then_inc(a_s[l], 1)

                    def turn(s, h, n_win):
                        pe.wait_ge(a_e[l], s + 1)
                        if not isinstance(s, int) or s > 0:
                            pe.wait_ge(a_t_act[l], s)
                            pe.wait_ge(a_t_dve[l], s)
                        for n in range((n_win + CTX) // P):
                            bank, at = (4, n * P) if n < 4 else (5, 0)
                            if not n_win:
                                bank, at = 4 + n, 0
                            mm = pe.transpose(ps[:, bank, at:at + P], prob[h % 2][:, n * P:(n + 1) * P], ident[:, :])
                        mm.then_inc(a_t[l], 1)

                    def values(s, b, h, n_win):
                        pe.wait_ge(a_t_act[l], s + 1)
                        pe.wait_ge(a_t_dve[l], s + 1)
                        g, n_all = h // 4, (n_win + CTX) // P
                        for n in range(n_all):
                            tile = b + n if n < n_win // P else NX + 2 + n - n_win // P
                            mm = pe.matmul(ps[:, 6, DH * h:DH * (h + 1)], prob_t[h % 2][:, n, :],
                                           v_tm[:, tile, g * DH:(g + 1) * DH], start=n == 0, stop=n == n_all - 1)
                        mm.then_inc(a_pv[l], 1)

                    def turn_out(b):
                        pe.wait_ge(a_att[l], b + 1)
                        if not isinstance(b, int) or b > 0:
                            pe.wait_ge(a_out[l], b)
                        att = att_tm.rearrange("p h d -> p (h d)")
                        for j in range(4):
                            mm = pe.transpose(ps[:, 7, j * P:(j + 1) * P], att[:, j * P:(j + 1) * P], ident[:, :])
                        mm.then_inc(a_att_tr[l], 1)

                    def query_block(b, u, n_win, next_win):
                        s0 = b * HEADS
                        for h in range(HEADS):
                            turn(s0 + h, h, n_win)
                            if h + 2 < HEADS:
                                scores(s0 + h + 2, b, u, h + 2, n_win)
                            elif next_win is not None:
                                pe.wait_ge(a_q[l], b + 2)
                                scores(s0 + h + 2, b + 1, 1 - u, h + 2 - HEADS, next_win)
                            if h == 0 and (not isinstance(b, int) or b > 0):
                                pe.wait_ge(a_att[l], b)
                            values(s0 + h, b, h, n_win)
                            if h == 1 and (not isinstance(b, int) or b > 0):
                                turn_out(b - 1)

                    pe.wait_ge(a_q[l], 1)
                    scores(0, 0, 0, 0, WIN)
                    scores(1, 0, 0, 1, WIN)
                    query_blocks(pe, query_block)
                    turn_out(layer_tiles(l) - 1)

                def mlstm(l):
                    nt = layer_tiles(l)
                    pe.wait_ge(a_out[l], nt)
                    pe.wait_ge(m_init[l], 1)

                    def front(n, d, tile, outputs):
                        pe.wait_ge(m_st[l], n + 1)
                        if outputs:
                            c = n - 2 * (NTILE - nt)
                            first = isinstance(c, int) and c == 0
                            if not first:
                                pe.wait_ge(m_y[l], c)
                            for h in range(MH):
                                mm = pe.matmul(ps[:, 1, h * P:(h + 1) * P], sel[:, d * MH + h, :], row_m[:, bass.ts(tile, P)], start=True, stop=True)
                            mm.then_inc(m_m[l], 1)
                            if not first:
                                pe.wait_ge(m_qs[l], c)
                            for h in range(MH):
                                mm = pe.matmul(ps[:, 2, h * P:(h + 1) * P], sel[:, d * MH + h, :], row_i[:, bass.ts(tile, P)], start=True, stop=True)
                            mm.then_inc(m_w[l], 1)
                        if not isinstance(n, int) or n > 0:
                            pe.wait_ge(m_kw[l], n)
                        for h in range(MH):
                            mm = pe.transpose(ps[:, 3, h * P:(h + 1) * P], qk_st[d][:, MH + h, :], ident[:, :])
                        mm.then_inc(m_k[l], 1)

                    def scores(n, d):
                        c = n - 2 * (NTILE - nt)
                        if not isinstance(c, int) or c > 0:
                            pe.wait_ge(m_p[l], c)
                        for h in range(MH):
                            mm = pe.matmul(ps[:, 0, h * P:(h + 1) * P], qk_st[d][:, MH + h, :], qk_st[d][:, h, :], start=True, stop=True)
                        mm.then_inc(m_s[l], 1)

                    def back(n, d, tile, outputs):
                        if outputs:
                            c = n - 2 * (NTILE - nt)
                            pe.wait_ge(m_p[l], c + 1)
                            pe.wait_ge(m_qs[l], c + 1)
                            if not isinstance(c, int) or c > 0:
                                pe.wait_ge(m_h[l], c)
                            if not isinstance(n, int) or n >= 2:
                                pe.wait_ge(m_c[l], n - 1)
                            for h in range(MH):
                                o = ps[:, 4 + h // 2, (MD + 1) * (h % 2):(MD + 1) * (h % 2 + 1)]
                                pe.matmul(o, p_t[d][:, h, :], mv_tm[:, tile, h, :], start=True, stop=False)
                                mm = pe.matmul(o, q_w[d][:, h, :], c_state[:, d * MH + h, :], start=False, stop=True)
                            mm.then_inc(m_num[l], 1)
                        pe.wait_ge(m_kw[l], n + 1)
                        if not isinstance(n, int) or n > 0:
                            pe.wait_ge(m_c[l], n)
                        for h in range(MH):
                            mm = pe.matmul(ps[:, 6 + h // 2, (MD + 1) * (h % 2):(MD + 1) * (h % 2 + 1)],
                                           k_w[d][:, h, :], mv_tm[:, tile, h, :], start=True, stop=True)
                        mm.then_inc(m_del[l], 1)

                    def ahead(n, d, tile, outputs):
                        front(n, d, tile, outputs)
                        if outputs:
                            scores(n, d)

                    def step(j, tiles, outputs, next_tile, next_outputs):
                        ahead(2 * j + 1, 1, tiles[1], outputs)
                        back(2 * j, 0, tiles[0], outputs)
                        if next_tile is not None:
                            ahead(2 * j + 2, 0, next_tile, next_outputs)
                        back(2 * j + 1, 1, tiles[1], outputs)

                    ahead(0, 0, NX, nt > NX)
                    mlstm_steps(pe, step, nt > NX)

                def output(l):
                    nt = layer_tiles(l)
                    pe.wait_ge(m_h[l], 2 * nt)
                    pe.wait_ge(m_c[l], 2 * NTILE)

                    def turn(t, u):
                        pe.wait_ge(p_hz[l], t + 1)
                        if not isinstance(t, int) or t >= 2:
                            pe.wait_ge(p_ev[l], t - 1)
                        for j in range(MH):
                            mm = pe.transpose(ps[:, 4 + u, j * P:(j + 1) * P], h_z[u][:, j * P:(j + 1) * P], ident[:, :])
                        mm.then_inc(p_tr[l], 1)

                    def product(t, u):
                        pe.wait_ge(p_ev[l], t + 1)
                        pe.wait_ge(p_att[l], t + 1)
                        if not isinstance(t, int) or t >= 2:
                            pe.wait_ge(p_gated[l], t - 1)
                        for c in range(2):
                            for k in range(KT):
                                mm = pe.matmul(ps[:, 2 * u + c, :], mix_st[u][:, k, :], w_out[:, k, 512 * c:512 * (c + 1)],
                                               start=k == 0, stop=k == KT - 1)
                        mm.then_inc(p_mm[l], 1)

                    turn(0, 0)
                    pe.wait_ge(p_w[l], 16)
                    turn(1, 1)
                    product(0, 0)
                    turn(2, 0)
                    product(1, 1)
                    last = NX // 2 if nt > NX else NX // 2 - 1
                    with pe.Fori(1, last) as i:
                        turn(2 * i + 1, 1)
                        product(2 * i, 0)
                        turn(2 * i + 2, 0)
                        product(2 * i + 1, 1)
                    turn(nt - 1, 1)
                    product(nt - 2, 0)
                    product(nt - 1, 1)

                modulation()
                norm_tm(l)
                ft(l)
                spread_gates(l)
                attention(l)
                mlstm(l)
                output(l)

            @block.vector
            def _(dve):
                def bcast(col, n):
                    return col.unsqueeze(2).to_broadcast([col.shape[0], col.shape[1], n])

                def setup():
                    dve.memset(minus_half[:, :], -0.5)
                    dve.memset(k_scale[:, :], LN_KSCALE)
                    dve.memset(ones[:, :], 1.0)
                    dve.memset(m_dec[:, :], 0.0).then_inc(setup_dve, 1)
                    dve.wait_ge(const_ld, CONST_ALL)
                    dve.tensor_copy(ident_bf[:, :], ident[:, :]).then_inc(setup_dve, 1)
                    dve.tensor_scalar(neg_sink[:, :, :], sink[:, :, :], -1.0, None, ALU.mult).then_inc(setup_dve, 1)

                def modulation():
                    dve.wait_ge(ada_use, 6)
                    if l == 0:
                        dve.wait_ge(const_ld, CONST_ALL)
                    got = ps[:, 0, 0:6 * KT].rearrange("p (k v) -> p v k", v=2)
                    dve.tensor_tensor(mod[:, :, :], got, b_ada[:, l, :].unsqueeze(1).to_broadcast([P, 2, 3 * KT]), ALU.add).then_inc(mod_sum, 1)
                    dve.wait_ge(mod_sum, 1)
                    dve.scalar_tensor_tensor(out=mod_scale[:, :, :], in0=mod[:, :, KT:2 * KT], scalar=1.0,
                                             in1=norm_g[:, l, :].unsqueeze(1).to_broadcast([P, 2, KT]), op0=ALU.add, op1=ALU.mult).then_inc(ada_done, 1)

                def spread_gates(l):
                    n_v = 2 if l < DEPTH - 1 else 1
                    dve.wait_ge(ft_mm[l], F_TILES)
                    for v in range(n_v):
                        for k in range(KT):
                            ins = dve.tensor_scalar(gate_diag[:, v, k, :], ident[:, :], mod[:, v, 2 * KT + k:2 * KT + k + 1], None, ALU.mult)
                    ins.then_inc(gt_diag, 1)
                    dve.wait_ge(gt_mm, 1)
                    for v in range(n_v):
                        ins = dve.tensor_copy((gate, gate_c)[v], ps_flat[:, 2048 + 1024 * v:3072 + 1024 * v])
                    ins.then_inc(gt_ev, 1)

                def norm_tm(l):
                    def scale_rows(t, u):
                        dve.wait_ge(nt_sq[l], t + 1)
                        dve.tensor_scalar(stat[:, 1, u:u + 1], stat[:, 0, u:u + 1], 1.0 / D_MODEL, EPS, ALU.mult, ALU.add)\
                            .then_inc(nt_ms[l], 1)
                        dve.wait_ge(nt_rs[l], t + 1)
                        if not isinstance(t, int) or t >= 2:
                            dve.wait_ge(nt_tr[l], t - 1)
                        dve.tensor_scalar(xs[u], xt[u], stat[:, 2, u:u + 1], None, ALU.mult).then_inc(nt_xs[l], 1)

                    def modulate(t, u, v):
                        dve.wait_ge(nt_tr[l], t + 1)
                        if not isinstance(t, int) or t >= 2:
                            dve.wait_ge(nt_v[l], t - 1)
                            dve.wait_ge(nt_cp[l], t - 1)
                        for k in range(4, KT):
                            ins = dve.tensor_scalar(xst[u][:, k, :], ps[:, 2 * u + 1, (k - 4) * P:(k - 3) * P],
                                                    mod_scale[:, v, k:k + 1], mod[:, v, k:k + 1], ALU.mult, ALU.add)
                        ins.then_inc(nt_ev_dve[l], 1)

                    def outputs(t, u, gates=True):
                        dve.wait_ge(nt_mv[l], t + 1)
                        dve.tensor_copy(mv_tm[:, t, :, 0:MD], ps[:, 4, :].rearrange("p (h d) -> p h d", h=MH))\
                            .then_inc(nt_mv_ev[l], 1)
                        if gates:
                            dve.wait_ge(nt_mo[l], t + 1)
                            if not isinstance(t, int) or t >= 2:
                                dve.wait_ge(nt_o_st[l][u], 16 * ((t - u) // 2) if isinstance(t, int) else 8 * (t - u))
                            dve.tensor_copy(o_st[u], ps[:, 6, :]).then_inc(nt_mo_ev[l], 1)
                        dve.wait_ge(nt_v[l], t + 1)
                        dve.tensor_copy(v_tm[:, t + 1 if not isinstance(t, int) or t < NX else t + 2, :], ps[:, 7, 0:P])\
                            .then_inc(nt_v_ev[l], 1)

                    dve.memset(kz, 0.0)
                    dve.memset(v_tm[:, 0, :], 0.0)
                    dve.memset(v_tm[:, NX + 1, :], 0.0)
                    dve.memset(mv_tm[:, :, :, MD:MD + 1], 1.0).then_inc(pads[l], 1)
                    for t in range(2):
                        scale_rows(t, t)
                        modulate(t, t, 0)
                    scale_rows(2, 0)
                    outputs(0, 0)
                    def tile(t, u):
                        modulate(t + 2, u, 0)
                        scale_rows(t + 3, 1 - u)
                        outputs(t + 1, 1 - u)

                    pairs(dve, NX // 2 - 1, tile)
                    modulate(8, 0, 1)
                    scale_rows(9, 1)
                    outputs(7, 1)
                    modulate(9, 1, 1)
                    outputs(8, 0, l < DEPTH - 1)
                    outputs(9, 1, l < DEPTH - 1)

                def rope(l, r, n, u, dest, ctx_dest):
                    if ctx_dest is not None:
                        dve.wait_ge(ft_ev[l], n + 1)
                        for at, rows in ctx_dest:
                            dve.tensor_copy(at, cst[u][rows, SEQ:NTOK])
                    dve.wait_ge(ft_rot[l], r + 1)
                    dve.wait_ge(ft_rope_a[l], r + 1)
                    dve.tensor_tensor(rope_b[u], ps_flat[:, 3072:4096], sin_t, ALU.mult).then_inc(ft_rotfree[l], 1)
                    dve.wait_ge(ft_rotfree[l], r + 1)
                    for at, rows in dest:
                        ins = dve.tensor_tensor(at, rope_a[u][rows, :], rope_b[u][rows, :], ALU.add)
                    ins.then_inc(ft_rope[l], 1)

                def gate_scans(l):
                    ch = g_chain[l]
                    dve.wait_ge(g_ln[l], 1)
                    ch.start(1)
                    fwd, bwd = slice(0, MH), slice(32, 32 + MH)
                    tiles_w, tiles_m, tiles_i, tiles_b, tiles_a = [
                        r.rearrange("p (t n) -> p t n", n=P) for r in (row_w, row_m, row_i, row_b, row_a)]
                    dve.scalar_tensor_tensor(out=row_b, in0=row_b, scalar=0.0, in1=row_i, op0=ALU.min, op1=ALU.subtract)
                    ch(dve, dve.memset(row_m, 1.0))
                    dve.memset(tiles_m[fwd, :, 0:1], 0.0)
                    ch(dve, dve.memset(tiles_m[bwd, :, P - 1:P], 0.0))
                    dve.tensor_tensor_scan(row_i[fwd], row_m[fwd], row_b[fwd], 0.0, ALU.mult, ALU.add)
                    dve.tensor_tensor_scan(row_i[bwd, ::-1], row_m[bwd, ::-1], row_b[bwd, ::-1], 0.0, ALU.mult, ALU.add)
                    ch(dve, dve.memset(row_w, 0.0))
                    dve.tensor_tensor(row_a, row_a, row_i, ALU.subtract)
                    dve.tensor_copy(tiles_w[fwd, 1:, 0], tiles_i[fwd, 0:NTILE - 1, P - 1])
                    dve.tensor_copy(tiles_w[fwd, 0:1, 0], tiles_i[fwd, NTILE - 1:, P - 1])
                    ch(dve, dve.tensor_copy(tiles_w[bwd, 0:NTILE - 1, P - 1], tiles_i[bwd, 1:, 0]))
                    dve.tensor_tensor_scan(row_m[bwd, ::-1], row_w[bwd, ::-1], row_a[bwd, ::-1], -BIG, ALU.add, ALU.max)
                    ch(dve, dve.tensor_tensor_scan(row_m[fwd, SEQ:], row_w[fwd, SEQ:], row_a[fwd, SEQ:], -BIG, ALU.add, ALU.max))
                    ch(dve, dve.tensor_tensor_scan(row_m[fwd, 0:SEQ], row_w[fwd, 0:SEQ], row_a[fwd, 0:SEQ], row_m[fwd, NTOK - 1:],
                                                   ALU.add, ALU.max))
                    dve.tensor_tensor(m_state[fwd, 1:NTILE], tiles_w[fwd, 1:, 0], tiles_m[fwd, 0:NTILE - 1, P - 1], ALU.add)
                    dve.tensor_tensor(m_state[fwd, 0:1], tiles_w[fwd, 0:1, 0], tiles_m[fwd, NTILE - 1:, P - 1], ALU.add)
                    dve.tensor_tensor(m_state[bwd, 0:NTILE - 1], tiles_w[bwd, 0:NTILE - 1, P - 1], tiles_m[bwd, 1:, 0], ALU.add)
                    ch(dve, dve.memset(m_state[bwd, NTILE - 1:NTILE], -BIG))
                    ch(dve, dve.memset(m_state[fwd, NX:NX + 1], -BIG))
                    for r, end in ((fwd, P - 1), (bwd, 0)):
                        m_last = tiles_m[r, :, end]
                        dve.tensor_tensor(tiles_w[r], tiles_a[r], bcast(m_last, P), ALU.subtract)
                        dve.tensor_tensor(m_dec[r, 0:NTILE], m_state[r, 0:NTILE], m_last, ALU.subtract)
                        ins = dve.tensor_tensor(row_b[r], row_i[r], row_m[r], ALU.add)
                    ch(dve, ins)
                    for r in (fwd, bwd):
                        ins = dve.tensor_tensor(tiles_i[r], bcast(m_state[r, 0:NTILE], P), tiles_m[r], ALU.subtract)
                    ins.then_inc(g_rows[l], 1)

                def conv(l, c, u):
                    n = N_MQ + c
                    dve.wait_ge(ft_ev[l], n + 1)
                    if not isinstance(c, int) or c > 0:
                        dve.wait_ge(ft_silu[l], c)
                    ch = ft_chain[l]
                    ch.start((CONV_K - 1) * c)
                    w = conv_w[:, l, :, :].rearrange("p c k -> p (c k)")

                    def tap(k):
                        return w[:, bass.ds(c * CONV_K + k, 1)]

                    a = acc[:, 0:ACC_LEN]
                    ch(dve, dve.tensor_scalar(a, cst[u][:, 0:ACC_LEN], tap(0), None, ALU.mult))
                    for k in range(1, CONV_K):
                        ins = dve.scalar_tensor_tensor(out=a, in0=cst[u][:, k:k + ACC_LEN], scalar=tap(k), in1=a,
                                                       op0=ALU.mult, op1=ALU.add)
                        if k < CONV_K - 1:
                            ch(dve, ins)
                    ins.then_inc(ft_conv[l], 1)
                    assert ch.n == CONV_K - 1

                def ft(l):
                    nt = layer_tiles(l)
                    ch = g_chain[l]
                    dve.wait_ge(ft_ev[l], 1)
                    ch.start(0)
                    ch(dve, dve.tensor_scalar(row_b, row_b, gate_b[:, l, 1:2], None, ALU.add))
                    dve.scalar_tensor_tensor(out=row_m, in0=row_b, scalar=-1.0, in1=row_b, op0=ALU.mult, op1=ALU.min)\
                        .then_inc(g_abs[l], 1)
                    dve.wait_ge(ft_trig[l], 32)
                    halves = [slice(g * DH, (g + 1) * DH) for g in range(KV)]
                    rope(l, 0, N_K, 1, [(kz[r, g, P:P + SEQ], r) for g, r in enumerate(halves)],
                         [(kz[r, g, KPAD:KPAD + CTX], r) for g, r in enumerate(halves)])
                    everything = slice(0, P)
                    with dve.Fori(0, 2) as j:
                        for u in range(2):
                            n = 2 * j + u
                            rope(l, n + 1, N_Q + n, u, [(q_flat[:, n, 0:SEQ], everything)],
                                 [(q_flat[:, n, SEQ:NTOK], everything)] if nt > NX else None)
                    gate_scans(l)
                    for u in range(2):
                        dve.wait_ge(ft_az_st[l][u], 32)
                        dve.memset(cst[u][:, 0:2], 0.0)
                        dve.memset(cst[u][:, SEQ + 2:SEQ + 6], 0.0)
                        ins = dve.memset(cst[u][:, CONV_LEN - 2:CONV_LEN], 0.0)
                    ins.then_inc(pads[l], 1)
                    pairs(dve, 4, lambda c, u: conv(l, c, u))
                    for n in range(3):
                        dve.wait_ge(g_tr[l], n + 1)
                        dve.tensor_copy(cols[:, n].rearrange("p t r -> p (t r)"), ps[:, n, 0:36 * NTILE]).then_inc(g_cols[l], 1)
                    dve.wait_ge(g_tr[l], 4)
                    dve.tensor_copy(decay_b[:, :, :].rearrange("p n j -> p (n j)"), ps[:, 3, 0:2 * MH * NTILE]).then_inc(g_cols[l], 1)

                def attention(l):
                    ch, fin = a_chain[l], a_fin[l]

                    def head_max(s, u, h, n_win):
                        dve.wait_ge(a_s[l], s + 1)
                        r = h % 2
                        at = ps_flat[:, 1024 * r + P:1024 * r + P + NKEY] if n_win else ps[:, 2 * r + 1, 0:CTX]
                        ch.start(s)
                        ch(dve, dve.tensor_reduce(row_max[:, u, h:h + 1], at, AX_X, ALU.max, negate=True))
                        dve.tensor_scalar(neg_max[:, u, h:h + 1], row_max[:, u, h:h + 1], DH ** -0.5, neg_sink[:, l, h:h + 1],
                                          ALU.mult, ALU.min).then_inc(a_nm[l], 1)

                    def divide(b, u):
                        fin.start(2 * b)
                        dve.wait_ge(a_sink_e[l], b + 1)
                        fin(dve, dve.tensor_tensor(lsum[:, u, :], lsum[:, u, :], sink_e[:, u, :], ALU.add))
                        fin(dve, dve.reciprocal(recip[:, u, :], lsum[:, u, :]))
                        dve.wait_ge(a_pv[l], HEADS * b + HEADS)
                        if not isinstance(b, int) or b > 0:
                            dve.wait_ge(a_att_tr[l], b)
                        dve.tensor_tensor(att_tm, ps[:, 6, :].rearrange("p (h d) -> p h d", h=HEADS), bcast(recip[:, u, :], DH), ALU.mult)\
                            .then_inc(a_att[l], 1)

                    def gate_out(b, u):
                        dve.wait_ge(a_att_tr[l], b + 1)
                        dve.wait_ge(a_az[l][u], (8 * (b - u) if not isinstance(b, int) else 16 * (b // 2)) + 16)
                        dve.tensor_tensor(att_t[:, :, b, :], ps[:, 7, :].rearrange("p (j n) -> p j n", j=4), az_st[u], ALU.mult)\
                            .then_inc(a_out[l], 1)

                    def query_block(b, u, n_win, next_win):
                        s0 = HEADS * b
                        if not isinstance(b, int) or b > 0:
                            divide(b - 1, 1 - u)
                        for h in range(HEADS):
                            dve.wait_ge(a_t[l], s0 + h + 1)
                            n = 4 if n_win else 1
                            dve.tensor_copy(prob_t[h % 2][:, 0:n, :], ps[:, 4, 0:n * P].rearrange("p (n q) -> p n q", n=n))\
                                .then_inc(a_t_dve[l], 1)
                            if h + 2 < HEADS:
                                head_max(s0 + h + 2, u, h + 2, n_win)
                            elif next_win is not None:
                                head_max(s0 + h + 2, 1 - u, h + 2 - HEADS, next_win)
                            if h == HEADS - 3:
                                dve.wait_ge(a_nm[l], s0 + HEADS)
                                dve.tensor_tensor(sink_e[:, u, :], neg_max[:, u, :], sink[:, l, :], ALU.add).then_inc(a_sink[l], 1)
                            if h == 2 and (not isinstance(b, int) or b > 0):
                                gate_out(b - 1, 1 - u)

                    head_max(0, 0, 0, WIN)
                    head_max(1, 0, 1, WIN)
                    query_blocks(dve, query_block)
                    last = layer_tiles(l) - 1
                    divide(last, last % 2)
                    gate_out(last, last % 2)

                def mlstm(l):
                    nt = layer_tiles(l)
                    ch = m_chain[l]
                    dve.wait_ge(a_out[l], nt)
                    dve.wait_ge(a_pv[l], HEADS * nt)
                    dve.memset(c_state, 0.0).then_inc(m_init[l], 1)

                    def before(n, d, tile):
                        c = n - 2 * (NTILE - nt)
                        dve.wait_ge(m_m[l], c + 1)
                        if not isinstance(c, int) or c >= 2:
                            dve.wait_ge(m_d[l], c - 1)
                        a_col = cols[:, 0].rearrange("p t r -> p (t r)")
                        for h in range(MH):
                            ins = dve.scalar_tensor_tensor(out=dec_y[d][:, h, :], in0=ps[:, 1, h * P:(h + 1) * P],
                                                           scalar=a_col[:, bass.ds(tile * 36 + 32 * d + h, 1)], in1=tri[:, d, :],
                                                           op0=ALU.subtract, op1=ALU.max)
                        ins.then_inc(m_y[l], 1)
                        dve.wait_ge(m_w[l], c + 1)
                        if not isinstance(c, int) or c >= 2:
                            dve.wait_ge(m_num[l], c - 1)
                        dve.tensor_tensor(q_w[d], ps[:, 2, :].rearrange("p (h t) -> p h t", h=MH), qk_st[d][:, 0:MH, :], ALU.mult)\
                            .then_inc(m_qs[l], 1)

                    def weigh(n, d):
                        c = n - 2 * (NTILE - nt)
                        dve.wait_ge(m_s[l], c + 1)
                        dve.wait_ge(m_d[l], c + 1)
                        dve.tensor_tensor(p_t[d], ps[:, 0, :].rearrange("p (h t) -> p h t", h=MH), dec_y[d], ALU.mult)\
                            .then_inc(m_p[l], 1)

                    def after(n, d, tile, outputs):
                        dve.wait_ge(m_del[l], n + 1)
                        dec = decay_b[:, :, :].rearrange("p n j -> p (n j)")
                        for h in range(MH):
                            c_h = c_state[:, d * MH + h, :]
                            ins = dve.scalar_tensor_tensor(out=c_h, in0=c_h, scalar=dec[:, bass.ds((d * MH + h) * NTILE + tile, 1)],
                                                           in1=ps[:, 6 + h // 2, (MD + 1) * (h % 2):(MD + 1) * (h % 2 + 1)],
                                                           op0=ALU.mult, op1=ALU.add)
                        ins.then_inc(m_c[l], 1)
                        if not outputs:
                            return
                        c = n - 2 * (NTILE - nt)
                        ch.start(4 * c)
                        dve.wait_ge(m_num[l], c + 1)
                        num = ps[:, 4:6, 0:2 * (MD + 1)].rearrange("p b (h v) -> p b h v", h=2)
                        ch(dve, dve.tensor_copy(den[:, d, 0, :].rearrange("p (b h) -> p b h", b=2), num[:, :, :, MD]))
                        ch(dve, dve.scalar_tensor_tensor(out=den[:, d, 1, :], in0=den[:, d, 0, :], scalar=-1.0, in1=den[:, d, 0, :],
                                                         op0=ALU.mult, op1=ALU.max))
                        ch(dve, dve.tensor_tensor(den[:, d, 2, :], den[:, d, 1, :], cols[:, 2, tile, 32 * d:32 * d + MH], ALU.max))
                        ch(dve, dve.reciprocal(den[:, d, 3, :], den[:, d, 2, :]))
                        r = den[:, d, 3, :].rearrange("p (b h) -> p b h", b=2).unsqueeze(3).to_broadcast([P, 2, 2, MD])
                        dve.tensor_tensor(h_dir[d][:, tile, :].rearrange("p (b h v) -> p b h v", b=2, h=2), num[:, :, :, 0:MD], r, ALU.mult)\
                            .then_inc(m_h[l], 1)
                        assert ch.n == 4

                    def ahead(n, d, tile, outputs):
                        if outputs:
                            before(n, d, tile)
                            weigh(n, d)

                    def step(j, tiles, outputs, next_tile, next_outputs):
                        ahead(2 * j + 1, 1, tiles[1], outputs)
                        after(2 * j, 0, tiles[0], outputs)
                        if next_tile is not None:
                            ahead(2 * j + 2, 0, next_tile, next_outputs)
                        after(2 * j + 1, 1, tiles[1], outputs)

                    ahead(0, 0, NX, nt > NX)
                    mlstm_steps(dve, step, nt > NX)

                def output(l):
                    nt = layer_tiles(l)

                    def heads_norm(t, u):
                        dve.wait_ge(p_sig[l], t + 1)
                        dve.wait_ge(p_sum[l], t + 1)
                        dve.tensor_tensor(h_g[u], h_sum[u], o_in[u], ALU.mult).then_inc(p_hg[l], 1)
                        dve.wait_ge(p_sq[l], t + 1)
                        dve.tensor_scalar(stat[:, 1, 0:MH], stat[:, 0, 0:MH], 1.0 / MD, EPS, ALU.mult, ALU.add).then_inc(p_ms[l], 1)
                        dve.wait_ge(p_rs[l], t + 1)
                        if not isinstance(t, int) or t > 0:
                            dve.wait_ge(p_hz[l], t)
                        dve.tensor_tensor(h_n.rearrange("p (h v) -> p h v", h=MH), h_g[u].rearrange("p (h v) -> p h v", h=MH),
                                          bcast(stat[:, 2, 0:MH], MD), ALU.mult).then_inc(p_hn[l], 1)

                    def residual(t, u, gate):
                        dve.wait_ge(p_mm[l], t + 1)
                        if not isinstance(t, int) or t > 0:
                            dve.wait_ge(p_new[l], t)
                        dve.tensor_tensor(gated, ps_flat[:, 1024 * u:1024 * u + 1024], gate, ALU.mult).then_inc(p_gated[l], 1)
                        dve.wait_ge(p_gated[l], t + 1)
                        dve.wait_ge(p_x[l][u], (8 * (t - u) if not isinstance(t, int) else 16 * (t // 2)) + 16)
                        if not isinstance(t, int) or t >= 2:
                            dve.wait_ge(p_store[l][u], 8 * (t - u) if not isinstance(t, int) else 16 * (t // 2))
                        dve.tensor_tensor(x_new[u], gated, x_in[u], ALU.add).then_inc(p_new[l], 1)
                        if l == DEPTH - 1:
                            dve.wait_ge(f_sq, t + 1)
                            dve.tensor_scalar(stat[:, 1, 4:5], stat[:, 0, 4:5], 1.0 / D_MODEL, EPS, ALU.mult, ALU.add).then_inc(f_ms, 1)
                            dve.wait_ge(f_rs, t + 1)
                            dve.scalar_tensor_tensor(out=x_new[u], in0=x_new[u], scalar=stat[:, 2, 4:5], in1=final_g,
                                                     op0=ALU.mult, op1=ALU.mult).then_inc(f_x, 1)

                    if l == DEPTH - 1:
                        dve.wait_ge(p_fg[l], 16)
                    heads_norm(0, 0)
                    heads_norm(1, 1)
                    def tile(t, u):
                        heads_norm(t + 2, u)
                        residual(t, u, gate)

                    pairs(dve, NX // 2 - 1, tile)
                    for t in range(NX - 2, nt):
                        if t + 2 < nt:
                            heads_norm(t + 2, t % 2)
                        residual(t, t % 2, gate if t < NX else gate_c)

                if l == 0:
                    setup()
                modulation()
                norm_tm(l)
                ft(l)
                spread_gates(l)
                attention(l)
                mlstm(l)
                output(l)

            @block.scalar
            def _(act):
                def modulation():
                    if l == 0:
                        act.wait_ge(const_ld, CONST_ALL)
                        act.activation(scc[:, :, :], cc[:, :, :], ACT.Silu).then_inc(silu_c, 1)

                def norm_tm(l):
                    def squares(t, u):
                        act.wait_ge(nt_ld[l][u], (8 * (t - u) if not isinstance(t, int) else 16 * (t // 2)) + 16)
                        act.activation(junk[u], xt[u], ACT.Square, accum_out=stat[:, 0, u:u + 1]).then_inc(nt_sq[l], 1)

                    def modulate(t, u, v):
                        act.wait_ge(nt_tr[l], t + 1)
                        if not isinstance(t, int) or t >= 2:
                            act.wait_ge(nt_v[l], t - 1)
                            act.wait_ge(nt_cp[l], t - 1)
                        for k in range(4):
                            ins = act.activation(xst[u][:, k, :], ps[:, 2 * u, k * P:(k + 1) * P], ACT.Identity,
                                                 bias=mod[:, v, k:k + 1], scale=mod_scale[:, v, k:k + 1])
                        ins.then_inc(nt_ev_act[l], 1)

                    def gate(t, u):
                        act.wait_ge(nt_mz[l], t + 1)
                        if not isinstance(t, int) or t >= 2:
                            act.wait_ge(nt_z_st[l][u], 16 * (t // 2) if isinstance(t, int) else 8 * (t - u))
                        act.activation(z_st[u], ps[:, 5, :], ACT.Silu).then_inc(nt_mz_ev[l], 1)

                    for t in range(2):
                        squares(t, t)
                    act.wait_ge(ada_done, 1)
                    for t in range(2):
                        modulate(t, t, 0)
                    squares(2, 0)
                    gate(0, 0)
                    def tile(t, u):
                        modulate(t + 2, u, 0)
                        squares(t + 3, 1 - u)
                        gate(t + 1, 1 - u)

                    pairs(act, NX // 2 - 1, tile)
                    modulate(8, 0, 1)
                    squares(9, 1)
                    gate(7, 1)
                    modulate(9, 1, 1)
                    if l < DEPTH - 1:
                        gate(8, 0)
                        gate(9, 1)

                def ft(l):
                    nt = layer_tiles(l)
                    for stored in (nt_z_st[l], nt_o_st[l]):
                        for u in range(2):
                            act.wait_ge(stored[u], 16 * (nt // 2))
                    act.wait_ge(ft_mm[l], 1)
                    act.activation(row_a, ps_flat[0:36, 0:NTOK], ACT.Identity, bias=gate_b[:, l, 0:1])
                    act.activation(row_b, ps_flat[64:100, 0:NTOK], ACT.Copy).then_inc(ft_ev[l], 1)
                    act.wait_ge(g_abs[l], 1)
                    ch = g_act_chain[l]
                    ch(act, act.activation(row_w, row_m, ACT.Exp))
                    act.activation(row_i, row_w, ACT.Ln, bias=1.0).then_inc(g_ln[l], 1)

                    def raw(r, n, u, ntok):
                        act.wait_ge(ft_mm[l], n + 1)
                        if not isinstance(r, int) or r >= 2:
                            act.wait_ge(ft_rope[l], r - 1)
                        act.activation(cst[u][:, 0:ntok], ps_flat[:, 1536 * u:1536 * u + ntok], ACT.Copy).then_inc(ft_ev[l], 1)

                    raw(0, N_K, 1, NTOK)
                    raw(1, N_Q, 0, nt * P)
                    raw(2, N_Q + 1, 1, nt * P)
                    raw(3, N_Q + 2, 0, nt * P)
                    raw(4, N_Q + 3, 1, nt * P)
                    for j in range(4):
                        u = j % 2
                        act.wait_ge(ft_mm[l], N_AZ + j + 1)
                        if j < 2:
                            act.wait_ge(ft_rope[l], 4 + u)
                        else:
                            act.wait_ge(ft_az_st[l][u], 16)
                        act.activation(cst[u][:, 0:nt * P], ps_flat[:, 1536 * u:1536 * u + nt * P], ACT.Silu).then_inc(ft_ev[l], 1)
                        act.wait_ge(ft_ev[l], N_AZ + j + 1)
                        act.dma_start(az_dram[l][j, :, 0:nt, :], cst[u][:, 0:nt * P].rearrange("p (t n) -> p t n", n=P))\
                            .then_inc(ft_az_st[l][u], 16)
                    act.wait_ge(g_rows[l], 1)
                    act.activation(row_w, row_w, ACT.Exp, bias=k_scale[0:36, :]).then_inc(g_exp[l], 1)
                    act.activation(row_i, row_i, ACT.Exp).then_inc(g_exp[l], 1)
                    act.activation(row_b, row_b, ACT.Exp, scale=-1.0).then_inc(g_exp[l], 1)
                    act.activation(m_dec[:, :], m_dec[:, :], ACT.Exp).then_inc(g_exp[l], 1)
                    act.wait_ge(pads[l], 2)
                    act.wait_ge(ft_rope[l], 5)

                    def taps_in(c, u, ntok):
                        act.wait_ge(ft_mm[l], N_MQ + c + 1)
                        if not isinstance(c, int) or c >= 2:
                            act.wait_ge(ft_conv[l], c - 1)
                        if ntok > SEQ:
                            act.activation(cst[u][:, SEQ + 6:SEQ + 6 + CTX], ps_flat[:, 1536 * u + SEQ:1536 * u + NTOK], ACT.Copy)
                        act.activation(cst[u][:, 2:2 + SEQ], ps_flat[:, 1536 * u:1536 * u + SEQ], ACT.Copy).then_inc(ft_ev[l], 1)

                    def silu(c, ntok):
                        act.wait_ge(ft_conv[l], c + 1)
                        bias = conv_b[:, l, bass.ds(c, 1)]
                        ins = act.activation(mqk_flat[:, c, 0:SEQ], acc[:, 0:SEQ], ACT.Silu, bias=bias)
                        if ntok > SEQ:
                            ins = act.activation(mqk_flat[:, c, SEQ:NTOK], acc[:, SEQ + 4:ACC_LEN], ACT.Silu, bias=bias)
                        ins.then_inc(ft_silu[l], 1)

                    def pair(i, ntok):
                        for u in range(2):
                            taps_in(2 * i + u, u, ntok)
                        for u in range(2):
                            silu(2 * i + u, ntok)

                    for i in range(2):
                        pair(i, nt * P)
                    with act.Fori(2, 4) as i:
                        pair(i, NTOK)

                def attention(l):
                    def exps(s, u, h, n_win):
                        act.wait_ge(a_nm[l], s + 1)
                        r, n = h % 2, n_win + CTX
                        at = ps_flat[:, 1024 * r + P:1024 * r + P + NKEY] if n_win else ps[:, 2 * r + 1, 0:CTX]
                        act.activation(prob[r][:, 0:n], at, ACT.Exp, bias=neg_max[:, u, h:h + 1], scale=DH ** -0.5,
                                       accum_out=lsum[:, u, h:h + 1]).then_inc(a_e[l], 1)

                    def query_block(b, u, n_win, next_win):
                        s0 = HEADS * b
                        for h in range(HEADS):
                            act.wait_ge(a_t[l], s0 + h + 1)
                            n = 4 if n_win else 1
                            act.activation(prob_t[h % 2][:, n, :], ps[:, 5, 0:P], ACT.Copy).then_inc(a_t_act[l], 1)
                            if h + 2 < HEADS:
                                exps(s0 + h + 2, u, h + 2, n_win)
                            elif next_win is not None:
                                exps(s0 + h + 2, 1 - u, h + 2 - HEADS, next_win)
                            if h == HEADS - 2:
                                act.wait_ge(a_sink[l], b + 1)
                                act.activation(sink_e[:, u, :], sink_e[:, u, :], ACT.Exp).then_inc(a_sink_e[l], 1)

                    exps(0, 0, 0, WIN)
                    exps(1, 0, 1, WIN)
                    query_blocks(act, query_block)

                def mlstm(l):
                    nt = layer_tiles(l)

                    def weigh_keys(n, d, tile):
                        act.wait_ge(m_k[l], n + 1)
                        if not isinstance(n, int) or n >= 2:
                            act.wait_ge(m_del[l], n - 1)
                        w_col = cols[:, 1].rearrange("p t r -> p (t r)")
                        for h in range(MH):
                            ins = act.activation(k_w[d][:, h, :], ps[:, 3, h * P:(h + 1) * P], ACT.Copy,
                                                 scale=w_col[:, bass.ds(tile * 36 + 32 * d + h, 1)])
                        ins.then_inc(m_kw[l], 1)

                    def decays(n, d):
                        c = n - 2 * (NTILE - nt)
                        act.wait_ge(m_y[l], c + 1)
                        act.activation(dec_y[d], dec_y[d], ACT.Exp, scale=-1.0, bias=k_scale[:, :]).then_inc(m_d[l], 1)

                    def step(j, tiles, outputs):
                        for d in range(2):
                            if outputs:
                                decays(2 * j + d, d)
                            weigh_keys(2 * j + d, d, tiles[d])

                    act.wait_ge(m_init[l], 1)
                    for j in range(NC):
                        step(j, (NX + j, NX + NC - 1 - j), l < DEPTH - 1)
                    if l == DEPTH - 1:
                        step(NC, (0, NX - 1), True)
                    with act.Fori(0 if l < DEPTH - 1 else 1, NX) as i:
                        step(i + NC, (i, i * -1 + (NX - 1)), True)

                def output(l):
                    nt = layer_tiles(l)

                    def gate(t, u):
                        act.wait_ge(p_o[l][u], (8 * (t - u) if not isinstance(t, int) else 16 * (t // 2)) + 16)
                        act.activation(o_in[u], o_in[u], ACT.Sigmoid).then_inc(p_sig[l], 1)
                        act.wait_ge(p_hg[l], t + 1)
                        if not isinstance(t, int) or t > 0:
                            act.wait_ge(p_ms[l], t)
                        for h in range(MH):
                            ins = act.activation(sq_junk[:, h * P:(h + 1) * P], h_g[u][:, h * MD:(h + 1) * MD], ACT.Square,
                                                 accum_out=stat[:, 0, h:h + 1])
                        ins.then_inc(p_sq[l], 1)

                    def gains(t, u):
                        act.wait_ge(p_tr[l], t + 1)
                        if not isinstance(t, int) or t >= 2:
                            act.wait_ge(p_mm[l], t - 1)
                        for j in range(MH):
                            ins = act.activation(mix_st[u][:, 4 + j, :], ps[:, 4 + u, j * P:(j + 1) * P], ACT.Copy,
                                                 scale=head_g[:, l, j:j + 1])
                        ins.then_inc(p_ev[l], 1)

                    def last_norm(t, u):
                        if l < DEPTH - 1:
                            return
                        act.wait_ge(p_new[l], t + 1)
                        act.activation(sq_last, x_new[u], ACT.Square, accum_out=stat[:, 0, 4:5]).then_inc(f_sq, 1)

                    act.wait_ge(m_del[l], 2 * NTILE)
                    gate(0, 0)
                    gate(1, 1)
                    gains(0, 0)
                    gains(1, 1)
                    with act.Fori(0, NX // 2 - 1) as i:
                        for u in range(2):
                            gate(2 * i + u + 2, u)
                            last_norm(2 * i + u, u)
                            gains(2 * i + u + 2, u)
                    for t in range(NX - 2, nt):
                        if t + 2 < nt:
                            gate(t + 2, t % 2)
                        last_norm(t, t % 2)
                        if t + 2 < nt:
                            gains(t + 2, t % 2)

                modulation()
                norm_tm(l)
                ft(l)
                attention(l)
                mlstm(l)
                output(l)

            @block.gpsimd
            def _(pool):
                def inverse_root(dst, src, n):
                    return pool.tensor_tensor(dst, src, minus_half[:, 0:n], ALU.pow)

                def norm_tm(l):
                    def roots(t, u):
                        pool.wait_ge(nt_ms[l], t + 1)
                        inverse_root(stat[:, 2, u:u + 1], stat[:, 1, u:u + 1], 1).then_inc(nt_rs[l], 1)

                    def keep(t, u):
                        pool.wait_ge(nt_ev_act[l], t + 1)
                        pool.wait_ge(nt_ev_dve[l], t + 1)
                        pool.tensor_copy(xn_t[:, :, t, :], xst[u]).then_inc(nt_cp[l], 1)

                    roots(0, 0)
                    roots(1, 1)
                    keep(0, 0)
                    with pool.Fori(0, NX // 2) as i:
                        for u in range(2):
                            roots(2 * i + u + 2, u)
                            keep(2 * i + u + 1, 1 - u)
                    keep(NTILE - 1, 1)

                def ft(l):
                    def rope(r, n, u):
                        pool.wait_ge(ft_ev[l], n + 1)
                        if not isinstance(r, int) or r >= 2:
                            pool.wait_ge(ft_rope[l], r - 1)
                        pool.tensor_tensor(rope_a[u], cst[u][:, 0:SEQ], cos_t, ALU.mult).then_inc(ft_rope_a[l], 1)

                    pool.wait_ge(ft_trig[l], 32)
                    rope(0, N_K, 1)
                    rope(1, N_Q, 0)
                    rope(2, N_Q + 1, 1)
                    rope(3, N_Q + 2, 0)
                    rope(4, N_Q + 3, 1)

                def attention(l):
                    def stage(b, u):
                        if not isinstance(b, int) or b >= 2:
                            pool.wait_ge(a_s[l], HEADS * (b - 1))
                        pool.tensor_copy(q_st[u], q_t[:, :, b, :]).then_inc(a_q[l], 1)

                    pool.wait_ge(ft_rope[l], 5)
                    pool.wait_ge(ft_mm[l], F_TILES)
                    stage(0, 0)
                    stage(1, 1)
                    with pool.Fori(1, NX // 2) as i:
                        for u in range(2):
                            stage(2 * i + u, u)
                    for b in range(NX, layer_tiles(l)):
                        stage(b, b % 2)

                def mlstm(l):
                    nt = layer_tiles(l)

                    def stage(n, d, tile):
                        if not isinstance(n, int) or n >= 2:
                            c = n - 2 * (NTILE - nt)
                            pool.wait_ge(m_k[l], n - 1)
                            if not isinstance(c, int) or c >= 2:
                                pool.wait_ge(m_qs[l], c - 1)
                                pool.wait_ge(m_s[l], c - 1)
                        pool.tensor_copy(qk_st[d], mqk_t[:, :, tile, :]).then_inc(m_st[l], 1)

                    pool.wait_ge(m_init[l], 1)
                    pool.wait_ge(ft_silu[l], 8)

                    def step(j, tiles):
                        for d in range(2):
                            stage(2 * j + d, d, tiles[d])

                    for j in range(NC):
                        step(j, (NX + j, NX + NC - 1 - j))
                    first = 0
                    if l == DEPTH - 1:
                        step(NC, (0, NX - 1))
                        first = 1
                    with pool.Fori(first, NX) as i:
                        step(i + NC, (i, i * -1 + (NX - 1)))

                def output(l):
                    nt = layer_tiles(l)
                    pool.wait_ge(m_h[l], 2 * nt)
                    pool.wait_ge(m_del[l], 2 * NTILE)

                    def join(t, u):
                        if not isinstance(t, int) or t >= 2:
                            pool.wait_ge(p_hg[l], t - 1)
                        pool.tensor_tensor(h_sum[u], h_dir[0][:, t, :], h_dir[1][:, t, :], ALU.add).then_inc(p_sum[l], 1)

                    def attended(t, u):
                        if not isinstance(t, int) or t >= 2:
                            pool.wait_ge(p_mm[l], t - 1)
                        pool.tensor_copy(mix_st[u][:, 0:4, :], att_t[:, :, t, :]).then_inc(p_att[l], 1)

                    def heads(t, u):
                        pool.wait_ge(p_ms[l], t + 1)
                        inverse_root(stat[:, 2, 0:MH], stat[:, 1, 0:MH], MH).then_inc(p_rs[l], 1)
                        pool.wait_ge(p_hn[l], t + 1)
                        pool.wait_ge(p_z[l][u], (8 * (t - u) if not isinstance(t, int) else 16 * (t // 2)) + 16)
                        if not isinstance(t, int) or t >= 2:
                            pool.wait_ge(p_tr[l], t - 1)
                        pool.tensor_tensor(h_z[u], h_n, z_in[u], ALU.mult).then_inc(p_hz[l], 1)

                    def last_root(t):
                        if l < DEPTH - 1:
                            return
                        pool.wait_ge(f_ms, t + 1)
                        inverse_root(stat[:, 2, 4:5], stat[:, 1, 4:5], 1).then_inc(f_rs, 1)

                    for t in range(2):
                        join(t, t)
                        heads(t, t)
                        attended(t, t)
                    with pool.Fori(0, NX // 2 - 1) as i:
                        for u in range(2):
                            t = 2 * i + u
                            join(t + 2, u)
                            heads(t + 2, u)
                            attended(t + 2, u)
                            last_root(t)
                    for t in range(NX - 2, nt):
                        if t + 2 < nt:
                            join(t + 2, t % 2)
                            heads(t + 2, t % 2)
                            attended(t + 2, t % 2)
                        last_root(t)

                if l == 0:
                    pool.wait_ge(setup_dve, 1)
                norm_tm(l)
                ft(l)
                attention(l)
                mlstm(l)
                output(l)

        def second_block(number, block, sems):
            def sem(name):
                sems.append(nc.alloc_semaphore(name=f"{name}_{number}"))
                return sems[-1]

            const2 = sem("const2")
            CONST2 = [(alibi[:, :], "alibi"), (slope, "slope"), (pw_w, "pw_w"), (fnet_w, "fnet_w"), (dft_c, "dft_c"),
                      (sgu_rows, "sgu_rows"), (sgu_w, "sgu_w"), (lam_in, "lam"), (dw_w, "dw_w"), (dw_b, "dw_b"),
                      (cln_g, "cln_g"), (cln_b, "cln_b"), (pw_b, "pw_b"), (fnet_b, "fnet_b"), (subln_g, "subln_g"),
                      (norm1_g, "norm1_g"), (norm2_g, "norm2_g"), (sgu_b, "sgu_b"), (mean64, "mean64")]
            CONST2_ALL = 16 * len(CONST2)
            setup2, lam_sum, lam_e, sub_ready = sem("setup2"), sem("lam_sum"), sem("lam_e"), sem("sub_ready")
            x_ld = [sem(f"x_ld{u}") for u in range(2)]
            norm_sems = {n: {k: sem(f"n{n}_{k}") for k in ("sq", "ms", "rs", "xs", "tr", "ev_act", "ev_dve")} for n in ("1", "2", "f")}
            w2_ld = [sem(f"w2_ld{n}") for n in range(4)]
            cv_mm, cv_sig, cv_z, cv_acc = sem("cv_mm"), sem("cv_sig"), sem("cv_z"), sem("cv_acc")
            cv_tap = sem("cv_tap")
            c_mm, c_ev, v_mm, v_ev, uv_mm, uv_ev = [sem(n) for n in ("c_mm", "c_ev", "v_mm", "v_ev", "uv_mm", "uv_ev")]
            qk_mm, qk_ev = sem("qk_mm"), sem("qk_ev")
            ln_act, ln_rs, ln_v = Chain(sem("ln_act")), sem("ln_rs"), sem("ln_v")
            ln_pool = Chain(sem("ln_pool"))
            ln_var = sem("ln_var")
            d_q, d_s, d_nm, d_e = sem("d_q"), [sem(f"d_s{m}") for m in range(2)], [sem(f"d_nm{m}") for m in range(2)], \
                [sem(f"d_e{m}") for m in range(2)]
            d_w, d_t, d_t_act, d_pv, d_o = [sem(n) for n in ("d_w", "d_t", "d_t_act", "d_pv", "d_o")]
            d_ms, d_rs, d_on, d_att, d_y = [sem(n) for n in ("d_ms", "d_rs", "d_on", "d_att", "d_y")]
            d_chain, d_fin = Chain(sem("d_chain")), Chain(sem("d_fin"))
            rep_ld, rep_round, qk_lo_ev, rep_mm, rep_ev, q_mm = [sem(n) for n in ("rep_ld", "rep_round", "qk_lo_ev", "rep_mm", "rep_ev", "q_mm")]
            tab_ld = [sem(f"tab_ld{n}") for n in range(2)]
            cw_mm, cw_ev, u_mm, u_ev = sem("cw_mm"), sem("cw_ev"), sem("u_mm"), sem("u_ev")
            dft_mm, dft_odd, dft_y = sem("dft_mm"), sem("dft_odd"), sem("dft_y")
            mu_mm, mu_x, mu_sq, var_mm, var_ln, var_rs, cn_z, cn_silu, pw_mm, pw_ev = [sem(n) for n in (
                "mu_mm", "mu_x", "mu_sq", "var_mm", "var_ln", "var_rs", "cn_z", "cn_silu", "pw_mm", "pw_ev")]
            sg_mm, sg_u, sg_tr, sg_ev = [sem(n) for n in ("sg_mm", "sg_u", "sg_tr", "sg_ev")]
            wo_ld, y_rd, wo_mm, x_add = [sem(f"wo_ld{c}") for c in range(2)], sem("y_rd"), sem("wo_mm"), sem("x_add")
            xn_hi, xn_lo = sem("xn_hi"), sem("xn_lo")
            up_ld, dn_ld = [sem(f"up_ld{u}") for u in range(2)], sem("dn_ld")
            up_hi, up_lo, dn_hi, dn_lo = [sem(n) for n in ("up_hi", "up_lo", "dn_hi", "dn_lo")]
            up_mm, up_relu, up_h, dn_mm, dn_add = [sem(n) for n in ("up_mm", "up_relu", "up_h", "dn_mm", "dn_add")]
            h_chain = Chain(sem("h_chain"))
            fg_ld, out_ready, out_st = sem("fg_ld"), sem("out_ready"), [sem(f"out_st{u}") for u in range(2)]
            GROUPS, FT = D_FF // FG, FG // P

            def pairs_with_ends(eng, n, body):
                for t in range(2):
                    body(t, t)
                with eng.Fori(1, n - 1) as i:
                    for u in range(2):
                        body(2 * i + u, u)
                for t in range(2 * n - 2, 2 * n):
                    body(t, t % 2)

            @block.sync
            def _(sp):
                def load_x(t, u):
                    if not isinstance(t, int) or t >= 2:
                        sp.wait_ge(x_ld[u], 8 * (t - u) if not isinstance(t, int) else 16 * (t // 2))
                    sp.dma_start(x_res[:, t, :], x_dram[DEPTH][t]).then_inc(x_ld[u], 16)

                load_x(0, 0)
                load_x(1, 1)
                for view, name in CONST2:
                    sp.dma_start(view, A[name]).then_inc(const2, 16)
                for n in range(2):
                    sp.dma_start(w_in2[n], A["w_in2"][n]).then_inc(w2_ld[n], 16)
                with sp.Fori(1, NX // 2) as i:
                    for u in range(2):
                        load_x(2 * i + u, u)
                sp.wait_ge(cv_mm, 4)
                sp.dma_start(w_in2[0], A["w_in2"][2]).then_inc(w2_ld[2], 16)
                sp.wait_ge(c_mm, 2)
                sp.wait_ge(v_mm, NX)
                sp.dma_start(w_in2[1], A["w_in2"][3]).then_inc(w2_ld[3], 16)
                sp.wait_ge(cv_z, 2)
                sp.dma_start(rep_raw, A["rep"]).then_inc(rep_ld, 16)
                sp.wait_ge(d_pv, 4 * NX)
                sp.dma_start(cos_s, A["cos_s"]).then_inc(tab_ld[0], 16)
                sp.dma_start(sin_s, A["sin_s"]).then_inc(tab_ld[1], 16)
                for c in range(2):
                    sp.dma_start(w_out2[:, c], A["w_out2"][c]).then_inc(wo_ld[c], 16)

                def load_up(g, u):
                    sp.dma_start(w_up[u], A["w_up"][g]).then_inc(up_ld[u], 16)

                def load_down(g):
                    sp.dma_start(w_down, A["w_down"][g]).then_inc(dn_ld, 16)

                def next_loads(g, u):
                    sp.wait_ge(up_mm, FT * g)
                    load_up(g + 1, 1 - u)
                    sp.wait_ge(dn_mm, 16 * g)
                    load_down(g)

                sp.wait_ge(dft_y, 2)
                sp.wait_ge(pw_mm, 4)
                sp.wait_ge(sg_mm, 4)
                load_up(0, 0)
                load_up(1, 1)
                sp.wait_ge(wo_mm, NX)
                load_down(0)
                next_loads(1, 1)
                with sp.Fori(1, GROUPS // 2 - 1) as i:
                    for u in range(2):
                        next_loads(2 * i + u, u)
                next_loads(GROUPS - 2, 0)
                sp.wait_ge(dn_mm, 16 * (GROUPS - 1))
                load_down(GROUPS - 1)
                sp.dma_start(final_g2, A["final_g2"]).then_inc(fg_ld, 16)

                def store(t, u):
                    sp.wait_ge(out_ready, t + 1)
                    sp.dma_start(out[t], out_s[u]).then_inc(out_st[u], 16)

                pairs(sp, NX // 2, store)
                for u in range(2):
                    sp.wait_ge(out_st[u], 16 * (NX // 2))

            @block.tensor
            def _(pe):
                def turn(n, xs, t, u):
                    s = norm_sems[n]
                    pe.wait_ge(s["xs"], t + 1)
                    if not isinstance(t, int) or t >= 2:
                        pe.wait_ge(s["ev_act"], t - 1)
                        pe.wait_ge(s["ev_dve"], t - 1)
                    for k in range(KT):
                        mm = pe.transpose(ps[:, 2 * u + k // 4, (k % 4) * P:(k % 4 + 1) * P], xs[u][:, k * P:(k + 1) * P], ident[:, :])
                    mm.then_inc(s["tr"], 1)

                def ft_tile(bank, w, done):
                    for c in range(2):
                        for k in range(KT):
                            mm = pe.matmul(ps[:, bank + c, :], w[:, k, :], xn2_t[:, k, 512 * c:512 * (c + 1)],
                                           start=k == 0, stop=k == KT - 1)
                    mm.then_inc(done, 1)

                def tm_tile(bank, t, w, width, done):
                    for k in range(KT):
                        mm = pe.matmul(ps[:, bank, 0:width], xn2_t[:, k, t * P:(t + 1) * P], w[:, k, :], start=k == 0, stop=k == KT - 1)
                    mm.then_inc(done, 1)

                def projections():
                    pe.wait_ge(norm_sems["1"]["ev_act"], NX)
                    pe.wait_ge(norm_sems["1"]["ev_dve"], NX)
                    pe.wait_ge(w2_ld[0], 16)
                    for n in range(4):
                        ft_tile(2 * n, w_in2[0][:, :, n * P:(n + 1) * P], cv_mm)
                    pe.wait_ge(w2_ld[1], 16)
                    for j in range(2):
                        pe.wait_ge(cv_sig, j + 1)
                        ft_tile(4 * j, w_in2[1][:, :, j * P:(j + 1) * P], c_mm)
                    pe.wait_ge(cv_z, 1)
                    for t in range(NX):
                        if t >= 2:
                            pe.wait_ge(v_ev, t - 1)
                        tm_tile(2 + t % 2, t, w_in2[1][:, :, GW:2 * GW], GW, v_mm)
                    pe.wait_ge(cv_z, 2)
                    pe.wait_ge(w2_ld[2], 16)
                    for t in range(NX):
                        if t >= 2:
                            pe.wait_ge(uv_ev, t - 1)
                        tm_tile(6 + t % 2, t, w_in2[0], 512, uv_mm)
                    pe.wait_ge(w2_ld[3], 16)
                    pe.wait_ge(c_ev, 2)
                    pe.wait_ge(v_ev, NX)
                    for n, bank in enumerate((0, 4, 2)):
                        ft_tile(bank, w_in2[1][:, :, n * P:(n + 1) * P], qk_mm)
                    pe.wait_ge(uv_ev, NX)
                    ft_tile(6, w_in2[1][:, :, 3 * P:4 * P], qk_mm)

                def attention():
                    pe.wait_ge(qk_ev, 4)

                    for n in range(8):
                        pe.wait_ge(qk_lo_ev, 3 + n // 4)
                        if n == 0:
                            pe.wait_ge(rep_round, 1)
                        if n >= 2:
                            pe.wait_ge(rep_ev, n - 1)
                        rows = slice(32 * (n % 4), 32 * (n % 4) + 32)
                        for c in range(2):
                            at = ps[:, 2 * (n % 2) + c, :]
                            pe.matmul(at, rep_k[rows, 0, :], qk_hi[1][rows, n // 4, 512 * c:512 * (c + 1)], start=True, stop=False)
                            mm = pe.matmul(at, rep_k[rows, 1, :], qk_lo[1][rows, n // 4, 512 * c:512 * (c + 1)], start=False, stop=True)
                        mm.then_inc(rep_mm, 1)

                    def queries(b, j):
                        for r in range(4):
                            at = ps[:, 7, r * P:(r + 1) * P]
                            pe.matmul(at, rep_q[:, r, 0, :], qk_hi[0][:, j, bass.ts(b, P)], start=True, stop=False)
                            mm = pe.matmul(at, rep_q[:, r, 1, :], qk_lo[0][:, j, bass.ts(b, P)], start=False, stop=True)
                        mm.then_inc(q_mm, 1)

                    def scores(s, b, u, h):
                        if h == 0:
                            pe.wait_ge(d_q, 2 * b + 2)
                        for m in range(2):
                            if not isinstance(s, int) or s > 0:
                                pe.wait_ge(d_e[m], s)
                            for c in range(2):
                                pe.matmul(ps[:, 2 * m + c, :], q2_st[u][:, 2 * h + m, :], k2_st[:, 2 * h + m, 512 * c:512 * (c + 1)],
                                          start=True, stop=False)
                                mm = pe.matmul(ps[:, 2 * m + c, :], slope[:, h, :],
                                               alibi[:, bass.ds(b * -P + (SEQ - P + 512 * c), 512)], start=False, stop=True)
                            mm.then_inc(d_s[m], 1)

                    def turn_p(s, h):
                        pe.wait_ge(d_w, s + 1)
                        if not isinstance(s, int) or s > 0:
                            pe.wait_ge(d_t_act, s)
                        for n in range(NX):
                            mm = pe.transpose(ps[:, 4 + n // 4, (n % 4) * P:(n % 4 + 1) * P], prob2[h % 2][0][:, n * P:(n + 1) * P], ident[:, :])
                        mm.then_inc(d_t, 1)

                    def values(s, b, h):
                        pe.wait_ge(d_t_act, s + 1)
                        if h == 0 and (not isinstance(b, int) or b > 0):
                            pe.wait_ge(d_o, b)
                        for n in range(NX):
                            mm = pe.matmul(ps[:, 6, DH * h:DH * (h + 1)], w_t[h % 2][:, n, :], v2_tm[:, n, DH * h:DH * (h + 1)],
                                           start=n == 0, stop=n == NX - 1)
                        mm.then_inc(d_pv, 1)

                    def turn_out(b):
                        pe.wait_ge(d_on, b + 1)
                        for j in range(2):
                            mm = pe.transpose(ps[:, 7, j * P:(j + 1) * P], o_tm[:, j * P:(j + 1) * P], ident[:, :])
                        mm.then_inc(d_att, 1)

                    def query_block(b, u):
                        for h in range(4):
                            s = 4 * b + h
                            if h < 3:
                                scores(s + 1, b, u, h + 1)
                            elif not isinstance(b, int) or b < NX - 1:
                                scores(s + 1, b + 1, 1 - u, 0)
                            if h > 0:
                                values(s - 1, b, h - 1)
                            elif not isinstance(b, int) or b > 0:
                                values(s - 1, b - 1, 3)
                            turn_p(s, h)
                            last = isinstance(b, int) and b == NX - 1
                            first = isinstance(b, int) and b == 0
                            if h == 0 and not last:
                                pe.wait_ge(d_q, 2 * b + 2)
                                queries(b + 1, 0)
                            if h == 1 and not first:
                                if not last:
                                    pe.wait_ge(d_q, 2 * b + 3)
                                turn_out(b - 1)
                            if h == 2 and not last:
                                if first:
                                    pe.wait_ge(d_q, 2 * b + 3)
                                else:
                                    pe.wait_ge(d_y, b)
                                queries(b + 1, 1)

                    queries(0, 0)
                    pe.wait_ge(d_q, 1)
                    queries(0, 1)
                    pe.wait_ge(rep_ev, 8)
                    scores(0, 0, 0, 0)
                    pairs_with_ends(pe, NX // 2, query_block)
                    values(4 * NX - 1, NX - 1, 3)
                    turn_out(NX - 1)

                def mixers():
                    pe.wait_ge(d_y, NX)
                    pe.wait_ge(d_e[1], 4 * NX)

                    def group_mean(src, n, done):
                        for c in range(2):
                            mm = pe.matmul(ps[:, 2 * n + c, :], mean64, src[:, n, 512 * c:512 * (c + 1)], start=True, stop=True)
                        mm.then_inc(done, 1)

                    pe.wait_ge(cv_acc, 2)
                    for j in range(2):
                        group_mean(dw_acc, j, mu_mm)
                    for j in range(2):
                        for m in range(2):
                            mm = pe.matmul(ps[:, 4 + j, m * P:(m + 1) * P], dft_c[:, m, :], fnet_w[:, j, :], start=True, stop=True)
                    mm.then_inc(cw_mm, 1)
                    pe.wait_ge(cw_ev, 1)
                    for t in range(NX):
                        if t >= 2:
                            pe.wait_ge(u_ev, t - 1)
                        for j in range(2):
                            mm = pe.matmul(ps[:, 6 + t % 2, 2 * P * j:2 * P * (j + 1)], c2_t[:, j, t * P:(t + 1) * P],
                                           chan_w[:, j].rearrange("p m e -> p (m e)"), start=True, stop=True)
                        mm.then_inc(u_mm, 1)
                    for j in range(2):
                        pe.wait_ge(mu_sq, j + 1)
                        group_mean(z_flat, j, var_mm)
                    pe.wait_ge(u_ev, NX)
                    pe.wait_ge(cn_silu, 2)
                    for e in range(2):
                        for c in range(2):
                            for k in range(2):
                                mm = pe.matmul(ps[:, 2 * e + c, :], pw_w[:, k, e * P:(e + 1) * P], z_flat[:, k, 512 * c:512 * (c + 1)],
                                               start=k == 0, stop=k == 1)
                            mm.then_inc(pw_mm, 1)
                    pe.wait_ge(ln_v, 1)
                    for g in range(4):
                        v_g = uv_tm[:, :, GW + DH * g:GW + DH * (g + 1)]
                        pe.matmul(ps[:, 4 + g, :], sgu_w[:, g, :], v_g, start=True, stop=True).then_inc(sg_mm, 1)
                    pe.wait_ge(sg_u, 4)
                    pe.wait_ge(pw_ev, 4)
                    for n in range(4):
                        j, half = n // 2, n % 2
                        for i in range(4):
                            mm = pe.transpose(ps[:, n, i * P:(i + 1) * P], uv_tm[:, 4 * half + i, j * P:(j + 1) * P], ident[:, :])
                        mm.then_inc(sg_tr, 1)
                    for n in range(2):
                        pe.wait_ge(tab_ld[n], 16)
                    for j in range(2):
                        a, b = (4, 5) if j == 0 else (6, 7)
                        for k in range(NX):
                            pe.matmul(ps[:, a, :], u_tm[:, k, j, 0, :], cos_s[:, k, 0:HALF], start=k == 0, stop=k == NX - 1)
                        for k in range(NX):
                            pe.matmul(ps[:, b, 0:1], u_tm[:, k, j, 0, :], cos_s[:, k, HALF:HALF + 1], start=k == 0, stop=k == NX - 1)
                        for k in range(NX):
                            mm = pe.matmul(ps[:, b, 1:HALF], u_tm[:, k, j, 1, :], sin_s[:, k, :], start=k == 0, stop=k == NX - 1)
                        mm.then_inc(dft_mm, 1)

                def output():
                    def product(t, u):
                        pe.wait_ge(y_rd, t + 1)
                        if not isinstance(t, int) or t >= 2:
                            pe.wait_ge(x_add, t - 1)
                        for c in range(2):
                            if isinstance(t, int) and t == 0:
                                pe.wait_ge(wo_ld[c], 16)
                            for k in range(KT):
                                mm = pe.matmul(ps[:, 4 + 2 * u + c, :], y_st[u][:, k, :], w_out2[:, c, k, :], start=k == 0, stop=k == KT - 1)
                        mm.then_inc(wo_mm, 1)

                    pe.wait_ge(sg_ev, 4)
                    for t in range(4):
                        product(t, t % 2)
                        if t >= 2:
                            turn("2", nx_s2, t - 2, t % 2)
                    with pe.Fori(2, NX // 2) as i:
                        for u in range(2):
                            product(2 * i + u, u)
                            turn("2", nx_s2, 2 * i + u - 2, u)
                    for t in range(NX - 2, NX):
                        turn("2", nx_s2, t, t % 2)

                def mlp():
                    pe.wait_ge(xn_lo, NX)
                    pe.wait_ge(x_add, NX)

                    def up(g, u):
                        pe.wait_ge(up_lo, g + 1)
                        for n in range(FT):
                            i = FT * g + n
                            if not isinstance(i, int) or i >= 2:
                                pe.wait_ge(up_relu, i - 1)
                            for c in range(2):
                                at, cols = ps[:, 2 * (n % 2) + c, :], slice(512 * c, 512 * (c + 1))
                                for k in range(KT):
                                    hi, lo = w_up_hi[u][:, k, n * P:(n + 1) * P], w_up_lo[u][:, k, n * P:(n + 1) * P]
                                    x_hi, x_lo = xn2_hi[k // 4][:, k % 4, cols], xn2_lo[k // 4][:, k % 4, cols]
                                    pe.matmul(at, hi, x_hi, start=k == 0, stop=False)
                                    pe.matmul(at, hi, x_lo, start=False, stop=False)
                                    mm = pe.matmul(at, lo, x_hi, start=False, stop=k == KT - 1)
                            mm.then_inc(up_mm, 1)

                    def down(g, u):
                        pe.wait_ge(dn_lo, g + 1)
                        pe.wait_ge(up_h, FT * g + FT)
                        for t in range(NX):
                            for c in range(2):
                                i = 16 * g + 2 * t + c
                                if not isinstance(i, int) or i >= 4:
                                    pe.wait_ge(dn_add, i - 3)
                                at, cols, rows = ps[:, 4 + (2 * t + c) % 4, :], slice(512 * c, 512 * (c + 1)), slice(t * P, (t + 1) * P)
                                for k in range(FT):
                                    pe.matmul(at, h_hi[u][:, k, rows], w_down_hi[:, k, cols], start=k == 0, stop=False)
                                    pe.matmul(at, h_hi[u][:, k, rows], w_down_lo[:, k, cols], start=False, stop=False)
                                    mm = pe.matmul(at, h_lo[u][:, k, rows], w_down_hi[:, k, cols], start=False, stop=k == FT - 1)
                                mm.then_inc(dn_mm, 1)

                    up(0, 0)
                    up(1, 1)
                    down(0, 0)
                    with pe.Fori(1, GROUPS // 2) as i:
                        up(2 * i, 0)
                        down(2 * i - 1, 1)
                        up(2 * i + 1, 1)
                        down(2 * i, 0)
                    down(GROUPS - 1, 1)

                pe.wait_ge(const2, CONST2_ALL)
                pairs(pe, NX // 2, lambda t, u: turn("1", nx_s, t, u))
                projections()
                attention()
                mixers()
                output()
                mlp()

            @block.vector
            def _(dve):
                def bcast(col, n):
                    return col.unsqueeze(2).to_broadcast([col.shape[0], col.shape[1], n])

                def mean_square(n, t):
                    s = norm_sems[n]
                    dve.wait_ge(s["sq"], t + 1)
                    dve.tensor_scalar(stat[:, 1, bass.ds(t, 1)], stat[:, 0, bass.ds(t, 1)], 1.0 / D_MODEL, EPS, ALU.mult, ALU.add)\
                        .then_inc(s["ms"], 1)

                def scale_rows(n, xs, t, u):
                    s = norm_sems[n]
                    mean_square(n, t)
                    dve.wait_ge(s["rs"], t + 1)
                    if not isinstance(t, int) or t >= 2:
                        dve.wait_ge(s["tr"], t - 1)
                    dve.tensor_scalar(xs[u], x_res[:, t, :], stat[:, 2, bass.ds(t, 1)], None, ALU.mult).then_inc(s["xs"], 1)

                def gain(n, g, t, u, dst):
                    s = norm_sems[n]
                    dve.wait_ge(s["tr"], t + 1)
                    dve.tensor_tensor(dst[:, 4:8, bass.ts(t, P)], ps[:, 2 * u + 1, :].rearrange("p (k n) -> p k n", k=4),
                                      bcast(g[:, 4:8], P), ALU.mult).then_inc(s["ev_dve"], 1)

                def setup():
                    dve.memset(eps_col[:, :], EPS)
                    dve.memset(z_pad[:, :, 0:DW_K // 2], 0.0)
                    dve.memset(z_pad[:, :, SEQ + DW_K // 2:], 0.0).then_inc(setup2, 1)
                    dve.wait_ge(const2, CONST2_ALL)
                    dve.tensor_scalar(sub_g[:, :], subln_g, 1.0 - LAM_INIT, None, ALU.mult).then_inc(sub_ready, 1)
                    dve.tensor_tensor(lam_p, lam_in[:, 0:4:2], lam_in[:, 1:4:2], ALU.mult).then_inc(setup2, 1)
                    dve.wait_ge(setup2, 2)
                    dve.tensor_reduce(lam_s[:, :], lam_p, AX_X, ALU.add).then_inc(lam_sum, 1)

                def convolution():
                    for j in range(2):
                        dve.wait_ge(cv_mm, 2 * j + 2)
                        dve.wait_ge(cv_sig, j + 1)
                        dve.tensor_tensor(z_pad[:, j, DW_K // 2:DW_K // 2 + SEQ], ps_flat[:, 2048 * j + 1024:2048 * j + 2048], sig[j], ALU.mult)\
                            .then_inc(cv_z, 1)
                    dve.wait_ge(cv_z, 2)
                    for k in range(DW_K):
                        for j in range(2):
                            src, tap = z_pad[:, j, k:k + SEQ], dw_w[:, j, k:k + 1]
                            if k:
                                dve.wait_ge(cv_tap, 2 * k + j - 1)
                                ins = dve.scalar_tensor_tensor(out=dw_acc[:, j], in0=src, scalar=tap, in1=dw_acc[:, j], op0=ALU.mult, op1=ALU.add)
                            else:
                                ins = dve.tensor_scalar(dw_acc[:, j], src, tap, dw_b[:, j:j + 1], ALU.mult, ALU.add)
                            ins.then_inc(cv_acc if k == DW_K - 1 else cv_tap, 1)

                def attention():
                    ch, fin = d_chain, d_fin
                    dve.wait_ge(lam_e, 1)
                    dve.scalar_tensor_tensor(out=neg_lam[:, :], in0=lam_s[:, 1:2], scalar=-LAM_INIT, in1=lam_s[:, 0:1],
                                             op0=ALU.add, op1=ALU.subtract).then_inc(setup2, 1)
                    dve.wait_ge(setup2, 3)

                    def maxima(s, u, h):
                        for m in range(2):
                            dve.wait_ge(d_s[m], s + 1)
                            dve.tensor_reduce(neg_max[:, u, 2 * h + m:2 * h + m + 1], ps_flat[:, 1024 * m:1024 * (m + 1)], AX_X, ALU.max, negate=True)\
                                .then_inc(d_nm[m], 1)

                    def combine(s, u, h):
                        dve.wait_ge(d_e[1], s + 1)
                        dve.wait_ge(d_e[0], s + 1)
                        ch.start(2 * s)
                        c = recip[:, u, 2 * h + 1:2 * h + 2]
                        ch(dve, dve.reciprocal(c, lsum[:, u, 2 * h + 1:2 * h + 2]))
                        ch(dve, dve.scalar_tensor_tensor(out=row_max[:, u, h:h + 1], in0=lsum[:, u, 2 * h:2 * h + 1], scalar=neg_lam[:, :], in1=c,
                                                         op0=ALU.mult, op1=ALU.mult))
                        p0, p1 = prob2[h % 2]
                        dve.scalar_tensor_tensor(out=p0, in0=p1, scalar=row_max[:, u, h:h + 1], in1=p0, op0=ALU.mult, op1=ALU.add)\
                            .then_inc(d_w, 1)

                    def finish(b, u):
                        fin.start(3 * b)
                        fin(dve, dve.reciprocal(den[:, u, 0, :], lsum[:, u, 0:8:2]))
                        dve.wait_ge(d_pv, 4 * b + 4)
                        if not isinstance(b, int) or b > 0:
                            dve.wait_ge(d_att, b)
                        o = o_tm.rearrange("p (h d) -> p h d", h=4)
                        dve.tensor_tensor(o, ps[:, 6, 0:GW].rearrange("p (h d) -> p h d", h=4), bcast(den[:, u, 0, :], DH), ALU.mult)\
                            .then_inc(d_o, 1)
                        dve.wait_ge(d_o, b + 1)
                        fin(dve, dve.tensor_tensor(o_sq, o_tm, o_tm, ALU.mult))
                        fin(dve, dve.tensor_reduce(den[:, u, 1, :], o_sq.rearrange("p (h d) -> p h d", h=4), AX_X, ALU.add))
                        dve.tensor_scalar(den[:, u, 2, :], den[:, u, 1, :], 1.0 / DH, EPS, ALU.mult, ALU.add).then_inc(d_ms, 1)
                        dve.wait_ge(d_rs, b + 1)
                        dve.tensor_tensor(o, o, bcast(den[:, u, 3, :], DH), ALU.mult).then_inc(d_on, 1)

                    def query_block(b, u):
                        for h in range(4):
                            s = 4 * b + h
                            combine(s, u, h)
                            if h < 3:
                                maxima(s + 1, u, h + 1)
                            elif not isinstance(b, int) or b < NX - 1:
                                maxima(s + 1, 1 - u, 0)
                            if h == 0 and (not isinstance(b, int) or b > 0):
                                finish(b - 1, 1 - u)

                    maxima(0, 0, 0)
                    pairs_with_ends(dve, NX // 2, query_block)
                    finish(NX - 1, 1)

                def mixers():
                    for j in range(2):
                        dve.wait_ge(mu_mm, j + 1)
                        dve.tensor_tensor(dw_acc[:, j], dw_acc[:, j], ps_flat[:, 1024 * j:1024 * (j + 1)], ALU.subtract).then_inc(mu_x, 1)
                    for j in range(2):
                        dve.wait_ge(var_rs, j + 1)
                        dve.tensor_tensor(dw_acc[:, j], dw_acc[:, j], z_flat[:, j], ALU.mult).then_inc(cn_z, 1)
                    for g in range(4):
                        dve.wait_ge(sg_mm, g + 1)
                        u = uv_tm[:, :, DH * g:DH * (g + 1)]
                        dve.scalar_tensor_tensor(out=u, in0=ps[:, 4 + g, :].rearrange("p (n c) -> p n c", n=NX), scalar=sgu_b[:, g:g + 1], in1=u,
                                                 op0=ALU.add, op1=ALU.mult).then_inc(sg_u, 1)
                    for n in range(4):
                        dve.wait_ge(sg_tr, n + 1)
                        dve.tensor_copy(y_t[:, 6 + n // 2, 512 * (n % 2):512 * (n % 2 + 1)], ps[:, n, :]).then_inc(sg_ev, 1)
                    for j in range(2):
                        dve.wait_ge(dft_mm, j + 1)
                        dve.wait_ge(dft_odd, j + 1)
                        a, y, b = ps[:, (4, 6)[j], :], y_t[:, 4 + j, :], fnet_b[:, j:j + 1]
                        dve.tensor_scalar(y[:, 0:1], a[:, 0:1], b, None, ALU.add)
                        dve.tensor_scalar(y[:, HALF:HALF + 1], odd[j][:, 0:1], b, None, ALU.add)
                        dve.scalar_tensor_tensor(out=y[:, 1:HALF], in0=a[:, 1:HALF], scalar=b, in1=odd[j][:, 1:HALF], op0=ALU.add, op1=ALU.add)
                        dve.scalar_tensor_tensor(out=y[:, :HALF:-1], in0=a[:, 1:HALF], scalar=b, in1=odd[j][:, 1:HALF], op0=ALU.add, op1=ALU.subtract)\
                            .then_inc(dft_y, 1)

                def output():
                    def residual(t, u):
                        dve.wait_ge(wo_mm, t + 1)
                        dve.tensor_tensor(x_res[:, t, :], x_res[:, t, :], ps_flat[:, 2048 + 1024 * u:3072 + 1024 * u], ALU.add).then_inc(x_add, 1)

                    residual(0, 0)
                    residual(1, 1)
                    for t in range(2):
                        scale_rows("2", nx_s2, t, t)
                        residual(t + 2, t)
                    with dve.Fori(0, 2) as i:
                        for u in range(2):
                            gain("2", norm2_g, 2 * i + u, u, xn2_raw)
                            scale_rows("2", nx_s2, 2 * i + u + 2, u)
                            residual(2 * i + u + 4, u)
                    for t in range(4, NX):
                        gain("2", norm2_g, t, t % 2, xn2_raw)
                        if t + 2 < NX:
                            scale_rows("2", nx_s2, t + 2, t % 2)

                def mlp():
                    def hidden(g, u):
                        for n in range(FT):
                            h = h_raw[u][:, n, :]
                            dve.wait_ge(up_relu, FT * g + n + 1)
                            h_chain.start(2 * (FT * g + n))
                            h_chain(dve, dve.tensor_tensor(h, h, h, ALU.mult))
                            h_chain(dve, dve.tensor_copy(h_hi[u][:, n, :], h))
                            dve.tensor_tensor(h_lo[u][:, n, :], h, h_hi[u][:, n, :].bitcast(F32), ALU.subtract).then_inc(up_h, 1)

                    def adds(g):
                        for t in range(NX):
                            for c in range(2):
                                dve.wait_ge(dn_mm, 16 * g + 2 * t + c + 1)
                                x = x_res[:, t, 512 * c:512 * (c + 1)]
                                dve.tensor_tensor(x, x, ps[:, 4 + (2 * t + c) % 4, :], ALU.add).then_inc(dn_add, 1)

                    hidden(0, 0)
                    hidden(1, 1)
                    adds(0)
                    with dve.Fori(1, GROUPS // 2) as i:
                        hidden(2 * i, 0)
                        adds(2 * i - 1)
                        hidden(2 * i + 1, 1)
                        adds(2 * i)
                    adds(GROUPS - 1)

                def last_norm(t, u):
                    mean_square("f", t)
                    dve.wait_ge(norm_sems["f"]["rs"], t + 1)
                    if not isinstance(t, int) or t >= 2:
                        dve.wait_ge(out_st[u], 8 * (t - u) if not isinstance(t, int) else 16 * (t // 2))
                    dve.scalar_tensor_tensor(out=out_s[u], in0=x_res[:, t, :], scalar=stat[:, 2, bass.ds(t, 1)], in1=final_g2,
                                             op0=ALU.mult, op1=ALU.mult).then_inc(out_ready, 1)

                setup()
                for t in range(2):
                    scale_rows("1", nx_s, t, t)
                with dve.Fori(0, NX // 2 - 1) as i:
                    for u in range(2):
                        gain("1", norm1_g, 2 * i + u, u, xn2_t)
                        scale_rows("1", nx_s, 2 * i + u + 2, u)
                for t in range(NX - 2, NX):
                    gain("1", norm1_g, t, t % 2, xn2_t)
                convolution()
                attention()
                mixers()
                output()
                mlp()
                dve.wait_ge(fg_ld, 16)
                pairs(dve, NX // 2, last_norm)

            @block.scalar
            def _(act):
                def squares(n, xs, t, u):
                    s = norm_sems[n]
                    if n == "1":
                        act.wait_ge(x_ld[u], 8 * (t - u) + 16 if not isinstance(t, int) else 16 * (t // 2) + 16)
                    elif n == "2":
                        act.wait_ge(x_add, t + 1)
                    else:
                        act.wait_ge(dn_add, 16 * (GROUPS - 1) + 2 * t + 2)
                    if not isinstance(t, int) or t >= 2:
                        act.wait_ge(s["tr"] if n != "f" else s["ms"], t - 1)
                    act.activation(xs[u], x_res[:, t, :], ACT.Square, accum_out=stat[:, 0, bass.ds(t, 1)]).then_inc(s["sq"], 1)

                def gain(n, g, t, u):
                    s = norm_sems[n]
                    dst = xn2_t if n == "1" else xn2_raw
                    act.wait_ge(s["tr"], t + 1)
                    for k in range(4):
                        ins = act.activation(dst[:, k, bass.ts(t, P)], ps[:, 2 * u, k * P:(k + 1) * P], ACT.Copy, scale=g[:, k:k + 1])
                    ins.then_inc(s["ev_act"], 1)

                def high(t):
                    s = norm_sems["2"]
                    act.wait_ge(s["ev_act"], t + 1)
                    act.wait_ge(s["ev_dve"], t + 1)
                    for n in range(2):
                        ins = act.activation(xn2_hi[n][:, :, bass.ts(t, P)], xn2_raw[:, 4 * n:4 * n + 4, bass.ts(t, P)], ACT.Copy)
                    ins.then_inc(xn_hi, 1)

                def norm(n, xs, g):
                    for t in range(2):
                        squares(n, xs, t, t)
                    with act.Fori(0, NX // 2 - 1) as i:
                        for u in range(2):
                            gain(n, g, 2 * i + u, u)
                            squares(n, xs, 2 * i + u + 2, u)
                            if n == "2":
                                high(2 * i + u)
                    for t in range(NX - 2, NX):
                        gain(n, g, t, t % 2)
                        if n == "2":
                            high(t)

                def projections():
                    for j in range(2):
                        act.wait_ge(cv_mm, 2 * j + 1)
                        act.activation(sig[j], ps_flat[:, 2048 * j:2048 * j + 1024], ACT.Sigmoid).then_inc(cv_sig, 1)
                    for j in range(2):
                        act.wait_ge(c_mm, j + 1)
                        act.activation(c2_t[:, j, :], ps_flat[:, 2048 * j:2048 * j + 1024], ACT.Copy).then_inc(c_ev, 1)
                    for t in range(NX):
                        act.wait_ge(v_mm, t + 1)
                        act.activation(v2_tm[:, t, :], ps[:, 2 + t % 2, 0:GW], ACT.Copy).then_inc(v_ev, 1)
                    for t in range(NX):
                        act.wait_ge(uv_mm, t + 1)
                        act.activation(uv_tm[:, t, 0:GW], ps[:, 6 + t % 2, 0:GW], ACT.Copy)
                        act.activation(uv_tm[:, t, GW:], ps[:, 6 + t % 2, GW:], ACT.Copy, accum_out=stat2[:, 0, t:t + 1]).then_inc(uv_ev, 1)
                    ch = ln_act
                    act.wait_ge(uv_ev, NX)
                    ch(act, act.activation(stat2[:, 1, :], stat2[:, 0, :], ACT.Copy, scale=-1.0 / GW))
                    for n, bank in enumerate((0, 4, 2, 6)):
                        act.wait_ge(qk_mm, n + 1)
                        dst = q2_t[:, n, :] if n < 2 else k2_t[:, n - 2, :]
                        scale = 32 ** -0.5 if n < 2 else 1.0
                        act.activation(dst, ps_flat[:, 512 * bank:512 * bank + 1024], ACT.Copy, scale=scale)
                        act.activation(qk_hi[n // 2][:, n % 2, :], ps_flat[:, 512 * bank:512 * bank + 1024], ACT.Copy, scale=scale).then_inc(qk_ev, 1)
                        if n < 2:
                            for t in range(4 * n, 4 * n + 4):
                                v = uv_tm[:, t, GW:]
                                ins = act.activation(v, v, ACT.Identity, bias=stat2[:, 1, t:t + 1])
                            ch(act, ins)
                        else:
                            for t in range(4 * n - 8, 4 * n - 4):
                                ins = act.activation(v_sq[:, t, :], uv_tm[:, t, GW:], ACT.Square, accum_out=stat2[:, 2, t:t + 1])
                            ch(act, ins)
                    act.activation(stat2[:, 3, :], stat2[:, 2, :], ACT.Identity, scale=1.0 / GW, bias=eps_col[:, :]).then_inc(ln_var, 1)

                def attention():
                    act.wait_ge(lam_sum, 1)
                    act.activation(lam_s[:, :], lam_s[:, :], ACT.Exp).then_inc(lam_e, 1)

                    def exps(s, u, h):
                        for m in range(2):
                            act.wait_ge(d_nm[m], s + 1)
                            if m == 0 and (not isinstance(s, int) or s >= 2):
                                act.wait_ge(d_t, s - 1)
                            act.activation(prob2[h % 2][m], ps_flat[:, 1024 * m:1024 * (m + 1)], ACT.Exp, bias=neg_max[:, u, 2 * h + m:2 * h + m + 1],
                                           accum_out=lsum[:, u, 2 * h + m:2 * h + m + 1]).then_inc(d_e[m], 1)

                    def evacuate(s, h):
                        act.wait_ge(d_t, s + 1)
                        act.activation(w_t[h % 2].rearrange("p n q -> p (n q)"), ps_flat[:, 2048:3072], ACT.Copy).then_inc(d_t_act, 1)

                    def gains(b):
                        act.wait_ge(d_att, b + 1)
                        for j in range(2):
                            ins = act.activation(y_t[:, j, bass.ts(b, P)], ps[:, 7, j * P:(j + 1) * P], ACT.Copy, scale=sub_g[:, :])
                        ins.then_inc(d_y, 1)

                    def query_block(b, u):
                        for h in range(4):
                            s = 4 * b + h
                            if h < 3:
                                exps(s + 1, u, h + 1)
                            elif not isinstance(b, int) or b < NX - 1:
                                exps(s + 1, 1 - u, 0)
                            evacuate(s, h)
                            last = isinstance(b, int) and b == NX - 1
                            if h in (0, 2) and not last:
                                queries(b + 1, 1 - u, h // 2)
                            if h == 1 and (not isinstance(b, int) or b > 0):
                                gains(b - 1)

                    def queries(b, u, j):
                        act.wait_ge(q_mm, 2 * b + j + 1)
                        act.activation(q2_st[u][:, 4 * j:4 * j + 4, :].rearrange("p r q -> p (r q)"), ps[:, 7, :], ACT.Copy).then_inc(d_q, 1)

                    act.wait_ge(rep_ld, 16)
                    act.activation(rep, rep_raw, ACT.Copy).then_inc(rep_round, 1)
                    for n in range(8):
                        act.wait_ge(rep_mm, n + 1)
                        act.activation(k2_st[:, n, :], ps_flat[:, 1024 * (n % 2):1024 * (n % 2 + 1)], ACT.Copy).then_inc(rep_ev, 1)
                    for j in range(2):
                        queries(0, 0, j)
                    act.wait_ge(sub_ready, 1)
                    exps(0, 0, 0)
                    pairs_with_ends(act, NX // 2, query_block)
                    gains(NX - 1)

                def mixers():
                    act.wait_ge(cw_mm, 1)
                    for j in range(2):
                        ins = act.activation(chan_w[:, j], ps[:, 4 + j, 0:2 * P].rearrange("p (m e) -> p m e", m=2), ACT.Copy)
                    ins.then_inc(cw_ev, 1)
                    for j in range(2):
                        act.wait_ge(mu_x, j + 1)
                        act.activation(z_flat[:, j], dw_acc[:, j], ACT.Square).then_inc(mu_sq, 1)
                    for t in range(NX):
                        act.wait_ge(u_mm, t + 1)
                        act.activation(u_tm[:, t].rearrange("p j m e -> p (j m e)"), ps[:, 6 + t % 2, :], ACT.Copy).then_inc(u_ev, 1)
                    for j in range(2):
                        act.wait_ge(var_mm, j + 1)
                        act.activation(z_flat[:, j], ps_flat[:, 1024 * j:1024 * (j + 1)], ACT.Ln, bias=eps_col[:, :]).then_inc(var_ln, 1)
                    for j in range(2):
                        act.wait_ge(var_ln, j + 1)
                        act.activation(z_flat[:, j], z_flat[:, j], ACT.Exp, scale=-0.5).then_inc(var_rs, 1)
                    for j in range(2):
                        act.wait_ge(cn_z, j + 1)
                        act.activation(z_flat[:, j], dw_acc[:, j], ACT.Silu, scale=cln_g[:, j:j + 1], bias=cln_b[:, j:j + 1]).then_inc(cn_silu, 1)
                    for n in range(4):
                        act.wait_ge(pw_mm, n + 1)
                        e, c = n // 2, n % 2
                        act.activation(dw_acc[:, e, 512 * c:512 * (c + 1)], ps[:, n, :], ACT.Identity, bias=pw_b[:, e:e + 1]).then_inc(pw_ev, 1)
                    for j in range(2):
                        act.wait_ge(dft_mm, j + 1)
                        act.activation(odd[j], ps[:, (5, 7)[j], :], ACT.Copy).then_inc(dft_odd, 1)

                def mlp():
                    def high_up(g, u):
                        act.wait_ge(up_ld[u], 8 * (g - u) + 16)
                        act.activation(w_up_hi[u], w_up[u], ACT.Copy).then_inc(up_hi, 1)

                    def high_down(g):
                        act.wait_ge(dn_ld, 16 * g + 16)
                        act.activation(w_down_hi, w_down, ACT.Copy).then_inc(dn_hi, 1)

                    def relu(g, u, n):
                        act.wait_ge(up_mm, FT * g + n + 1)
                        if n == 0 and (not isinstance(g, int) or g >= 2):
                            act.wait_ge(dn_mm, 16 * g - 16)
                        act.activation(h_raw[u][:, n, :], ps_flat[:, 1024 * (n % 2):1024 * (n % 2 + 1)], ACT.Relu).then_inc(up_relu, 1)

                    def group(g, u, more=True):
                        relu(g, u, 0)
                        high_down(g - 1)
                        relu(g, u, 1)
                        if more:
                            high_up(g + 1, 1 - u)

                    high_up(0, 0)
                    high_up(1, 1)
                    for n in range(FT):
                        relu(0, 0, n)
                    group(1, 1)
                    with act.Fori(1, GROUPS // 2 - 1) as i:
                        for u in range(2):
                            group(2 * i + u, u)
                    group(GROUPS - 2, 0)
                    group(GROUPS - 1, 1, False)
                    high_down(GROUPS - 1)

                act.wait_ge(const2, CONST2_ALL)
                act.wait_ge(setup2, 1)
                norm("1", nx_s, norm1_g)
                projections()
                attention()
                mixers()
                norm("2", nx_s2, norm2_g)
                mlp()
                pairs(act, NX // 2, lambda t, u: squares("f", nx_s2, t, u))

            @block.gpsimd
            def _(pool):
                def root(n, t):
                    s = norm_sems[n]
                    pool.wait_ge(s["ms"], t + 1)
                    pool.tensor_tensor(stat[:, 2, bass.ds(t, 1)], stat[:, 1, bass.ds(t, 1)], minus_half[:, 0:1], ALU.pow).then_inc(s["rs"], 1)

                def spatial_norm():
                    ch = ln_pool
                    v = uv_tm[:, :, GW:]
                    pool.wait_ge(ln_var, 1)
                    for c in range(2):
                        ins = pool.tensor_tensor(stat2[:, 4, 4 * c:4 * c + 4], stat2[:, 3, 4 * c:4 * c + 4], minus_half[:, :], ALU.pow)
                    ch(pool, ins)
                    ch(pool, pool.tensor_tensor(v, v, stat2[:, 4, :].unsqueeze(2).to_broadcast([P, NX, GW]), ALU.mult))
                    ch(pool, pool.tensor_tensor(v, v, sgu_rows[:, 0:1, :].to_broadcast([P, NX, GW]), ALU.mult))
                    pool.tensor_tensor(v, v, sgu_rows[:, 1:2, :].to_broadcast([P, NX, GW]), ALU.add).then_inc(ln_v, 1)

                def attention():
                    def root_heads(b, u):
                        pool.wait_ge(d_ms, b + 1)
                        pool.tensor_tensor(den[:, u, 3, :], den[:, u, 2, :], minus_half[:, :], ALU.pow).then_inc(d_rs, 1)

                    for n in range(4):
                        pool.wait_ge(qk_ev, n + 1)
                        at = (q2_t, k2_t)[n // 2][:, n % 2, :]
                        pool.tensor_tensor(qk_lo[n // 2][:, n % 2, :], at, qk_hi[n // 2][:, n % 2, :].bitcast(F32), ALU.subtract).then_inc(qk_lo_ev, 1)
                    spatial_norm()
                    with pool.Fori(0, NX // 2) as i:
                        for u in range(2):
                            root_heads(2 * i + u, u)

                def output():
                    def stage(t, u):
                        if not isinstance(t, int) or t >= 2:
                            pool.wait_ge(wo_mm, t - 1)
                        pool.tensor_copy(y_st[u], y_t[:, :, bass.ts(t, P)]).then_inc(y_rd, 1)

                    def low(t):
                        pool.wait_ge(xn_hi, t + 1)
                        for n in range(2):
                            cols = bass.ts(t, P)
                            ins = pool.tensor_tensor(xn2_lo[n][:, :, cols], xn2_raw[:, 4 * n:4 * n + 4, cols], xn2_hi[n][:, :, cols].bitcast(F32),
                                                     ALU.subtract)
                        ins.then_inc(xn_lo, 1)

                    pool.wait_ge(sg_ev, 4)
                    pool.wait_ge(pw_ev, 4)
                    pool.wait_ge(dft_y, 2)
                    stage(0, 0)
                    stage(1, 1)
                    for t in range(2, 4):
                        stage(t, t % 2)
                        root("2", t - 2)
                    with pool.Fori(2, NX // 2) as i:
                        for u in range(2):
                            stage(2 * i + u, u)
                            root("2", 2 * i + u - 2)
                            low(2 * i + u - 4)
                    for t in range(NX - 2, NX):
                        root("2", t)
                        low(t - 2)
                    for t in range(NX - 2, NX):
                        low(t)

                def mlp():
                    def low_up(g, u):
                        pool.wait_ge(up_hi, g + 1)
                        pool.tensor_tensor(w_up_lo[u], w_up[u], w_up_hi[u].bitcast(F32), ALU.subtract).then_inc(up_lo, 1)

                    def low_down(g):
                        pool.wait_ge(dn_hi, g + 1)
                        pool.tensor_tensor(w_down_lo, w_down, w_down_hi.bitcast(F32), ALU.subtract).then_inc(dn_lo, 1)

                    low_up(0, 0)
                    low_up(1, 1)
                    with pool.Fori(0, GROUPS // 2 - 1) as i:
                        for u in range(2):
                            low_down(2 * i + u)
                            low_up(2 * i + u + 2, u)
                    low_down(GROUPS - 2)
                    low_down(GROUPS - 1)

                with pool.Fori(0, NX) as t:
                    root("1", t)
                attention()
                output()
                mlp()
                with pool.Fori(0, NX) as t:
                    root("f", t)

        def run_block(number, program):
            sems = []
            with nc.Block() as block:
                program(number, block, sems)
            nc.clear_and_free_semaphores(sems)
            nc.all_engine_barrier()

        for l in range(DEPTH):
            run_block(l, first_block_layer)
        run_block(DEPTH, second_block)


def kernel(**inputs):
    import concourse.bacc as bacc
    from concourse.bass_utils import run_bass_kernel_spmd

    nc = bacc.Bacc("TRN2", target_bir_lowering=False, num_devices=1)
    arrays = {f"in_{k}": v for k, v in host_layout(inputs).items()}
    access = {k[3:]: nc.dram_tensor(k, v.shape, mybir.dt.from_np(v.dtype), kind="ExternalInput").ap() for k, v in arrays.items()}
    out = nc.dram_tensor("out", (NX, P, D_MODEL), F32, kind="ExternalOutput").ap()
    build(nc, access, out)
    result = run_bass_kernel_spmd(nc, [arrays], core_ids=[0])
    return result.results[0]["out"].reshape(1, SEQ, D_MODEL)
```

```python
from contextlib import ExitStack

import numpy as np

import concourse.bass as bass
from concourse import mybir

F32 = mybir.dt.float32
BF16 = mybir.dt.bfloat16
F16 = mybir.dt.float16
F32R = mybir.dt.float32r
ACT = mybir.ActivationFunctionType
ALU = mybir.AluOpType
AX_X = mybir.AxisListType.X

P = 128
D_MODEL = 1024
KT = D_MODEL // P
SEQ, CTX = 1024, 256
NX, NC = SEQ // P, CTX // P
NTOK = SEQ + CTX
NTILE = NX + NC
DEPTH = 2
HEADS, KV, DH = 8, 2, 64
MH, MD = 4, 128
MW = MH * MD
CONV_K = 5
EPS = 1e-6
BIG = 1e30
WIN = 3 * P
NKEY = WIN + CTX
F_TILES = 18
N_GATE, N_K, N_Q, N_AZ, N_MQ, N_MK = 0, 1, 2, 6, 10, 14
CONV_LEN = SEQ + CTX + 8
ACC_LEN = CONV_LEN - 4
GW = D_MODEL // 4
DW_K = 31
D_FF = 4 * D_MODEL
FG = 2 * P
ALIBI_LEN = SEQ - P + SEQ
LAM_INIT = float(0.8 - 0.6 * np.exp(0.0))
SMALL = 3264
LN_KSCALE = float(-0.5 * np.log(MD))


class Chain:

    def __init__(self, sem):
        self.sem, self.base, self.n = sem, 0, 0

    def start(self, base):
        self.base, self.n = base, 0

    def __call__(self, eng, ins):
        ins.then_inc(self.sem, 1)
        self.n += 1
        eng.wait_ge(self.sem, self.base + self.n)


def host_constants():
    f = np.float32
    out = {"ident": np.eye(P, dtype=f)}
    rot = np.zeros((P, P), f)
    for b in range(0, P, 32):
        for j in range(16):
            rot[b + 16 + j, b + j] = -1.0
            rot[b + j, b + 16 + j] = 1.0
    out["rot"] = rot
    sel = np.zeros((36, 2 * MH, P), f)
    for d in range(2):
        for h in range(MH):
            sel[32 * d + h, d * MH + h] = 1.0
    out["sel"] = sel
    sel_hl = np.zeros((100, 2 * MH, P), f)
    sel_hl[0:36], sel_hl[64:100] = sel, sel
    out["sel_hl"] = sel_hl
    pick = np.zeros((2, 2, P), f)
    pick[0, 0], pick[1, 1] = 1.0, 1.0
    out["pick"] = pick
    s, t = np.arange(P)[:, None], np.arange(P)[None, :]
    out["tri"] = np.stack([np.where(s <= t, 0.0, BIG), np.where(s >= t, 0.0, BIG)], 1).astype(f)
    half = DH // 2
    inv = (10000.0 ** (-np.arange(0, half, 2, dtype=f) / f(half))).astype(f)
    tok = np.arange(SEQ)
    ang = np.concatenate([np.tile((tok // 64).astype(f)[None] * inv[:, None], (2, 1)),
                          np.tile((tok % 64).astype(f)[None] * inv[:, None], (2, 1))], 0)
    ang = np.tile(ang.astype(f), (2, 1)).astype(np.float64)
    out["cos"], out["sin"] = np.cos(ang).astype(f), np.sin(ang).astype(f)
    q, k = np.arange(P)[:, None], np.arange(WIN)[None, :] - P
    band = np.abs(q - k) <= P
    mask = np.zeros((P, NX, WIN), f)
    for b in range(NX):
        kpos = b * P + k
        mask[:, b] = np.where(band & (kpos >= 0) & (kpos < SEQ), 0.0, -BIG)
    out["wmask"] = mask[:, (0, 1, NX - 1)]
    out["alibi"] = np.abs(np.arange(P)[:, None] - (np.arange(ALIBI_LEN)[None, :] - (SEQ - P))).astype(np.float16)
    slopes = 2.0 ** (-8.0 * (np.arange(4) + 1) / 4)
    out["slope"] = (-slopes[None, :, None] * np.eye(P)[:, None, :]).astype(np.float16)
    n = np.arange(SEQ)
    ang = 2 * np.pi * ((n[:, None] * n[None, :]) % SEQ) / SEQ
    half = SEQ // 2
    out["cos_s"] = np.cos(ang[:, 0:half + 1]).reshape(NX, P, half + 1).transpose(1, 0, 2).astype(f)
    out["sin_s"] = np.sin(ang[:, 1:half]).reshape(NX, P, half - 1).transpose(1, 0, 2).astype(f)
    c = np.arange(DH)
    ang = 2 * np.pi * ((c[:, None] * c[None, :]) % DH) / DH
    norm = (SEQ * DH) ** -0.5
    diag = np.eye(P // DH)
    out["dft_c"] = np.stack([np.kron(diag, np.cos(ang) * norm), np.kron(diag, -np.sin(ang) * norm)], 1).astype(f)
    out["mean64"] = np.kron(diag, np.full((DH, DH), 1.0 / DH)).astype(f)
    high, low = np.repeat([1, 1, 0, 0], 32), np.repeat([0, 0, 1, 1], 32)
    rows, four = np.arange(P)[:, None, None], np.arange(4)[None, :, None]
    copy = rows == 32 * four + np.arange(P)[None, None, :] % 32
    rep_q = np.stack([copy * high, copy * low], 2).astype(f)
    copy = rows[:, :, 0] % 32 == np.arange(P)[None, :] % 32
    high, low = np.repeat([1, 0, 1, 0], 32), np.repeat([0, 1, 0, 1], 32)
    out["rep"] = np.concatenate([rep_q, np.stack([copy * high, copy * low], 1).astype(f)[:, None]], 1)
    return out


def pairs(eng, n, body):
    for t in range(2):
        body(t, t)
    with eng.Fori(1, n) as i:
        for u in range(2):
            body(2 * i + u, u)


def host_layout(inputs):
    f = np.float32

    def rows(w):
        return w.reshape(w.shape[0] // P, P, w.shape[1]).transpose(1, 0, 2)

    def cols(v):
        v = v.reshape(v.shape[:-1] + (v.shape[-1] // P, P))
        return np.moveaxis(v, -1, 0)

    def spread(v):
        return np.broadcast_to(v[None], (P,) + v.shape)

    i = {k: np.asarray(v) for k, v in inputs.items()}
    o = dict(host_constants())
    o["wmask"] = (o["wmask"].view(np.uint32) >> 16).astype(np.uint16)
    o["xall"] = np.concatenate([i["x"][0], i["ctx"][0]], 0).reshape(NTILE, P, D_MODEL)
    o["cc"] = np.stack([cols(i["c"][0]), cols(i["c_ctx"])], 2)
    o["w_ada"] = np.stack([np.stack([rows(w[:, 512 * b:512 * b + 512]) for b in range(6)]) for w in i["w_ada"]])
    o["b_ada"] = np.broadcast_to(i["b_ada"][None], (2,) + i["b_ada"].shape)
    o["norm_g"], o["conv_b"], o["head_g"] = cols(i["norm_g"]), cols(i["conv_b"]), cols(i["head_g"])
    o["conv_w"] = cols(i["conv_w"]).transpose(0, 1, 3, 2)
    gate = np.zeros((36, DEPTH, 2), f)
    for d in range(2):
        for n in range(2):
            at = 2 * MH * n + MH * d
            gate[32 * d:32 * d + MH, :, n] = i["gate_b"][:, at:at + MH].T
    o["gate_b"] = gate
    o["sink"], o["final_g"] = spread(i["sink"]), spread(i["final_g"])
    cut = np.cumsum((HEADS * DH, KV * DH, KV * DH, HEADS * DH, MW, MW, MW, MW, MW, 2 * MH, 2 * MH))
    w_tm, w_v, w_ft = [], [], []
    for w in i["w_in"]:
        aq, ak, av, az, mq, mk, mv, mo, mz, mi, mf, _ = np.split(w, cut, 1)
        w_tm.append(np.stack([rows(m) for m in (mv, mz, mo)]))
        w_v.append(rows(av))
        gates = np.zeros((D_MODEL, P), f)
        for n, m in enumerate((mi, mf)):
            for d in range(2):
                gates[:, 64 * n + 32 * d:64 * n + 32 * d + MH] = m[:, MH * d:MH * (d + 1)]
        q = [np.concatenate([aq[:, DH * j:DH * (j + 1)], aq[:, DH * (j + 4):DH * (j + 5)]], 1) for j in range(4)]
        w_ft.append(np.stack([rows(m) for m in [gates, ak] + q + sum([np.split(m, 4, 1) for m in (az, mq, mk)], [])]))
    o["w_tm"], o["w_v"], o["w_ft"] = np.stack(w_tm), np.stack(w_v), np.stack(w_ft)
    o["w_out"] = np.stack([rows(w) for w in i["w_out"]])
    two = {k[:-2]: v[0] for k, v in i.items() if k.endswith("_2") and k != "final_g_2"}
    w = two["w_in"]
    hq, hk, hv, ha, hg, hc, hu, hvv = np.split(w, 8, 1)
    blocks = (np.concatenate([hg[:, 0:P], ha[:, 0:P], hg[:, P:], ha[:, P:]], 1), np.concatenate([hc, hv], 1),
              np.concatenate([hu, hvv], 1), np.concatenate([hq, hk], 1))
    o["w_in2"] = np.stack([rows(b) for b in blocks])
    o["w_out2"] = np.stack([rows(b) for b in np.split(two["w_out"], 2, 1)])
    o["w_up"] = np.stack([rows(b) for b in np.split(two["w_up"], D_FF // FG, 1)])
    o["w_down"] = np.stack([rows(b) for b in np.split(two["w_down"], D_FF // FG, 0)])
    o["lam"] = spread(np.stack([two[n] for n in ("lam_q1", "lam_k1", "lam_q2", "lam_k2")]))
    o["subln_g"] = np.tile(two["subln_g"], 2)[:, None]
    o["norm1_g"], o["norm2_g"], o["final_g2"] = cols(two["norm1_g"]), cols(two["norm2_g"]), spread(i["final_g_2"])
    o["dw_w"] = cols(two["conv_dw_w"]).transpose(0, 2, 1)
    for name, src in (("dw_b", "conv_dw_b"), ("cln_g", "conv_ln_g"), ("cln_b", "conv_ln_b"), ("pw_b", "conv_pw_b"), ("fnet_b", "fnet_b")):
        o[name] = cols(two[src])
    o["pw_w"] = rows(two["conv_pw_w"])
    fw = np.zeros((P, 2, P), f)
    for g in range(4):
        at = DH * (g % 2)
        fw[at:at + DH, g // 2, at:at + DH] = two["fnet_w"][g]
    o["fnet_w"] = fw
    o["sgu_rows"] = spread(np.stack([two["sgu_ln_g"], two["sgu_ln_b"]]))
    o["sgu_w"] = two["sgu_w"].transpose(2, 0, 1)
    o["sgu_b"] = two["sgu_b"].T
    return {k: np.ascontiguousarray(v) for k, v in o.items()}




def build(nc, A, out):
    with ExitStack() as ctx:
        def sb(name, shape, dt=F32):
            return ctx.enter_context(nc.sbuf_tensor(f"{name}_sb", shape, dt))

        ident = sb("ident", [P, P])
        rot = sb("rot", [P, P])
        small = sb("small", [P, SMALL])
        sel = small[0:36, 0:1024].rearrange("p (n m) -> p n m", n=2 * MH)
        tri = sb("tri", [P, 2, P])
        ident_bf = sb("ident_bf", [P, P], BF16)
        cc = sb("cc", [P, KT, 2])
        scc = sb("scc", [P, KT, 2])
        mod = sb("mod", [P, 2, 2 * KT])
        norm_g = sb("norm_g", [P, DEPTH, KT])
        mod_scale = sb("mod_scale", [P, 2, KT])
        pick = small[:, 1024 + 3 * NTILE * 36:][:, 0:2 * P].rearrange("p (v m) -> p v m", v=2)
        gate_rows = small[:, 0:D_MODEL]
        conv_w = sb("conv_w", [P, DEPTH, KT, CONV_K])
        conv_b = sb("conv_b", [P, DEPTH, KT])
        gate_b = sb("gate_b", [36, DEPTH, 2])
        head_g = sb("head_g", [P, DEPTH, MH])
        sink = sb("sink", [P, DEPTH, HEADS])
        neg_sink = sb("neg_sink", [P, DEPTH, HEADS])
        minus_half = sb("minus_half", [P, MH])
        k_scale = sb("k_scale", [P, 1])
        stat = sb("stat", [P, 4, 8])
        cols = small[:, 1024:1024 + 3 * NTILE * 36].rearrange("p (n t r) -> p n t r", n=3, t=NTILE)
        decay_b = sb("decay_b", [P, 2 * MH, NTILE])
        m_state = sb("m_state", [36, 16])
        m_dec = sb("m_dec", [36, NTILE])
        lsum = sb("lsum", [P, 2, HEADS])
        neg_max = sb("neg_max", [P, 2, HEADS])
        row_max = sb("row_max", [P, 2, HEADS])
        sink_e = sb("sink_e", [P, 2, HEADS])
        recip = sb("recip", [P, 2, HEADS])
        den = sb("den", [P, 2, 4, MH])

        ARENA = 47700
        arena = sb("arena", [P, ARENA])
        arena_at = nc.sbuf_base - 4 * ARENA
        XN, QKV, MV, MQK, G, S, WFT = 0, 10240, 19968, 25136, 35376, 41776, 45652

        def shaped(v, shape):
            if len(shape) == 1:
                return v
            names = "abcde"[:len(shape)]
            return v.rearrange(f"p ({' '.join(names)}) -> p {' '.join(names)}",
                               **{c: s for c, s in zip(names[1:], shape[1:])})

        def part(at, *shape):
            n = int(np.prod(shape))
            assert at + n <= ARENA, (at, shape)
            return shaped(arena[:, at:at + n], shape)

        def rounded(name, at, *shape):
            n = int(np.prod(shape))
            assert at + n <= ARENA, (at, shape)
            return shaped(nc.alloc_sbuf_tensor_at(f"{name}_sb", [P, n], F32R, offset=arena_at + 4 * at)[:, :], shape)

        xn_t = part(XN, KT, NTILE, P)
        xn_flat = part(XN, KT, NTOK)
        att_t = part(XN, 4, NTILE, P)
        h_dir = [part(XN + 5120, NTILE, MW), part(QKV, NTILE, MW)]
        q_t = part(QKV, 4, NTILE, P)
        q_flat = part(QKV, 4, NTOK)
        k_raw = part(QKV + 5120, P + KV * NTOK)
        v_tm = part(QKV + 8192, NTILE + 2, P)
        mv_tm = part(MV, NTILE, MH, MD + 1)
        mqk_t = part(MQK, 2 * MH, NTILE, P)
        mqk_flat = part(MQK, 2 * MH, NTOK)
        ada_w = [part(XN + 4096 * u, KT, 512) for u in range(2)]
        ada_b, mod_rows = arena[0:2, MV:MV + 3 * D_MODEL], arena[0:2, MV + 3 * D_MODEL:MV + 5 * D_MODEL]
        w_mv, w_mz, w_mo = part(MQK, KT, 512), part(MQK + 4096, KT, 512), part(QKV, KT, 512)
        w_v = part(QKV + 4096, KT, P)
        xt = [part(G + 1024 * u, D_MODEL) for u in range(2)]
        xs = [part(G + 2048 + 1024 * u, D_MODEL) for u in range(2)]
        xst = [part(G + 4096 + 1024 * u, KT, P) for u in range(2)]
        junk = [part(G + 6144 + 3072 * u, D_MODEL) for u in range(2)]
        z_st = [part(G + 7168 + 512 * u, MW) for u in range(2)]
        o_st = [part(G + 8192 + 512 * u, MW) for u in range(2)]
        w_ft = [part(WFT + 1024 * u, KT, P) for u in range(2)]
        cst = [part(S + 1292 * u, 1292) for u in range(2)]
        acc = part(S + 2584, 1292)
        cos_t, sin_t = part(MQK, SEQ), part(MQK + 1024, SEQ)
        rope_a = [part(MQK + 2048 + 1024 * u, SEQ) for u in range(2)]
        rope_b = [part(MQK + 4096 + 1024 * u, SEQ) for u in range(2)]
        row_a, row_b, row_m, row_w, row_i = [arena[0:36, G + NTOK * n:G + NTOK * (n + 1)] for n in range(5)]
        row_hl = [rounded(f"row_hl{n}", G + NTOK * n, NTOK) for n in range(2)]
        sel_raw, sel_hl = part(G + 3 * NTOK, 2 * MH, P), rounded("sel_hl", G + 3 * NTOK, 2 * MH, P)
        prob = [part(XN + 5120 + NKEY * u, NKEY) for u in range(2)]
        prob_t = [part(XN + 6400 + NKEY * u, NKEY // P, P) for u in range(2)]
        q_hl = [rounded(f"q_hl{g}", XN + 7680 + 512 * g, 4, P) for g in range(KV)]
        k_hi = rounded("k1_hi", S + 512 + 3 * WIN // 2, P + KV * NTOK)
        k_lo = rounded("k1_lo", QKV + 5120, P + KV * NTOK)
        az_st = [part(XN + 8704 + 512 * u, 4, P) for u in range(2)]
        att_tm = part(S, HEADS, DH)
        wmask = part(S + 512, 3 * WIN // 2).bitcast(BF16).rearrange("p (b k) -> p b k", b=3)
        c_state = part(QKV + 5120, 2 * MH, MD + 1)
        qk_st = [part(QKV + 6152 + 1024 * d, 2 * MH, P) for d in range(2)]
        dec_y = [part(QKV + 8200 + 512 * d, MH, P) for d in range(2)]
        p_t = [part(S + 512 * d, MH, P) for d in range(2)]
        q_w = [part(S + 1024 + 512 * d, MH, P) for d in range(2)]
        k_w = [part(S + 2048 + 512 * d, MH, P) for d in range(2)]
        w_out = part(MQK, KT, D_MODEL)
        mix_st = [part(MV + 1024 * u, KT, P) for u in range(2)]
        x_new = [part(MV + 2048 + 1024 * u, D_MODEL) for u in range(2)]
        gated = part(MV + 4096, D_MODEL)
        x_in = [part(G + 1024 * u, D_MODEL) for u in range(2)]
        o_in = [part(G + 2048 + 512 * u, MW) for u in range(2)]
        z_in = [part(G + 3072 + 512 * u, MW) for u in range(2)]
        h_sum = [part(G + 4096 + 512 * u, MW) for u in range(2)]
        h_g = [part(G + 5120 + 512 * u, MW) for u in range(2)]
        gate, gate_c, final_g = part(WFT, D_MODEL), part(WFT + 1024, D_MODEL), part(WFT + 1024, D_MODEL)
        sq_junk = part(S, D_MODEL)
        sq_last = part(S + 2560, D_MODEL)
        h_n = part(S + 1024, MW)
        h_z = [part(S + 1536 + 512 * u, MW) for u in range(2)]

        ps = ctx.enter_context(nc.psum_tensor("ps", [P, 8, 512], F32))
        ps_flat = ps[:, :, :].rearrange("p b n -> p (b n)")

        X2, XNT, YT, W2, M2 = 0, 8192, 16384, 24576, 32768
        x_res = part(X2, NX, D_MODEL)
        xn2_t = part(XNT, KT, SEQ)
        y_t = part(YT, KT, SEQ)
        nx_s = [part(YT + 1024 * u, D_MODEL) for u in range(2)]
        w_in2 = [part(W2 + 4096 * u, KT, 512) for u in range(2)]
        q2_t, k2_t = part(M2, 2, SEQ), part(M2 + 2048, 2, SEQ)
        v2_tm = part(M2 + 4096, NX, GW)
        z_pad = part(M2 + 6144, 2, SEQ + DW_K - 1)
        z_flat = part(M2 + 6144, 2, SEQ)
        c2_t = part(M2 + 8256, 2, SEQ)
        uv_tm = part(M2 + 10304, NX, 2 * GW)
        o_tm, o_sq = part(M2 + 14400, GW), part(M2 + 14656, GW)
        dw_acc = y_t[:, 2:4, :]
        sig = [part(YT + 4096 + 1024 * u, SEQ) for u in range(2)]
        v_sq = part(W2, NX, GW)
        prob2 = [[part(W2 + 2048 * u + 1024 * m, SEQ) for m in range(2)] for u in range(2)]
        w_t = [part(W2 + 4096 + 1024 * u, NX, P) for u in range(2)]
        q2_st = [rounded(f"q2_st{u}", W2 + 6144 + 1024 * u, 8, P) for u in range(2)]
        qk_hi = [rounded("q_hi", YT + 6144, 2, SEQ), rounded("k_hi", W2 + 2048, 2, SEQ)]
        qk_lo = [rounded("q_lo", M2, 2, SEQ), rounded("k_lo", M2 + 2048, 2, SEQ)]
        k2_st = rounded("k2_st", XNT, 8, SEQ)
        rep_raw = part(YT + 4096, 5, 2, P)
        rep = rounded("rep", YT + 4096, 5, 2, P)
        rep_q, rep_k = rep[:, 0:4], rep[:, 4]
        HALF = SEQ // 2
        cos_s = arena[:, XNT:XNT + KT * (HALF + 1)].rearrange("p (k n) -> p k n", k=KT)
        sin_s = arena[:, XNT + KT * (HALF + 1):XNT + 8192].rearrange("p (k n) -> p k n", k=KT)
        u_tm = part(M2, NX, 2, 2, P)
        odd = [part(M2 + 6144 + 512 * j, HALF) for j in range(2)]
        w_out2 = part(W2, 2, KT, 512)
        y_st = [part(M2 + 8192 + 1024 * u, KT, P) for u in range(2)]
        nx_s2 = [part(M2 + 12288 + 1024 * u, D_MODEL) for u in range(2)]
        xn2_raw = y_t
        xn2_hi = [rounded(f"xn2_hi{n}", XNT + 4096 * n, 4, SEQ) for n in range(2)]
        xn2_lo = [rounded(f"xn2_lo{n}", YT + 4096 * n, 4, SEQ) for n in range(2)]
        w_up = [part(M2 + 4096 * u, KT, FG) for u in range(2)]
        w_up_hi = [rounded(f"w_up_hi{u}", M2 + 4096 * u + 2048, KT, FG) for u in range(2)]
        w_up_lo = [rounded(f"w_up_lo{u}", M2 + 4096 * u, KT, FG) for u in range(2)]
        w_down, w_down_hi = part(W2, FG // P, D_MODEL), rounded("w_down_hi", W2 + 2048, FG // P, D_MODEL)
        w_down_lo = rounded("w_down_lo", W2, FG // P, D_MODEL)
        w_last = part(M2, FG // P, D_MODEL)
        w_last_hi, w_last_lo = [w.rearrange("p k n -> p (k n)").rearrange("p (k n) -> p k n", k=FG // P) for w in (w_up_hi[0], w_up_lo[0])]
        h_at = (W2 + 4096, M2 + 8192)
        h_raw = [part(at, FG // P, SEQ) for at in h_at]
        h_hi = [rounded(f"h_hi{u}", at + 2048, FG // P, SEQ) for u, at in enumerate(h_at)]
        h_lo = [rounded(f"h_lo{u}", at, FG // P, SEQ) for u, at in enumerate(h_at)]
        final_g2 = part(YT + 4096, D_MODEL)
        out_s = [part(YT + 5120 + 1024 * u, D_MODEL) for u in range(2)]
        alibi = sb("alibi", [P, ALIBI_LEN], F16)
        stat2 = sb("stat2", [P, 6, 8])
        eps_col = sb("eps_col", [P, 1])
        neg_lam = sb("neg_lam", [P, 1])
        lam_s = sb("lam_s", [P, 2])
        sub_g = sb("sub_g", [P, 1])
        at2 = 0

        def small_part(*shape):
            nonlocal at2
            n = int(np.prod(shape))
            at2 += n
            assert at2 <= SMALL, at2
            v = small[:, at2 - n:at2]
            return v if len(shape) == 1 else v.rearrange(
                f"p ({' '.join('abc'[:len(shape)])}) -> p {' '.join('abc'[:len(shape)])}",
                **{c: s for c, s in zip("bc", shape[1:])})

        slope = small_part(4 * P // 2).bitcast(F16).rearrange("p (h q) -> p h q", h=4)
        pw_w, fnet_w, dft_c = small_part(2, GW), small_part(2, P), small_part(2, P)
        chan_w = small_part(2, 2, P)
        sgu_rows, sgu_w = small_part(2, GW), small_part(4, P)
        lam_in, lam_p = small_part(4, 32), small_part(2, 32)
        dw_w, dw_b = small_part(2, DW_K), small_part(2)
        cln_g, cln_b, pw_b, fnet_b = [small_part(2) for _ in range(4)]
        subln_g, norm1_g, norm2_g, sgu_b = small_part(1), small_part(KT), small_part(KT), small_part(4)
        mean64 = small_part(P)

        def dram(name, shape):
            return nc.dram_tensor(f"{name}_dram", shape, F32).ap()

        z_dram = [dram(f"z_{l}", [NTILE, P, MW]) for l in range(DEPTH)]
        o_dram = [dram(f"o_{l}", [NTILE, P, MW]) for l in range(DEPTH)]
        az_dram = [dram(f"az_{l}", [4, P, NTILE, P]) for l in range(DEPTH)]
        x_dram = [A["xall"]] + [dram(f"x_{l + 1}", [NTILE, P, D_MODEL]) for l in range(DEPTH)]

        def layer_tiles(l):
            return NTILE if l < DEPTH - 1 else NX

        def first_block_layer(l, block, sems):

            def sem(name):
                sems.append(nc.alloc_semaphore(name=f"{name}_{l}"))
                return sems[-1]

            def sem_per_layer(name):
                return {l: sem(name)}

            def sem_per_slot(name):
                return {l: [sem(f"{name}{u}") for u in range(2)]}

            const_ld = sem("const_ld")
            CONSTS = [(ident[:, :], "ident"), (rot[:, :], "rot"), (sel[:, :, :], "sel"), (tri[:, :, :], "tri"),
                      (cc[:, :, :], "cc"), (pick[64:66, :, :], "pick"), (norm_g[:, :, :], "norm_g"),
                      (conv_w[:, :, :, :], "conv_w"), (conv_b[:, :, :], "conv_b"), (gate_b[:, :, :], "gate_b"),
                      (head_g[:, :, :], "head_g"), (sink[:, :, :], "sink")]
            CONST_ALL = 16 * len(CONSTS)
            setup_dve = sem("setup_dve")
            ada_ld, ada_use = [sem(f"ada_ld{u}") for u in range(2)], sem("ada_use")
            silu_c, ada_b_ld, ada_row = sem("silu_c"), sem("ada_b_ld"), sem("ada_row")
            mod_tr, mod_col, ada_done = sem("mod_tr"), sem("mod_col"), sem("ada_done")
            gt_mm, gt_ev = sem("gt_mm"), sem("gt_ev")
            nt_w = {l: [sem(f"nt_w{n}") for n in range(4)]}
            nt_ld = sem_per_slot("nt_ld")
            nt_sq, nt_ms, nt_rs, nt_xs, nt_tr = [sem_per_layer(n) for n in ("nt_sq", "nt_ms", "nt_rs", "nt_xs", "nt_tr")]
            nt_ev_act, nt_ev_dve, nt_cp = [sem_per_layer(n) for n in ("nt_ev_act", "nt_ev_dve", "nt_cp")]
            nt_mv, nt_mz, nt_mo, nt_v = [sem_per_layer(n) for n in ("nt_mv", "nt_mz", "nt_mo", "nt_v")]
            nt_mv_ev, nt_mz_ev, nt_mo_ev, nt_v_ev = [sem_per_layer(n) for n in ("nt_mv_ev", "nt_mz_ev", "nt_mo_ev", "nt_v_ev")]
            nt_z_st, nt_o_st = sem_per_slot("nt_z_st"), sem_per_slot("nt_o_st")
            pads = sem_per_layer("pads")
            ft_w = sem_per_slot("ft_w")
            ft_trig, ft_mm, ft_ev, ft_rot, ft_rope_a, ft_rope, ft_conv, ft_silu = [sem_per_layer(n) for n in (
                "ft_trig", "ft_mm", "ft_ev", "ft_rot", "ft_rope_a", "ft_rope", "ft_conv", "ft_silu")]
            ft_rotfree = sem_per_layer("ft_rotfree")
            ft_az_st = sem_per_slot("ft_az_st")
            ft_chain = {l: Chain(sem("ft_chain"))}
            g_abs, g_ln, g_rows, g_exp, g_tr, g_cols = [sem_per_layer(n) for n in (
                "g_abs", "g_ln", "g_rows", "g_exp", "g_tr", "g_cols")]
            g_chain = {l: Chain(sem("g_chain"))}
            g_act_chain = {l: Chain(sem("g_act_chain"))}
            a_mask = sem_per_layer("a_mask")
            a_az = sem_per_slot("a_az")
            a_q, a_s, a_nm, a_e, a_t, a_t_act, a_t_dve, a_pv = [sem_per_layer(n) for n in (
                "a_q", "a_s", "a_nm", "a_e", "a_t", "a_t_act", "a_t_dve", "a_pv")]
            a_sink, a_sink_e, a_att, a_att_tr, a_out = [sem_per_layer(n) for n in (
                "a_sink", "a_sink_e", "a_att", "a_att_tr", "a_out")]
            a_qh, a_kh, a_kl, a_k, a_t2 = [sem_per_layer(n) for n in ("a_qh", "a_kh", "a_kl", "a_k", "a_t2")]
            a_chain, a_fin = {l: Chain(sem("a_chain"))}, {l: Chain(sem("a_fin"))}
            m_st, m_s, m_k, m_m, m_w, m_y, m_d, m_kw, m_qs, m_p, m_num, m_del, m_c, m_h, m_init = [sem_per_layer(n) for n in (
                "m_st", "m_s", "m_k", "m_m", "m_w", "m_y", "m_d", "m_kw", "m_qs", "m_p", "m_num", "m_del", "m_c", "m_h", "m_init")]
            m_chain = {l: Chain(sem("m_chain"))}
            m_inv = sem_per_layer("m_inv")
            m_sel_ld, m_zero, m_high, m_rows = sem("m_sel_ld"), sem("m_zero"), sem("m_high"), sem("m_rows")
            p_w, p_fg = sem_per_layer("p_w"), sem_per_layer("p_fg")
            p_x, p_o, p_z, p_store = [sem_per_slot(n) for n in ("p_x", "p_o", "p_z", "p_store")]
            p_sig, p_sum, p_hg, p_sq, p_ms, p_rs, p_hn, p_hz, p_tr, p_ev, p_att, p_mm, p_gated, p_new = [sem_per_layer(n) for n in (
                "p_sig", "p_sum", "p_hg", "p_sq", "p_ms", "p_rs", "p_hn", "p_hz", "p_tr", "p_ev", "p_att", "p_mm", "p_gated", "p_new")]
            f_sq, f_ms, f_rs, f_x = sem("f_sq"), sem("f_ms"), sem("f_rs"), sem("f_x")

            def query_blocks(eng, body):
                nt = layer_tiles(l)
                for b in range(2):
                    body(b, b, WIN, WIN)
                with eng.Fori(1, NX // 2 - 1) as i:
                    for u in range(2):
                        body(2 * i + u, u, WIN, WIN)
                for b in range(NX - 2, nt):
                    body(b, b % 2, WIN if b < NX else 0, None if b == nt - 1 else WIN if b + 1 < NX else 0)

            def turned(n_win):
                return (2, 3) if n_win else (1, 1)

            def mlstm_steps(eng, step, ctx_outputs):
                for j in range(NC):
                    step(j, (NX + j, NTILE - 1 - j), ctx_outputs, NX + j + 1 if j < NC - 1 else 0, ctx_outputs or j == NC - 1)
                step(NC, (0, NX - 1), True, 1, True)
                with eng.Fori(1, NX - 1) as i:
                    step(i + NC, (i, i * -1 + (NX - 1)), True, i + 1, True)
                step(NC + NX - 1, (NX - 1, 0), True, None, False)

            @block.sync
            def _(sp):
                if l == 0:
                    for view, name in CONSTS:
                        sp.dma_start(view, A[name]).then_inc(const_ld, 16)

                def modulation():
                    sp.dma_start(ada_b, A["b_ada"][:, l, :]).then_inc(ada_b_ld, 16)
                    for n in range(6):
                        if n >= 2:
                            sp.wait_ge(ada_use, n - 1)
                        sp.dma_start(ada_w[n % 2], A["w_ada"][l, n]).then_inc(ada_ld[n % 2], 16)
                        if n == 1:
                            for u in range(2):
                                sp.dma_start(xt[u], x_dram[l][u]).then_inc(nt_ld[l][u], 16)

                def norm_tm(l):
                    sp.dma_start(w_mv, A["w_tm"][l, 0]).then_inc(nt_w[l][0], 16)
                    sp.dma_start(w_mz, A["w_tm"][l, 1]).then_inc(nt_w[l][1], 16)
                    sp.dma_start(w_mo, A["w_tm"][l, 2]).then_inc(nt_w[l][2], 16)
                    sp.dma_start(w_v, A["w_v"][l]).then_inc(nt_w[l][3], 16)

                    for u in range(2):
                        sp.dma_start(w_ft[u], A["w_ft"][l, u]).then_inc(ft_w[l][u], 16)

                    def load_x(t, u):
                        sp.dma_start(xt[u], x_dram[l][t]).then_inc(nt_ld[l][u], 16)

                    def store(t, u):
                        sp.wait_ge(nt_mz_ev[l], t + 1)
                        sp.dma_start(z_dram[l][t], z_st[u]).then_inc(nt_z_st[l][u], 16)
                        sp.wait_ge(nt_mo_ev[l], t + 1)
                        sp.dma_start(o_dram[l][t], o_st[u]).then_inc(nt_o_st[l][u], 16)

                    with sp.Fori(0, NX // 2) as i:
                        for u in range(2):
                            sp.wait_ge(nt_xs[l], 2 * i + u + 1)
                            load_x(2 * i + u + 2, u)
                            store(2 * i + u, u)
                    if l < DEPTH - 1:
                        for t in range(NX, NTILE):
                            store(t, t % 2)

                def ft(l):
                    sp.wait_ge(nt_mv[l], NTILE)
                    sp.dma_start(cos_t, A["cos"]).then_inc(ft_trig[l], 16)
                    sp.dma_start(sin_t, A["sin"]).then_inc(ft_trig[l], 16)
                    with sp.Fori(1, F_TILES // 2) as i:
                        for u in range(2):
                            sp.wait_ge(ft_mm[l], 2 * i + u - 1)
                            sp.dma_start(w_ft[u], A["w_ft"][l, 2 * i + u]).then_inc(ft_w[l][u], 16)

                def attention(l):
                    sp.wait_ge(ft_silu[l], 8)
                    sp.dma_start(wmask, A["wmask"].bitcast(BF16)).then_inc(a_mask[l], 16)
                    for u in range(2):
                        sp.wait_ge(ft_az_st[l][u], 16 * 2)

                    def load_az(b, u):
                        sp.dma_start(az_st[u], az_dram[l][:, :, b, :].rearrange("j p n -> p j n")).then_inc(a_az[l][u], 16)

                    load_az(0, 0)
                    load_az(1, 1)
                    sp.wait_ge(g_cols[l], 4)
                    sp.dma_start(sel_raw[0:100, :, :], A["sel_hl"]).then_inc(m_sel_ld, 16)
                    with sp.Fori(0, NX // 2 - 1) as i:
                        for u in range(2):
                            sp.wait_ge(a_out[l], 2 * i + u + 1)
                            load_az(2 * i + u + 2, u)
                    if l < DEPTH - 1:
                        for t in range(NX, NTILE):
                            sp.wait_ge(a_out[l], t - 1)
                            load_az(t, t % 2)

                def output(l):
                    nt = layer_tiles(l)
                    sp.wait_ge(m_st[l], 2 * NTILE)
                    sp.dma_start(w_out, A["w_out"][l]).then_inc(p_w[l], 16)
                    if l == DEPTH - 1:
                        sp.dma_start(final_g, A["final_g"]).then_inc(p_fg[l], 16)
                    sp.wait_ge(m_h[l], 2 * nt)
                    sp.wait_ge(m_del[l], 2 * NTILE)
                    sp.wait_ge(m_w[l], 2 * nt)
                    for s in (nt_z_st, nt_o_st):
                        for u in range(2):
                            sp.wait_ge(s[l][u], 16 * (nt // 2))

                    def load(t, u):
                        sp.dma_start(o_in[u], o_dram[l][t]).then_inc(p_o[l][u], 16)
                        sp.dma_start(z_in[u], z_dram[l][t]).then_inc(p_z[l][u], 16)

                    def load_x(t, u):
                        sp.dma_start(x_in[u], x_dram[l][t]).then_inc(p_x[l][u], 16)

                    def store(t, u):
                        sp.wait_ge(p_new[l], t + 1) if l == 0 else sp.wait_ge(f_x, t + 1)
                        sp.dma_start(x_dram[l + 1][t], x_new[u]).then_inc(p_store[l][u], 16)

                    def next_loads(t, u):
                        sp.wait_ge(p_hz[l], t + 1)
                        load(t + 2, u)

                    for t in range(2):
                        load(t, t)
                        load_x(t, t)
                    next_loads(0, 0)
                    with sp.Fori(0, NX // 2 - 2) as i:
                        for u in range(2):
                            next_loads(2 * i + u + 1, 1 - u)
                            store(2 * i + u, u)
                            load_x(2 * i + u + 2, u)
                    for t in range(NX - 4, nt):
                        if t + 3 < nt:
                            next_loads(t + 1, (t + 1) % 2)
                        store(t, t % 2)
                        if t + 2 < nt:
                            load_x(t + 2, t % 2)
                    for u in range(2):
                        sp.wait_ge(p_store[l][u], 16 * (nt // 2))

                modulation()
                norm_tm(l)
                ft(l)
                attention(l)
                output(l)

            @block.tensor
            def _(pe):
                def modulation():
                    if l == 0:
                        pe.wait_ge(silu_c, 1)
                        pe.wait_ge(const_ld, CONST_ALL)
                    for n in range(6):
                        pe.wait_ge(ada_ld[n % 2], 16 * (n // 2 + 1))
                        for k in range(KT):
                            mm = pe.matmul(ps[0:2, n, :], scc[:, k, :], ada_w[n % 2][:, k, :], start=k == 0, stop=k == KT - 1)
                        mm.then_inc(ada_use, 1)
                    pe.wait_ge(ada_row, 4)
                    for f in range(2 * KT):
                        mm = pe.transpose(ps[:, 6, 2 * f:2 * f + 2], mod_rows[:, f * P:(f + 1) * P], ident[0:2, 0:2])
                    mm.then_inc(mod_tr, 1)

                def spread_gates(l):
                    pe.wait_ge(ft_ev[l], F_TILES)
                    pe.wait_ge(ada_row, 6)
                    for v in range(2 if l < DEPTH - 1 else 1):
                        for n in range(2):
                            mm = pe.matmul(ps[:, 4 + 2 * v + n, :], pick[64:66, v, :], gate_rows[64:66, 512 * n:512 * (n + 1)],
                                           start=True, stop=True)
                    mm.then_inc(gt_mm, 1)

                def norm_tm(l):
                    def turn(t, u):
                        pe.wait_ge(nt_xs[l], t + 1)
                        for k in range(KT):
                            mm = pe.transpose(ps[:, 2 * u + k // 4, (k % 4) * P:(k % 4 + 1) * P],
                                              xs[u][:, k * P:(k + 1) * P], ident[:, :])
                        mm.then_inc(nt_tr[l], 1)

                    def products(t, u, gates=True):
                        pe.wait_ge(nt_ev_act[l], t + 1)
                        pe.wait_ge(nt_ev_dve[l], t + 1)
                        for n, w, width, done, free in ((0, w_mv, 512, nt_mv, nt_mv_ev), (1, w_mz, 512, nt_mz, nt_mz_ev),
                                                        (2, w_mo, 512, nt_mo, nt_mo_ev), (3, w_v, P, nt_v, nt_v_ev)):
                            if n in (1, 2) and not gates:
                                continue
                            pe.wait_ge(nt_w[l][n], 16)
                            if not isinstance(t, int) or t > 0:
                                pe.wait_ge(free[l], t)
                            for k in range(KT):
                                mm = pe.matmul(ps[:, 4 + n, 0:width], xst[u][:, k, :], w[:, k, :],
                                               start=k == 0, stop=k == KT - 1)
                            mm.then_inc(done[l], 1)

                    pe.wait_ge(ada_done, 1)
                    turn(0, 0)
                    turn(1, 1)
                    products(0, 0)
                    turn(2, 0)
                    products(1, 1)
                    with pe.Fori(1, NX // 2) as i:
                        turn(2 * i + 1, 1)
                        products(2 * i, 0)
                        turn(2 * i + 2, 0)
                        products(2 * i + 1, 1)
                    turn(9, 1)
                    products(8, 0, l < DEPTH - 1)
                    products(9, 1, l < DEPTH - 1)

                def ft(l):
                    nt = layer_tiles(l)
                    for s, n in ((nt_ev_act, NTILE), (nt_ev_dve, NTILE), (nt_mv_ev, NTILE), (nt_mz_ev, nt), (nt_mo_ev, nt), (nt_v_ev, NTILE)):
                        pe.wait_ge(s[l], n)
                    pe.wait_ge(nt_cp[l], NTILE)

                    def tile(n, i, u, ntok):
                        pe.wait_ge(ft_w[l][u], 16 * i + 16)
                        if not isinstance(n, int) or n >= 2:
                            pe.wait_ge(ft_ev[l], n - 1)
                        for c, at in enumerate(range(0, ntok, 512)):
                            size = min(512, ntok - at)
                            for k in range(KT):
                                mm = pe.matmul(ps[:, 3 * u + c, 0:size], w_ft[u][:, k, :], xn_flat[:, k, at:at + size],
                                               start=k == 0, stop=k == KT - 1)
                        mm.then_inc(ft_mm[l], 1)

                    def rotate(r, n, u):
                        pe.wait_ge(ft_ev[l], n + 1)
                        if not isinstance(r, int) or r > 0:
                            pe.wait_ge(ft_rotfree[l], r)
                        for c in range(2):
                            mm = pe.matmul(ps[:, 6 + c, :], rot[:, :], cst[u][:, 512 * c:512 * c + 512], start=True, stop=True)
                        mm.then_inc(ft_rot[l], 1)

                    tile(N_GATE, 0, 0, NTOK)
                    tile(N_K, 0, 1, NTOK)
                    rotate(0, N_K, 1)
                    with pe.Fori(0, 2) as j:
                        for u in range(2):
                            tile(N_Q + 2 * j + u, j + N_Q // 2, u, nt * P)
                        for u in range(2):
                            rotate(2 * j + u + 1, N_Q + 2 * j + u, u)
                    with pe.Fori(N_AZ // 2, N_MK // 2) as j:
                        for u in range(2):
                            tile(2 * j + u, j, u, nt * P)
                    with pe.Fori(N_MK // 2, F_TILES // 2) as j:
                        for u in range(2):
                            tile(2 * j + u, j, u, NTOK)
                    pe.wait_ge(g_exp[l], 4)
                    pe.wait_ge(ft_rotfree[l], 5)
                    pe.wait_ge(ft_ev[l], F_TILES)
                    for n, row in enumerate((row_a, row_w, row_b)):
                        for t in range(NTILE):
                            mm = pe.transpose(ps[:, n, 36 * t:36 * t + 36], row[:, t * P:(t + 1) * P], ident[0:36, 0:36])
                        mm.then_inc(g_tr[l], 1)
                    for n in range(2 * MH):
                        mm = pe.matmul(ps[:, 3, NTILE * n:NTILE * (n + 1)], sel[:, n, :], m_dec[:, :], start=True, stop=True)
                    mm.then_inc(g_tr[l], 1)

                def attention(l):
                    pe.wait_ge(g_cols[l], 4)
                    pe.wait_ge(ft_rope[l], 5)
                    pe.wait_ge(a_mask[l], 16)

                    def scores(s, b, u, h, n_win):
                        r, j, g = h % 2, h % 4, h // 4
                        if j == 0:
                            pe.wait_ge(a_q[l], 2 * b + g + 1)
                            if isinstance(b, int) and b == 0:
                                pe.wait_ge(a_k[l], g + 1)
                        if n_win:
                            win, edge = bass.ds(b * P + g * NTOK, WIN), isinstance(b, int) and (b > 0) + (b == NX - 1)
                            pe.matmul(ps[:, 2 * r, P:512], q_hl[g][:, j, :], k_hi[:, win], start=True, stop=False)
                            pe.matmul(ps[:, 2 * r, P:512], q_hl[g][:, j, :], k_lo[:, win], start=False, stop=False)
                            pe.matmul(ps[:, 2 * r, P:512], ident_bf[:, :], wmask[:, edge if isinstance(b, int) else 1, :],
                                      start=False, stop=True)
                        ctx = slice(P + g * NTOK + SEQ, P + (g + 1) * NTOK)
                        pe.matmul(ps[:, 2 * r + 1, 0:CTX], q_hl[g][:, j, :], k_hi[:, ctx], start=True, stop=False)
                        pe.matmul(ps[:, 2 * r + 1, 0:CTX], q_hl[g][:, j, :], k_lo[:, ctx], start=False, stop=True)\
                            .then_inc(a_s[l], 1)

                    def turn(s, h, n_win):
                        pe.wait_ge(a_e[l], s + 1)
                        n = 0
                        for bank, tiles, copied, done in zip((4, 5), turned(n_win), (a_t_dve, a_t_act), (a_t, a_t2)):
                            if not isinstance(s, int) or s > 0:
                                pe.wait_ge(copied[l], s)
                            for at in range(tiles):
                                mm = pe.transpose(ps[:, bank, at * P:(at + 1) * P], prob[h % 2][:, n * P:(n + 1) * P], ident[:, :])
                                n += 1
                            mm.then_inc(done[l], 1)

                    def values(s, b, h, n_win):
                        pe.wait_ge(a_t_act[l], s + 1)
                        pe.wait_ge(a_t_dve[l], s + 1)
                        g, n_all = h // 4, (n_win + CTX) // P
                        for n in range(n_all):
                            tile = b + n if n < n_win // P else NX + 2 + n - n_win // P
                            mm = pe.matmul(ps[:, 6, DH * h:DH * (h + 1)], prob_t[h % 2][:, n, :],
                                           v_tm[:, tile, g * DH:(g + 1) * DH], start=n == 0, stop=n == n_all - 1)
                        mm.then_inc(a_pv[l], 1)

                    def turn_out(b):
                        pe.wait_ge(a_att[l], b + 1)
                        if not isinstance(b, int) or b > 0:
                            pe.wait_ge(a_out[l], b)
                        att = att_tm.rearrange("p h d -> p (h d)")
                        for j in range(4):
                            mm = pe.transpose(ps[:, 7, j * P:(j + 1) * P], att[:, j * P:(j + 1) * P], ident[:, :])
                        mm.then_inc(a_att_tr[l], 1)

                    def query_block(b, u, n_win, next_win):
                        s0 = b * HEADS
                        later = not isinstance(b, int) or b > 0
                        for h in range(HEADS):
                            turn(s0 + h, h, n_win)
                            if h + 2 < HEADS:
                                scores(s0 + h + 2, b, u, h + 2, n_win)
                            elif next_win is not None:
                                scores(s0 + h + 2, b + 1, 1 - u, h + 2 - HEADS, next_win)
                            if h == 1 and later:
                                pe.wait_ge(a_att[l], b)
                            if h > 0:
                                values(s0 + h - 1, b, h - 1, n_win)
                            elif later:
                                values(s0 - 1, b - 1, HEADS - 1, 0 if isinstance(b, int) and b > NX else WIN)
                            if h == 2 and later:
                                turn_out(b - 1)

                    scores(0, 0, 0, 0, WIN)
                    scores(1, 0, 0, 1, WIN)
                    pe.wait_ge(gt_ev, 1)
                    query_blocks(pe, query_block)
                    last = layer_tiles(l) - 1
                    values(HEADS * last + HEADS - 1, last, HEADS - 1, WIN if last < NX else 0)
                    turn_out(last)

                def mlstm(l):
                    nt = layer_tiles(l)
                    pe.wait_ge(a_out[l], nt)
                    pe.wait_ge(m_init[l], 1)
                    pe.wait_ge(m_high, 3)
                    pe.wait_ge(m_rows, 2)

                    def front(n, d, tile, outputs):
                        pe.wait_ge(m_st[l], n + 1)
                        if outputs:
                            c = n - 2 * (NTILE - nt)
                            first = isinstance(c, int) and c == 0
                            if not first:
                                pe.wait_ge(m_y[l], c)
                            for h in range(MH):
                                mm = pe.matmul(ps[:, 1, h * P:(h + 1) * P], sel_hl[0:100, d * MH + h, :], row_hl[0][0:100, bass.ts(tile, P)],
                                               start=True, stop=True)
                            mm.then_inc(m_m[l], 1)
                            if not first:
                                pe.wait_ge(m_qs[l], c)
                            for h in range(MH):
                                mm = pe.matmul(ps[:, 2, h * P:(h + 1) * P], sel_hl[0:100, d * MH + h, :], row_hl[1][0:100, bass.ts(tile, P)],
                                               start=True, stop=True)
                            mm.then_inc(m_w[l], 1)
                        if not isinstance(n, int) or n > 0:
                            pe.wait_ge(m_kw[l], n)
                        for h in range(MH):
                            mm = pe.transpose(ps[:, 3, h * P:(h + 1) * P], qk_st[d][:, MH + h, :], ident[:, :])
                        mm.then_inc(m_k[l], 1)

                    def scores(n, d):
                        c = n - 2 * (NTILE - nt)
                        if not isinstance(c, int) or c > 0:
                            pe.wait_ge(m_p[l], c)
                        for h in range(MH):
                            mm = pe.matmul(ps[:, 0, h * P:(h + 1) * P], qk_st[d][:, MH + h, :], qk_st[d][:, h, :], start=True, stop=True)
                        mm.then_inc(m_s[l], 1)

                    def back(n, d, tile, outputs):
                        if outputs:
                            c = n - 2 * (NTILE - nt)
                            pe.wait_ge(m_p[l], c + 1)
                            pe.wait_ge(m_qs[l], c + 1)
                            if not isinstance(c, int) or c > 0:
                                pe.wait_ge(m_h[l], c)
                            if not isinstance(n, int) or n >= 2:
                                pe.wait_ge(m_c[l], n - 1)
                            for h in range(MH):
                                o = ps[:, 4 + h // 2, (MD + 1) * (h % 2):(MD + 1) * (h % 2 + 1)]
                                pe.matmul(o, p_t[d][:, h, :], mv_tm[:, tile, h, :], start=True, stop=False)
                                mm = pe.matmul(o, q_w[d][:, h, :], c_state[:, d * MH + h, :], start=False, stop=True)
                            mm.then_inc(m_num[l], 1)
                        pe.wait_ge(m_kw[l], n + 1)
                        if not isinstance(n, int) or n > 0:
                            pe.wait_ge(m_c[l], n)
                        for h in range(MH):
                            mm = pe.matmul(ps[:, 6 + h // 2, (MD + 1) * (h % 2):(MD + 1) * (h % 2 + 1)],
                                           k_w[d][:, h, :], mv_tm[:, tile, h, :], start=True, stop=True)
                        mm.then_inc(m_del[l], 1)

                    def ahead(n, d, tile, outputs):
                        front(n, d, tile, outputs)
                        if outputs:
                            scores(n, d)

                    def step(j, tiles, outputs, next_tile, next_outputs):
                        ahead(2 * j + 1, 1, tiles[1], outputs)
                        back(2 * j, 0, tiles[0], outputs)
                        if next_tile is not None:
                            ahead(2 * j + 2, 0, next_tile, next_outputs)
                        back(2 * j + 1, 1, tiles[1], outputs)

                    ahead(0, 0, NX, nt > NX)
                    mlstm_steps(pe, step, nt > NX)

                def output(l):
                    nt = layer_tiles(l)

                    def turn(t, u):
                        pe.wait_ge(p_hz[l], t + 1)
                        if not isinstance(t, int) or t >= 2:
                            pe.wait_ge(p_ev[l], t - 1)
                        for j in range(MH):
                            mm = pe.transpose(ps[:, 4 + u, j * P:(j + 1) * P], h_z[u][:, j * P:(j + 1) * P], ident[:, :])
                        mm.then_inc(p_tr[l], 1)

                    def first_half(t, u):
                        for c in range(2):
                            for k in range(4):
                                pe.matmul(ps[:, 2 * u + c, :], att_t[:, k, t, :], w_out[:, k, 512 * c:512 * (c + 1)], start=k == 0, stop=False)

                    def second_half(t, u):
                        pe.wait_ge(p_ev[l], t + 1)
                        for c in range(2):
                            for k in range(4, KT):
                                mm = pe.matmul(ps[:, 2 * u + c, :], mix_st[u][:, k, :], w_out[:, k, 512 * c:512 * (c + 1)],
                                               start=False, stop=k == KT - 1)
                        mm.then_inc(p_mm[l], 1)

                    def product(t, u):
                        pe.wait_ge(p_ev[l], t + 1)
                        pe.wait_ge(p_att[l], t - 1)
                        pe.wait_ge(p_gated[l], t - 1)
                        for c in range(2):
                            for k in range(KT):
                                mm = pe.matmul(ps[:, 2 * u + c, :], mix_st[u][:, k, :], w_out[:, k, 512 * c:512 * (c + 1)],
                                               start=k == 0, stop=k == KT - 1)
                        mm.then_inc(p_mm[l], 1)

                    pe.wait_ge(p_w[l], 16)
                    for t in range(2):
                        first_half(t, t)
                    pe.wait_ge(m_h[l], 2 * nt)
                    pe.wait_ge(m_c[l], 2 * NTILE)
                    turn(0, 0)
                    turn(1, 1)
                    second_half(0, 0)
                    second_half(1, 1)
                    turn(2, 0)
                    last = NX // 2 if nt > NX else NX // 2 - 1
                    with pe.Fori(1, last) as i:
                        turn(2 * i + 1, 1)
                        product(2 * i, 0)
                        turn(2 * i + 2, 0)
                        product(2 * i + 1, 1)
                    turn(nt - 1, 1)
                    product(nt - 2, 0)
                    product(nt - 1, 1)

                modulation()
                norm_tm(l)
                ft(l)
                spread_gates(l)
                attention(l)
                mlstm(l)
                output(l)

            @block.vector
            def _(dve):
                def bcast(col, n):
                    return col.unsqueeze(2).to_broadcast([col.shape[0], col.shape[1], n])

                def setup():
                    dve.memset(minus_half[:, :], -0.5)
                    dve.memset(k_scale[:, :], LN_KSCALE)
                    dve.memset(m_dec[:, :], 0.0).then_inc(setup_dve, 1)
                    dve.wait_ge(const_ld, CONST_ALL)
                    dve.tensor_copy(ident_bf[:, :], ident[:, :]).then_inc(setup_dve, 1)
                    dve.tensor_scalar(neg_sink[:, :, :], sink[:, :, :], -1.0, None, ALU.mult).then_inc(setup_dve, 1)

                def scale_rows(t, u):
                    dve.wait_ge(nt_sq[l], t + 1)
                    dve.tensor_scalar(stat[:, 1, u:u + 1], stat[:, 0, u:u + 1], 1.0 / D_MODEL, EPS, ALU.mult, ALU.add)\
                        .then_inc(nt_ms[l], 1)
                    dve.wait_ge(nt_rs[l], t + 1)
                    if not isinstance(t, int) or t >= 2:
                        dve.wait_ge(nt_tr[l], t - 1)
                    dve.tensor_scalar(xs[u], xt[u], stat[:, 2, u:u + 1], None, ALU.mult).then_inc(nt_xs[l], 1)

                def modulation():
                    for t in range(2):
                        scale_rows(t, t)
                    dve.wait_ge(ada_b_ld, 16)
                    for n in range(6):
                        dve.wait_ge(ada_use, n + 1)
                        to = mod_rows[:, 512 * n:512 * (n + 1)] if n < 4 else gate_rows[64:66, 512 * (n - 4):512 * (n - 3)]
                        dve.tensor_tensor(to, ps[0:2, n, :], ada_b[:, 512 * n:512 * (n + 1)], ALU.add).then_inc(ada_row, 1)
                    dve.wait_ge(mod_tr, 1)
                    if l == 0:
                        dve.wait_ge(const_ld, CONST_ALL)
                    got = ps[:, 6, 0:4 * KT].rearrange("p (k v) -> p v k", v=2)
                    dve.tensor_copy(mod[:, :, :], got).then_inc(mod_col, 1)
                    dve.wait_ge(mod_col, 1)
                    dve.scalar_tensor_tensor(out=mod_scale[:, :, :], in0=mod[:, :, KT:2 * KT], scalar=1.0,
                                             in1=norm_g[:, l, :].unsqueeze(1).to_broadcast([P, 2, KT]), op0=ALU.add, op1=ALU.mult).then_inc(ada_done, 1)

                def spread_gates(l):
                    n_v = 2 if l < DEPTH - 1 else 1
                    dve.wait_ge(ft_mm[l], F_TILES)
                    dve.wait_ge(gt_mm, 1)
                    for v in range(n_v):
                        ins = dve.tensor_copy((gate, gate_c)[v], ps_flat[:, 2048 + 1024 * v:3072 + 1024 * v])
                    ins.then_inc(gt_ev, 1)

                def norm_tm(l):
                    def modulate(t, u, v):
                        dve.wait_ge(nt_tr[l], t + 1)
                        if not isinstance(t, int) or t >= 2:
                            dve.wait_ge(nt_v[l], t - 1)
                            dve.wait_ge(nt_cp[l], t - 1)
                        for k in range(4, KT):
                            ins = dve.tensor_scalar(xst[u][:, k, :], ps[:, 2 * u + 1, (k - 4) * P:(k - 3) * P],
                                                    mod_scale[:, v, k:k + 1], mod[:, v, k:k + 1], ALU.mult, ALU.add)
                        ins.then_inc(nt_ev_dve[l], 1)

                    def outputs(t, u, gates=True):
                        dve.wait_ge(nt_mv[l], t + 1)
                        dve.tensor_copy(mv_tm[:, t, :, 0:MD], ps[:, 4, :].rearrange("p (h d) -> p h d", h=MH))\
                            .then_inc(nt_mv_ev[l], 1)
                        if gates:
                            dve.wait_ge(nt_mo[l], t + 1)
                            if not isinstance(t, int) or t >= 2:
                                dve.wait_ge(nt_o_st[l][u], 16 * ((t - u) // 2) if isinstance(t, int) else 8 * (t - u))
                            dve.tensor_copy(o_st[u], ps[:, 6, :]).then_inc(nt_mo_ev[l], 1)
                        dve.wait_ge(nt_v[l], t + 1)
                        dve.tensor_copy(v_tm[:, t + 1 if not isinstance(t, int) or t < NX else t + 2, :], ps[:, 7, 0:P])\
                            .then_inc(nt_v_ev[l], 1)

                    dve.memset(v_tm[:, 0, :], 0.0)
                    dve.memset(v_tm[:, NX + 1, :], 0.0)
                    dve.memset(mv_tm[:, :, :, MD:MD + 1], 1.0).then_inc(pads[l], 1)
                    for t in range(2):
                        modulate(t, t, 0)
                    scale_rows(2, 0)
                    outputs(0, 0)
                    def tile(t, u):
                        modulate(t + 2, u, 0)
                        scale_rows(t + 3, 1 - u)
                        outputs(t + 1, 1 - u)

                    pairs(dve, NX // 2 - 1, tile)
                    modulate(8, 0, 1)
                    scale_rows(9, 1)
                    outputs(7, 1)
                    modulate(9, 1, 1)
                    outputs(8, 0, l < DEPTH - 1)
                    outputs(9, 1, l < DEPTH - 1)

                def rope(l, r, n, u, dest, ctx_dest):
                    if ctx_dest is not None:
                        dve.wait_ge(ft_ev[l], n + 1)
                        for at, rows in ctx_dest:
                            dve.tensor_copy(at, cst[u][rows, SEQ:NTOK])
                    dve.wait_ge(ft_rot[l], r + 1)
                    dve.wait_ge(ft_rope_a[l], r + 1)
                    dve.tensor_tensor(rope_b[u], ps_flat[:, 3072:4096], sin_t, ALU.mult).then_inc(ft_rotfree[l], 1)
                    dve.wait_ge(ft_rotfree[l], r + 1)
                    for at, rows in dest:
                        ins = dve.tensor_tensor(at, rope_a[u][rows, :], rope_b[u][rows, :], ALU.add)
                    ins.then_inc(ft_rope[l], 1)

                def gate_scans(l):
                    ch = g_chain[l]
                    dve.wait_ge(g_ln[l], 1)
                    ch.start(1)
                    fwd, bwd = slice(0, MH), slice(32, 32 + MH)
                    tiles_w, tiles_m, tiles_i, tiles_b, tiles_a = [
                        r.rearrange("p (t n) -> p t n", n=P) for r in (row_w, row_m, row_i, row_b, row_a)]
                    dve.scalar_tensor_tensor(out=row_b, in0=row_b, scalar=0.0, in1=row_i, op0=ALU.min, op1=ALU.subtract)
                    ch(dve, dve.memset(row_m, 1.0))
                    dve.memset(tiles_m[fwd, :, 0:1], 0.0)
                    ch(dve, dve.memset(tiles_m[bwd, :, P - 1:P], 0.0))
                    dve.tensor_tensor_scan(row_i[fwd], row_m[fwd], row_b[fwd], 0.0, ALU.mult, ALU.add)
                    dve.tensor_tensor_scan(row_i[bwd, ::-1], row_m[bwd, ::-1], row_b[bwd, ::-1], 0.0, ALU.mult, ALU.add)
                    ch(dve, dve.memset(row_w, 0.0))
                    dve.tensor_tensor(row_a, row_a, row_i, ALU.subtract)
                    dve.tensor_copy(tiles_w[fwd, 1:, 0], tiles_i[fwd, 0:NTILE - 1, P - 1])
                    dve.tensor_copy(tiles_w[fwd, 0:1, 0], tiles_i[fwd, NTILE - 1:, P - 1])
                    ch(dve, dve.tensor_copy(tiles_w[bwd, 0:NTILE - 1, P - 1], tiles_i[bwd, 1:, 0]))
                    dve.tensor_tensor_scan(row_m[bwd, ::-1], row_w[bwd, ::-1], row_a[bwd, ::-1], -BIG, ALU.add, ALU.max)
                    ch(dve, dve.tensor_tensor_scan(row_m[fwd, SEQ:], row_w[fwd, SEQ:], row_a[fwd, SEQ:], -BIG, ALU.add, ALU.max))
                    ch(dve, dve.tensor_tensor_scan(row_m[fwd, 0:SEQ], row_w[fwd, 0:SEQ], row_a[fwd, 0:SEQ], row_m[fwd, NTOK - 1:],
                                                   ALU.add, ALU.max))
                    dve.tensor_tensor(m_state[fwd, 1:NTILE], tiles_w[fwd, 1:, 0], tiles_m[fwd, 0:NTILE - 1, P - 1], ALU.add)
                    dve.tensor_tensor(m_state[fwd, 0:1], tiles_w[fwd, 0:1, 0], tiles_m[fwd, NTILE - 1:, P - 1], ALU.add)
                    dve.tensor_tensor(m_state[bwd, 0:NTILE - 1], tiles_w[bwd, 0:NTILE - 1, P - 1], tiles_m[bwd, 1:, 0], ALU.add)
                    ch(dve, dve.memset(m_state[bwd, NTILE - 1:NTILE], -BIG))
                    ch(dve, dve.memset(m_state[fwd, NX:NX + 1], -BIG))
                    for r, end in ((fwd, P - 1), (bwd, 0)):
                        m_last = tiles_m[r, :, end]
                        dve.tensor_tensor(tiles_w[r], tiles_a[r], bcast(m_last, P), ALU.subtract)
                        dve.tensor_tensor(m_dec[r, 0:NTILE], m_state[r, 0:NTILE], m_last, ALU.subtract)
                        ins = dve.tensor_tensor(row_b[r], row_i[r], row_m[r], ALU.add)
                    ch(dve, ins)
                    for r in (fwd, bwd):
                        ins = dve.tensor_tensor(tiles_i[r], bcast(m_state[r, 0:NTILE], P), tiles_m[r], ALU.subtract)
                    ins.then_inc(g_rows[l], 1)

                def conv(l, c, u):
                    n = N_MQ + c
                    dve.wait_ge(ft_ev[l], n + 1)
                    if not isinstance(c, int) or c > 0:
                        dve.wait_ge(ft_silu[l], c)
                    ch = ft_chain[l]
                    ch.start((CONV_K - 1) * c)
                    w = conv_w[:, l, :, :].rearrange("p c k -> p (c k)")

                    def tap(k):
                        return w[:, bass.ds(c * CONV_K + k, 1)]

                    a = acc[:, 0:ACC_LEN]
                    ch(dve, dve.tensor_scalar(a, cst[u][:, 0:ACC_LEN], tap(0), None, ALU.mult))
                    for k in range(1, CONV_K):
                        ins = dve.scalar_tensor_tensor(out=a, in0=cst[u][:, k:k + ACC_LEN], scalar=tap(k), in1=a,
                                                       op0=ALU.mult, op1=ALU.add)
                        if k < CONV_K - 1:
                            ch(dve, ins)
                    ins.then_inc(ft_conv[l], 1)
                    assert ch.n == CONV_K - 1

                def ft(l):
                    nt = layer_tiles(l)
                    ch = g_chain[l]
                    dve.wait_ge(ft_ev[l], 1)
                    ch.start(0)
                    ch(dve, dve.tensor_scalar(row_b, row_b, gate_b[:, l, 1:2], None, ALU.add))
                    dve.scalar_tensor_tensor(out=row_m, in0=row_b, scalar=-1.0, in1=row_b, op0=ALU.mult, op1=ALU.min)\
                        .then_inc(g_abs[l], 1)
                    dve.wait_ge(ft_trig[l], 32)
                    halves = [slice(g * DH, (g + 1) * DH) for g in range(KV)]
                    rope(l, 0, N_K, 1, [(k_raw[r, P + g * NTOK:][:, 0:SEQ], r) for g, r in enumerate(halves)],
                         [(k_raw[r, P + g * NTOK + SEQ:][:, 0:CTX], r) for g, r in enumerate(halves)])
                    everything = slice(0, P)
                    with dve.Fori(0, 2) as j:
                        for u in range(2):
                            n = 2 * j + u
                            rope(l, n + 1, N_Q + n, u, [(q_flat[:, n, 0:SEQ], everything)],
                                 [(q_flat[:, n, SEQ:NTOK], everything)] if nt > NX else None)
                    gate_scans(l)
                    for u in range(2):
                        dve.wait_ge(ft_az_st[l][u], 32)
                        dve.memset(cst[u][:, 0:2], 0.0)
                        dve.memset(cst[u][:, SEQ + 2:SEQ + 6], 0.0)
                        ins = dve.memset(cst[u][:, CONV_LEN - 2:CONV_LEN], 0.0)
                    ins.then_inc(pads[l], 1)
                    pairs(dve, 4, lambda c, u: conv(l, c, u))
                    for n in range(3):
                        dve.wait_ge(g_tr[l], n + 1)
                        dve.tensor_copy(cols[:, n].rearrange("p t r -> p (t r)"), ps[:, n, 0:36 * NTILE]).then_inc(g_cols[l], 1)
                    dve.wait_ge(g_tr[l], 4)
                    dve.tensor_copy(decay_b[:, :, :].rearrange("p n j -> p (n j)"), ps[:, 3, 0:2 * MH * NTILE]).then_inc(g_cols[l], 1)

                def attention(l):
                    ch, fin = a_chain[l], a_fin[l]

                    def head_max(s, u, h, n_win):
                        dve.wait_ge(a_s[l], s + 1)
                        r = h % 2
                        at = ps_flat[:, 1024 * r + P:1024 * r + P + NKEY] if n_win else ps[:, 2 * r + 1, 0:CTX]
                        ch.start(s)
                        ch(dve, dve.tensor_reduce(row_max[:, u, h:h + 1], at, AX_X, ALU.max, negate=True))
                        dve.tensor_scalar(neg_max[:, u, h:h + 1], row_max[:, u, h:h + 1], DH ** -0.5, neg_sink[:, l, h:h + 1],
                                          ALU.mult, ALU.min).then_inc(a_nm[l], 1)

                    def divide(b, u):
                        fin.start(2 * b)
                        dve.wait_ge(a_sink_e[l], b + 1)
                        fin(dve, dve.tensor_tensor(lsum[:, u, :], lsum[:, u, :], sink_e[:, u, :], ALU.add))
                        fin(dve, dve.reciprocal(recip[:, u, :], lsum[:, u, :]))
                        dve.wait_ge(a_pv[l], HEADS * b + HEADS)
                        if not isinstance(b, int) or b > 0:
                            dve.wait_ge(a_att_tr[l], b)
                        dve.tensor_tensor(att_tm, ps[:, 6, :].rearrange("p (h d) -> p h d", h=HEADS), bcast(recip[:, u, :], DH), ALU.mult)\
                            .then_inc(a_att[l], 1)

                    def gate_out(b, u):
                        dve.wait_ge(a_att_tr[l], b + 1)
                        dve.wait_ge(a_az[l][u], (8 * (b - u) if not isinstance(b, int) else 16 * (b // 2)) + 16)
                        dve.tensor_tensor(att_t[:, :, b, :], ps[:, 7, :].rearrange("p (j n) -> p j n", j=4), az_st[u], ALU.mult)\
                            .then_inc(a_out[l], 1)

                    def query_block(b, u, n_win, next_win):
                        s0 = HEADS * b
                        later = not isinstance(b, int) or b > 0
                        for h in range(HEADS):
                            dve.wait_ge(a_t[l], s0 + h + 1)
                            n = turned(n_win)[0]
                            dve.tensor_copy(prob_t[h % 2][:, 0:n, :], ps[:, 4, 0:n * P].rearrange("p (n q) -> p n q", n=n))\
                                .then_inc(a_t_dve[l], 1)
                            if h + 2 < HEADS:
                                head_max(s0 + h + 2, u, h + 2, n_win)
                            elif next_win is not None:
                                head_max(s0 + h + 2, 1 - u, h + 2 - HEADS, next_win)
                            if h == HEADS - 3:
                                dve.wait_ge(a_nm[l], s0 + HEADS)
                                dve.tensor_tensor(sink_e[:, u, :], neg_max[:, u, :], sink[:, l, :], ALU.add).then_inc(a_sink[l], 1)
                            if h == 0 and later:
                                divide(b - 1, 1 - u)
                            if h == 3 and later:
                                gate_out(b - 1, 1 - u)
                            if h % 4 == 3 and next_win is not None:
                                split_queries(b + 1, h // 4)
                            if isinstance(b, int) and b == NX - 1 and h in (4, 5):
                                low_rows(h - 4)

                    def low_rows(n):
                        dve.wait_ge(m_high, n + 1)
                        dve.tensor_tensor(row_hl[n][64:100, :], (row_m, row_i)[n], row_hl[n][0:36, :].bitcast(F32), ALU.subtract).then_inc(m_rows, 1)

                    def rows(g):
                        return slice(g * DH, (g + 1) * DH)

                    def split_keys(g):
                        own, other, at = rows(g), rows(1 - g), slice(P + g * NTOK, P + (g + 1) * NTOK)
                        dve.tensor_copy(k_hi[other, at], k_raw[own, at])
                        dve.wait_ge(a_kh[l], g + 1)
                        dve.tensor_tensor(k_lo[other, at], k_raw[own, at], k_hi[own, at].bitcast(F32), ALU.subtract).then_inc(a_kl[l], 1)
                        if g == 0:
                            dve.wait_ge(a_kl[l], 1)
                            dve.tensor_tensor(k_lo[own, at], k_raw[own, at], k_hi[own, at].bitcast(F32), ALU.subtract).then_inc(a_k[l], 1)

                    def split_queries(b, g):
                        dve.wait_ge(a_qh[l], 2 * b + g + 1)
                        dve.tensor_tensor(q_hl[g][rows(1 - g), :, :], q_t[rows(g), :, b, :], q_hl[g][rows(g), :, :].bitcast(F32), ALU.subtract)\
                            .then_inc(a_q[l], 1)

                    dve.wait_ge(ft_silu[l], 8)
                    for k in (k_hi, k_lo):
                        dve.tensor_scalar(k[:, 0:P], ident[:, :], 0.0, None, ALU.mult)
                    split_queries(0, 0)
                    split_keys(0)
                    spread_gates(l)
                    head_max(0, 0, 0, WIN)
                    head_max(1, 0, 1, WIN)
                    split_queries(0, 1)
                    split_keys(1)
                    query_blocks(dve, query_block)
                    last = layer_tiles(l) - 1
                    divide(last, last % 2)
                    gate_out(last, last % 2)

                def mlstm(l):
                    nt = layer_tiles(l)
                    ch = m_chain[l]
                    dve.wait_ge(a_out[l], nt)
                    dve.wait_ge(a_pv[l], HEADS * nt)
                    dve.memset(c_state, 0.0).then_inc(m_init[l], 1)

                    def before(n, d, tile):
                        c = n - 2 * (NTILE - nt)
                        dve.wait_ge(m_m[l], c + 1)
                        if not isinstance(c, int) or c >= 2:
                            dve.wait_ge(m_d[l], c - 1)
                        a_col = cols[:, 0].rearrange("p t r -> p (t r)")
                        for h in range(MH):
                            ins = dve.scalar_tensor_tensor(out=dec_y[d][:, h, :], in0=ps[:, 1, h * P:(h + 1) * P],
                                                           scalar=a_col[:, bass.ds(tile * 36 + 32 * d + h, 1)], in1=tri[:, d, :],
                                                           op0=ALU.subtract, op1=ALU.max)
                        ins.then_inc(m_y[l], 1)
                        dve.wait_ge(m_w[l], c + 1)
                        if not isinstance(c, int) or c >= 2:
                            dve.wait_ge(m_num[l], c - 1)
                        dve.tensor_tensor(q_w[d], ps[:, 2, :].rearrange("p (h t) -> p h t", h=MH), qk_st[d][:, 0:MH, :], ALU.mult)\
                            .then_inc(m_qs[l], 1)

                    def weigh(n, d):
                        c = n - 2 * (NTILE - nt)
                        dve.wait_ge(m_s[l], c + 1)
                        dve.wait_ge(m_d[l], c + 1)
                        dve.tensor_tensor(p_t[d], ps[:, 0, :].rearrange("p (h t) -> p h t", h=MH), dec_y[d], ALU.mult)\
                            .then_inc(m_p[l], 1)

                    def denominators(n, d, tile):
                        c = n - 2 * (NTILE - nt)
                        ch.start(3 * c)
                        dve.wait_ge(m_num[l], c + 1)
                        num = ps[:, 4:6, 0:2 * (MD + 1)].rearrange("p b (h v) -> p b h v", h=2)
                        ch(dve, dve.tensor_copy(den[:, d, 0, :].rearrange("p (b h) -> p b h", b=2), num[:, :, :, MD]))
                        ch(dve, dve.scalar_tensor_tensor(out=den[:, d, 1, :], in0=den[:, d, 0, :], scalar=-1.0, in1=den[:, d, 0, :],
                                                         op0=ALU.mult, op1=ALU.max))
                        ch(dve, dve.tensor_tensor(den[:, d, 2, :], den[:, d, 1, :], cols[:, 2, tile, 32 * d:32 * d + MH], ALU.max))
                        dve.reciprocal(den[:, d, 3, :], den[:, d, 2, :]).then_inc(m_inv[l], 1)

                    def after(n, d, tile, outputs):
                        if outputs:
                            denominators(n, d, tile)
                        dve.wait_ge(m_del[l], n + 1)
                        dec = decay_b[:, :, :].rearrange("p n j -> p (n j)")
                        for h in range(MH):
                            c_h = c_state[:, d * MH + h, :]
                            ins = dve.scalar_tensor_tensor(out=c_h, in0=c_h, scalar=dec[:, bass.ds((d * MH + h) * NTILE + tile, 1)],
                                                           in1=ps[:, 6 + h // 2, (MD + 1) * (h % 2):(MD + 1) * (h % 2 + 1)],
                                                           op0=ALU.mult, op1=ALU.add)
                        ins.then_inc(m_c[l], 1)

                    def ahead(n, d, tile, outputs):
                        if outputs:
                            before(n, d, tile)
                            weigh(n, d)

                    def step(j, tiles, outputs, next_tile, next_outputs):
                        ahead(2 * j + 1, 1, tiles[1], outputs)
                        after(2 * j, 0, tiles[0], outputs)
                        if next_tile is not None:
                            ahead(2 * j + 2, 0, next_tile, next_outputs)
                        after(2 * j + 1, 1, tiles[1], outputs)

                    ahead(0, 0, NX, nt > NX)
                    mlstm_steps(dve, step, nt > NX)

                def output(l):
                    nt = layer_tiles(l)

                    def heads_norm(t, u):
                        dve.wait_ge(p_sig[l], t + 1)
                        dve.wait_ge(p_sum[l], t + 1)
                        dve.tensor_tensor(h_g[u], h_sum[u], o_in[u], ALU.mult).then_inc(p_hg[l], 1)
                        dve.wait_ge(p_sq[l], t + 1)
                        dve.tensor_scalar(stat[:, 1, 0:MH], stat[:, 0, 0:MH], 1.0 / MD, EPS, ALU.mult, ALU.add).then_inc(p_ms[l], 1)
                        dve.wait_ge(p_rs[l], t + 1)
                        if not isinstance(t, int) or t > 0:
                            dve.wait_ge(p_hz[l], t)
                        dve.tensor_tensor(h_n.rearrange("p (h v) -> p h v", h=MH), h_g[u].rearrange("p (h v) -> p h v", h=MH),
                                          bcast(stat[:, 2, 0:MH], MD), ALU.mult).then_inc(p_hn[l], 1)

                    def residual(t, u, gate):
                        dve.wait_ge(p_mm[l], t + 1)
                        if not isinstance(t, int) or t > 0:
                            dve.wait_ge(p_new[l], t)
                        dve.tensor_tensor(gated, ps_flat[:, 1024 * u:1024 * u + 1024], gate, ALU.mult).then_inc(p_gated[l], 1)
                        dve.wait_ge(p_gated[l], t + 1)
                        dve.wait_ge(p_x[l][u], (8 * (t - u) if not isinstance(t, int) else 16 * (t // 2)) + 16)
                        if not isinstance(t, int) or t >= 2:
                            dve.wait_ge(p_store[l][u], 8 * (t - u) if not isinstance(t, int) else 16 * (t // 2))
                        dve.tensor_tensor(x_new[u], gated, x_in[u], ALU.add).then_inc(p_new[l], 1)
                        if l == DEPTH - 1:
                            dve.wait_ge(f_sq, t + 1)
                            dve.tensor_scalar(stat[:, 1, 4:5], stat[:, 0, 4:5], 1.0 / D_MODEL, EPS, ALU.mult, ALU.add).then_inc(f_ms, 1)
                            dve.wait_ge(f_rs, t + 1)
                            dve.scalar_tensor_tensor(out=x_new[u], in0=x_new[u], scalar=stat[:, 2, 4:5], in1=final_g,
                                                     op0=ALU.mult, op1=ALU.mult).then_inc(f_x, 1)

                    if l == DEPTH - 1:
                        dve.wait_ge(p_fg[l], 16)
                    for t in range(3):
                        heads_norm(t, t % 2)
                    def tile(t, u):
                        heads_norm(t + 3, 1 - u)
                        residual(t, u, gate)

                    pairs(dve, NX // 2 - 2, tile)
                    for t in range(NX - 4, nt):
                        if t + 3 < nt:
                            heads_norm(t + 3, (t + 3) % 2)
                        residual(t, t % 2, gate if t < NX else gate_c)

                if l == 0:
                    setup()
                modulation()
                norm_tm(l)
                ft(l)
                attention(l)
                mlstm(l)
                output(l)

            @block.scalar
            def _(act):
                def modulation():
                    if l == 0:
                        act.wait_ge(const_ld, CONST_ALL)
                        act.activation(scc[:, :, :], cc[:, :, :], ACT.Silu).then_inc(silu_c, 1)

                def norm_tm(l):
                    def squares(t, u):
                        act.wait_ge(nt_ld[l][u], (8 * (t - u) if not isinstance(t, int) else 16 * (t // 2)) + 16)
                        act.activation(junk[u], xt[u], ACT.Square, accum_out=stat[:, 0, u:u + 1]).then_inc(nt_sq[l], 1)

                    def modulate(t, u, v):
                        act.wait_ge(nt_tr[l], t + 1)
                        if not isinstance(t, int) or t >= 2:
                            act.wait_ge(nt_v[l], t - 1)
                            act.wait_ge(nt_cp[l], t - 1)
                        for k in range(4):
                            ins = act.activation(xst[u][:, k, :], ps[:, 2 * u, k * P:(k + 1) * P], ACT.Identity,
                                                 bias=mod[:, v, k:k + 1], scale=mod_scale[:, v, k:k + 1])
                        ins.then_inc(nt_ev_act[l], 1)

                    def gate(t, u):
                        act.wait_ge(nt_mz[l], t + 1)
                        if not isinstance(t, int) or t >= 2:
                            act.wait_ge(nt_z_st[l][u], 16 * (t // 2) if isinstance(t, int) else 8 * (t - u))
                        act.activation(z_st[u], ps[:, 5, :], ACT.Silu).then_inc(nt_mz_ev[l], 1)

                    for t in range(2):
                        squares(t, t)
                    act.wait_ge(ada_done, 1)
                    for t in range(2):
                        modulate(t, t, 0)
                    squares(2, 0)
                    gate(0, 0)
                    def tile(t, u):
                        modulate(t + 2, u, 0)
                        squares(t + 3, 1 - u)
                        gate(t + 1, 1 - u)

                    pairs(act, NX // 2 - 1, tile)
                    modulate(8, 0, 1)
                    squares(9, 1)
                    gate(7, 1)
                    modulate(9, 1, 1)
                    if l < DEPTH - 1:
                        gate(8, 0)
                        gate(9, 1)

                def ft(l):
                    nt = layer_tiles(l)
                    for stored in (nt_z_st[l], nt_o_st[l]):
                        for u in range(2):
                            act.wait_ge(stored[u], 16 * (nt // 2))
                    act.wait_ge(ft_mm[l], 1)
                    act.activation(row_a, ps_flat[0:36, 0:NTOK], ACT.Identity, bias=gate_b[:, l, 0:1])
                    act.activation(row_b, ps_flat[64:100, 0:NTOK], ACT.Copy).then_inc(ft_ev[l], 1)
                    act.wait_ge(g_abs[l], 1)
                    ch = g_act_chain[l]
                    ch(act, act.activation(row_w, row_m, ACT.Exp))
                    act.activation(row_i, row_w, ACT.Ln, bias=1.0).then_inc(g_ln[l], 1)

                    def raw(r, n, u, ntok):
                        act.wait_ge(ft_mm[l], n + 1)
                        if not isinstance(r, int) or r >= 2:
                            act.wait_ge(ft_rope[l], r - 1)
                        act.activation(cst[u][:, 0:ntok], ps_flat[:, 1536 * u:1536 * u + ntok], ACT.Copy).then_inc(ft_ev[l], 1)

                    raw(0, N_K, 1, NTOK)
                    raw(1, N_Q, 0, nt * P)
                    raw(2, N_Q + 1, 1, nt * P)
                    raw(3, N_Q + 2, 0, nt * P)
                    raw(4, N_Q + 3, 1, nt * P)
                    for j in range(4):
                        u = j % 2
                        act.wait_ge(ft_mm[l], N_AZ + j + 1)
                        if j < 2:
                            act.wait_ge(ft_rope[l], 4 + u)
                        else:
                            act.wait_ge(ft_az_st[l][u], 16)
                        act.activation(cst[u][:, 0:nt * P], ps_flat[:, 1536 * u:1536 * u + nt * P], ACT.Silu).then_inc(ft_ev[l], 1)
                        act.wait_ge(ft_ev[l], N_AZ + j + 1)
                        act.dma_start(az_dram[l][j, :, 0:nt, :], cst[u][:, 0:nt * P].rearrange("p (t n) -> p t n", n=P))\
                            .then_inc(ft_az_st[l][u], 16)
                    act.wait_ge(g_rows[l], 1)
                    act.activation(row_w, row_w, ACT.Exp, bias=k_scale[0:36, :]).then_inc(g_exp[l], 1)
                    act.activation(row_i, row_i, ACT.Exp).then_inc(g_exp[l], 1)
                    act.activation(row_b, row_b, ACT.Exp, scale=-1.0).then_inc(g_exp[l], 1)
                    act.activation(m_dec[:, :], m_dec[:, :], ACT.Exp).then_inc(g_exp[l], 1)
                    act.wait_ge(pads[l], 2)
                    act.wait_ge(ft_rope[l], 5)

                    def taps_in(c, u, ntok):
                        act.wait_ge(ft_mm[l], N_MQ + c + 1)
                        if not isinstance(c, int) or c >= 2:
                            act.wait_ge(ft_conv[l], c - 1)
                        if ntok > SEQ:
                            act.activation(cst[u][:, SEQ + 6:SEQ + 6 + CTX], ps_flat[:, 1536 * u + SEQ:1536 * u + NTOK], ACT.Copy)
                        act.activation(cst[u][:, 2:2 + SEQ], ps_flat[:, 1536 * u:1536 * u + SEQ], ACT.Copy).then_inc(ft_ev[l], 1)

                    def silu(c, ntok):
                        act.wait_ge(ft_conv[l], c + 1)
                        bias = conv_b[:, l, bass.ds(c, 1)]
                        ins = act.activation(mqk_flat[:, c, 0:SEQ], acc[:, 0:SEQ], ACT.Silu, bias=bias)
                        if ntok > SEQ:
                            ins = act.activation(mqk_flat[:, c, SEQ:NTOK], acc[:, SEQ + 4:ACC_LEN], ACT.Silu, bias=bias)
                        ins.then_inc(ft_silu[l], 1)

                    def pair(i, ntok):
                        for u in range(2):
                            taps_in(2 * i + u, u, ntok)
                        for u in range(2):
                            silu(2 * i + u, ntok)

                    for i in range(2):
                        pair(i, nt * P)
                    with act.Fori(2, 4) as i:
                        pair(i, NTOK)

                def attention(l):
                    def exps(s, u, h, n_win):
                        act.wait_ge(a_nm[l], s + 1)
                        r, n = h % 2, n_win + CTX
                        at = ps_flat[:, 1024 * r + P:1024 * r + P + NKEY] if n_win else ps[:, 2 * r + 1, 0:CTX]
                        act.activation(prob[r][:, 0:n], at, ACT.Exp, bias=neg_max[:, u, h:h + 1], scale=DH ** -0.5,
                                       accum_out=lsum[:, u, h:h + 1]).then_inc(a_e[l], 1)

                    def query_block(b, u, n_win, next_win):
                        s0 = HEADS * b
                        for h in range(HEADS):
                            act.wait_ge(a_t2[l], s0 + h + 1)
                            m, n = turned(n_win)
                            act.activation(prob_t[h % 2][:, m:m + n, :], ps[:, 5, 0:n * P].rearrange("p (n q) -> p n q", n=n), ACT.Copy)\
                                .then_inc(a_t_act[l], 1)
                            if h + 2 < HEADS:
                                exps(s0 + h + 2, u, h + 2, n_win)
                            elif next_win is not None:
                                exps(s0 + h + 2, 1 - u, h + 2 - HEADS, next_win)
                            if h == HEADS - 2:
                                act.wait_ge(a_sink[l], b + 1)
                                act.activation(sink_e[:, u, :], sink_e[:, u, :], ACT.Exp).then_inc(a_sink_e[l], 1)

                    act.wait_ge(ft_silu[l], 8)
                    for g in range(KV):
                        own, at = slice(g * DH, (g + 1) * DH), slice(P + g * NTOK, P + (g + 1) * NTOK)
                        act.activation(k_hi[own, at], k_raw[own, at], ACT.Copy).then_inc(a_kh[l], 1)
                    exps(0, 0, 0, WIN)
                    exps(1, 0, 1, WIN)
                    query_blocks(act, query_block)

                def mlstm(l):
                    nt = layer_tiles(l)

                    def weigh_keys(n, d, tile):
                        act.wait_ge(m_k[l], n + 1)
                        if not isinstance(n, int) or n >= 2:
                            act.wait_ge(m_del[l], n - 1)
                        w_col = cols[:, 1].rearrange("p t r -> p (t r)")
                        for h in range(MH):
                            ins = act.activation(k_w[d][:, h, :], ps[:, 3, h * P:(h + 1) * P], ACT.Copy,
                                                 scale=w_col[:, bass.ds(tile * 36 + 32 * d + h, 1)])
                        ins.then_inc(m_kw[l], 1)

                    def decays(n, d):
                        c = n - 2 * (NTILE - nt)
                        act.wait_ge(m_y[l], c + 1)
                        act.activation(dec_y[d], dec_y[d], ACT.Exp, scale=-1.0, bias=k_scale[:, :]).then_inc(m_d[l], 1)

                    def divide(n, d, tile):
                        act.wait_ge(m_inv[l], n - 2 * (NTILE - nt) + 1)
                        for h in range(MH):
                            num = ps[:, 4 + h // 2, (MD + 1) * (h % 2):(MD + 1) * (h % 2) + MD]
                            ins = act.activation(h_dir[d][:, tile, h * MD:(h + 1) * MD], num, ACT.Copy, scale=den[:, d, 3, h:h + 1])
                        ins.then_inc(m_h[l], 1)

                    def ahead(n, d, tile, outputs):
                        if outputs:
                            decays(n, d)
                        weigh_keys(n, d, tile)

                    def step(j, tiles, outputs, next_tile, next_outputs):
                        ahead(2 * j + 1, 1, tiles[1], outputs)
                        if outputs:
                            divide(2 * j, 0, tiles[0])
                        if next_tile is not None:
                            ahead(2 * j + 2, 0, next_tile, next_outputs)
                        if outputs:
                            divide(2 * j + 1, 1, tiles[1])

                    act.wait_ge(m_init[l], 1)
                    ahead(0, 0, NX, nt > NX)
                    mlstm_steps(act, step, nt > NX)

                def output(l):
                    nt = layer_tiles(l)

                    def gate(t, u):
                        act.wait_ge(p_o[l][u], (8 * (t - u) if not isinstance(t, int) else 16 * (t // 2)) + 16)
                        act.activation(o_in[u], o_in[u], ACT.Sigmoid).then_inc(p_sig[l], 1)
                        act.wait_ge(p_hg[l], t + 1)
                        if not isinstance(t, int) or t > 0:
                            act.wait_ge(p_ms[l], t)
                        for h in range(MH):
                            ins = act.activation(sq_junk[:, h * P:(h + 1) * P], h_g[u][:, h * MD:(h + 1) * MD], ACT.Square,
                                                 accum_out=stat[:, 0, h:h + 1])
                        ins.then_inc(p_sq[l], 1)

                    def gains(t, u):
                        act.wait_ge(p_tr[l], t + 1)
                        if not isinstance(t, int) or t >= 2:
                            act.wait_ge(p_mm[l], t - 1)
                        for j in range(MH):
                            ins = act.activation(mix_st[u][:, 4 + j, :], ps[:, 4 + u, j * P:(j + 1) * P], ACT.Copy,
                                                 scale=head_g[:, l, j:j + 1])
                        ins.then_inc(p_ev[l], 1)

                    def last_norm(t, u):
                        if l < DEPTH - 1:
                            return
                        act.wait_ge(p_new[l], t + 1)
                        act.activation(sq_last, x_new[u], ACT.Square, accum_out=stat[:, 0, 4:5]).then_inc(f_sq, 1)

                    act.wait_ge(m_del[l], 2 * NTILE)
                    gate(0, 0)
                    gate(1, 1)
                    gains(0, 0)
                    gains(1, 1)
                    gate(2, 0)
                    with act.Fori(0, NX // 2 - 2) as i:
                        for u in range(2):
                            gate(2 * i + u + 3, 1 - u)
                            last_norm(2 * i + u, u)
                            gains(2 * i + u + 2, u)
                    for t in range(NX - 4, nt):
                        if t + 3 < nt:
                            gate(t + 3, (t + 3) % 2)
                        last_norm(t, t % 2)
                        if t + 2 < nt:
                            gains(t + 2, t % 2)

                modulation()
                norm_tm(l)
                ft(l)
                attention(l)
                mlstm(l)
                output(l)

            @block.gpsimd
            def _(pool):
                def inverse_root(dst, src, n):
                    return pool.tensor_tensor(dst, src, minus_half[:, 0:n], ALU.pow)

                def norm_tm(l):
                    def roots(t, u):
                        pool.wait_ge(nt_ms[l], t + 1)
                        inverse_root(stat[:, 2, u:u + 1], stat[:, 1, u:u + 1], 1).then_inc(nt_rs[l], 1)

                    def keep(t, u):
                        pool.wait_ge(nt_ev_act[l], t + 1)
                        pool.wait_ge(nt_ev_dve[l], t + 1)
                        pool.tensor_copy(xn_t[:, :, t, :], xst[u]).then_inc(nt_cp[l], 1)

                    roots(0, 0)
                    roots(1, 1)
                    keep(0, 0)
                    with pool.Fori(0, NX // 2) as i:
                        for u in range(2):
                            roots(2 * i + u + 2, u)
                            keep(2 * i + u + 1, 1 - u)
                    keep(NTILE - 1, 1)

                def ft(l):
                    def rope(r, n, u):
                        pool.wait_ge(ft_ev[l], n + 1)
                        if not isinstance(r, int) or r >= 2:
                            pool.wait_ge(ft_rope[l], r - 1)
                        pool.tensor_tensor(rope_a[u], cst[u][:, 0:SEQ], cos_t, ALU.mult).then_inc(ft_rope_a[l], 1)

                    pool.wait_ge(ft_trig[l], 32)
                    rope(0, N_K, 1)
                    rope(1, N_Q, 0)
                    rope(2, N_Q + 1, 1)
                    rope(3, N_Q + 2, 0)
                    rope(4, N_Q + 3, 1)

                def attention(l):
                    def round_queries(b):
                        for g in range(KV):
                            if not isinstance(b, int) or b > 0:
                                pool.wait_ge(a_s[l], HEADS * (b - 1) + 4 * g + 4)
                            own = slice(g * DH, (g + 1) * DH)
                            pool.tensor_copy(q_hl[g][own, :, :], q_t[own, :, b, :]).then_inc(a_qh[l], 1)

                    pool.wait_ge(ft_rope[l], 5)
                    pool.wait_ge(ft_mm[l], F_TILES)
                    round_queries(0)
                    own, at = slice(DH, P), slice(P + NTOK, P + 2 * NTOK)
                    pool.wait_ge(a_kh[l], 2)
                    pool.wait_ge(a_kl[l], 2)
                    pool.tensor_tensor(k_lo[own, at], k_raw[own, at], k_hi[own, at].bitcast(F32), ALU.subtract).then_inc(a_k[l], 1)
                    round_queries(1)
                    pool.wait_ge(g_cols[l], 4)
                    for b in range(2, layer_tiles(l)):
                        round_queries(b)
                        n = b // 2 - 1
                        if b > 6:
                            continue
                        pool.wait_ge(a_qh[l], 2 * b + 2)
                        if b == 6:
                            pool.wait_ge(m_sel_ld, 16)
                            pool.tensor_copy(sel_hl[0:100, :, :], sel_raw[0:100, :, :]).then_inc(m_high, 1)
                            pool.wait_ge(m_high, 3)
                        elif b % 2 == 0:
                            zeros = v_tm[32:64, 0:1, :].to_broadcast([32, NTILE, P])
                            pool.tensor_copy(row_hl[n][32:64, :].rearrange("p (t n) -> p t n", n=P), zeros).then_inc(m_zero, 1)
                            pool.wait_ge(m_zero, n + 1)
                        else:
                            pool.tensor_copy(row_hl[n][0:36, :], (row_m, row_i)[n]).then_inc(m_high, 1)
                            pool.wait_ge(m_high, n + 1)

                def mlstm(l):
                    nt = layer_tiles(l)

                    def stage(n, d, tile):
                        if not isinstance(n, int) or n >= 2:
                            c = n - 2 * (NTILE - nt)
                            pool.wait_ge(m_k[l], n - 1)
                            if not isinstance(c, int) or c >= 2:
                                pool.wait_ge(m_qs[l], c - 1)
                                pool.wait_ge(m_s[l], c - 1)
                        pool.tensor_copy(qk_st[d], mqk_t[:, :, tile, :]).then_inc(m_st[l], 1)

                    pool.wait_ge(a_s[l], HEADS * nt)
                    pool.wait_ge(a_pv[l], HEADS * (nt - 1))
                    pool.wait_ge(ft_silu[l], 8)

                    def step(j, tiles):
                        for d in range(2):
                            stage(2 * j + d, d, tiles[d])

                    for j in range(NC):
                        step(j, (NX + j, NX + NC - 1 - j))
                    first = 0
                    if l == DEPTH - 1:
                        step(NC, (0, NX - 1))
                        first = 1
                    with pool.Fori(first, NX) as i:
                        step(i + NC, (i, i * -1 + (NX - 1)))

                def output(l):
                    nt = layer_tiles(l)
                    pool.wait_ge(m_h[l], 2 * nt)
                    pool.wait_ge(m_del[l], 2 * NTILE)

                    def join(t, u):
                        if not isinstance(t, int) or t >= 2:
                            pool.wait_ge(p_hg[l], t - 1)
                        pool.tensor_tensor(h_sum[u], h_dir[0][:, t, :], h_dir[1][:, t, :], ALU.add).then_inc(p_sum[l], 1)

                    def attended(t, u):
                        pool.wait_ge(p_mm[l], t - 1)
                        pool.tensor_copy(mix_st[u][:, 0:4, :], att_t[:, :, t, :]).then_inc(p_att[l], 1)

                    def heads(t, u):
                        pool.wait_ge(p_ms[l], t + 1)
                        inverse_root(stat[:, 2, 0:MH], stat[:, 1, 0:MH], MH).then_inc(p_rs[l], 1)
                        pool.wait_ge(p_hn[l], t + 1)
                        pool.wait_ge(p_z[l][u], (8 * (t - u) if not isinstance(t, int) else 16 * (t // 2)) + 16)
                        if not isinstance(t, int) or t >= 2:
                            pool.wait_ge(p_tr[l], t - 1)
                        pool.tensor_tensor(h_z[u], h_n, z_in[u], ALU.mult).then_inc(p_hz[l], 1)

                    def last_root(t):
                        if l < DEPTH - 1:
                            return
                        pool.wait_ge(f_ms, t + 1)
                        inverse_root(stat[:, 2, 4:5], stat[:, 1, 4:5], 1).then_inc(f_rs, 1)

                    for t in range(3):
                        join(t, t % 2)
                        heads(t, t % 2)
                    with pool.Fori(0, NX // 2 - 2) as i:
                        for u in range(2):
                            t = 2 * i + u
                            join(t + 3, 1 - u)
                            heads(t + 3, 1 - u)
                            attended(t + 2, u)
                            last_root(t)
                    for t in range(NX - 4, nt):
                        if t + 3 < nt:
                            join(t + 3, (t + 3) % 2)
                            heads(t + 3, (t + 3) % 2)
                        if t + 2 < nt:
                            attended(t + 2, t % 2)
                        last_root(t)

                if l == 0:
                    pool.wait_ge(setup_dve, 1)
                norm_tm(l)
                ft(l)
                attention(l)
                mlstm(l)
                output(l)

        def second_block(number, block, sems):
            def sem(name):
                sems.append(nc.alloc_semaphore(name=f"{name}_{number}"))
                return sems[-1]

            const2 = sem("const2")
            FIRST2 = [(norm1_g, "norm1_g"), (lam_in, "lam"), (subln_g, "subln_g")]
            first2, FIRST2_ALL = sem("first2"), 16 * len(FIRST2)
            CONST2 = [(alibi[:, :], "alibi"), (slope, "slope"), (pw_w, "pw_w"), (fnet_w, "fnet_w"), (dft_c, "dft_c"),
                      (sgu_rows, "sgu_rows"), (sgu_w, "sgu_w"), (dw_w, "dw_w"), (dw_b, "dw_b"),
                      (cln_g, "cln_g"), (cln_b, "cln_b"), (pw_b, "pw_b"), (fnet_b, "fnet_b"), (norm2_g, "norm2_g"),
                      (sgu_b, "sgu_b"), (mean64, "mean64")]
            CONST2_ALL = 16 * len(CONST2)
            setup2, lam_sum, lam_e, sub_ready = sem("setup2"), sem("lam_sum"), sem("lam_e"), sem("sub_ready")
            x_ld = [sem(f"x_ld{u}") for u in range(2)]
            norm_sems = {n: {k: sem(f"n{n}_{k}") for k in ("sq", "ms", "rs", "xs", "tr", "ev_act", "ev_dve")} for n in ("1", "2", "f")}
            w2_ld = [sem(f"w2_ld{n}") for n in range(4)]
            cv_mm, cv_sig, cv_z, cv_acc = sem("cv_mm"), sem("cv_sig"), sem("cv_z"), sem("cv_acc")
            cv_tap = sem("cv_tap")
            c_mm, c_ev, v_mm, v_ev, uv_mm, uv_ev = [sem(n) for n in ("c_mm", "c_ev", "v_mm", "v_ev", "uv_mm", "uv_ev")]
            qk_mm, qk_ev = sem("qk_mm"), sem("qk_ev")
            ln_act, ln_rs, ln_v = Chain(sem("ln_act")), sem("ln_rs"), sem("ln_v")
            ln_pool = Chain(sem("ln_pool"))
            ln_var = sem("ln_var")
            d_q, d_s, d_nm, d_e = sem("d_q"), [sem(f"d_s{m}") for m in range(2)], [sem(f"d_nm{m}") for m in range(2)], \
                [sem(f"d_e{m}") for m in range(2)]
            d_w, d_t, d_t_act, d_pv, d_o = [sem(n) for n in ("d_w", "d_t", "d_t_act", "d_pv", "d_o")]
            d_ms, d_rs, d_on, d_att, d_y = [sem(n) for n in ("d_ms", "d_rs", "d_on", "d_att", "d_y")]
            d_chain, d_fin = Chain(sem("d_chain")), Chain(sem("d_fin"))
            rep_ld, rep_round, qk_lo_ev, rep_mm, rep_ev, q_mm = [sem(n) for n in ("rep_ld", "rep_round", "qk_lo_ev", "rep_mm", "rep_ev", "q_mm")]
            tab_ld = [sem(f"tab_ld{n}") for n in range(2)]
            cw_mm, cw_ev, u_mm, u_ev = sem("cw_mm"), sem("cw_ev"), sem("u_mm"), sem("u_ev")
            dft_mm, dft_odd, dft_y = sem("dft_mm"), sem("dft_odd"), sem("dft_y")
            mu_mm, mu_x, mu_sq, var_mm, var_ln, var_rs, cn_z, cn_silu, pw_mm, pw_ev = [sem(n) for n in (
                "mu_mm", "mu_x", "mu_sq", "var_mm", "var_ln", "var_rs", "cn_z", "cn_silu", "pw_mm", "pw_ev")]
            sg_mm, sg_u, sg_tr, sg_ev = [sem(n) for n in ("sg_mm", "sg_u", "sg_tr", "sg_ev")]
            wo_ld, y_rd, wo_mm, x_add = [sem(f"wo_ld{c}") for c in range(2)], sem("y_rd"), sem("wo_mm"), sem("x_add")
            xn_hi, xn_lo = sem("xn_hi"), sem("xn_lo")
            up_ld, dn_ld = [sem(f"up_ld{u}") for u in range(2)], sem("dn_ld")
            up_hi, up_lo, dn_hi, dn_lo = [sem(n) for n in ("up_hi", "up_lo", "dn_hi", "dn_lo")]
            up_mm, up_relu, up_h, dn_mm, dn_add = [sem(n) for n in ("up_mm", "up_relu", "up_h", "dn_mm", "dn_add")]
            h_chain = Chain(sem("h_chain"))
            fg_ld, out_ready, out_st = sem("fg_ld"), sem("out_ready"), [sem(f"out_st{u}") for u in range(2)]
            GROUPS, FT = D_FF // FG, FG // P

            last_ld, up_first = sem("last_ld"), sem("up_first")

            def pairs_with_ends(eng, n, body):
                for t in range(2):
                    body(t, t)
                with eng.Fori(1, n - 1) as i:
                    for u in range(2):
                        body(2 * i + u, u)
                for t in range(2 * n - 2, 2 * n):
                    body(t, t % 2)

            @block.sync
            def _(sp):
                def load_x(t, u):
                    if not isinstance(t, int) or t >= 2:
                        sp.wait_ge(x_ld[u], 8 * (t - u) if not isinstance(t, int) else 16 * (t // 2))
                    sp.dma_start(x_res[:, t, :], x_dram[DEPTH][t]).then_inc(x_ld[u], 16)

                for t in range(2):
                    load_x(t, t)
                for u in range(2):
                    sp.wait_ge(x_ld[u], 16)
                sp.dma_start(w_in2[0], A["w_in2"][0]).then_inc(w2_ld[0], 16)
                with sp.Fori(1, NX // 2) as i:
                    for u in range(2):
                        load_x(2 * i + u, u)
                for view, name in CONST2:
                    sp.dma_start(view, A[name]).then_inc(const2, 16)
                sp.dma_start(w_in2[1], A["w_in2"][1]).then_inc(w2_ld[1], 16)
                sp.wait_ge(cv_mm, 4)
                sp.dma_start(w_in2[0], A["w_in2"][2]).then_inc(w2_ld[2], 16)
                sp.wait_ge(c_mm, 2)
                sp.wait_ge(v_mm, NX)
                sp.dma_start(w_in2[1], A["w_in2"][3]).then_inc(w2_ld[3], 16)
                sp.wait_ge(cv_z, 2)
                sp.dma_start(rep_raw, A["rep"]).then_inc(rep_ld, 16)
                sp.wait_ge(d_pv, 4 * NX)
                sp.dma_start(cos_s, A["cos_s"]).then_inc(tab_ld[0], 16)
                sp.dma_start(sin_s, A["sin_s"]).then_inc(tab_ld[1], 16)
                for c in range(2):
                    sp.dma_start(w_out2[:, c], A["w_out2"][c]).then_inc(wo_ld[c], 16)

                def load_up(g, u):
                    sp.dma_start(w_up[u], A["w_up"][g]).then_inc(up_ld[u], 16)

                def load_down(g):
                    sp.dma_start(w_down, A["w_down"][g]).then_inc(dn_ld, 16)

                def next_loads(g, u):
                    sp.wait_ge(up_mm, FT * g)
                    load_up(g + 1, 1 - u)
                    sp.wait_ge(dn_mm, 16 * g)
                    load_down(g)

                sp.wait_ge(dft_y, 2)
                sp.wait_ge(pw_mm, 4)
                sp.wait_ge(sg_mm, 4)
                load_up(0, 0)
                load_up(1, 1)
                sp.wait_ge(wo_mm, NX)
                load_down(0)
                next_loads(1, 1)
                with sp.Fori(1, GROUPS // 2 - 1) as i:
                    for u in range(2):
                        next_loads(2 * i + u, u)
                next_loads(GROUPS - 2, 0)
                sp.wait_ge(up_mm, FT * (GROUPS - 1))
                sp.dma_start(w_last, A["w_down"][GROUPS - 1]).then_inc(last_ld, 16)
                sp.wait_ge(dn_mm, 16 * (GROUPS - 1))
                sp.dma_start(final_g2, A["final_g2"]).then_inc(fg_ld, 16)

                def store(t, u):
                    sp.wait_ge(out_ready, t + 1)
                    sp.dma_start(out[t], out_s[u]).then_inc(out_st[u], 16)

                pairs(sp, NX // 2, store)
                for u in range(2):
                    sp.wait_ge(out_st[u], 16 * (NX // 2))

            @block.tensor
            def _(pe):
                def turn(n, xs, t, u):
                    s = norm_sems[n]
                    pe.wait_ge(s["xs"], t + 1)
                    if not isinstance(t, int) or t >= 2:
                        pe.wait_ge(s["ev_act"], t - 1)
                        pe.wait_ge(s["ev_dve"], t - 1)
                    for k in range(KT):
                        mm = pe.transpose(ps[:, 2 * u + k // 4, (k % 4) * P:(k % 4 + 1) * P], xs[u][:, k * P:(k + 1) * P], ident[:, :])
                    mm.then_inc(s["tr"], 1)

                def ft_tile(bank, w, done):
                    for c in range(2):
                        for k in range(KT):
                            mm = pe.matmul(ps[:, bank + c, :], w[:, k, :], xn2_t[:, k, 512 * c:512 * (c + 1)],
                                           start=k == 0, stop=k == KT - 1)
                    mm.then_inc(done, 1)

                def tm_tile(bank, t, w, width, done):
                    for k in range(KT):
                        mm = pe.matmul(ps[:, bank, 0:width], xn2_t[:, k, t * P:(t + 1) * P], w[:, k, :], start=k == 0, stop=k == KT - 1)
                    mm.then_inc(done, 1)

                def projections():
                    pe.wait_ge(norm_sems["1"]["ev_act"], NX)
                    pe.wait_ge(norm_sems["1"]["ev_dve"], NX)
                    pe.wait_ge(w2_ld[0], 16)
                    for n in range(4):
                        ft_tile(2 * n, w_in2[0][:, :, n * P:(n + 1) * P], cv_mm)
                    pe.wait_ge(w2_ld[1], 16)
                    for j in range(2):
                        pe.wait_ge(cv_sig, j + 1)
                        ft_tile(4 * j, w_in2[1][:, :, j * P:(j + 1) * P], c_mm)
                    pe.wait_ge(cv_z, 1)
                    for t in range(NX):
                        if t >= 2:
                            pe.wait_ge(v_ev, t - 1)
                        tm_tile(2 + t % 2, t, w_in2[1][:, :, GW:2 * GW], GW, v_mm)
                    pe.wait_ge(cv_z, 2)
                    pe.wait_ge(w2_ld[2], 16)
                    for t in range(NX):
                        if t >= 2:
                            pe.wait_ge(uv_ev, t - 1)
                        tm_tile(6 + t % 2, t, w_in2[0], 512, uv_mm)
                    pe.wait_ge(w2_ld[3], 16)
                    pe.wait_ge(c_ev, 2)
                    pe.wait_ge(v_ev, NX)
                    for n, bank in enumerate((0, 4, 2)):
                        ft_tile(bank, w_in2[1][:, :, n * P:(n + 1) * P], qk_mm)
                    pe.wait_ge(uv_ev, NX)
                    ft_tile(6, w_in2[1][:, :, 3 * P:4 * P], qk_mm)

                def attention():
                    pe.wait_ge(qk_ev, 4)

                    for n in range(8):
                        pe.wait_ge(qk_lo_ev, 3 + n // 4)
                        if n == 0:
                            pe.wait_ge(rep_round, 1)
                        if n >= 2:
                            pe.wait_ge(rep_ev, n - 1)
                        rows = slice(32 * (n % 4), 32 * (n % 4) + 32)
                        for c in range(2):
                            at = ps[:, 2 * (n % 2) + c, :]
                            pe.matmul(at, rep_k[rows, 0, :], qk_hi[1][rows, n // 4, 512 * c:512 * (c + 1)], start=True, stop=False)
                            mm = pe.matmul(at, rep_k[rows, 1, :], qk_lo[1][rows, n // 4, 512 * c:512 * (c + 1)], start=False, stop=True)
                        mm.then_inc(rep_mm, 1)

                    def queries(b, j):
                        for r in range(4):
                            at = ps[:, 7, r * P:(r + 1) * P]
                            pe.matmul(at, rep_q[:, r, 0, :], qk_hi[0][:, j, bass.ts(b, P)], start=True, stop=False)
                            mm = pe.matmul(at, rep_q[:, r, 1, :], qk_lo[0][:, j, bass.ts(b, P)], start=False, stop=True)
                        mm.then_inc(q_mm, 1)

                    def scores(s, b, u, h, m):
                        if h == 0 and m == 0:
                            pe.wait_ge(d_q, 2 * b + 2)
                        if not isinstance(s, int) or s > 0:
                            pe.wait_ge(d_e[m], s)
                        for c in range(2):
                            pe.matmul(ps[:, 2 * m + c, :], q2_st[u][:, 2 * h + m, :], k2_st[:, 2 * h + m, 512 * c:512 * (c + 1)],
                                      start=True, stop=False)
                            mm = pe.matmul(ps[:, 2 * m + c, :], slope[:, h, :],
                                           alibi[:, bass.ds(b * -P + (SEQ - P + 512 * c), 512)], start=False, stop=True)
                        mm.then_inc(d_s[m], 1)

                    def turn_p(s, h):
                        pe.wait_ge(d_w, s + 1)
                        if not isinstance(s, int) or s > 0:
                            pe.wait_ge(d_t_act, s)
                        for n in range(NX):
                            mm = pe.transpose(ps[:, 4 + n // 4, (n % 4) * P:(n % 4 + 1) * P], prob2[h % 2][0][:, n * P:(n + 1) * P], ident[:, :])
                        mm.then_inc(d_t, 1)

                    def values(s, b, h):
                        pe.wait_ge(d_t_act, s + 1)
                        if h == 0 and (not isinstance(b, int) or b > 0):
                            pe.wait_ge(d_o, b)
                        for n in range(NX):
                            mm = pe.matmul(ps[:, 6, DH * h:DH * (h + 1)], w_t[h % 2][:, n, :], v2_tm[:, n, DH * h:DH * (h + 1)],
                                           start=n == 0, stop=n == NX - 1)
                        mm.then_inc(d_pv, 1)

                    def turn_out(b):
                        pe.wait_ge(d_on, b + 1)
                        for j in range(2):
                            mm = pe.transpose(ps[:, 7, j * P:(j + 1) * P], o_tm[:, j * P:(j + 1) * P], ident[:, :])
                        mm.then_inc(d_att, 1)

                    def query_block(b, u):
                        last, first = isinstance(b, int) and b == NX - 1, isinstance(b, int) and b == 0
                        for h in range(4):
                            s = 4 * b + h
                            following = (s + 2, b, u, h + 2) if h < 2 else (s + 2, b + 1, 1 - u, h - 2)
                            more = h < 2 or not last
                            if more:
                                scores(*following, 0)
                            turn_p(s, h)
                            if more:
                                scores(*following, 1)
                            if h > 0:
                                values(s - 1, b, h - 1)
                            elif not first:
                                values(s - 1, b - 1, 3)
                            if h == 0 and not last:
                                pe.wait_ge(d_q, 2 * b + 2)
                                if not isinstance(b, int) or b >= 2:
                                    pe.wait_ge(d_y, b - 1)
                                queries(b + 1, 0)
                            if h == 1 and not last:
                                pe.wait_ge(d_q, 2 * b + 3)
                                queries(b + 1, 1)
                            if h == 3 and not first:
                                if last:
                                    pe.wait_ge(d_y, b - 1)
                                else:
                                    pe.wait_ge(d_q, 2 * b + 4)
                                turn_out(b - 1)

                    queries(0, 0)
                    pe.wait_ge(d_q, 1)
                    queries(0, 1)
                    pe.wait_ge(rep_ev, 8)
                    for h in range(2):
                        for m in range(2):
                            scores(h, 0, 0, h, m)
                    pairs_with_ends(pe, NX // 2, query_block)
                    values(4 * NX - 1, NX - 1, 3)
                    pe.wait_ge(d_y, NX - 1)
                    turn_out(NX - 1)

                def mixers():
                    pe.wait_ge(d_y, NX)
                    pe.wait_ge(d_e[1], 4 * NX)

                    def group_mean(src, n, done):
                        for c in range(2):
                            mm = pe.matmul(ps[:, 2 * n + c, :], mean64, src[:, n, 512 * c:512 * (c + 1)], start=True, stop=True)
                        mm.then_inc(done, 1)

                    pe.wait_ge(cv_acc, 2)
                    for j in range(2):
                        group_mean(dw_acc, j, mu_mm)
                    for j in range(2):
                        for m in range(2):
                            mm = pe.matmul(ps[:, 4 + j, m * P:(m + 1) * P], dft_c[:, m, :], fnet_w[:, j, :], start=True, stop=True)
                    mm.then_inc(cw_mm, 1)
                    pe.wait_ge(cw_ev, 1)
                    for t in range(NX):
                        if t >= 2:
                            pe.wait_ge(u_ev, t - 1)
                        for j in range(2):
                            mm = pe.matmul(ps[:, 6 + t % 2, 2 * P * j:2 * P * (j + 1)], c2_t[:, j, t * P:(t + 1) * P],
                                           chan_w[:, j].rearrange("p m e -> p (m e)"), start=True, stop=True)
                        mm.then_inc(u_mm, 1)
                    for j in range(2):
                        pe.wait_ge(mu_sq, j + 1)
                        group_mean(z_flat, j, var_mm)
                    pe.wait_ge(u_ev, NX)
                    pe.wait_ge(cn_silu, 2)
                    for e in range(2):
                        for c in range(2):
                            for k in range(2):
                                mm = pe.matmul(ps[:, 2 * e + c, :], pw_w[:, k, e * P:(e + 1) * P], z_flat[:, k, 512 * c:512 * (c + 1)],
                                               start=k == 0, stop=k == 1)
                            mm.then_inc(pw_mm, 1)
                    pe.wait_ge(ln_v, 1)
                    for g in range(4):
                        v_g = uv_tm[:, :, GW + DH * g:GW + DH * (g + 1)]
                        pe.matmul(ps[:, 4 + g, :], sgu_w[:, g, :], v_g, start=True, stop=True).then_inc(sg_mm, 1)
                    pe.wait_ge(sg_u, 4)
                    pe.wait_ge(pw_ev, 4)
                    for n in range(4):
                        j, half = n // 2, n % 2
                        for i in range(4):
                            mm = pe.transpose(ps[:, n, i * P:(i + 1) * P], uv_tm[:, 4 * half + i, j * P:(j + 1) * P], ident[:, :])
                        mm.then_inc(sg_tr, 1)
                    for n in range(2):
                        pe.wait_ge(tab_ld[n], 16)
                    for j in range(2):
                        a, b = (4, 5) if j == 0 else (6, 7)
                        for k in range(NX):
                            pe.matmul(ps[:, a, :], u_tm[:, k, j, 0, :], cos_s[:, k, 0:HALF], start=k == 0, stop=k == NX - 1)
                        for k in range(NX):
                            pe.matmul(ps[:, b, 0:1], u_tm[:, k, j, 0, :], cos_s[:, k, HALF:HALF + 1], start=k == 0, stop=k == NX - 1)
                        for k in range(NX):
                            mm = pe.matmul(ps[:, b, 1:HALF], u_tm[:, k, j, 1, :], sin_s[:, k, :], start=k == 0, stop=k == NX - 1)
                        mm.then_inc(dft_mm, 1)

                def output():
                    def product(t, u):
                        pe.wait_ge(y_rd, t + 1)
                        if not isinstance(t, int) or t >= 2:
                            pe.wait_ge(x_add, t - 1)
                        for c in range(2):
                            if isinstance(t, int) and t == 0:
                                pe.wait_ge(wo_ld[c], 16)
                            for k in range(KT):
                                mm = pe.matmul(ps[:, 4 + 2 * u + c, :], y_st[u][:, k, :], w_out2[:, c, k, :], start=k == 0, stop=k == KT - 1)
                        mm.then_inc(wo_mm, 1)

                    pe.wait_ge(sg_ev, 4)
                    for t in range(4):
                        product(t, t % 2)
                        if t >= 2:
                            turn("2", nx_s2, t - 2, t % 2)
                    with pe.Fori(2, NX // 2) as i:
                        for u in range(2):
                            product(2 * i + u, u)
                            turn("2", nx_s2, 2 * i + u - 2, u)
                    for t in range(NX - 2, NX):
                        turn("2", nx_s2, t, t % 2)

                def mlp():
                    pe.wait_ge(xn_lo, NX)
                    pe.wait_ge(x_add, NX)

                    def up(g, u):
                        if isinstance(g, int) and g == 0:
                            pe.wait_ge(up_first, 1)
                        else:
                            pe.wait_ge(up_lo, g)
                        for n in range(FT):
                            i = FT * g + n
                            if not isinstance(i, int) or i >= 2:
                                pe.wait_ge(up_relu, i - 1)
                            for c in range(2):
                                at, cols = ps[:, 2 * (n % 2) + c, :], slice(512 * c, 512 * (c + 1))
                                for k in range(KT):
                                    hi, lo = w_up_hi[u][:, k, n * P:(n + 1) * P], w_up_lo[u][:, k, n * P:(n + 1) * P]
                                    x_hi, x_lo = xn2_hi[k // 4][:, k % 4, cols], xn2_lo[k // 4][:, k % 4, cols]
                                    pe.matmul(at, hi, x_hi, start=k == 0, stop=False)
                                    pe.matmul(at, hi, x_lo, start=False, stop=False)
                                    mm = pe.matmul(at, lo, x_hi, start=False, stop=k == KT - 1)
                            mm.then_inc(up_mm, 1)

                    def down(g, u, hi=w_down_hi, lo=w_down_lo):
                        pe.wait_ge(dn_lo, g + 1)
                        pe.wait_ge(up_h, FT * g + FT)
                        for t in range(NX):
                            for c in range(2):
                                i = 16 * g + 2 * t + c
                                if not isinstance(i, int) or i >= 4:
                                    pe.wait_ge(dn_add, i - 3)
                                at, cols, rows = ps[:, 4 + (2 * t + c) % 4, :], slice(512 * c, 512 * (c + 1)), slice(t * P, (t + 1) * P)
                                for k in range(FT):
                                    pe.matmul(at, h_hi[u][:, k, rows], hi[:, k, cols], start=k == 0, stop=False)
                                    pe.matmul(at, h_hi[u][:, k, rows], lo[:, k, cols], start=False, stop=False)
                                    mm = pe.matmul(at, h_lo[u][:, k, rows], hi[:, k, cols], start=False, stop=k == FT - 1)
                                mm.then_inc(dn_mm, 1)

                    up(0, 0)
                    up(1, 1)
                    down(0, 0)
                    with pe.Fori(1, GROUPS // 2) as i:
                        up(2 * i, 0)
                        down(2 * i - 1, 1)
                        up(2 * i + 1, 1)
                        down(2 * i, 0)
                    down(GROUPS - 1, 1, w_last_hi, w_last_lo)

                pairs(pe, NX // 2, lambda t, u: turn("1", nx_s, t, u))
                pe.wait_ge(const2, CONST2_ALL)
                projections()
                attention()
                mixers()
                output()
                mlp()

            @block.vector
            def _(dve):
                def bcast(col, n):
                    return col.unsqueeze(2).to_broadcast([col.shape[0], col.shape[1], n])

                def mean_square(n, t):
                    s = norm_sems[n]
                    dve.wait_ge(s["sq"], t + 1)
                    dve.tensor_scalar(stat[:, 1, bass.ds(t, 1)], stat[:, 0, bass.ds(t, 1)], 1.0 / D_MODEL, EPS, ALU.mult, ALU.add)\
                        .then_inc(s["ms"], 1)

                def scale_rows(n, xs, t, u):
                    s = norm_sems[n]
                    mean_square(n, t)
                    dve.wait_ge(s["rs"], t + 1)
                    if not isinstance(t, int) or t >= 2:
                        dve.wait_ge(s["tr"], t - 1)
                    dve.tensor_scalar(xs[u], x_res[:, t, :], stat[:, 2, bass.ds(t, 1)], None, ALU.mult).then_inc(s["xs"], 1)

                def gain(n, g, t, u, dst):
                    s = norm_sems[n]
                    dve.wait_ge(s["tr"], t + 1)
                    dve.tensor_tensor(dst[:, 4:8, bass.ts(t, P)], ps[:, 2 * u + 1, :].rearrange("p (k n) -> p k n", k=4),
                                      bcast(g[:, 4:8], P), ALU.mult).then_inc(s["ev_dve"], 1)

                def setup():
                    dve.memset(eps_col[:, :], EPS)
                    dve.memset(z_pad[:, :, 0:DW_K // 2], 0.0)
                    dve.memset(z_pad[:, :, SEQ + DW_K // 2:], 0.0).then_inc(setup2, 1)

                def lambdas():
                    dve.wait_ge(first2, FIRST2_ALL)
                    dve.tensor_scalar(sub_g[:, :], subln_g, 1.0 - LAM_INIT, None, ALU.mult).then_inc(sub_ready, 1)
                    dve.tensor_tensor(lam_p, lam_in[:, 0:4:2], lam_in[:, 1:4:2], ALU.mult).then_inc(setup2, 1)
                    dve.wait_ge(setup2, 2)
                    dve.tensor_reduce(lam_s[:, :], lam_p, AX_X, ALU.add).then_inc(lam_sum, 1)

                def convolution():
                    dve.wait_ge(const2, CONST2_ALL)
                    for j in range(2):
                        dve.wait_ge(cv_mm, 2 * j + 2)
                        dve.wait_ge(cv_sig, j + 1)
                        dve.tensor_tensor(z_pad[:, j, DW_K // 2:DW_K // 2 + SEQ], ps_flat[:, 2048 * j + 1024:2048 * j + 2048], sig[j], ALU.mult)\
                            .then_inc(cv_z, 1)
                    dve.wait_ge(cv_z, 2)
                    for k in range(DW_K):
                        for j in range(2):
                            src, tap = z_pad[:, j, k:k + SEQ], dw_w[:, j, k:k + 1]
                            if k:
                                dve.wait_ge(cv_tap, 2 * k + j - 1)
                                ins = dve.scalar_tensor_tensor(out=dw_acc[:, j], in0=src, scalar=tap, in1=dw_acc[:, j], op0=ALU.mult, op1=ALU.add)
                            else:
                                ins = dve.tensor_scalar(dw_acc[:, j], src, tap, dw_b[:, j:j + 1], ALU.mult, ALU.add)
                            ins.then_inc(cv_acc if k == DW_K - 1 else cv_tap, 1)

                def attention():
                    ch, fin = d_chain, d_fin
                    dve.wait_ge(lam_e, 1)
                    dve.scalar_tensor_tensor(out=neg_lam[:, :], in0=lam_s[:, 1:2], scalar=-LAM_INIT, in1=lam_s[:, 0:1],
                                             op0=ALU.add, op1=ALU.subtract).then_inc(setup2, 1)
                    dve.wait_ge(setup2, 3)

                    def maximum(s, u, h, m):
                        dve.wait_ge(d_s[m], s + 1)
                        dve.tensor_reduce(neg_max[:, u, 2 * h + m:2 * h + m + 1], ps_flat[:, 1024 * m:1024 * (m + 1)], AX_X, ALU.max, negate=True)\
                            .then_inc(d_nm[m], 1)

                    def combine(s, u, h):
                        dve.wait_ge(d_e[1], s + 1)
                        dve.wait_ge(d_e[0], s + 1)
                        ch.start(2 * s)
                        c = recip[:, u, 2 * h + 1:2 * h + 2]
                        ch(dve, dve.reciprocal(c, lsum[:, u, 2 * h + 1:2 * h + 2]))
                        ch(dve, dve.scalar_tensor_tensor(out=row_max[:, u, h:h + 1], in0=lsum[:, u, 2 * h:2 * h + 1], scalar=neg_lam[:, :], in1=c,
                                                         op0=ALU.mult, op1=ALU.mult))
                        p0, p1 = prob2[h % 2]
                        dve.scalar_tensor_tensor(out=p0, in0=p1, scalar=row_max[:, u, h:h + 1], in1=p0, op0=ALU.mult, op1=ALU.add)\
                            .then_inc(d_w, 1)

                    def finish(b, u):
                        fin.start(3 * b)
                        fin(dve, dve.reciprocal(den[:, u, 0, :], lsum[:, u, 0:8:2]))
                        dve.wait_ge(d_pv, 4 * b + 4)
                        if not isinstance(b, int) or b > 0:
                            dve.wait_ge(d_att, b)
                        o = o_tm.rearrange("p (h d) -> p h d", h=4)
                        dve.tensor_tensor(o, ps[:, 6, 0:GW].rearrange("p (h d) -> p h d", h=4), bcast(den[:, u, 0, :], DH), ALU.mult)\
                            .then_inc(d_o, 1)
                        dve.wait_ge(d_o, b + 1)
                        fin(dve, dve.tensor_tensor(o_sq, o_tm, o_tm, ALU.mult))
                        fin(dve, dve.tensor_reduce(den[:, u, 1, :], o_sq.rearrange("p (h d) -> p h d", h=4), AX_X, ALU.add))
                        dve.tensor_scalar(den[:, u, 2, :], den[:, u, 1, :], 1.0 / DH, EPS, ALU.mult, ALU.add).then_inc(d_ms, 1)
                        dve.wait_ge(d_rs, b + 1)
                        dve.tensor_tensor(o, o, bcast(den[:, u, 3, :], DH), ALU.mult).then_inc(d_on, 1)

                    def query_block(b, u):
                        for h in range(4):
                            s = 4 * b + h
                            last = isinstance(b, int) and b == NX - 1
                            combine(s, u, h)
                            if h < 3 or not last:
                                maximum(s + 1, *((u, h + 1) if h < 3 else (1 - u, 0)), 1)
                            if h < 2 or not last:
                                maximum(s + 2, *((u, h + 2) if h < 2 else (1 - u, h - 2)), 0)
                            if h == 1 and (not isinstance(b, int) or b > 0):
                                finish(b - 1, 1 - u)

                    for h, m in ((0, 0), (0, 1), (1, 0)):
                        maximum(h, 0, h, m)
                    pairs_with_ends(dve, NX // 2, query_block)
                    finish(NX - 1, 1)

                def mixers():
                    for j in range(2):
                        dve.wait_ge(mu_mm, j + 1)
                        dve.tensor_tensor(dw_acc[:, j], dw_acc[:, j], ps_flat[:, 1024 * j:1024 * (j + 1)], ALU.subtract).then_inc(mu_x, 1)
                    for j in range(2):
                        dve.wait_ge(var_rs, j + 1)
                        dve.tensor_tensor(dw_acc[:, j], dw_acc[:, j], z_flat[:, j], ALU.mult).then_inc(cn_z, 1)
                    for g in range(4):
                        dve.wait_ge(sg_mm, g + 1)
                        u = uv_tm[:, :, DH * g:DH * (g + 1)]
                        dve.scalar_tensor_tensor(out=u, in0=ps[:, 4 + g, :].rearrange("p (n c) -> p n c", n=NX), scalar=sgu_b[:, g:g + 1], in1=u,
                                                 op0=ALU.add, op1=ALU.mult).then_inc(sg_u, 1)
                    for n in range(4):
                        dve.wait_ge(sg_tr, n + 1)
                        dve.tensor_copy(y_t[:, 6 + n // 2, 512 * (n % 2):512 * (n % 2 + 1)], ps[:, n, :]).then_inc(sg_ev, 1)
                    for j in range(2):
                        dve.wait_ge(dft_mm, j + 1)
                        dve.wait_ge(dft_odd, j + 1)
                        a, y, b = ps[:, (4, 6)[j], :], y_t[:, 4 + j, :], fnet_b[:, j:j + 1]
                        dve.tensor_scalar(y[:, 0:1], a[:, 0:1], b, None, ALU.add)
                        dve.tensor_scalar(y[:, HALF:HALF + 1], odd[j][:, 0:1], b, None, ALU.add)
                        dve.scalar_tensor_tensor(out=y[:, 1:HALF], in0=a[:, 1:HALF], scalar=b, in1=odd[j][:, 1:HALF], op0=ALU.add, op1=ALU.add)
                        dve.scalar_tensor_tensor(out=y[:, :HALF:-1], in0=a[:, 1:HALF], scalar=b, in1=odd[j][:, 1:HALF], op0=ALU.add, op1=ALU.subtract)\
                            .then_inc(dft_y, 1)

                def output():
                    def residual(t, u):
                        dve.wait_ge(wo_mm, t + 1)
                        dve.tensor_tensor(x_res[:, t, :], x_res[:, t, :], ps_flat[:, 2048 + 1024 * u:3072 + 1024 * u], ALU.add).then_inc(x_add, 1)

                    residual(0, 0)
                    residual(1, 1)
                    for t in range(2):
                        scale_rows("2", nx_s2, t, t)
                        residual(t + 2, t)
                    with dve.Fori(0, 2) as i:
                        for u in range(2):
                            gain("2", norm2_g, 2 * i + u, u, xn2_raw)
                            scale_rows("2", nx_s2, 2 * i + u + 2, u)
                            residual(2 * i + u + 4, u)
                    for t in range(4, NX):
                        gain("2", norm2_g, t, t % 2, xn2_raw)
                        if t + 2 < NX:
                            scale_rows("2", nx_s2, t + 2, t % 2)

                def last_scale(t, u):
                    dve.wait_ge(norm_sems["f"]["rs"], t + 1)
                    if t >= 2:
                        dve.wait_ge(out_st[u], 16 * (t // 2))
                    dve.scalar_tensor_tensor(out=out_s[u], in0=x_res[:, t, :], scalar=stat[:, 2, bass.ds(t, 1)], in1=final_g2,
                                             op0=ALU.mult, op1=ALU.mult).then_inc(out_ready, 1)

                def mlp():
                    def hidden(g, u):
                        for n in range(FT):
                            h = h_raw[u][:, n, :]
                            dve.wait_ge(up_relu, FT * g + n + 1)
                            h_chain.start(2 * (FT * g + n))
                            h_chain(dve, dve.tensor_tensor(h, h, h, ALU.mult))
                            h_chain(dve, dve.tensor_copy(h_hi[u][:, n, :], h))
                            dve.tensor_tensor(h_lo[u][:, n, :], h, h_hi[u][:, n, :].bitcast(F32), ALU.subtract).then_inc(up_h, 1)

                    def adds(g, tiles=range(NX)):
                        for t in tiles:
                            for c in range(2):
                                dve.wait_ge(dn_mm, 16 * g + 2 * t + c + 1)
                                x = x_res[:, t, 512 * c:512 * (c + 1)]
                                dve.tensor_tensor(x, x, ps[:, 4 + (2 * t + c) % 4, :], ALU.add).then_inc(dn_add, 1)

                    dve.wait_ge(up_hi, 1)
                    dve.tensor_tensor(w_up_lo[0], w_up[0], w_up_hi[0].bitcast(F32), ALU.subtract).then_inc(up_first, 1)
                    hidden(0, 0)
                    hidden(1, 1)
                    adds(0)
                    with dve.Fori(1, GROUPS // 2) as i:
                        hidden(2 * i, 0)
                        adds(2 * i - 1)
                        hidden(2 * i + 1, 1)
                        adds(2 * i)
                    dve.wait_ge(fg_ld, 16)
                    for t in range(NX + 2):
                        if t < NX:
                            adds(GROUPS - 1, (t,))
                        if 1 <= t <= NX:
                            mean_square("f", t - 1)
                        if t >= 2:
                            last_scale(t - 2, t % 2)

                setup()
                for t in range(2):
                    scale_rows("1", nx_s, t, t)
                lambdas()
                with dve.Fori(0, NX // 2 - 1) as i:
                    for u in range(2):
                        gain("1", norm1_g, 2 * i + u, u, xn2_t)
                        scale_rows("1", nx_s, 2 * i + u + 2, u)
                for t in range(NX - 2, NX):
                    gain("1", norm1_g, t, t % 2, xn2_t)
                convolution()
                attention()
                mixers()
                output()
                mlp()

            @block.scalar
            def _(act):
                def squares(n, xs, t, u):
                    s = norm_sems[n]
                    if n == "1":
                        act.wait_ge(x_ld[u], 8 * (t - u) + 16 if not isinstance(t, int) else 16 * (t // 2) + 16)
                    elif n == "2":
                        act.wait_ge(x_add, t + 1)
                    else:
                        act.wait_ge(dn_add, 16 * (GROUPS - 1) + 2 * t + 2)
                    if not isinstance(t, int) or t >= 2:
                        act.wait_ge(s["tr"] if n != "f" else s["ms"], t - 1)
                    act.activation(xs[u], x_res[:, t, :], ACT.Square, accum_out=stat[:, 0, bass.ds(t, 1)]).then_inc(s["sq"], 1)

                def gain(n, g, t, u):
                    s = norm_sems[n]
                    dst = xn2_t if n == "1" else xn2_raw
                    act.wait_ge(s["tr"], t + 1)
                    for k in range(4):
                        ins = act.activation(dst[:, k, bass.ts(t, P)], ps[:, 2 * u, k * P:(k + 1) * P], ACT.Copy, scale=g[:, k:k + 1])
                    ins.then_inc(s["ev_act"], 1)

                def high(t):
                    s = norm_sems["2"]
                    act.wait_ge(s["ev_act"], t + 1)
                    act.wait_ge(s["ev_dve"], t + 1)
                    for n in range(2):
                        ins = act.activation(xn2_hi[n][:, :, bass.ts(t, P)], xn2_raw[:, 4 * n:4 * n + 4, bass.ts(t, P)], ACT.Copy)
                    ins.then_inc(xn_hi, 1)

                def high_up(g, u):
                    act.wait_ge(up_ld[u], 8 * (g - u) + 16)
                    act.activation(w_up_hi[u], w_up[u], ACT.Copy).then_inc(up_hi, 1)

                def norm(n, xs, g):
                    for t in range(2):
                        squares(n, xs, t, t)
                    if n == "1":
                        act.wait_ge(first2, FIRST2_ALL)
                        act.wait_ge(setup2, 1)
                    with act.Fori(0, NX // 2 - 1) as i:
                        for u in range(2):
                            gain(n, g, 2 * i + u, u)
                            squares(n, xs, 2 * i + u + 2, u)
                            if n == "2":
                                high(2 * i + u)
                    for t in range(NX - 2, NX):
                        if n == "2" and t == NX - 2:
                            high_up(0, 0)
                        gain(n, g, t, t % 2)
                        if n == "2":
                            high(t)

                def projections():
                    act.wait_ge(const2, CONST2_ALL)
                    for j in range(2):
                        act.wait_ge(cv_mm, 2 * j + 1)
                        act.activation(sig[j], ps_flat[:, 2048 * j:2048 * j + 1024], ACT.Sigmoid).then_inc(cv_sig, 1)
                    for j in range(2):
                        act.wait_ge(c_mm, j + 1)
                        act.activation(c2_t[:, j, :], ps_flat[:, 2048 * j:2048 * j + 1024], ACT.Copy).then_inc(c_ev, 1)
                    for t in range(NX):
                        act.wait_ge(v_mm, t + 1)
                        act.activation(v2_tm[:, t, :], ps[:, 2 + t % 2, 0:GW], ACT.Copy).then_inc(v_ev, 1)
                    for t in range(NX):
                        act.wait_ge(uv_mm, t + 1)
                        act.activation(uv_tm[:, t, 0:GW], ps[:, 6 + t % 2, 0:GW], ACT.Copy)
                        act.activation(uv_tm[:, t, GW:], ps[:, 6 + t % 2, GW:], ACT.Copy, accum_out=stat2[:, 0, t:t + 1]).then_inc(uv_ev, 1)
                    ch = ln_act
                    act.wait_ge(uv_ev, NX)
                    ch(act, act.activation(stat2[:, 1, :], stat2[:, 0, :], ACT.Copy, scale=-1.0 / GW))
                    for n, bank in enumerate((0, 4, 2, 6)):
                        act.wait_ge(qk_mm, n + 1)
                        dst = q2_t[:, n, :] if n < 2 else k2_t[:, n - 2, :]
                        scale = 32 ** -0.5 if n < 2 else 1.0
                        act.activation(dst, ps_flat[:, 512 * bank:512 * bank + 1024], ACT.Copy, scale=scale)
                        act.activation(qk_hi[n // 2][:, n % 2, :], ps_flat[:, 512 * bank:512 * bank + 1024], ACT.Copy, scale=scale).then_inc(qk_ev, 1)
                        if n < 2:
                            for t in range(4 * n, 4 * n + 4):
                                v = uv_tm[:, t, GW:]
                                ins = act.activation(v, v, ACT.Identity, bias=stat2[:, 1, t:t + 1])
                            ch(act, ins)
                        else:
                            for t in range(4 * n - 8, 4 * n - 4):
                                ins = act.activation(v_sq[:, t, :], uv_tm[:, t, GW:], ACT.Square, accum_out=stat2[:, 2, t:t + 1])
                            ch(act, ins)
                    act.activation(stat2[:, 3, :], stat2[:, 2, :], ACT.Identity, scale=1.0 / GW, bias=eps_col[:, :]).then_inc(ln_var, 1)

                def attention():
                    act.wait_ge(lam_sum, 1)
                    act.activation(lam_s[:, :], lam_s[:, :], ACT.Exp).then_inc(lam_e, 1)

                    def exp(s, u, h, m):
                        act.wait_ge(d_nm[m], s + 1)
                        if m == 0 and (not isinstance(s, int) or s >= 2):
                            act.wait_ge(d_t, s - 1)
                        act.activation(prob2[h % 2][m], ps_flat[:, 1024 * m:1024 * (m + 1)], ACT.Exp, bias=neg_max[:, u, 2 * h + m:2 * h + m + 1],
                                       accum_out=lsum[:, u, 2 * h + m:2 * h + m + 1]).then_inc(d_e[m], 1)

                    def evacuate(s, h):
                        act.wait_ge(d_t, s + 1)
                        act.activation(w_t[h % 2].rearrange("p n q -> p (n q)"), ps_flat[:, 2048:3072], ACT.Copy).then_inc(d_t_act, 1)

                    def gains(b):
                        act.wait_ge(d_att, b + 1)
                        for j in range(2):
                            ins = act.activation(y_t[:, j, bass.ts(b, P)], ps[:, 7, j * P:(j + 1) * P], ACT.Copy, scale=sub_g[:, :])
                        ins.then_inc(d_y, 1)

                    def query_block(b, u):
                        for h in range(4):
                            s = 4 * b + h
                            last = isinstance(b, int) and b == NX - 1
                            if h < 3 or not last:
                                exp(s + 1, *((u, h + 1) if h < 3 else (1 - u, 0)), 1)
                            if h < 2 or not last:
                                exp(s + 2, *((u, h + 2) if h < 2 else (1 - u, h - 2)), 0)
                            evacuate(s, h)
                            if h < 2 and not last:
                                queries(b + 1, 1 - u, h)
                            if h == 3 and (not isinstance(b, int) or b > 0):
                                gains(b - 1)

                    def queries(b, u, j):
                        act.wait_ge(q_mm, 2 * b + j + 1)
                        act.activation(q2_st[u][:, 4 * j:4 * j + 4, :].rearrange("p r q -> p (r q)"), ps[:, 7, :], ACT.Copy).then_inc(d_q, 1)

                    act.wait_ge(rep_ld, 16)
                    act.activation(rep, rep_raw, ACT.Copy).then_inc(rep_round, 1)
                    for n in range(8):
                        act.wait_ge(rep_mm, n + 1)
                        act.activation(k2_st[:, n, :], ps_flat[:, 1024 * (n % 2):1024 * (n % 2 + 1)], ACT.Copy).then_inc(rep_ev, 1)
                    for j in range(2):
                        queries(0, 0, j)
                    act.wait_ge(sub_ready, 1)
                    for h, m in ((0, 0), (0, 1), (1, 0)):
                        exp(h, 0, h, m)
                    pairs_with_ends(act, NX // 2, query_block)
                    gains(NX - 1)

                def mixers():
                    act.wait_ge(cw_mm, 1)
                    for j in range(2):
                        ins = act.activation(chan_w[:, j], ps[:, 4 + j, 0:2 * P].rearrange("p (m e) -> p m e", m=2), ACT.Copy)
                    ins.then_inc(cw_ev, 1)
                    for j in range(2):
                        act.wait_ge(mu_x, j + 1)
                        act.activation(z_flat[:, j], dw_acc[:, j], ACT.Square).then_inc(mu_sq, 1)
                    for t in range(NX):
                        act.wait_ge(u_mm, t + 1)
                        act.activation(u_tm[:, t].rearrange("p j m e -> p (j m e)"), ps[:, 6 + t % 2, :], ACT.Copy).then_inc(u_ev, 1)
                    for j in range(2):
                        act.wait_ge(var_mm, j + 1)
                        act.activation(z_flat[:, j], ps_flat[:, 1024 * j:1024 * (j + 1)], ACT.Ln, bias=eps_col[:, :]).then_inc(var_ln, 1)
                    for j in range(2):
                        act.wait_ge(var_ln, j + 1)
                        act.activation(z_flat[:, j], z_flat[:, j], ACT.Exp, scale=-0.5).then_inc(var_rs, 1)
                    for j in range(2):
                        act.wait_ge(cn_z, j + 1)
                        act.activation(z_flat[:, j], dw_acc[:, j], ACT.Silu, scale=cln_g[:, j:j + 1], bias=cln_b[:, j:j + 1]).then_inc(cn_silu, 1)
                    for n in range(4):
                        act.wait_ge(pw_mm, n + 1)
                        e, c = n // 2, n % 2
                        act.activation(dw_acc[:, e, 512 * c:512 * (c + 1)], ps[:, n, :], ACT.Identity, bias=pw_b[:, e:e + 1]).then_inc(pw_ev, 1)
                    for j in range(2):
                        act.wait_ge(dft_mm, j + 1)
                        act.activation(odd[j], ps[:, (5, 7)[j], :], ACT.Copy).then_inc(dft_odd, 1)

                def mlp():
                    def high_down(g):
                        act.wait_ge(dn_ld, 16 * g + 16)
                        act.activation(w_down_hi, w_down, ACT.Copy).then_inc(dn_hi, 1)

                    def relu(g, u, n):
                        act.wait_ge(up_mm, FT * g + n + 1)
                        if n == 0 and (not isinstance(g, int) or g >= 2):
                            act.wait_ge(dn_mm, 16 * g - 16)
                        act.activation(h_raw[u][:, n, :], ps_flat[:, 1024 * (n % 2):1024 * (n % 2 + 1)], ACT.Relu).then_inc(up_relu, 1)

                    def group(g, u, more=True):
                        relu(g, u, 0)
                        high_down(g - 1)
                        relu(g, u, 1)
                        if more:
                            high_up(g + 1, 1 - u)

                    high_up(1, 1)
                    for n in range(FT):
                        relu(0, 0, n)
                    group(1, 1)
                    with act.Fori(1, GROUPS // 2 - 1) as i:
                        for u in range(2):
                            group(2 * i + u, u)
                    group(GROUPS - 2, 0)
                    group(GROUPS - 1, 1, False)
                    act.wait_ge(last_ld, 16)
                    act.activation(w_last_hi, w_last, ACT.Copy).then_inc(dn_hi, 1)

                for view, name in FIRST2:
                    act.dma_start(view, A[name]).then_inc(first2, 16)
                norm("1", nx_s, norm1_g)
                projections()
                attention()
                mixers()
                norm("2", nx_s2, norm2_g)
                mlp()
                pairs(act, NX // 2, lambda t, u: squares("f", nx_s2, t, u))

            @block.gpsimd
            def _(pool):
                def root(n, t):
                    s = norm_sems[n]
                    pool.wait_ge(s["ms"], t + 1)
                    pool.tensor_tensor(stat[:, 2, bass.ds(t, 1)], stat[:, 1, bass.ds(t, 1)], minus_half[:, 0:1], ALU.pow).then_inc(s["rs"], 1)

                def spatial_norm():
                    ch = ln_pool
                    v = uv_tm[:, :, GW:]
                    pool.wait_ge(ln_var, 1)
                    for c in range(2):
                        ins = pool.tensor_tensor(stat2[:, 4, 4 * c:4 * c + 4], stat2[:, 3, 4 * c:4 * c + 4], minus_half[:, :], ALU.pow)
                    ch(pool, ins)
                    ch(pool, pool.tensor_tensor(v, v, stat2[:, 4, :].unsqueeze(2).to_broadcast([P, NX, GW]), ALU.mult))
                    ch(pool, pool.tensor_tensor(v, v, sgu_rows[:, 0:1, :].to_broadcast([P, NX, GW]), ALU.mult))
                    pool.tensor_tensor(v, v, sgu_rows[:, 1:2, :].to_broadcast([P, NX, GW]), ALU.add).then_inc(ln_v, 1)

                def attention():
                    def root_heads(b, u):
                        pool.wait_ge(d_ms, b + 1)
                        pool.tensor_tensor(den[:, u, 3, :], den[:, u, 2, :], minus_half[:, :], ALU.pow).then_inc(d_rs, 1)

                    for n in range(4):
                        pool.wait_ge(qk_ev, n + 1)
                        at = (q2_t, k2_t)[n // 2][:, n % 2, :]
                        pool.tensor_tensor(qk_lo[n // 2][:, n % 2, :], at, qk_hi[n // 2][:, n % 2, :].bitcast(F32), ALU.subtract).then_inc(qk_lo_ev, 1)
                    spatial_norm()
                    with pool.Fori(0, NX // 2) as i:
                        for u in range(2):
                            root_heads(2 * i + u, u)

                def output():
                    def stage(t, u):
                        if not isinstance(t, int) or t >= 2:
                            pool.wait_ge(wo_mm, t - 1)
                        pool.tensor_copy(y_st[u], y_t[:, :, bass.ts(t, P)]).then_inc(y_rd, 1)

                    def low(t):
                        pool.wait_ge(xn_hi, t + 1)
                        for n in range(2):
                            cols = bass.ts(t, P)
                            ins = pool.tensor_tensor(xn2_lo[n][:, :, cols], xn2_raw[:, 4 * n:4 * n + 4, cols], xn2_hi[n][:, :, cols].bitcast(F32),
                                                     ALU.subtract)
                        ins.then_inc(xn_lo, 1)

                    pool.wait_ge(sg_ev, 4)
                    pool.wait_ge(pw_ev, 4)
                    pool.wait_ge(dft_y, 2)
                    stage(0, 0)
                    stage(1, 1)
                    for t in range(2, 4):
                        stage(t, t % 2)
                        root("2", t - 2)
                    with pool.Fori(2, NX // 2) as i:
                        for u in range(2):
                            stage(2 * i + u, u)
                            root("2", 2 * i + u - 2)
                            low(2 * i + u - 4)
                    for t in range(NX - 2, NX):
                        root("2", t)
                        low(t - 2)
                    for t in range(NX - 2, NX):
                        low(t)

                def mlp():
                    def low_up(g, u):
                        pool.wait_ge(up_hi, g + 1)
                        pool.tensor_tensor(w_up_lo[u], w_up[u], w_up_hi[u].bitcast(F32), ALU.subtract).then_inc(up_lo, 1)

                    def low_down(g):
                        pool.wait_ge(dn_hi, g + 1)
                        pool.tensor_tensor(w_down_lo, w_down, w_down_hi.bitcast(F32), ALU.subtract).then_inc(dn_lo, 1)

                    low_up(1, 1)
                    with pool.Fori(0, GROUPS // 2 - 1) as i:
                        for u in range(2):
                            low_down(2 * i + u)
                            low_up(2 * i + u + 2, u)
                    low_down(GROUPS - 2)
                    pool.wait_ge(dn_hi, GROUPS)
                    pool.tensor_tensor(w_last_lo, w_last, w_last_hi.bitcast(F32), ALU.subtract).then_inc(dn_lo, 1)

                with pool.Fori(0, NX) as t:
                    root("1", t)
                attention()
                output()
                mlp()
                with pool.Fori(0, NX) as t:
                    root("f", t)

        def run_block(number, program):
            sems = []
            with nc.Block() as block:
                program(number, block, sems)
            nc.clear_and_free_semaphores(sems)
            nc.all_engine_barrier()

        for l in range(DEPTH):
            run_block(l, first_block_layer)
        run_block(DEPTH, second_block)


def kernel(**inputs):
    import concourse.bacc as bacc
    from concourse.bass_utils import run_bass_kernel_spmd

    nc = bacc.Bacc("TRN2", target_bir_lowering=False, num_devices=1)
    arrays = {f"in_{k}": v for k, v in host_layout(inputs).items()}
    access = {k[3:]: nc.dram_tensor(k, v.shape, mybir.dt.from_np(v.dtype), kind="ExternalInput").ap() for k, v in arrays.items()}
    out = nc.dram_tensor("out", (NX, P, D_MODEL), F32, kind="ExternalOutput").ap()
    build(nc, access, out)
    result = run_bass_kernel_spmd(nc, [arrays], core_ids=[0])
    return result.results[0]["out"].reshape(1, SEQ, D_MODEL)
```
